# Optimizing a Trainium2 kernel written in Bass

```python
import math
import jax, jax.numpy as jnp
from jax import lax
import numpy as np
import jax
import jax.numpy as jnp

D_MODEL = 1024
BATCH = 1
SEQ = 512
DEPTH = 2

WIDTH_A = D_MODEL // 2
HEAD_DIM_A = 64
N_HEADS_A = WIDTH_A // HEAD_DIM_A
DILATED_BRANCHES = ((128, 1), (512, 4), (2048, 16))
ROPE_THETA = 10000.0

WIDTH_R = D_MODEL // 4
N_HEADS_R = 4
V_DIM_R = WIDTH_R // N_HEADS_R
QK_DIM_R = V_DIM_R // 2
RET_CHUNK = 128

WIDTH_G = D_MODEL // 4
N_HEADS_G = 4
V_DIM_G = WIDTH_G // N_HEADS_G
QK_DIM_G = V_DIM_G // 2
GLA_LOW_RANK = 16
GLA_TAU = 16.0
GLA_CHUNK = 64

MIX_WIDTH = WIDTH_A + WIDTH_R + WIDTH_G
PROJ_SIZES = (WIDTH_A, WIDTH_A, WIDTH_A,
              N_HEADS_R * QK_DIM_R, N_HEADS_R * QK_DIM_R, WIDTH_R, WIDTH_R,
              N_HEADS_G * QK_DIM_G, N_HEADS_G * QK_DIM_G, WIDTH_G, WIDTH_G, GLA_LOW_RANK)
PROJ_WIDTH = sum(PROJ_SIZES)

D_FF = 128 * ((8 * D_MODEL // 3 + 127) // 128)
CONV_WIDTH = 3

DEEPNORM_ALPHA = (2 * DEPTH) ** 0.25
DEEPNORM_BETA = (8 * DEPTH) ** -0.25
LN_EPS = 1e-5
HEAD_NORM_EPS = 1e-6


def layer_norm(x, g, b):
    xf = x.astype(jnp.float32)
    mu = xf.mean(-1, keepdims=True)
    var = jnp.square(xf - mu).mean(-1, keepdims=True)
    y = (xf - mu) * lax.rsqrt(var + LN_EPS)
    return (y * g.astype(jnp.float32) + b.astype(jnp.float32)).astype(x.dtype)

def head_norm(t):
    t = t.astype(jnp.float32)
    mu = t.mean(-1, keepdims=True)
    var = jnp.square(t - mu).mean(-1, keepdims=True)
    return (t - mu) * lax.rsqrt(var + HEAD_NORM_EPS)

def split_heads(t, n_heads):
    b, s, _ = t.shape
    return t.reshape(b, s, n_heads, -1).transpose(0, 2, 1, 3)

def merge_heads(t):
    b, h, s, d = t.shape
    return t.transpose(0, 2, 1, 3).reshape(b, s, h * d)

def rope_tables(seq, dim):
    inv = 1.0 / (ROPE_THETA ** (jnp.arange(0, dim, 2, dtype=jnp.float32) / dim))
    ang = jnp.arange(seq, dtype=jnp.float32)[:, None] * inv[None, :]
    return jnp.cos(ang), jnp.sin(ang)

def apply_rope(t, cos, sin):
    c = cos.astype(t.dtype)
    s = sin.astype(t.dtype)
    t1, t2 = jnp.split(t, 2, axis=-1)
    return jnp.concatenate([t1 * c - t2 * s, t1 * s + t2 * c], axis=-1)

def dilated_branch(q, k, v, window, dilation):
    b, h, s, d = q.shape
    blk = window // dilation
    unit = blk * dilation
    s_pad = -(-s // unit) * unit
    nb = s_pad // unit

    def to_blocks(t):
        t = jnp.pad(t, ((0, 0), (0, 0), (0, s_pad - s), (0, 0)))
        t = t.reshape(b, h, nb, blk, dilation, d)
        return t.transpose(0, 1, 4, 2, 3, 5)

    def with_prev(t):
        prev = jnp.pad(t, ((0, 0), (0, 0), (0, 0), (1, 0), (0, 0), (0, 0)))[:, :, :, :-1]
        return jnp.concatenate([prev, t], axis=4)

    def from_blocks(t):
        t = jnp.moveaxis(t, 2, 4)
        return t.reshape(b, h, s_pad, *t.shape[5:])[:, :, :s]

    qb = to_blocks(q)
    kk = with_prev(to_blocks(k))
    vv = with_prev(to_blocks(v)).astype(jnp.float32)
    scores = jnp.einsum('bhrnqd,bhrnkd->bhrnqk', qb, kk).astype(jnp.float32) * (d ** -0.5)
    qi = jnp.arange(blk)[:, None]
    kj = jnp.arange(2 * blk)[None, :]
    band = (kj >= qi) & (kj <= qi + blk)
    has_prev = (jnp.arange(nb) > 0)[:, None, None] | (kj >= blk)[None]
    mask = band[None] & has_prev
    scores = jnp.where(mask, scores, -jnp.inf)
    m = scores.max(-1)
    p = jnp.exp(scores - m[..., None])
    l = p.sum(-1)
    o = jnp.einsum('bhrnqk,bhrnkd->bhrnqd', p, vv) / l[..., None]
    return from_blocks(o), from_blocks(m), from_blocks(l)

def dilated_attention(q, k, v):
    outs, maxes, denoms = zip(*[dilated_branch(q, k, v, w, r) for (w, r) in DILATED_BRANCHES])
    m_all = jnp.stack(maxes)
    l_all = jnp.stack(denoms)
    o_all = jnp.stack(outs)
    wts = l_all * jnp.exp(m_all - m_all.max(0))
    wts = wts / wts.sum(0)
    return jnp.einsum('gbhs,gbhsd->bhsd', wts, o_all)

def retention(q, k, v):
    b, h, s, dk = q.shape
    dv = v.shape[-1]
    c = RET_CHUNK
    n = s // c
    lg = jnp.log(1.0 - jnp.power(2.0, -5.0 - jnp.arange(h, dtype=jnp.float32)))
    idx = jnp.arange(c, dtype=jnp.float32)
    dist = idx[:, None] - idx[None, :]
    decay_intra = jnp.where(dist >= 0, jnp.exp(lg[:, None, None] * jnp.maximum(dist, 0.0)), 0.0)
    q_dec = jnp.exp(lg[:, None] * (idx + 1.0))
    k_dec = jnp.exp(lg[:, None] * (c - 1.0 - idx))
    chunk_dec = jnp.exp(lg * c)
    qc = q.reshape(b, h, n, c, dk)
    kc = k.reshape(b, h, n, c, dk)
    vc = v.reshape(b, h, n, c, dv)
    scores = jnp.einsum('bhncd,bhnsd->bhncs', qc, kc) * decay_intra[:, None]
    intra = jnp.einsum('bhncs,bhnse->bhnce', scores, vc)
    kv = jnp.einsum('bhnsd,bhnse->nbhde', kc * k_dec[:, None, :, None], vc)

    def step(state, kv_n):
        return chunk_dec[:, None, None] * state + kv_n, state

    _, prev = lax.scan(step, jnp.zeros((b, h, dk, dv), jnp.float32), kv)
    inter = jnp.einsum('bhncd,nbhde->bhnce', qc * q_dec[:, None, :, None], prev)
    return (intra + inter).reshape(b, h, s, dv)

def gated_linear_attention(q, k, v, log_alpha):
    b, h, s, dk = q.shape
    dv = v.shape[-1]
    c = GLA_CHUNK
    n = s // c
    qc = q.reshape(b, h, n, c, dk)
    kc = k.reshape(b, h, n, c, dk)
    vc = v.reshape(b, h, n, c, dv)
    cum = jnp.cumsum(log_alpha.reshape(b, h, n, c, dk), axis=3)
    q_t = qc * jnp.exp(cum)
    k_t = kc * jnp.exp(-cum)
    causal = jnp.tril(jnp.ones((c, c), dtype=bool))
    att = jnp.where(causal, jnp.einsum('bhncd,bhnsd->bhncs', q_t, k_t), 0.0)
    intra = jnp.einsum('bhncs,bhnse->bhnce', att, vc)
    last = cum[:, :, :, -1:]
    kv = jnp.einsum('bhnsd,bhnse->nbhde', kc * jnp.exp(last - cum), vc)
    chunk_dec = jnp.moveaxis(jnp.exp(last[:, :, :, 0]), 2, 0)

    def step(state, xs):
        dec, kv_n = xs
        return dec[..., None] * state + kv_n, state

    _, prev = lax.scan(step, jnp.zeros((b, h, dk, dv), jnp.float32), (chunk_dec, kv))
    inter = jnp.einsum('bhncd,nbhde->bhnce', q_t, prev)
    return (intra + inter).reshape(b, h, s, dv)

def hybrid_mixer(x, w_in, w_alpha, b_alpha, mix_scale, w_out, cos_a, sin_a, cos_r, sin_r):
    f32 = jnp.float32
    proj = x @ w_in
    split_points = np.cumsum(PROJ_SIZES)[:-1].tolist()
    qa, ka, va, qr, kr, vr, gr, qg, kg, vg, rg, ag = jnp.split(proj, split_points, axis=-1)

    qa = apply_rope(split_heads(qa, N_HEADS_A), cos_a, sin_a)
    ka = apply_rope(split_heads(ka, N_HEADS_A), cos_a, sin_a)
    va = split_heads(va, N_HEADS_A)
    ya = merge_heads(head_norm(dilated_attention(qa, ka, va)))

    qr = apply_rope(split_heads(qr, N_HEADS_R), cos_r, sin_r).astype(f32)
    kr = apply_rope(split_heads(kr, N_HEADS_R), cos_r, sin_r).astype(f32) * (QK_DIM_R ** -0.5)
    vr = split_heads(vr, N_HEADS_R).astype(f32)
    yr = merge_heads(head_norm(retention(qr, kr, vr))) * jax.nn.silu(gr.astype(f32))

    log_alpha = jax.nn.log_sigmoid((ag @ w_alpha + b_alpha).astype(f32)) / GLA_TAU
    qg = split_heads(qg, N_HEADS_G).astype(f32) * (QK_DIM_G ** -0.5)
    kg = split_heads(kg, N_HEADS_G).astype(f32)
    vg = split_heads(vg, N_HEADS_G).astype(f32)
    og = gated_linear_attention(qg, kg, vg, split_heads(log_alpha, N_HEADS_G))
    yg = merge_heads(head_norm(og)) * jax.nn.silu(rg.astype(f32))

    y = jnp.concatenate([ya, yr, yg], axis=-1) * mix_scale.astype(f32)
    return y.astype(x.dtype) @ w_out

def causal_dwconv(u, w, bias):
    ch = u.shape[-1]
    y = lax.conv_general_dilated(u, w[:, None, :].astype(u.dtype), window_strides=(1,),
                                 padding=((CONV_WIDTH - 1, 0),),
                                 dimension_numbers=('NWC', 'WIO', 'NWC'),
                                 feature_group_count=ch)
    return y + bias.astype(u.dtype)

def conv_glu_ffn(x, w_up, conv_w, conv_b, w_down):
    u = causal_dwconv(x @ w_up, conv_w, conv_b)
    gate, val = jnp.split(u, 2, axis=-1)
    return (jax.nn.silu(gate) * val) @ w_down

def first_inputs(seed: int = 0) -> dict:
    key = jax.random.key(seed)
    ks = jax.random.split(key, 15)
    f32 = jnp.float32

    def nrm(k, shape, scale):
        return jax.random.normal(k, shape, f32) * scale

    hg = N_HEADS_G * QK_DIM_G
    return {
        "x": nrm(ks[0], (BATCH, SEQ, D_MODEL), 1.0),
        "w_in": nrm(ks[1], (DEPTH, D_MODEL, PROJ_WIDTH), D_MODEL ** -0.5),
        "w_alpha": nrm(ks[2], (DEPTH, GLA_LOW_RANK, hg), GLA_LOW_RANK ** -0.5),
        "b_alpha": nrm(ks[3], (DEPTH, hg), 0.1),
        "mix_scale": 1.0 + nrm(ks[4], (DEPTH, MIX_WIDTH), 0.02),
        "w_out": nrm(ks[5], (DEPTH, MIX_WIDTH, D_MODEL), MIX_WIDTH ** -0.5 * DEEPNORM_BETA),
        "ln1_g": 1.0 + nrm(ks[6], (DEPTH, D_MODEL), 0.02),
        "ln1_b": nrm(ks[7], (DEPTH, D_MODEL), 0.02),
        "w_up": nrm(ks[8], (DEPTH, D_MODEL, 2 * D_FF), D_MODEL ** -0.5),
        "conv_w": nrm(ks[9], (DEPTH, CONV_WIDTH, 2 * D_FF), CONV_WIDTH ** -0.5),
        "conv_b": nrm(ks[10], (DEPTH, 2 * D_FF), 0.02),
        "w_down": nrm(ks[11], (DEPTH, D_FF, D_MODEL), D_FF ** -0.5 * DEEPNORM_BETA),
        "ln2_g": 1.0 + nrm(ks[12], (DEPTH, D_MODEL), 0.02),
        "ln2_b": nrm(ks[13], (DEPTH, D_MODEL), 0.02),
    }

def first_block(x, w_in, w_alpha, b_alpha, mix_scale, w_out, ln1_g, ln1_b,
              w_up, conv_w, conv_b, w_down, ln2_g, ln2_b):
    seq = x.shape[1]
    cos_a, sin_a = rope_tables(seq, HEAD_DIM_A)
    cos_r, sin_r = rope_tables(seq, QK_DIM_R)
    for l in range(DEPTH):
        mix = hybrid_mixer(x, w_in[l], w_alpha[l], b_alpha[l], mix_scale[l], w_out[l],
                           cos_a, sin_a, cos_r, sin_r)
        x = layer_norm(DEEPNORM_ALPHA * x + mix, ln1_g[l], ln1_b[l])
        ffn = conv_glu_ffn(x, w_up[l], conv_w[l], conv_b[l], w_down[l])
        x = layer_norm(DEEPNORM_ALPHA * x + ffn, ln2_g[l], ln2_b[l])
    return x


A_WIDTH = 512
A_CONV = 3
B_WIDTH = 512
B_CONV = 31
C_HEADS = 8
C_HEAD_DIM = 64
IDX_HEADS = 8
IDX_DIM = 32
TOPK_MAX = 256
DIFF_HEADS = 4
DIFF_HEAD_DIM = 64
NUM_BUCKETS = 32
MAX_DISTANCE = 128
N_ATTN_HEADS = C_HEADS + DIFF_HEADS
N_GROUPS = 4
EXPERTS_PER_GROUP = 8
N_EXPERTS = N_GROUPS * EXPERTS_PER_GROUP
TOP_E = 2
D_EXPERT = 512
Q_BLOCK = 128
MOE_BLOCK = 128
EPS = 1e-6
N_EVEN = (DEPTH + 1) // 2
N_ODD = DEPTH // 2

AB_SIZES = (A_WIDTH, A_WIDTH, A_WIDTH, B_WIDTH, B_WIDTH)
AB_IN = 3 * A_WIDTH + 2 * B_WIDTH
C_WIDTH = C_HEADS * C_HEAD_DIM
DIFF_QK = DIFF_HEADS * 2 * DIFF_HEAD_DIM
DIFF_V = DIFF_HEADS * 2 * DIFF_HEAD_DIM
CD_SIZES = (C_WIDTH, C_WIDTH, C_WIDTH, IDX_HEADS * IDX_DIM, IDX_DIM, IDX_HEADS, DIFF_QK, DIFF_QK, DIFF_V)
CD_IN = 3 * C_WIDTH + IDX_HEADS * IDX_DIM + IDX_DIM + IDX_HEADS + 2 * DIFF_QK + DIFF_V


def rmsnorm(x, g):
    xf = x.astype(jnp.float32)
    y = xf * lax.rsqrt(jnp.mean(xf * xf, axis=-1, keepdims=True) + EPS)
    return (y * g.astype(jnp.float32)).astype(x.dtype)

def layernorm(x, g, b):
    xf = x.astype(jnp.float32)
    mu = jnp.mean(xf, axis=-1, keepdims=True)
    var = jnp.mean(jnp.square(xf - mu), axis=-1, keepdims=True)
    y = (xf - mu) * lax.rsqrt(var + EPS) * g.astype(jnp.float32) + b.astype(jnp.float32)
    return y.astype(x.dtype)

def modulate(h, shift, scale):
    return h * (1 + scale[:, None, :]) + shift[:, None, :]

def split_cols(z, sizes):
    cuts = [int(v) for v in np.cumsum(sizes)[:-1]]
    return jnp.split(z, cuts, axis=-1)

def causal_depthwise_conv(u, w):
    width, ch = w.shape
    return lax.conv_general_dilated(u, w[:, None, :].astype(u.dtype), window_strides=(1,),
                                    padding=[(width - 1, 0)],
                                    dimension_numbers=('NWC', 'WIO', 'NWC'),
                                    feature_group_count=ch)

def rel_bucket(dist):
    max_exact = NUM_BUCKETS // 2
    n = jnp.maximum(dist, 0)
    log_ratio = jnp.log(jnp.maximum(n, 1).astype(jnp.float32) / max_exact) / math.log(MAX_DISTANCE / max_exact)
    large = max_exact + (log_ratio * (NUM_BUCKETS - max_exact)).astype(jnp.int32)
    return jnp.where(n < max_exact, n, jnp.minimum(large, NUM_BUCKETS - 1))

def conv_mixers(h, w_in, conv_a, conv_b, conv_b_bias, ln_g, ln_b, w_out):
    gate_b, gate_c, x_a, val_b, glu_gate = split_cols(h @ w_in, AB_SIZES)
    y_a = gate_b * causal_depthwise_conv(gate_c * x_a, conv_a)
    u = causal_depthwise_conv(val_b * jax.nn.sigmoid(glu_gate), conv_b) + conv_b_bias
    y_b = jax.nn.silu(layernorm(u, ln_g, ln_b))
    return jnp.concatenate([y_a, y_b], axis=-1) @ w_out

def attn_mixers(h, positions, w_in, rel_bias, diff_lam, diff_norm_g, w_out, lambda_init):
    bsz, seq, _ = h.shape
    n_blocks = seq // Q_BLOCK
    topk = min(TOPK_MAX, seq // 4)
    q_c, k_c, v_c, q_idx, k_idx, w_idx, q_d, k_d, v_d = split_cols(h @ w_in, CD_SIZES)
    q_c = q_c.reshape(bsz, seq, C_HEADS, C_HEAD_DIM)
    k_c = k_c.reshape(bsz, seq, C_HEADS, C_HEAD_DIM)
    v_c = v_c.reshape(bsz, seq, C_HEADS, C_HEAD_DIM)
    q_idx = q_idx.reshape(bsz, seq, IDX_HEADS, IDX_DIM)
    q_d = q_d.reshape(bsz, seq, DIFF_HEADS, 2, DIFF_HEAD_DIM)
    k_d = k_d.reshape(bsz, seq, DIFF_HEADS, 2, DIFF_HEAD_DIM)
    q1, q2 = q_d[..., 0, :], q_d[..., 1, :]
    k1, k2 = k_d[..., 0, :], k_d[..., 1, :]
    v_d = v_d.reshape(bsz, seq, DIFF_HEADS, 2 * DIFF_HEAD_DIM)
    lam_f = diff_lam.astype(jnp.float32)
    lam = jnp.exp(jnp.sum(lam_f[0] * lam_f[1])) - jnp.exp(jnp.sum(lam_f[2] * lam_f[3])) + lambda_init
    bias_c = rel_bias[:, :C_HEADS]
    bias_d = rel_bias[:, C_HEADS:]
    scale_c = C_HEAD_DIM ** -0.5
    scale_d = DIFF_HEAD_DIM ** -0.5
    scale_idx = (IDX_DIM * IDX_HEADS) ** -0.5
    gather_rows = jax.vmap(lambda a, i: a[i])

    def block(j):
        s0 = j * Q_BLOCK
        take = lambda a: lax.dynamic_slice_in_dim(a, s0, Q_BLOCK, axis=1)
        pos_q = take(positions)
        causal = positions[:, None, :] <= pos_q[:, :, None]
        rel = jnp.einsum('bqhd,bsd->bqhs', take(q_idx), k_idx)
        score = jnp.einsum('bqhs,bqh->bqs', jax.nn.relu(rel), take(w_idx)).astype(jnp.float32) * scale_idx
        score = jnp.where(causal, score, -jnp.inf)
        _, sel = lax.top_k(score, topk)
        k_sel = gather_rows(k_c, sel)
        v_sel = gather_rows(v_c, sel)
        pos_sel = gather_rows(positions, sel)
        dist_c = pos_q[:, :, None] - pos_sel
        logit_c = (jnp.einsum('bqhd,bqkhd->bhqk', take(q_c), k_sel).astype(jnp.float32) * scale_c
                   + jnp.moveaxis(bias_c[rel_bucket(dist_c)], -1, 1))
        logit_c = jnp.where((dist_c >= 0)[:, None], logit_c, -jnp.inf)
        p_c = jax.nn.softmax(logit_c, axis=-1).astype(v_sel.dtype)
        out_c = jnp.einsum('bhqk,bqkhd->bqhd', p_c, v_sel)
        dist_d = pos_q[:, :, None] - positions[:, None, :]
        b_d = jnp.moveaxis(bias_d[rel_bucket(dist_d)], -1, 1)
        mask_d = causal[:, None]

        def softmax_map(qb, kk):
            lg = jnp.einsum('bqhd,bshd->bhqs', qb, kk).astype(jnp.float32) * scale_d + b_d
            return jax.nn.softmax(jnp.where(mask_d, lg, -jnp.inf), axis=-1)

        attn = softmax_map(take(q1), k1) - lam * softmax_map(take(q2), k2)
        out_d = jnp.einsum('bhqs,bshd->bqhd', attn.astype(v_d.dtype), v_d)
        return out_c, out_d

    out_c, out_d = lax.map(block, jnp.arange(n_blocks))
    out_c = jnp.moveaxis(out_c, 0, 1).reshape(bsz, seq, C_WIDTH)
    out_d = jnp.moveaxis(out_d, 0, 1).reshape(bsz, seq, DIFF_HEADS, 2 * DIFF_HEAD_DIM)
    out_d = (rmsnorm(out_d, diff_norm_g) * (1 - lambda_init)).reshape(bsz, seq, DIFF_V)
    return jnp.concatenate([out_c, out_d], axis=-1) @ w_out

def hier_moe(h, wr_g, br_g, wr_e, br_e, w_gate, w_up, w_down):
    bsz, seq, d = h.shape
    n_tok = bsz * seq
    xf = h.reshape(n_tok, d)
    p_group = jax.nn.softmax((xf @ wr_g + br_g).astype(jnp.float32), axis=-1)
    p_top, g_sel = lax.top_k(p_group, 1)
    fine = (xf @ wr_e + br_e).astype(jnp.float32).reshape(n_tok, N_GROUPS, EXPERTS_PER_GROUP)
    fine = jnp.take_along_axis(fine, g_sel[:, :, None], axis=1)[:, 0]
    e_val, e_sel = lax.top_k(fine, TOP_E)
    gate = (p_top * jax.nn.softmax(e_val, axis=-1)).reshape(-1)
    expert_id = (g_sel * EXPERTS_PER_GROUP + e_sel).reshape(-1)
    token_id = jnp.repeat(jnp.arange(n_tok, dtype=jnp.int32), TOP_E)
    n_assign = n_tok * TOP_E
    order = jnp.argsort(expert_id)
    e_sorted = expert_id[order]
    counts = jnp.bincount(expert_id, length=N_EXPERTS)
    starts = jnp.cumsum(counts) - counts
    padded = (counts + MOE_BLOCK - 1) // MOE_BLOCK * MOE_BLOCK
    pad_end = jnp.cumsum(padded)
    pad_start = pad_end - padded
    dest = pad_start[e_sorted] + jnp.arange(n_assign, dtype=jnp.int32) - starts[e_sorted]
    n_blocks = -(-n_assign // MOE_BLOCK) + N_EXPERTS
    n_rows = n_blocks * MOE_BLOCK
    row_token = jnp.full((n_rows,), n_tok, jnp.int32).at[dest].set(token_id[order])
    row_gate = jnp.zeros((n_rows,), gate.dtype).at[dest].set(gate[order])
    block_expert = jnp.minimum(jnp.searchsorted(pad_end, jnp.arange(n_blocks, dtype=jnp.int32) * MOE_BLOCK, side='right'),
                               N_EXPERTS - 1)
    x_rows = jnp.concatenate([xf, jnp.zeros((1, d), xf.dtype)], axis=0)[row_token].reshape(n_blocks, MOE_BLOCK, d)

    def expert_block(args):
        xb, e = args
        return (jax.nn.silu(xb @ w_gate[e]) * (xb @ w_up[e])) @ w_down[e]

    y_rows = lax.map(expert_block, (x_rows, block_expert)).reshape(n_rows, d)
    y_rows = y_rows * row_gate[:, None].astype(y_rows.dtype)
    out = jnp.zeros((n_tok + 1, d), y_rows.dtype).at[row_token].add(y_rows)[:n_tok]
    return out.reshape(bsz, seq, d)

def second_inputs(seed: int = 0) -> dict:
    key = jax.random.key(seed)
    ks = jax.random.split(key, 32)
    f32 = jnp.float32

    def nrm(k, shape, scale):
        return jax.random.normal(k, shape, f32) * scale

    return {
        'x': nrm(ks[0], (BATCH, SEQ, D_MODEL), 1.0),
        'c': nrm(ks[1], (BATCH, D_MODEL), 1.0),
        'positions': jnp.broadcast_to(jnp.arange(SEQ, dtype=jnp.int32), (BATCH, SEQ)),
        'rel_bias': nrm(ks[2], (NUM_BUCKETS, N_ATTN_HEADS), 0.5),
        'norm_g': 1.0 + nrm(ks[3], (DEPTH, 2, D_MODEL), 0.1),
        'final_norm_g': 1.0 + nrm(ks[4], (D_MODEL,), 0.1),
        'ada_w': nrm(ks[5], (DEPTH, D_MODEL, 6 * D_MODEL), 0.5 * D_MODEL ** -0.5),
        'ada_b': nrm(ks[6], (DEPTH, 6 * D_MODEL), 0.02),
        'ab_w_in': nrm(ks[7], (N_EVEN, D_MODEL, AB_IN), D_MODEL ** -0.5),
        'ab_conv_a': nrm(ks[8], (N_EVEN, A_CONV, A_WIDTH), A_CONV ** -0.5),
        'ab_conv_b': nrm(ks[9], (N_EVEN, B_CONV, B_WIDTH), B_CONV ** -0.5),
        'ab_conv_b_bias': nrm(ks[10], (N_EVEN, B_WIDTH), 0.02),
        'ab_ln_g': 1.0 + nrm(ks[11], (N_EVEN, B_WIDTH), 0.1),
        'ab_ln_b': nrm(ks[12], (N_EVEN, B_WIDTH), 0.02),
        'ab_w_out': nrm(ks[13], (N_EVEN, A_WIDTH + B_WIDTH, D_MODEL), (A_WIDTH + B_WIDTH) ** -0.5),
        'cd_w_in': nrm(ks[14], (N_ODD, D_MODEL, CD_IN), D_MODEL ** -0.5),
        'diff_lam': nrm(ks[15], (N_ODD, 4, DIFF_HEAD_DIM), 0.1),
        'diff_norm_g': 1.0 + nrm(ks[16], (N_ODD, 2 * DIFF_HEAD_DIM), 0.1),
        'cd_w_out': nrm(ks[17], (N_ODD, C_WIDTH + DIFF_V, D_MODEL), (C_WIDTH + DIFF_V) ** -0.5),
        'moe_wr_g': nrm(ks[18], (DEPTH, D_MODEL, N_GROUPS), D_MODEL ** -0.5),
        'moe_br_g': nrm(ks[19], (DEPTH, N_GROUPS), 0.01),
        'moe_wr_e': nrm(ks[20], (DEPTH, D_MODEL, N_EXPERTS), D_MODEL ** -0.5),
        'moe_br_e': nrm(ks[21], (DEPTH, N_EXPERTS), 0.01),
        'moe_w_gate': nrm(ks[22], (DEPTH, N_EXPERTS, D_MODEL, D_EXPERT), D_MODEL ** -0.5),
        'moe_w_up': nrm(ks[23], (DEPTH, N_EXPERTS, D_MODEL, D_EXPERT), D_MODEL ** -0.5),
        'moe_w_down': nrm(ks[24], (DEPTH, N_EXPERTS, D_EXPERT, D_MODEL), D_EXPERT ** -0.5),
    }

def second_block(x, c, positions, rel_bias, norm_g, final_norm_g, ada_w, ada_b,
              ab_w_in, ab_conv_a, ab_conv_b, ab_conv_b_bias, ab_ln_g, ab_ln_b, ab_w_out,
              cd_w_in, diff_lam, diff_norm_g, cd_w_out,
              moe_wr_g, moe_br_g, moe_wr_e, moe_br_e, moe_w_gate, moe_w_up, moe_w_down):
    cond = jax.nn.silu(c)
    for i in range(DEPTH):
        mod = cond @ ada_w[i] + ada_b[i]
        sh1, sc1, g1, sh2, sc2, g2 = jnp.split(mod, 6, axis=-1)
        h = modulate(rmsnorm(x, norm_g[i, 0]), sh1, sc1)
        j = i // 2
        if i % 2 == 0:
            y = conv_mixers(h, ab_w_in[j], ab_conv_a[j], ab_conv_b[j], ab_conv_b_bias[j],
                            ab_ln_g[j], ab_ln_b[j], ab_w_out[j])
        else:
            lambda_init = 0.8 - 0.6 * math.exp(-0.3 * i)
            y = attn_mixers(h, positions, cd_w_in[j], rel_bias, diff_lam[j], diff_norm_g[j],
                            cd_w_out[j], lambda_init)
        x = x + g1[:, None, :] * y
        h = modulate(rmsnorm(x, norm_g[i, 1]), sh2, sc2)
        x = x + g2[:, None, :] * hier_moe(h, moe_wr_g[i], moe_br_g[i], moe_wr_e[i], moe_br_e[i],
                                          moe_w_gate[i], moe_w_up[i], moe_w_down[i])
    return rmsnorm(x, final_norm_g)


def setup_inputs(seed=0):
    out = dict(first_inputs(seed))
    for name, value in second_inputs(seed + 1).items():
        if name != "x":
            out[name + "_2"] = value
    return out


def reference(
    x, w_in, w_alpha, b_alpha, mix_scale, w_out, ln1_g, ln1_b, w_up, conv_w, conv_b, w_down,
    ln2_g, ln2_b, c_2, positions_2, rel_bias_2, norm_g_2, final_norm_g_2, ada_w_2, ada_b_2,
    ab_w_in_2, ab_conv_a_2, ab_conv_b_2, ab_conv_b_bias_2, ab_ln_g_2, ab_ln_b_2, ab_w_out_2,
    cd_w_in_2, diff_lam_2, diff_norm_g_2, cd_w_out_2, moe_wr_g_2, moe_br_g_2, moe_wr_e_2,
    moe_br_e_2, moe_w_gate_2, moe_w_up_2, moe_w_down_2,
):
    x = first_block(
        x, w_in, w_alpha, b_alpha, mix_scale, w_out, ln1_g, ln1_b, w_up, conv_w, conv_b, w_down,
        ln2_g, ln2_b,
    )
    return second_block(
        x, c_2, positions_2, rel_bias_2, norm_g_2, final_norm_g_2, ada_w_2, ada_b_2, ab_w_in_2,
        ab_conv_a_2, ab_conv_b_2, ab_conv_b_bias_2, ab_ln_g_2, ab_ln_b_2, ab_w_out_2, cd_w_in_2,
        diff_lam_2, diff_norm_g_2, cd_w_out_2, moe_wr_g_2, moe_br_g_2, moe_wr_e_2, moe_br_e_2,
        moe_w_gate_2, moe_w_up_2, moe_w_down_2,
    )


_drawn_inputs = setup_inputs


def setup_inputs(seed=0):
    import zlib

    import numpy as np

    out = dict(_drawn_inputs(seed))
    spreads = {}
    factors = {'b_alpha': 5.006,
     'mix_scale': 3.635,
     'conv_b': 4.278,
     'ab_conv_b_bias_2': 5.798,
     'ab_ln_g_2': 2.968,
     'ab_ln_b_2': 7.905,
     'diff_lam_2': 2.88,
     'diff_norm_g_2': 3.28,
     'moe_br_g_2': 37.185,
     'moe_br_e_2': 21.751}
    for name, (base, spread) in spreads.items():
        noise = np.random.default_rng([zlib.crc32(name.encode()), seed]).standard_normal(out[name].shape)
        drawn = base * np.exp(spread * noise) if base else spread * noise
        out[name] = jnp.asarray(drawn.astype(out[name].dtype))
    for name, factor in factors.items():
        out[name] = (out[name] * factor).astype(out[name].dtype)
    return out
```

```python
from contextlib import ExitStack

import numpy as np
import concourse.bass as bass
from concourse import mybir

F32 = mybir.dt.float32
I32 = mybir.dt.int32
U32 = mybir.dt.uint32
ALU = mybir.AluOpType
ACT = mybir.ActivationFunctionType
AX_X = mybir.AxisListType.X

P = 128
SEQ = 512
D = 1024
DEPTH = 2
TT = SEQ // P
KD = D // P
BANK = 512

HEADS_A, HD_A = 8, 64
HEADS_R, QK_R = 4, 32
HEADS_G, QK_G = 4, 32
GLA_CHUNK = 64
N_CHUNKS = SEQ // GLA_CHUNK
LOW_RANK = 16
COL_QA, COL_KA, COL_VA = 0, 512, 1024
COL_QR, COL_VR, COL_QG, COL_VG, COL_AG = 1536, 1792, 2304, 2560, 3072
PROJ = COL_AG + LOW_RANK
D_FF = P * ((8 * D // 3 + P - 1) // P)
FT = D_FF // P
ALPHA = (2 * DEPTH) ** 0.25
LN_EPS = 1e-5
NORM_EPS = 1e-6
NEG = -1.0e30


def rope_pair(dim, rows):
    inv = np.float32(1.0) / (np.float32(10000.0) ** (np.arange(0, dim, 2, dtype=np.float32) / np.float32(dim)))
    ang = np.arange(SEQ, dtype=np.float32)[:, None] * inv[None, :]
    half = dim // 2
    r = np.arange(rows) % dim
    cos = np.cos(ang).T[r % half]
    sin = np.sin(ang).T[r % half] * np.where(r < half, -1.0, 1.0)[:, None]
    other = np.where(r < half, np.arange(rows) + half, np.arange(rows) - half)
    perm = np.zeros((rows, rows), np.float32)
    perm[other, np.arange(rows)] = 1.0
    return cos.astype(np.float32), sin.astype(np.float32), perm


def constant_parts():
    parts = {}
    parts["ident"] = np.eye(P, dtype=np.float32)
    parts["cos_a"], parts["sin_a"], parts["perm_a"] = rope_pair(HD_A, P)
    parts["cos_r"], parts["sin_r"], parts["perm_r"] = rope_pair(QK_R, P)
    q = np.arange(SEQ)[:, None]
    k = np.arange(SEQ)[None, :]
    d = q - k
    count = ((d >= 0) & (d <= 128)).astype(np.float64) + ((d >= 0) & (d % 4 == 0)) + ((d >= 0) & (d % 16 == 0))
    logc = np.where(count > 0, np.log(np.maximum(count, 1)), NEG).astype(np.float32)
    parts["log_count"] = logc.reshape(TT, P, SEQ).transpose(1, 0, 2).reshape(P, TT * SEQ)
    lg = np.log(np.float32(1.0) - np.float32(2.0) ** (np.float32(-5.0) - np.arange(HEADS_R, dtype=np.float32)))
    dist = np.arange(SEQ)[None, :] - np.arange(P)[:, None]
    dec = np.where(dist[:, None, :] >= 0, np.exp(lg.astype(np.float64)[None, :, None] * np.maximum(dist, 0)[:, None, :]), 0.0)
    parts["decay"] = (dec * QK_R ** -0.5).astype(np.float32).reshape(P, HEADS_R * SEQ)
    kk = np.arange(P)[:, None]
    qq = np.arange(P)[None, :]
    same = kk // GLA_CHUNK == qq // GLA_CHUNK
    parts["gla_causal"] = ((kk <= qq) & same).astype(np.float32)
    t = np.arange(SEQ)
    parts["chunk_keep"] = np.broadcast_to((t % GLA_CHUNK != 0).astype(np.float32), (P, SEQ))
    parts["even_chunk"] = np.broadcast_to((t // GLA_CHUNK % 2 == 0).astype(np.float32), (P, SEQ))
    parts["odd_chunk"] = np.broadcast_to((t // GLA_CHUNK % 2 == 1).astype(np.float32), (P, SEQ))
    parts["head_block"] = (np.arange(P)[:, None] // QK_G == np.arange(256)[None, :] // 64).astype(np.float32)
    return parts


class Phase:

    def __init__(self, nc, name):
        self.nc, self.name = nc, name
        self.stack = ExitStack()
        self.sems = []

    def sem(self, name):
        s = self.nc.alloc_semaphore(f"{self.name}_{name}")
        self.sems.append(s)
        return s

    def sb(self, name, shape, dt=F32):
        return self.stack.enter_context(self.nc.sbuf_tensor(f"{self.name}_{name}", shape, dt))

    def block(self):
        return self.stack.enter_context(self.nc.Block(no_gpsimd_drain=True))

    def __enter__(self):
        return self

    def __exit__(self, *failed):
        if failed[0] is None:
            self.stack.close()
            self.nc.clear_and_free_semaphores(self.sems)
            self.nc.all_engine_barrier(sem_only=True)


class Chain:

    def __init__(self, eng, sem):
        self.eng, self.sem, self.n = eng, sem, 0

    def link(self, ins):
        self.n += 1
        ins.then_inc(self.sem, 1)
        self.eng.wait_ge(self.sem, self.n)


def load_phase(nc, G):
    with Phase(nc, "load") as ph:
        consts_loaded = ph.sem("consts_loaded")
        x_loaded = ph.sem("x_loaded")
        transposed = ph.sem("transposed")
        xt_written = ph.sem("xt_written")
        ones_set = ph.sem("ones_set")
        X, XT, ps, ident = G["X"], G["XT"], G["ps"], G["c"]["ident"]
        block = ph.block()

        @block.sync
        def _(sp):
            sp.dma_start(G["consts"][:, :], G["d"]["consts"][:, :]).then_inc(consts_loaded, 16)
            sp.dma_start(X[:, :, :], G["d"]["x"][0].rearrange("(t p) n -> p t n", p=P)).then_inc(x_loaded, 16)
            sp.wait_ge(consts_loaded, 16)
            sp.wait_ge(x_loaded, 16)

        @block.vector
        def _(dve):
            nc.vector.memset(G["ones_col"][:, :], 1.0).then_inc(ones_set, 1)
            nc.vector.memset(G["eps_ln"][:, :], LN_EPS).then_inc(ones_set, 1)
            nc.vector.memset(G["eps_norm"][:, :], NORM_EPS).then_inc(ones_set, 1)

        @block.tensor
        def _(pe):
            pe.wait_ge(consts_loaded, 16)
            pe.wait_ge(x_loaded, 16)
            for t in range(TT):
                for j in range(2):
                    for i in range(4):
                        k = 4 * j + i
                        last = nc.tensor.transpose(ps[2 * t + j][:, i * P:(i + 1) * P], X[:, t, k * P:(k + 1) * P], ident)
                    last.then_inc(transposed, 1)

        @block.scalar
        def _(act):
            for t in range(TT):
                for j in range(2):
                    act.wait_ge(transposed, 2 * t + j + 1)
                    nc.scalar.copy(XT[:, 4 * j:4 * j + 4, t * P:(t + 1) * P],
                                   ps[2 * t + j][:, :].rearrange("p (k n) -> p k n", k=4)).then_inc(xt_written, 1)


FM, TM, ROPE = "feature-major", "token-major", "feature-major, rotated"
PROJ_CHUNKS = [(COL_QA, 512, ROPE), (COL_KA, 512, ROPE), (COL_VA, 512, TM), (COL_QR, 256, ROPE),
               (COL_VR, 512, TM), (COL_QG, 256, FM), (COL_VG, 512, TM), (COL_AG, LOW_RANK, FM)]


def project_phase(nc, l, G, S):
    RING = 3
    jobs = []
    for c, (col, width, kind) in enumerate(PROJ_CHUNKS):
        for m in range(TT if kind == TM else -(-width // P)):
            jobs.append((c, m, kind, col))
    ropes = [i for i, j in enumerate(jobs) if j[2] == ROPE]
    BANKS = 4

    def rope_dest(i):
        c, m, _, col = jobs[i]
        if col == COL_QR:
            return (S["QR"] if m == 0 else S["KR"])[:, :]
        return (S["QA"] if col == COL_QA else S["KA"])[:, m, :]

    def plain_dest(i):
        c, m, kind, col = jobs[i]
        if kind == TM:
            return {COL_VA: S["VA"], COL_VR: S["VR"], COL_VG: S["VG"]}[col][:, m, :]
        if col == COL_QG:
            return (S["QG"] if m == 0 else S["KG"])[:, :]
        return S["AG"][:, :]

    with Phase(nc, "project") as ph:
        W = ph.sb("w_ring", [P, RING, KD, 512])
        raw = ph.sb("rope_raw", [P, 4, SEQ])
        cosp = ph.sb("rope_cos_part", [P, 2, SEQ])
        sinp = ph.sb("rope_sin_part", [P, 2, SEQ])
        w_loaded = [ph.sem(f"w_loaded{i}") for i in range(RING)]
        product_done = ph.sem("product_done")
        evacuated = ph.sem("evacuated")
        rotated = ph.sem("rotated")
        cos_done = ph.sem("cos_done")
        sin_done = ph.sem("sin_done")
        rope_done = ph.sem("rope_done")
        ps, XT = G["ps"], G["XT"]
        first_job = [next(i for i, j in enumerate(jobs) if j[0] == c) for c in range(len(PROJ_CHUNKS))] + [len(jobs)]
        block = ph.block()

        @block.sync
        def _(sp):
            for c, (col, width, _) in enumerate(PROJ_CHUNKS):
                if c >= RING:
                    sp.wait_ge(product_done, first_job[c - RING + 1])
                sp.dma_start(W[:, c % RING, :, 0:width],
                             G["d"]["w_in"][bass.ds(l, 1), :, col:col + width].rearrange("o (k p) n -> p (o k) n", p=P)
                             ).then_inc(w_loaded[c % RING], 16)

        @block.tensor
        def _(pe):
            def turn(r):
                i = ropes[r]
                pe.wait_ge(evacuated, i + 1)
                if r >= 2:
                    pe.wait_ge(sin_done, r - 1)
                perm = G["c"]["perm_r" if jobs[i][3] == COL_QR else "perm_a"]
                nc.tensor.matmul(ps[4 + r % 2][:, :], perm, raw[:, r % 4, :], start=True, stop=True).then_inc(rotated, 1)

            r = 0
            for i, (c, m, kind, col) in enumerate(jobs):
                width = min(PROJ_CHUNKS[c][1], 512)
                pe.wait_ge(w_loaded[c % RING], 16 * (c // RING + 1))
                if i >= BANKS:
                    pe.wait_ge(evacuated, i - BANKS + 1)
                for k in range(KD):
                    if kind == TM:
                        last = nc.tensor.matmul(ps[i % BANKS][:, 0:width], XT[:, k, m * P:(m + 1) * P],
                                                W[:, c % RING, k, 0:width], start=(k == 0), stop=(k == KD - 1))
                    else:
                        rows = min(P, width - m * P)
                        last = nc.tensor.matmul(ps[i % BANKS][0:rows, :], W[:, c % RING, k, m * P:m * P + rows],
                                                XT[:, k, :], start=(k == 0), stop=(k == KD - 1))
                last.then_inc(product_done, 1)
                if r < len(ropes) and ropes[r] < i:
                    turn(r)
                    r += 1

        @block.scalar
        def _(act):
            r = 0
            for i, (c, m, kind, col) in enumerate(jobs):
                act.wait_ge(product_done, i + 1)
                if kind == ROPE:
                    if r >= 4:
                        act.wait_ge(rotated, r - 3)
                        act.wait_ge(cos_done, r - 3)
                    nc.scalar.copy(raw[:, r % 4, :], ps[i % BANKS][:, :]).then_inc(evacuated, 1)
                    r += 1
                elif col == COL_QG and m == 0:
                    nc.scalar.mul(plain_dest(i), ps[i % BANKS][:, :], QK_G ** -0.5).then_inc(evacuated, 1)
                elif col == COL_AG:
                    nc.scalar.copy(plain_dest(i), ps[i % BANKS][0:LOW_RANK, :]).then_inc(evacuated, 1)
                else:
                    nc.scalar.copy(plain_dest(i), ps[i % BANKS][:, :]).then_inc(evacuated, 1)

        @block.gpsimd
        def _(pool):
            for r, i in enumerate(ropes):
                cos = G["c"]["cos_r" if jobs[i][3] == COL_QR else "cos_a"]
                pool.wait_ge(evacuated, i + 1)
                if r >= 2:
                    pool.wait_ge(rope_done, r - 1)
                nc.gpsimd.tensor_tensor(cosp[:, r % 2, :], raw[:, r % 4, :], cos, ALU.mult).then_inc(cos_done, 1)

        @block.vector
        def _(dve):
            for r, i in enumerate(ropes):
                sin = G["c"]["sin_r" if jobs[i][3] == COL_QR else "sin_a"]
                dve.wait_ge(rotated, r + 1)
                if r >= 2:
                    dve.wait_ge(rope_done, r - 1)
                nc.vector.tensor_tensor(sinp[:, r % 2, :], ps[4 + r % 2][:, :], sin, ALU.mult).then_inc(sin_done, 1)
                dve.wait_ge(sin_done, r + 1)
                dve.wait_ge(cos_done, r + 1)
                nc.vector.tensor_tensor(rope_dest(i), sinp[:, r % 2, :], cosp[:, r % 2, :], ALU.add).then_inc(rope_done, 1)


def dilated_phase(nc, G, S):
    units = [(h, t) for h in range(HEADS_A) for t in range(TT)]
    with Phase(nc, "dilated") as ph:
        SL = ph.sb("scores", [P, 2, SEQ])
        PR = ph.sb("probs", [P, 2, SEQ])
        PT = ph.sb("probs_t", [P, 2, TT, P])
        neg_max = ph.sb("neg_max", [P, len(units)])
        row_sum = ph.sb("row_sum", [P, len(units)])
        inv_sum = ph.sb("inv_sum", [P, len(units)])
        scores_done = ph.sem("scores_done")
        biased = ph.sem("biased")
        max_done = ph.sem("max_done")
        exp_done = ph.sem("exp_done")
        turned = ph.sem("turned")
        turned_copied = ph.sem("turned_copied")
        mixed = ph.sem("mixed")
        inv_done = ph.sem("inv_done")
        out_done = ph.sem("out_done")
        ps, ident = G["ps"], G["c"]["ident"]
        logc = G["c"]["log_count"].rearrange("p (t n) -> p t n", t=TT)
        block = ph.block()

        @block.tensor
        def _(pe):
            def scores(u):
                h, t = units[u]
                r = HD_A * (h % 2)
                if u >= 2:
                    pe.wait_ge(biased, u - 1)
                nc.tensor.matmul(ps[u % 2][:, 0:(t + 1) * P], S["QA"][r:r + HD_A, h // 2, t * P:(t + 1) * P],
                                 S["KA"][r:r + HD_A, h // 2, 0:(t + 1) * P], start=True, stop=True).then_inc(scores_done, 1)

            def turn(u):
                h, t = units[u]
                pe.wait_ge(exp_done, u + 1)
                if u >= 2:
                    pe.wait_ge(turned_copied, u - 1)
                for k in range(t + 1):
                    last = nc.tensor.transpose(ps[2 + u % 2][:, k * P:(k + 1) * P], PR[:, u % 2, k * P:(k + 1) * P], ident)
                last.then_inc(turned, 1)

            def mix(u):
                h, t = units[u]
                pe.wait_ge(turned_copied, u + 1)
                if u >= 2:
                    pe.wait_ge(out_done, u - 1)
                for k in range(t + 1):
                    last = nc.tensor.matmul(ps[4 + u % 2][:, 0:HD_A], PT[:, u % 2, k, :],
                                            S["VA"][:, k, h * HD_A:(h + 1) * HD_A], start=(k == 0), stop=(k == t))
                last.then_inc(mixed, 1)

            for i in range(len(units) + 2):
                if i < len(units):
                    scores(i)
                if 1 <= i <= len(units):
                    turn(i - 1)
                if i >= 2:
                    mix(i - 2)

        @block.vector
        def _(dve):
            def finish(u):
                h, t = units[u]
                dve.wait_ge(exp_done, u + 1)
                nc.vector.reciprocal(inv_sum[:, u:u + 1], row_sum[:, u:u + 1]).then_inc(inv_done, 1)
                dve.wait_ge(inv_done, u + 1)
                dve.wait_ge(mixed, u + 1)
                nc.vector.tensor_scalar(S["Y"][:, t, h * HD_A:(h + 1) * HD_A], ps[4 + u % 2][:, 0:HD_A],
                                        inv_sum[:, u:u + 1], None, ALU.mult).then_inc(out_done, 1)

            for u, (h, t) in enumerate(units):
                n = (t + 1) * P
                dve.wait_ge(scores_done, u + 1)
                if u >= 2:
                    dve.wait_ge(exp_done, u - 1)
                nc.vector.scalar_tensor_tensor(SL[:, u % 2, 0:n], ps[u % 2][:, 0:n], HD_A ** -0.5, logc[:, t, 0:n],
                                               ALU.mult, ALU.add).then_inc(biased, 1)
                dve.wait_ge(biased, u + 1)
                nc.vector.tensor_reduce(neg_max[:, u:u + 1], SL[:, u % 2, 0:n], AX_X, ALU.max, negate=True
                                        ).then_inc(max_done, 1)
                if u >= 2:
                    finish(u - 2)
            finish(len(units) - 2)
            finish(len(units) - 1)

        @block.scalar
        def _(act):
            def copy(u):
                n = units[u][1] + 1
                act.wait_ge(turned, u + 1)
                if u >= 2:
                    act.wait_ge(mixed, u - 1)
                nc.scalar.copy(PT[:, u % 2, 0:n, :], ps[2 + u % 2][:, 0:n * P].rearrange("p (k n) -> p k n", n=P)
                               ).then_inc(turned_copied, 1)

            for u, (h, t) in enumerate(units):
                n = (t + 1) * P
                act.wait_ge(max_done, u + 1)
                if u >= 2:
                    act.wait_ge(turned, u - 1)
                nc.scalar.activation(PR[:, u % 2, 0:n], SL[:, u % 2, 0:n], ACT.Exp, bias=neg_max[:, u:u + 1],
                                     accum_out=row_sum[:, u:u + 1]).then_inc(exp_done, 1)
                if u >= 1:
                    copy(u - 1)
            copy(len(units) - 1)


def retention_phase(nc, G, S):
    units = [(k, h) for k in range(TT) for h in range(HEADS_R)]
    with Phase(nc, "retention") as ph:
        SD = ph.sb("decayed", [P, TT, HEADS_R, SEQ])
        scores_done = ph.sem("scores_done")
        decayed = ph.sem("decayed_done")
        mixed = ph.sem("mixed")
        copied = ph.sem("copied")
        ps = G["ps"]
        decay = G["c"]["decay"].rearrange("p (h n) -> p h n", h=HEADS_R)
        block = ph.block()

        @block.tensor
        def _(pe):
            for u, (k, h) in enumerate(units):
                r = QK_R * h
                if u >= 4:
                    pe.wait_ge(decayed, u - 3)
                nc.tensor.matmul(ps[u % 4][:, 0:SEQ - k * P], S["KR"][r:r + QK_R, k * P:(k + 1) * P],
                                 S["QR"][r:r + QK_R, k * P:SEQ], start=True, stop=True, tile_position=(r, 0)
                                 ).then_inc(scores_done, 1)
            pe.wait_ge(decayed, len(units))
            for t in range(TT):
                for h in range(HEADS_R):
                    for k in range(t + 1):
                        last = nc.tensor.matmul(ps[4 + t][:, h * 64:(h + 1) * 64], SD[:, k, h, (t - k) * P:(t - k + 1) * P],
                                                S["VR"][:, k, h * 64:(h + 1) * 64], start=(k == 0), stop=(k == t))
                last.then_inc(mixed, 1)

        @block.vector
        def _(dve):
            for u, (k, h) in enumerate(units):
                n = SEQ - k * P
                dve.wait_ge(scores_done, u + 1)
                nc.vector.tensor_tensor(SD[:, k, h, 0:n], ps[u % 4][:, 0:n], decay[:, h, 0:n], ALU.mult).then_inc(decayed, 1)

        @block.scalar
        def _(act):
            for t in range(TT):
                act.wait_ge(mixed, t + 1)
                nc.scalar.copy(S["Y"][:, t, 512:768], ps[4 + t][:, 0:256]).then_inc(copied, 1)


def gla_phase(nc, l, G, S):
    with Phase(nc, "gla") as ph:
        wal = ph.sb("w_alpha", [LOW_RANK, P])
        bal = ph.sb("b_alpha", [P, 1])
        z = ph.sb("z", [P, SEQ])
        za = ph.sb("z_abs", [P, SEQ])
        ze = ph.sb("z_exp", [P, SEQ])
        zl = ph.sb("z_ln", [P, SEQ])
        zm = ph.sb("z_min", [P, SEQ])
        la = ph.sb("log_alpha", [P, SEQ])
        cum = ph.sb("cum", [P, SEQ])
        rest = ph.sb("rest", [P, SEQ])
        grow = ph.sb("exp_cum", [P, SEQ])
        shrink = ph.sb("exp_minus_cum", [P, SEQ])
        rest_exp = ph.sb("exp_rest", [P, SEQ])
        qt = ph.sb("q_t", [P, SEQ])
        qe = ph.sb("q_even", [P, SEQ])
        qo = ph.sb("q_odd", [P, SEQ])
        kt = ph.sb("k_t", [P, SEQ])
        kd = ph.sb("k_rest", [P, SEQ])
        kdt = ph.sb("k_rest_t", [P, TT, P])
        kv = ph.sb("kv", [P, N_CHUNKS, 256])
        state = ph.sb("state", [P, N_CHUNKS, 256])
        att = ph.sb("att", [P, HEADS_G, TT, P])
        loaded = ph.sem("loaded")
        z_done = ph.sem("z_done")
        act_step = ph.sem("act_step")
        ln_done = ph.sem("ln_done")
        dve_step = ph.sem("dve_step")
        cum_done = ph.sem("cum_done")
        rest_done = ph.sem("rest_done")
        grow_done = ph.sem("grow_done")
        shrink_done = ph.sem("shrink_done")
        rest_exp_done = ph.sem("rest_exp_done")
        keys_done = ph.sem("keys_done")
        queries_done = ph.sem("queries_done")
        k_rest_done = ph.sem("k_rest_done")
        k_rest_turned = ph.sem("k_rest_turned")
        k_rest_copied = ph.sem("k_rest_copied")
        kv_done = ph.sem("kv_done")
        state_done = ph.sem("state_done")
        att_done = ph.sem("att_done")
        masked = ph.sem("masked")
        mixed = ph.sem("mixed")
        copied = ph.sem("copied")
        split_done = ph.sem("split_done")
        ps, c = G["ps"], G["c"]
        kv_bank = lambda n: ps[(5, 7, 5, 7, 6, 4, 6, 4)[n]][:, 256 * (n // 2 % 2):256 * (n // 2 % 2) + 256]
        by_chunk = lambda a: a[:, :].rearrange("p (n s) -> p n s", s=GLA_CHUNK)
        block = ph.block()

        @block.sync
        def _(sp):
            sp.dma_start(wal[:, :], G["d"]["w_alpha"][bass.ds(l, 1), :, :].rearrange("o r n -> (o r) n")).then_inc(loaded, 16)
            sp.dma_start(bal[:, :], G["d"]["b_alpha"][bass.ds(l, 1), :].rearrange("o p -> p o")).then_inc(loaded, 16)

        @block.tensor
        def _(pe):
            pe.wait_ge(loaded, 32)
            nc.tensor.matmul(ps[0][:, :], wal[:, :], S["AG"][:, :], start=True, stop=True).then_inc(z_done, 1)
            pe.wait_ge(queries_done, 1)
            pe.wait_ge(keys_done, 1)
            for h in range(HEADS_G):
                r = QK_G * h
                for t in range(TT):
                    last = nc.tensor.matmul(ps[h][:, t * P:(t + 1) * P], kt[r:r + QK_G, t * P:(t + 1) * P],
                                            qt[r:r + QK_G, t * P:(t + 1) * P], start=True, stop=True, tile_position=(r, 0))
                last.then_inc(att_done, 1)
            pe.wait_ge(k_rest_done, 1)
            for t in range(TT):
                last = nc.tensor.transpose(ps[4][:, t * P:(t + 1) * P], kd[:, t * P:(t + 1) * P], c["ident"])
            last.then_inc(k_rest_turned, 1)
            pe.wait_ge(k_rest_copied, 1)
            for n in range(N_CHUNKS):
                r = GLA_CHUNK * (n % 2)
                nc.tensor.matmul(kv_bank(n), kdt[r:r + GLA_CHUNK, n // 2, :],
                                 S["VG"][r:r + GLA_CHUNK, n // 2, 0:256], start=True, stop=True).then_inc(kv_done, 1)
            pe.wait_ge(masked, HEADS_G)
            pe.wait_ge(split_done, 2)
            for t in range(TT):
                pe.wait_ge(state_done, 2 * t + 2)
                o = ps[t % 2]
                if t >= 2:
                    pe.wait_ge(copied, t - 1)
                nc.tensor.matmul(o[:, 0:256], qe[:, t * P:(t + 1) * P], state[:, 2 * t, :], start=True, stop=False,
                                 skip_group_check=True)
                nc.tensor.matmul(o[:, 0:256], qo[:, t * P:(t + 1) * P], state[:, 2 * t + 1, :], start=False, stop=False,
                                 skip_group_check=True)
                for h in range(HEADS_G):
                    last = nc.tensor.matmul(o[:, h * 64:(h + 1) * 64], att[:, h, t, :], S["VG"][:, t, h * 64:(h + 1) * 64],
                                            start=False, stop=True, skip_group_check=True)
                last.then_inc(mixed, 1)

        @block.scalar
        def _(act):
            chain = Chain(act, act_step)
            act.wait_ge(loaded, 32)
            act.wait_ge(z_done, 1)
            chain.link(nc.scalar.activation(z[:, :], ps[0][:, :], ACT.Identity, bias=bal[:, :]))
            chain.link(nc.scalar.activation(za[:, :], z[:, :], ACT.Abs))
            chain.link(nc.scalar.activation(ze[:, :], za[:, :], ACT.Exp, scale=-1.0))
            nc.scalar.activation(zl[:, :], ze[:, :], ACT.Ln, bias=G["ones_col"][:, :]).then_inc(ln_done, 1)
            act.wait_ge(cum_done, 1)
            nc.scalar.activation(grow[:, :], cum[:, :], ACT.Exp).then_inc(grow_done, 1)
            nc.scalar.activation(shrink[:, :], cum[:, :], ACT.Exp, scale=-1.0).then_inc(shrink_done, 1)
            act.wait_ge(rest_done, 1)
            nc.scalar.activation(rest_exp[:, :], rest[:, :], ACT.Exp).then_inc(rest_exp_done, 1)
            act.wait_ge(k_rest_turned, 1)
            nc.scalar.copy(kdt[:, :, :], ps[4][:, :].rearrange("p (t n) -> p t n", t=TT)).then_inc(k_rest_copied, 1)
            for t in range(TT):
                act.wait_ge(mixed, t + 1)
                nc.scalar.copy(S["Y"][:, t, 768:1024], ps[t % 2][:, 0:256]).then_inc(copied, 1)

        @block.vector
        def _(dve):
            chain = Chain(dve, dve_step)
            dve.wait_ge(act_step, 1)
            chain.link(nc.vector.tensor_scalar(zm[:, :], z[:, :], 0.0, 1.0 / 16.0, ALU.min, ALU.mult))
            dve.wait_ge(ln_done, 1)
            chain.link(nc.vector.scalar_tensor_tensor(la[:, :], zl[:, :], -1.0 / 16.0, zm[:, :], ALU.mult, ALU.add))
            nc.vector.tensor_tensor_scan(cum[:, :], c["chunk_keep"], la[:, :], 0.0, ALU.mult, ALU.add).then_inc(cum_done, 1)
            dve.wait_ge(cum_done, 1)
            last = by_chunk(cum)[:, :, GLA_CHUNK - 1:GLA_CHUNK].to_broadcast([P, N_CHUNKS, GLA_CHUNK])
            nc.vector.tensor_tensor(by_chunk(rest), last, by_chunk(cum), ALU.subtract).then_inc(rest_done, 1)
            dve.wait_ge(grow_done, 1)
            nc.vector.tensor_tensor(qt[:, :], S["QG"][:, :], grow[:, :], ALU.mult).then_inc(queries_done, 1)
            dve.wait_ge(shrink_done, 1)
            nc.vector.tensor_tensor(kt[:, :], S["KG"][:, :], shrink[:, :], ALU.mult).then_inc(keys_done, 1)
            dve.wait_ge(rest_exp_done, 1)
            nc.vector.tensor_tensor(kd[:, :], S["KG"][:, :], rest_exp[:, :], ALU.mult).then_inc(k_rest_done, 1)
            mask = c["gla_causal"].rearrange("p (o n) -> p o n", o=1).to_broadcast([P, TT, P])
            for h in range(HEADS_G):
                dve.wait_ge(att_done, h + 1)
                nc.vector.tensor_tensor(att[:, h, :, :], ps[h][:, :].rearrange("p (t n) -> p t n", t=TT), mask, ALU.mult
                                        ).then_inc(masked, 1)
            nc.vector.memset(state[:, 0, :], 0.0).then_inc(state_done, 1)
            for n in range(N_CHUNKS - 1):
                dve.wait_ge(kv_done, 4 * (n // 4) + 4)
                chain.link(nc.vector.tensor_tensor(kv[:, n, :], kv_bank(n), c["head_block"], ALU.mult))
                dve.wait_ge(state_done, n + 1)
                e = n * GLA_CHUNK + GLA_CHUNK - 1
                nc.vector.scalar_tensor_tensor(state[:, n + 1, :], state[:, n, :], grow[:, e:e + 1], kv[:, n, :],
                                               ALU.mult, ALU.add).then_inc(state_done, 1)

        @block.gpsimd
        def _(pool):
            pool.wait_ge(queries_done, 1)
            nc.gpsimd.tensor_tensor(qe[:, :], qt[:, :], c["even_chunk"], ALU.mult).then_inc(split_done, 1)
            nc.gpsimd.tensor_tensor(qo[:, :], qt[:, :], c["odd_chunk"], ALU.mult).then_inc(split_done, 1)


def head_norm_phase(nc, l, G, S):
    HN = 16
    with Phase(nc, "head_norm") as ph:
        sums = ph.sb("sums", [P, TT, HN])
        mean = ph.sb("mean", [P, TT, HN])
        cen = ph.sb("centred", [P, TT, D])
        sq = ph.sb("squares", [P, 2, D])
        sqs = ph.sb("square_sums", [P, TT, HN])
        std = ph.sb("std", [P, TT, HN])
        rstd = ph.sb("rstd", [P, TT, HN])
        gates = ph.sb("gates", [P, TT, 512])
        nrm = ph.sb("normed", [P, TT, D])
        scale_rows = ph.sb("scale_rows", [KD, P])
        scale = ph.sb("scale", [P, KD])
        loaded = ph.sem("loaded")
        dve_step = ph.sem("dve_step")
        centred = ph.sem("centred_done")
        squared = ph.sem("squared")
        squares_summed = ph.sem("squares_summed")
        std_done = ph.sem("std_done")
        gate_done = ph.sem("gate_done")
        normed = ph.sem("normed_done")
        gated = ph.sem("gated")
        scale_turned = ph.sem("scale_turned")
        scale_done = ph.sem("scale_done")
        turned = ph.sem("turned")
        copied = ph.sem("copied")
        ps, ident = G["ps"], G["c"]["ident"]
        heads = lambda a: a.rearrange("p (h e) -> p h e", h=HN)
        spread = lambda a: a.rearrange("p (h o) -> p h o", o=1).to_broadcast([P, HN, 64])
        block = ph.block()

        @block.sync
        def _(sp):
            sp.dma_start(scale_rows[:, :], G["d"]["mix_scale"][bass.ds(l, 1), :].rearrange("o (k p) -> (o k) p", p=P)
                         ).then_inc(loaded, 16)

        @block.vector
        def _(dve):
            chain = Chain(dve, dve_step)
            for t in range(TT):
                y = heads(S["Y"][:, t, :])
                chain.link(nc.vector.tensor_reduce(sums[:, t, :], y, AX_X, ALU.add))
                chain.link(nc.vector.tensor_scalar(mean[:, t, :], sums[:, t, :], 1.0 / 64, None, ALU.mult))
                nc.vector.tensor_tensor(heads(cen[:, t, :]), y, spread(mean[:, t, :]), ALU.subtract).then_inc(centred, 1)
            for t in range(TT):
                dve.wait_ge(squared, t + 1)
                nc.vector.tensor_reduce(sqs[:, t, :], heads(sq[:, t % 2, :]), AX_X, ALU.add).then_inc(squares_summed, 1)
            for t in range(TT):
                dve.wait_ge(std_done, 1)
                chain.link(nc.vector.reciprocal(rstd[:, t, :], std[:, t, :]))
                nc.vector.tensor_tensor(heads(nrm[:, t, :]), heads(cen[:, t, :]), spread(rstd[:, t, :]), ALU.mult
                                        ).then_inc(normed, 1)

        @block.scalar
        def _(act):
            for t in range(TT):
                act.wait_ge(centred, t + 1)
                if t >= 2:
                    act.wait_ge(squares_summed, t - 1)
                nc.scalar.activation(sq[:, t % 2, :], cen[:, t, :], ACT.Square).then_inc(squared, 1)
            for t in range(TT):
                nc.scalar.activation(gates[:, t, 0:256], S["VR"][:, t, 256:512], ACT.Silu).then_inc(gate_done, 1)
                nc.scalar.activation(gates[:, t, 256:512], S["VG"][:, t, 256:512], ACT.Silu).then_inc(gate_done, 1)
            act.wait_ge(squares_summed, TT)
            nc.scalar.activation(std[:, :, :], sqs[:, :, :], ACT.Sqrt, scale=1.0 / 64, bias=G["eps_norm"][:, :]
                                 ).then_inc(std_done, 1)
            act.wait_ge(scale_turned, 1)
            nc.scalar.copy(scale[:, :], ps[7][:, 0:KD]).then_inc(scale_done, 1)
            act.wait_ge(scale_done, 1)
            for t in range(TT):
                for k in range(KD):
                    act.wait_ge(turned, 2 * t + k // 4 + 1)
                    nc.scalar.activation(S["YT"][:, k, t * P:(t + 1) * P],
                                         ps[2 * (t % 2) + k // 4][:, (k % 4) * P:(k % 4 + 1) * P], ACT.Copy,
                                         scale=scale[:, k:k + 1]).then_inc(copied, 1)

        @block.gpsimd
        def _(pool):
            pool.wait_ge(gate_done, 2 * TT)
            for t in range(TT):
                pool.wait_ge(normed, t + 1)
                nc.gpsimd.tensor_tensor(nrm[:, t, 512:1024], nrm[:, t, 512:1024], gates[:, t, :], ALU.mult).then_inc(gated, 1)

        @block.tensor
        def _(pe):
            pe.wait_ge(loaded, 16)
            nc.tensor.transpose(ps[7][:, 0:KD], scale_rows[:, :], ident[0:KD, 0:KD]).then_inc(scale_turned, 1)
            for t in range(TT):
                pe.wait_ge(normed, t + 1)
                pe.wait_ge(gated, t + 1)
                if t >= 2:
                    pe.wait_ge(copied, KD * (t - 1))
                for j in range(2):
                    for i in range(4):
                        k = 4 * j + i
                        last = nc.tensor.transpose(ps[2 * (t % 2) + j][:, i * P:(i + 1) * P], nrm[:, t, k * P:(k + 1) * P], ident)
                    last.then_inc(turned, 1)


def output_norm_phase(nc, name, l, G, act_t, KT, w_dram, g_dram, b_dram):
    KS = 4
    RING = 3
    slots = [(s, min(KS, KT - s)) for s in range(0, KT, KS)]
    with Phase(nc, name) as ph:
        W = ph.sb("w_ring", [P, RING, KS, D])
        g_row = ph.sb("g_row", [P, D])
        b_row = ph.sb("b_row", [P, D])
        R = ph.sb("residual", [P, TT, D])
        stats = ph.sb("stats", [P, TT, 2, 6])
        mv = ph.sb("mean_var", [P, TT, 2])
        std = ph.sb("std", [P, TT])
        rstd = ph.sb("rstd", [P, TT])
        w_loaded = [ph.sem(f"w_loaded{i}") for i in range(RING)]
        rows_loaded = ph.sem("rows_loaded")
        slot_used = ph.sem("slot_used")
        product_done = ph.sem("product_done")
        summed = ph.sem("summed")
        dve_step = ph.sem("dve_step")
        var_done = ph.sem("var_done")
        std_done = ph.sem("std_done")
        normed = ph.sem("normed")
        scaled = ph.sem("scaled")
        shifted = ph.sem("shifted")
        turned = ph.sem("turned")
        copied = ph.sem("copied")
        ps, X, XT, ident = G["ps"], G["X"], G["XT"], G["c"]["ident"]
        block = ph.block()

        @block.sync
        def _(sp):
            for i, (k0, n) in enumerate(slots):
                if i >= RING:
                    sp.wait_ge(slot_used, i - RING + 1)
                sp.dma_start(W[:, i % RING, 0:n, :],
                             w_dram[bass.ds(l, 1), k0 * P:(k0 + n) * P, :].rearrange("o (k p) n -> p (o k) n", p=P)
                             ).then_inc(w_loaded[i % RING], 16)
                if i == 1:
                    sp.dma_start(g_row[:, :], g_dram[bass.ds(l, 1), :].to_broadcast([P, D])).then_inc(rows_loaded, 16)
                    sp.dma_start(b_row[:, :], b_dram[bass.ds(l, 1), :].to_broadcast([P, D])).then_inc(rows_loaded, 16)

        @block.tensor
        def _(pe):
            for i, (k0, n) in enumerate(slots):
                pe.wait_ge(w_loaded[i % RING], 16 * (i // RING + 1))
                for t in range(TT):
                    for c in range(2):
                        for k in range(n):
                            last = nc.tensor.matmul(ps[2 * t + c][:, :], act_t[:, k0 + k, t * P:(t + 1) * P],
                                                    W[:, i % RING, k, c * BANK:(c + 1) * BANK],
                                                    start=(k0 + k == 0), stop=(k0 + k == KT - 1))
                        if k0 + n == KT:
                            last.then_inc(product_done, 1)
                if k0 + n < KT:
                    last.then_inc(slot_used, 1)
            for t in range(TT):
                pe.wait_ge(shifted, t + 1)
                for j in range(2):
                    for i in range(4):
                        k = 4 * j + i
                        last = nc.tensor.transpose(ps[2 * t + j][:, i * P:(i + 1) * P], X[:, t, k * P:(k + 1) * P], ident)
                    last.then_inc(turned, 1)

        @block.vector
        def _(dve):
            chain = Chain(dve, dve_step)

            def stats_of(t):
                for c in range(2):
                    dve.wait_ge(product_done, 2 * t + c + 1)
                    half = R[:, t, c * BANK:(c + 1) * BANK]
                    nc.vector.scalar_tensor_tensor(half, X[:, t, c * BANK:(c + 1) * BANK], ALPHA, ps[2 * t + c][:, :],
                                                   ALU.mult, ALU.add).then_inc(summed, 1)
                    dve.wait_ge(summed, 2 * t + c + 1)
                    chain.link(nc.vector.bn_stats(stats[:, t, c, :], half))
                nc.vector.bn_aggr(mv[:, t, :], stats[:, t, :, :]).then_inc(var_done, 1)

            def norm(t):
                dve.wait_ge(std_done, t + 1)
                chain.link(nc.vector.reciprocal(rstd[:, t:t + 1], std[:, t:t + 1]))
                nc.vector.tensor_scalar(R[:, t, :], R[:, t, :], mv[:, t, 0:1], rstd[:, t:t + 1], ALU.subtract, ALU.mult
                                        ).then_inc(normed, 1)
                dve.wait_ge(normed, t + 1)
                dve.wait_ge(rows_loaded, 32)
                nc.vector.tensor_tensor(R[:, t, :], R[:, t, :], g_row[:, :], ALU.mult).then_inc(scaled, 1)

            for t in range(TT):
                stats_of(t)
                if t >= 1:
                    norm(t - 1)
            norm(TT - 1)

        @block.scalar
        def _(act):
            for t in range(TT):
                act.wait_ge(var_done, t + 1)
                nc.scalar.activation(std[:, t:t + 1], mv[:, t, 1:2], ACT.Sqrt, bias=G["eps_ln"][:, :]).then_inc(std_done, 1)
            for t in range(TT):
                for j in range(2):
                    act.wait_ge(turned, 2 * t + j + 1)
                    nc.scalar.copy(XT[:, 4 * j:4 * j + 4, t * P:(t + 1) * P],
                                   ps[2 * t + j][:, :].rearrange("p (k n) -> p k n", k=4)).then_inc(copied, 1)

        @block.gpsimd
        def _(pool):
            pool.wait_ge(rows_loaded, 32)
            for t in range(TT):
                pool.wait_ge(scaled, t + 1)
                nc.gpsimd.tensor_tensor(X[:, t, :], R[:, t, :], b_row[:, :], ALU.add).then_inc(shifted, 1)


def ffn_up_phase(nc, l, G, H):
    RING = 3
    PER = 2
    SLOTS = FT // PER
    jobs = [(j, v) for j in range(FT) for v in range(2)]
    BANKS = 6
    with Phase(nc, "ffn_up") as ph:
        W = ph.sb("w_ring", [P, RING, KD, 2, PER * P])
        taps_rows = ph.sb("taps_rows", [2 * FT, 4, P])
        taps = ph.sb("taps", [P, 4, 2 * FT])
        conv = ph.sb("conv", [P, 6, SEQ])
        gate = ph.sb("gate", [P, 2, SEQ])
        w_loaded = [ph.sem(f"w_loaded{i}") for i in range(RING)]
        taps_loaded = ph.sem("taps_loaded")
        taps_turned = ph.sem("taps_turned")
        taps_copied = ph.sem("taps_copied")
        product_done = ph.sem("product_done")
        last_tap = ph.sem("last_tap")
        dve_tap = ph.sem("dve_tap")
        conv_done = ph.sem("conv_done")
        silu_done = ph.sem("silu_done")
        glu_done = ph.sem("glu_done")
        ps, XT, ident = G["ps"], G["XT"], G["c"]["ident"]
        block = ph.block()

        @block.sync
        def _(sp):
            sp.dma_start(taps_rows[:, 0:3, :], G["d"]["conv_w"][bass.ds(l, 1), :, :].rearrange("o w (j p) -> j (o w) p", p=P)
                         ).then_inc(taps_loaded, 16)
            sp.dma_start(taps_rows[:, 3:4, :], G["d"]["conv_b"][bass.ds(l, 1), :].rearrange("o (j p) -> j o p", p=P)
                         ).then_inc(taps_loaded, 16)
            for s in range(SLOTS):
                if s >= RING:
                    sp.wait_ge(product_done, 2 * PER * (s - RING + 1))
                for v in range(2):
                    col = v * D_FF + s * PER * P
                    sp.dma_start(W[:, s % RING, :, v, :],
                                 G["d"]["w_up"][bass.ds(l, 1), :, col:col + PER * P].rearrange("o (k p) n -> p (o k) n", p=P)
                                 ).then_inc(w_loaded[s % RING], 16)

        @block.tensor
        def _(pe):
            pe.wait_ge(taps_loaded, 32)
            for w in range(4):
                last = nc.tensor.transpose(ps[7][:, w * P:w * P + 2 * FT], taps_rows[:, w, :], ident[0:2 * FT, 0:2 * FT])
            last.then_inc(taps_turned, 1)
            for i, (j, v) in enumerate(jobs):
                s, o = j // PER, j % PER
                pe.wait_ge(w_loaded[s % RING], 32 * (s // RING + 1))
                if i >= BANKS:
                    pe.wait_ge(conv_done, i - BANKS + 1)
                for k in range(KD):
                    last = nc.tensor.matmul(ps[i % BANKS][:, :], W[:, s % RING, k, v, o * P:(o + 1) * P], XT[:, k, :],
                                            start=(k == 0), stop=(k == KD - 1))
                last.then_inc(product_done, 1)

        @block.scalar
        def _(act):
            act.wait_ge(taps_turned, 1)
            nc.scalar.copy(taps[:, :, :], ps[7][:, :].rearrange("p (w j) -> p w j", w=4)[:, :, 0:2 * FT]).then_inc(taps_copied, 1)
            act.wait_ge(taps_copied, 1)

            def silu(j):
                act.wait_ge(conv_done, 2 * j + 1)
                if j >= 2:
                    act.wait_ge(glu_done, j - 1)
                nc.scalar.activation(gate[:, j % 2, :], conv[:, (2 * j) % 6, :], ACT.Silu).then_inc(silu_done, 1)

            for i, (j, v) in enumerate(jobs):
                ch = v * FT + j
                act.wait_ge(product_done, i + 1)
                if i >= 6:
                    act.wait_ge(glu_done, (i - 6) // 2 + 1)
                nc.scalar.activation(conv[:, i % 6, :], ps[i % BANKS][:, :], ACT.Identity, bias=taps[:, 3, ch:ch + 1],
                                     scale=taps[:, 2, ch:ch + 1]).then_inc(last_tap, 1)
                if v == 1:
                    silu(j)

        @block.vector
        def _(dve):
            dve.wait_ge(taps_copied, 1)
            for i, (j, v) in enumerate(jobs):
                ch = v * FT + j
                u = ps[i % BANKS]
                dve.wait_ge(last_tap, i + 1)
                nc.vector.scalar_tensor_tensor(conv[:, i % 6, 1:SEQ], u[:, 0:SEQ - 1], taps[:, 1, ch:ch + 1],
                                               conv[:, i % 6, 1:SEQ], ALU.mult, ALU.add).then_inc(dve_tap, 1)
                dve.wait_ge(dve_tap, i + 1)
                nc.vector.scalar_tensor_tensor(conv[:, i % 6, 2:SEQ], u[:, 0:SEQ - 2], taps[:, 0, ch:ch + 1],
                                               conv[:, i % 6, 2:SEQ], ALU.mult, ALU.add).then_inc(conv_done, 1)

        @block.gpsimd
        def _(pool):
            for j in range(FT):
                pool.wait_ge(silu_done, j + 1)
                pool.wait_ge(conv_done, 2 * j + 2)
                nc.gpsimd.tensor_tensor(H[:, j, :], gate[:, j % 2, :], conv[:, (2 * j + 1) % 6, :], ALU.mult).then_inc(glu_done, 1)


def first_block(nc, G):
    with nc.Fori(0, DEPTH) as l:
        with ExitStack() as ctx:
            sb = lambda name, shape: ctx.enter_context(nc.sbuf_tensor(name, shape, F32))
            S = {"Y": sb("mixed", [P, TT, D])}
            with ExitStack() as proj:
                sp = lambda name, shape: proj.enter_context(nc.sbuf_tensor(name, shape, F32))
                for n in ("VR", "VG"):
                    S[n] = sp(n, [P, TT, 512])
                with ExitStack() as heads:
                    sh = lambda name, shape: heads.enter_context(nc.sbuf_tensor(name, shape, F32))
                    for n in ("QA", "KA", "VA"):
                        S[n] = sh(n, [P, 4, SEQ])
                    for n in ("QR", "KR", "QG", "KG"):
                        S[n] = sh(n, [P, SEQ])
                    S["AG"] = sh("AG", [LOW_RANK, SEQ])
                    project_phase(nc, l, G, S)
                    dilated_phase(nc, G, S)
                    retention_phase(nc, G, S)
                    gla_phase(nc, l, G, S)
                S["YT"] = sp("mixed_t", [P, KD, SEQ])
                head_norm_phase(nc, l, G, S)
                output_norm_phase(nc, "mix_out", l, G, S["YT"], KD, G["d"]["w_out"], G["d"]["ln1_g"], G["d"]["ln1_b"])
        with ExitStack() as ctx:
            H = ctx.enter_context(nc.sbuf_tensor("hidden", [P, FT, SEQ], F32))
            ffn_up_phase(nc, l, G, H)
            output_norm_phase(nc, "ffn_down", l, G, H, FT, G["d"]["w_down"], G["d"]["ln2_g"], G["d"]["ln2_b"])


A_W = 512
CONV_A, CONV_B = 3, 31
HEADS_C, HD_C = 8, 64
IDX_HEADS, IDX_DIM = 8, 32
TOPK = min(256, SEQ // 4)
HEADS_D, HD_D = 4, 64
BUCKETS, MAX_DIST = 32, 128
HEADS_ALL = HEADS_C + HEADS_D
GROUPS, PER_GROUP = 4, 8
EXPERTS = GROUPS * PER_GROUP
D_EXP = 512
TOP_E = 2
SLOT_ROWS = P
MAX_BLOCKS = -(-SEQ // SLOT_ROWS)
SPARE = (SEQ * TOP_E - 1) // (SLOT_ROWS + 1)
BLOCKS = EXPERTS + SPARE
LAMBDA_INIT = 0.8 - 0.6 * float(np.exp(-0.3 * 1))
DROPPED = -3.0e38
FAR = float(2 ** 30)


def bucket_starts():
    n = np.arange(4 * MAX_DIST)
    exact = BUCKETS // 2
    ratio = np.log(np.maximum(n, 1).astype(np.float32) / np.float32(exact)) / np.float32(np.log(MAX_DIST / exact))
    large = exact + (ratio * np.float32(BUCKETS - exact)).astype(np.int32)
    b = np.where(n < exact, n, np.minimum(large, BUCKETS - 1))
    starts = np.array([np.flatnonzero(b >= i)[0] for i in range(BUCKETS)], np.float64)
    starts[0] = -FAR
    return starts


def constant_parts_2():
    parts = {}
    parts["ident"] = np.eye(P, dtype=np.float32)
    parts["ones"] = np.ones((P, P), np.float32)
    parts["before"] = (np.arange(P)[:, None] < np.arange(P)[None, :]).astype(np.float32)
    parts["bucket_start"] = np.tile(bucket_starts(), P // BUCKETS)[:, None].astype(np.float32)
    parts["tile_block"] = (np.arange(P)[:, None] // BUCKETS == np.arange(TT)[None, :]).astype(np.float32)
    parts["index_e"] = np.broadcast_to(np.arange(EXPERTS, dtype=np.float32), (P, EXPERTS))
    parts["index_e_less"] = np.broadcast_to(np.arange(EXPERTS, dtype=np.float32) - EXPERTS, (P, EXPERTS))
    parts["index_spare"] = np.broadcast_to(np.arange(SPARE, dtype=np.float32), (P, SPARE))
    parts["token_id"] = (np.arange(TT)[None, :] * P + np.arange(P)[:, None]).astype(np.float32)
    return parts


def row_of(ap, n):
    return ap.to_broadcast([P, n])


def second_load_phase(nc, G):
    with Phase(nc, "second_load") as ph:
        c_rows = ph.sb("c_rows", [KD, P])
        c_silu = ph.sb("c_silu", [KD, P])
        loaded = ph.sem("loaded")
        silu_done = ph.sem("silu_done")
        turned = ph.sem("turned")
        spread_done = ph.sem("spread_done")
        zero_rows = ph.sb("zero_rows", [P, D])
        zero_set = ph.sem("zero_set")
        cleared = ph.sem("cleared")
        ps = G["ps"]
        block = ph.block()

        @block.sync
        def _(sp):
            sp.dma_start(G["consts2"][:, :], G["d"]["consts2"][:, :]).then_inc(loaded, 16)
            sp.dma_start(c_rows[:, :], G["d"]["c_2"][:, :].rearrange("o (k p) -> (o k) p", p=P)).then_inc(loaded, 16)
            sp.wait_ge(zero_set, 1)
            for b in range(EXPERTS, BLOCKS):
                sp.dma_start(G["y_dram"][b * P:(b + 1) * P, :], zero_rows[:, :]).then_inc(cleared, 16)
            sp.wait_ge(cleared, 16 * SPARE)

        @block.gpsimd
        def _(pool):
            nc.gpsimd.memset(zero_rows[:, :], 0.0).then_inc(zero_set, 1)

        @block.scalar
        def _(act):
            act.wait_ge(loaded, 32)
            nc.scalar.activation(c_silu[:, :], c_rows[:, :], ACT.Silu).then_inc(silu_done, 1)

        @block.tensor
        def _(pe):
            pe.wait_ge(silu_done, 1)
            nc.tensor.transpose(ps[0][:, 0:KD], c_silu[:, :], G["c2"]["ident"][0:KD, 0:KD]).then_inc(turned, 1)

        @block.vector
        def _(dve):
            dve.wait_ge(turned, 1)
            nc.vector.tensor_copy(G["cond"][:, :, :], ps[0][:, 0:KD].rearrange("p (k o) -> p k o", o=1).to_broadcast([P, KD, P])
                                  ).then_inc(spread_done, 1)
            dve.wait_ge(spread_done, 1)


def ada_phase(nc, i, G):
    CH = 6 * D // BANK
    RING = 3
    with Phase(nc, f"ada{i}") as ph:
        W = ph.sb("w_ring", [P, RING, KD, BANK])
        bias = ph.sb("bias", [1, 6 * D])
        w_loaded = [ph.sem(f"w_loaded{r}") for r in range(RING)]
        bias_loaded = ph.sem("bias_loaded")
        product_done = ph.sem("product_done")
        copied = ph.sem("copied")
        ps = G["ps"]
        block = ph.block()

        @block.sync
        def _(sp):
            sp.dma_start(bias[:, :], G["d"]["ada_b_2"][i:i + 1, :]).then_inc(bias_loaded, 16)
            for c in range(CH):
                if c >= RING:
                    sp.wait_ge(product_done, c - RING + 1)
                sp.dma_start(W[:, c % RING, :, :],
                             G["d"]["ada_w_2"][i, :, c * BANK:(c + 1) * BANK].rearrange("(k p) n -> p k n", p=P)
                             ).then_inc(w_loaded[c % RING], 16)

        @block.tensor
        def _(pe):
            pe.wait_ge(bias_loaded, 16)
            for c in range(CH):
                pe.wait_ge(w_loaded[c % RING], 16 * (c // RING + 1))
                if c >= 4:
                    pe.wait_ge(copied, c - 3)
                for k in range(KD):
                    nc.tensor.matmul(ps[c % 4][:, :], G["cond"][:, k, :], W[:, c % RING, k, :], start=(k == 0), stop=False)
                nc.tensor.matmul(ps[c % 4][:, :], G["c2"]["ones"][0:1, :], bias[:, c * BANK:(c + 1) * BANK], start=False,
                                 stop=True).then_inc(product_done, 1)

        @block.scalar
        def _(act):
            for c in range(CH):
                act.wait_ge(product_done, c + 1)
                nc.scalar.copy(G["mod"][:, c * BANK:(c + 1) * BANK], ps[c % 4][:, :]).then_inc(copied, 1)


def norm_mod_phase(nc, name, G, g_dram, shift, scale, h_dram=None):
    with Phase(nc, name) as ph:
        gain = ph.sb("gain", [P, D])
        both = ph.sb("gain_scaled", [P, D])
        sq = ph.sb("squares", [P, D])
        ss = ph.sb("square_sum", [P, TT])
        std = ph.sb("std", [P, TT])
        rstd = ph.sb("rstd", [P, TT])
        part = ph.sb("scaled_rows", [P, TT, D])
        h = ph.sb("rows", [P, TT, D])
        loaded = ph.sem("loaded")
        squared = ph.sem("squared")
        std_done = ph.sem("std_done")
        gain_done = ph.sem("gain_done")
        inv_done = ph.sem("inv_done")
        scaled = ph.sem("scaled")
        shifted = ph.sem("shifted")
        turned = ph.sem("turned")
        copied = ph.sem("copied")
        stored = ph.sem("stored")
        ps, X, XT = G["ps"], G["X"], G["XT"]
        block = ph.block()

        @block.sync
        def _(sp):
            sp.dma_start(gain[:, :], row_of(g_dram, D)).then_inc(loaded, 16)
            if h_dram is not None:
                for t in range(TT):
                    sp.wait_ge(shifted, t + 1)
                    sp.dma_start(h_dram[t * P:(t + 1) * P, :], h[:, t, :]).then_inc(stored, 16)
                sp.wait_ge(stored, 16 * TT)

        @block.scalar
        def _(act):
            for t in range(TT):
                if t:
                    act.wait_ge(squared, t)
                nc.scalar.activation(sq[:, :], X[:, t, :], ACT.Square, accum_out=ss[:, t:t + 1]).then_inc(squared, 1)
            act.wait_ge(squared, TT)
            nc.scalar.activation(std[:, :], ss[:, :], ACT.Sqrt, scale=1.0 / D, bias=G["eps_norm"][:, :]).then_inc(std_done, 1)
            for t in range(TT):
                for j in range(2):
                    act.wait_ge(turned, 2 * t + j + 1)
                    nc.scalar.copy(XT[:, 4 * j:4 * j + 4, t * P:(t + 1) * P],
                                   ps[2 * t + j][:, :].rearrange("p (k n) -> p k n", k=4)).then_inc(copied, 1)

        @block.vector
        def _(dve):
            dve.wait_ge(loaded, 16)
            nc.vector.scalar_tensor_tensor(both[:, :], scale, 1.0, gain[:, :], ALU.add, ALU.mult).then_inc(gain_done, 1)
            dve.wait_ge(std_done, 1)
            nc.vector.reciprocal(rstd[:, :], std[:, :]).then_inc(inv_done, 1)
            dve.wait_ge(inv_done, 1)
            dve.wait_ge(gain_done, 1)
            for t in range(TT):
                nc.vector.scalar_tensor_tensor(part[:, t, :], X[:, t, :], rstd[:, t:t + 1], both[:, :], ALU.mult, ALU.mult
                                               ).then_inc(scaled, 1)

        @block.gpsimd
        def _(pool):
            for t in range(TT):
                pool.wait_ge(scaled, t + 1)
                nc.gpsimd.tensor_tensor(h[:, t, :], part[:, t, :], shift, ALU.add).then_inc(shifted, 1)

        @block.tensor
        def _(pe):
            for t in range(TT):
                pe.wait_ge(shifted, t + 1)
                for j in range(2):
                    for n in range(4):
                        k = 4 * j + n
                        last = nc.tensor.transpose(ps[2 * t + j][:, n * P:(n + 1) * P], h[:, t, k * P:(k + 1) * P], G["c2"]["ident"])
                    last.then_inc(turned, 1)


def conv_mix_phase(nc, G, YT):
    RING = 3
    GATE_B, GATE_C, X_A, VAL_B, GLU = range(5)
    order = [GLU, VAL_B, GATE_C, X_A, GATE_B]
    jobs = [(c, m) for c in range(5) for m in range(4)]
    BANKS = 6
    ROWS = 4 * CONV_B
    PAD_A, PAD_B = CONV_A - 1, CONV_B - 1
    with Phase(nc, "conv_mix") as ph:
        W = ph.sb("w_ring", [P, RING, KD, BANK])
        ta_rows = ph.sb("taps_a_rows", [4 * CONV_A, P])
        tb_rows = ph.sb("taps_b_rows", [ROWS, P])
        vec_rows = ph.sb("vector_rows", [12, P])
        taps_a = ph.sb("taps_a", [P, 4 * CONV_A])
        taps_b = ph.sb("taps_b", [P, ROWS])
        vecs = ph.sb("vectors", [P, 12])
        mean_w = ph.sb("mean_weights", [P, P])
        glu = ph.sb("glu", [P, 4, SEQ])
        gc = ph.sb("gate_c", [P, 4, SEQ])
        ub = ph.sb("u_b", [P, 4, PAD_B + SEQ])
        pa = ph.sb("p_a", [P, 4, PAD_A + SEQ])
        ca = ph.sb("conv_a", [P, 4, SEQ])
        cb = ph.sb("conv_b", [P, 4, SEQ])
        sq = ph.sb("squares", [P, 4, SEQ])
        std = ph.sb("std", [P, SEQ])
        rstd = ph.sb("rstd", [P, SEQ])
        w_loaded = [ph.sem(f"w_loaded{r}") for r in range(RING)]
        rows_loaded = ph.sem("rows_loaded")
        rows_turned = ph.sem("rows_turned")
        rows_copied = ph.sem("rows_copied")
        pads_set = ph.sem("pads_set")
        product_done = ph.sem("product_done")
        by_act = ph.sem("evacuated_by_act")
        by_dve = ph.sem("evacuated_by_dve")
        a_step = ph.sem("a_step")
        b_step = ph.sem("b_step")
        b_conv_done = ph.sem("b_conv_done")
        mean_done = ph.sem("mean_done")
        centred = ph.sem("centred")
        squared = ph.sem("squared")
        var_done = ph.sem("var_done")
        std_done = ph.sem("std_done")
        inv_done = ph.sem("inv_done")
        normed = ph.sem("normed")
        out_done = ph.sem("out_done")
        ps, XT, ident = G["ps"], G["XT"], G["c2"]["ident"]
        reader = ["act" if order[c] in (GLU, GATE_C) else "dve" for c, _ in jobs]
        count = {"act": 0, "dve": 0}
        freed = []
        for r in reader:
            count[r] += 1
            freed.append(count[r])
        block = ph.block()

        @block.sync
        def _(sp):
            sp.dma_start(ta_rows[:, :], G["d"]["ab_conv_a_2"][0].rearrange("w (m p) -> (w m) p", p=P)).then_inc(rows_loaded, 16)
            sp.dma_start(tb_rows[:, :], G["d"]["ab_conv_b_2"][0].rearrange("w (m p) -> (w m) p", p=P)).then_inc(rows_loaded, 16)
            for v, name in enumerate(("ab_conv_b_bias_2", "ab_ln_g_2", "ab_ln_b_2")):
                sp.dma_start(vec_rows[4 * v:4 * v + 4, :], G["d"][name][0:1, :].rearrange("o (m p) -> (o m) p", p=P)
                             ).then_inc(rows_loaded, 16)
            for c, part in enumerate(order):
                if c >= RING:
                    sp.wait_ge(product_done, 4 * (c - RING + 1))
                sp.dma_start(W[:, c % RING, :, :],
                             G["d"]["ab_w_in_2"][0, :, part * A_W:(part + 1) * A_W].rearrange("(k p) n -> p k n", p=P)
                             ).then_inc(w_loaded[c % RING], 16)

        @block.tensor
        def _(pe):
            pe.wait_ge(rows_loaded, 80)
            nc.tensor.transpose(ps[7][:, 0:ROWS], tb_rows[:, :], ident[0:ROWS, 0:ROWS])
            nc.tensor.transpose(ps[7][:, 128:128 + 12], ta_rows[:, :], ident[0:12, 0:12])
            nc.tensor.transpose(ps[7][:, 256:256 + 12], vec_rows[:, :], ident[0:12, 0:12]).then_inc(rows_turned, 1)
            for i, (c, m) in enumerate(jobs):
                pe.wait_ge(w_loaded[c % RING], 16 * (c // RING + 1))
                if i >= BANKS:
                    j = i - BANKS
                    pe.wait_ge(by_act if reader[j] == "act" else by_dve, freed[j])
                for k in range(KD):
                    last = nc.tensor.matmul(ps[i % BANKS][:, :], W[:, c % RING, k, m * P:(m + 1) * P], XT[:, k, :],
                                            start=(k == 0), stop=(k == KD - 1))
                last.then_inc(product_done, 1)
            pe.wait_ge(by_dve, count["dve"])
            for m in range(4):
                pe.wait_ge(b_conv_done, m + 1)
                last = nc.tensor.matmul(ps[6][:, :], mean_w[:, :], cb[:, m, :], start=(m == 0), stop=(m == 3))
            last.then_inc(mean_done, 1)
            for m in range(4):
                pe.wait_ge(squared, m + 1)
                last = nc.tensor.matmul(ps[7][:, :], mean_w[:, :], sq[:, m, :], start=(m == 0), stop=(m == 3))
            last.then_inc(var_done, 1)

        @block.scalar
        def _(act):
            act.wait_ge(rows_turned, 1)
            nc.scalar.copy(taps_b[:, :], ps[7][:, 0:ROWS]).then_inc(rows_copied, 1)
            nc.scalar.copy(taps_a[:, :], ps[7][:, 128:140]).then_inc(rows_copied, 1)
            nc.scalar.copy(vecs[:, :], ps[7][:, 256:268]).then_inc(rows_copied, 1)
            for i, (c, m) in enumerate(jobs):
                if order[c] == GLU:
                    act.wait_ge(product_done, i + 1)
                    nc.scalar.activation(glu[:, m, :], ps[i % BANKS][:, :], ACT.Sigmoid).then_inc(by_act, 1)
                elif order[c] == GATE_C:
                    act.wait_ge(product_done, i + 1)
                    nc.scalar.copy(gc[:, m, :], ps[i % BANKS][:, :]).then_inc(by_act, 1)
            for m in range(4):
                act.wait_ge(centred, m + 1)
                nc.scalar.activation(sq[:, m, :], cb[:, m, :], ACT.Square).then_inc(squared, 1)
            act.wait_ge(var_done, 1)
            nc.scalar.activation(std[:, :], ps[7][:, :], ACT.Sqrt, bias=G["eps_norm"][:, :]).then_inc(std_done, 1)
            act.wait_ge(rows_copied, 3)
            for m in range(4):
                act.wait_ge(normed, m + 1)
                nc.scalar.activation(YT[:, 4 + m, :], cb[:, m, :], ACT.Silu, scale=vecs[:, 4 + m:5 + m], bias=vecs[:, 8 + m:9 + m]
                                     ).then_inc(out_done, 1)

        @block.gpsimd
        def _(pool):
            nc.gpsimd.memset(ub[:, :, 0:PAD_B], 0.0).then_inc(pads_set, 1)
            nc.gpsimd.memset(pa[:, :, 0:PAD_A], 0.0).then_inc(pads_set, 1)
            nc.gpsimd.memset(mean_w[:, :], 1.0 / A_W).then_inc(pads_set, 1)

        @block.vector
        def _(dve):
            achain, bchain = Chain(dve, a_step), Chain(dve, b_step)
            dve.wait_ge(rows_copied, 3)
            dve.wait_ge(pads_set, 3)
            evac = 0

            def conv_b(m, first, last_tap):
                for w in range(first, last_tap):
                    tap = taps_b[:, 4 * w + m:4 * w + m + 1]
                    if w == 0:
                        bchain.link(nc.vector.tensor_scalar(cb[:, m, :], ub[:, m, 0:SEQ], tap, vecs[:, m:m + 1], ALU.mult, ALU.add))
                    else:
                        ins = nc.vector.scalar_tensor_tensor(cb[:, m, :], ub[:, m, w:w + SEQ], tap, cb[:, m, :], ALU.mult, ALU.add)
                        if w == CONV_B - 1:
                            ins.then_inc(b_conv_done, 1)
                        else:
                            bchain.link(ins)

            for i, (c, m) in enumerate(jobs):
                if reader[i] == "act":
                    continue
                evac += 1
                dve.wait_ge(product_done, i + 1)
                if order[c] == VAL_B:
                    dve.wait_ge(by_act, m + 1)
                    nc.vector.tensor_tensor(ub[:, m, PAD_B:], ps[i % BANKS][:, :], glu[:, m, :], ALU.mult).then_inc(by_dve, 1)
                    dve.wait_ge(by_dve, evac)
                    conv_b(m, 0, CONV_B // 2)
                elif order[c] == X_A:
                    dve.wait_ge(by_act, 4 + m + 1)
                    nc.vector.tensor_tensor(pa[:, m, PAD_A:], ps[i % BANKS][:, :], gc[:, m, :], ALU.mult).then_inc(by_dve, 1)
                    dve.wait_ge(by_dve, evac)
                    achain.link(nc.vector.tensor_scalar(ca[:, m, :], pa[:, m, 0:SEQ], taps_a[:, m:m + 1], None, ALU.mult))
                    for w in range(1, CONV_A):
                        achain.link(nc.vector.scalar_tensor_tensor(ca[:, m, :], pa[:, m, w:w + SEQ],
                                                                   taps_a[:, 4 * w + m:4 * w + m + 1], ca[:, m, :],
                                                                   ALU.mult, ALU.add))
                    conv_b(m, CONV_B // 2, CONV_B)
                else:
                    nc.vector.tensor_tensor(YT[:, m, :], ps[i % BANKS][:, :], ca[:, m, :], ALU.mult).then_inc(by_dve, 1)
            dve.wait_ge(mean_done, 1)
            for m in range(4):
                nc.vector.tensor_tensor(cb[:, m, :], cb[:, m, :], ps[6][:, :], ALU.subtract).then_inc(centred, 1)
            dve.wait_ge(std_done, 1)
            nc.vector.reciprocal(rstd[:, :], std[:, :]).then_inc(inv_done, 1)
            dve.wait_ge(inv_done, 1)
            dve.wait_ge(squared, 4)
            for m in range(4):
                nc.vector.tensor_tensor(cb[:, m, :], cb[:, m, :], rstd[:, :], ALU.mult).then_inc(normed, 1)


def gated_residual_phase(nc, name, G, YT, w_dram, gate):
    with Phase(nc, name) as ph:
        W = ph.sb("w", [P, 2, 4, D])
        part = ph.sb("gated", [P, 4, BANK])
        w_loaded = [ph.sem(f"w_loaded{r}") for r in range(2)]
        product_done = ph.sem("product_done")
        gated = ph.sem("gated_done")
        added = ph.sem("added")
        ps, X = G["ps"], G["X"]
        block = ph.block()

        @block.sync
        def _(sp):
            for s in range(2):
                sp.dma_start(W[:, s, :, :], w_dram[s * 4 * P:(s + 1) * 4 * P, :].rearrange("(k p) n -> p k n", p=P)
                             ).then_inc(w_loaded[s], 16)

        @block.tensor
        def _(pe):
            for s in range(2):
                pe.wait_ge(w_loaded[s], 16)
                for j in range(2 * TT):
                    t, c = j // 2, j % 2
                    for k in range(4):
                        last = nc.tensor.matmul(ps[j][:, :], YT[:, 4 * s + k, t * P:(t + 1) * P],
                                                W[:, s, k, c * BANK:(c + 1) * BANK], start=(s + k == 0), stop=(s == 1 and k == 3))
                    if s == 1:
                        last.then_inc(product_done, 1)

        @block.vector
        def _(dve):
            for j in range(2 * TT):
                c = j % 2
                dve.wait_ge(product_done, j + 1)
                if j >= 4:
                    dve.wait_ge(added, j - 3)
                nc.vector.tensor_tensor(part[:, j % 4, :], ps[j][:, :], gate[:, c * BANK:(c + 1) * BANK], ALU.mult
                                        ).then_inc(gated, 1)

        @block.gpsimd
        def _(pool):
            for j in range(2 * TT):
                t, c = j // 2, j % 2
                pool.wait_ge(gated, j + 1)
                xs = X[:, t, c * BANK:(c + 1) * BANK]
                nc.gpsimd.tensor_tensor(xs, xs, part[:, j % 4, :], ALU.add).then_inc(added, 1)


def router_phase(nc, i, G):
    LG = GROUPS + EXPERTS
    with Phase(nc, f"router{i}") as ph:
        wr = ph.sb("w_router", [P, KD, LG])
        br = ph.sb("b_router", [P, LG])
        L = ph.sb("logits", [P, TT, LG])
        small = lambda name, n=1: ph.sb(name, [P, TT, n])
        gmax, gexp, gsum, ptop = small("gmax"), small("gexp", GROUPS), small("gsum"), small("ptop")
        geq, gval, gidx, goh, gpen = (small("geq", GROUPS), small("gval", GROUPS), small("gidx"), small("goh", GROUPS),
                                      small("gpen", GROUPS))
        fine, fine2 = small("fine", EXPERTS), small("fine2", EXPERTS)
        top = [small("top0"), small("top1")]
        eq, val = small("eq", EXPERTS), small("val", EXPERTS)
        idx = [small("idx0"), small("idx1")]
        oh = [small("oh0", EXPERTS), small("oh1", EXPERTS)]
        both = small("both", EXPERTS)
        diff, dexp, dsum, dinv = small("diff"), small("dexp"), small("dsum"), small("dinv")
        rank = small("rank", EXPERTS)
        cnt = ph.sb("count", [P, EXPERTS])
        more = ph.sb("more", [P, 3, EXPERTS])
        spare = ph.sb("spare", [P, EXPERTS])
        spare_end = ph.sb("spare_end", [P, EXPERTS])
        spare_start = ph.sb("spare_start", [P, EXPERTS])
        ends_at = ph.sb("ends_at", [P, SPARE, EXPERTS])
        spare_exp = ph.sb("spare_expert", [P, SPARE])
        prod = small("prod", EXPERTS)
        r, b, blk, first, tmp, blkno, local = (small("r"), small("b"), small("blk"), small("first"), small("tmp"),
                                               small("blkno"), small("local"))
        place, yrow = small("place"), small("yrow")
        place_i = [ph.sb(f"place_i{k}", [P, TT], I32) for k in range(TOP_E)]
        tok = ph.sb("token_id", [P, TT], I32)
        zero = ph.sb("zero", [P, BLOCKS], I32)
        loaded = ph.sem("loaded")
        zero_set = ph.sem("zero_set")
        cleared = ph.sem("cleared")
        logits_done = ph.sem("logits_done")
        logits_read = ph.sem("logits_read")
        dve_step = ph.sem("dve_step")
        gmax_done = ph.sem("gmax_done")
        gexp_done = ph.sem("gexp_done")
        diff_done = ph.sem("diff_done")
        dexp_done = ph.sem("dexp_done")
        chosen = ph.sem("chosen")
        ranked = ph.sem("ranked")
        placed = ph.sem("placed")
        scattered = ph.sem("scattered")
        read_back = ph.sem("read_back")
        ps, XT, c2 = G["ps"], G["XT"], G["c2"]
        spread = lambda a, n: a.to_broadcast([P, TT, n])
        rows = lambda a, n: a.rearrange("p (o n) -> p o n", o=1).to_broadcast([P, TT, n])
        block = ph.block()

        @block.sync
        def _(sp):
            sp.dma_start(wr[:, :, 0:GROUPS], G["d"]["moe_wr_g_2"][i].rearrange("(k p) n -> p k n", p=P)).then_inc(loaded, 16)
            sp.dma_start(wr[:, :, GROUPS:LG], G["d"]["moe_wr_e_2"][i].rearrange("(k p) n -> p k n", p=P)).then_inc(loaded, 16)
            sp.dma_start(br[:, 0:GROUPS], row_of(G["d"]["moe_br_g_2"][i:i + 1, :], GROUPS)).then_inc(loaded, 16)
            sp.dma_start(br[:, GROUPS:LG], row_of(G["d"]["moe_br_e_2"][i:i + 1, :], EXPERTS)).then_inc(loaded, 16)
            sp.wait_ge(zero_set, 1)
            sp.dma_start(G["slot_dram"][:, :].rearrange("(p b) o -> p (b o)", p=P), zero[:, :]).then_inc(cleared, 16)
            sp.wait_ge(scattered, 16 * TT * TOP_E)
            sp.dma_start(G["slot_token"][:, :], G["slot_dram"][:, :].rearrange("(p b) o -> p (b o)", p=P)).then_inc(read_back, 16)
            sp.wait_ge(read_back, 16)

        @block.tensor
        def _(pe):
            pe.wait_ge(loaded, 64)
            for t in range(TT):
                for k in range(KD):
                    last = nc.tensor.matmul(ps[t][:, 0:LG], XT[:, k, t * P:(t + 1) * P], wr[:, k, :], start=(k == 0),
                                            stop=(k == KD - 1))
                last.then_inc(logits_done, 1)
            pe.wait_ge(chosen, 1)
            for t in range(TT + 1):
                for s in range(min(t + 1, TT)):
                    last = nc.tensor.matmul(ps[4][:, t * EXPERTS:(t + 1) * EXPERTS], c2["before" if s == t else "ones"],
                                            both[:, s, :], start=(s == 0), stop=(s == min(t, TT - 1)))
            last.then_inc(ranked, 1)

        @block.scalar
        def _(act):
            act.wait_ge(gmax_done, 1)
            nc.scalar.activation(gexp[:, :, :], gval[:, :, :], ACT.Exp).then_inc(gexp_done, 1)
            act.wait_ge(diff_done, 1)
            nc.scalar.activation(dexp[:, :, :], diff[:, :, :], ACT.Exp).then_inc(dexp_done, 1)

        @block.gpsimd
        def _(pool):
            nc.gpsimd.memset(zero[:, :], 0).then_inc(zero_set, 1)
            pool.wait_ge(cleared, 16)
            for k in range(TOP_E):
                pool.wait_ge(placed, k + 1)
                for t in range(TT):
                    pool.indirect_dma_start(G["slot_dram"][:, :], bass.IndirectOffsetOnAxis(ap=place_i[k][:, t:t + 1], axis=0),
                                            tok[:, t:t + 1], None).then_inc(scattered, 16)

        @block.vector
        def _(dve):
            V = nc.vector
            link = Chain(dve, dve_step).link
            dve.wait_ge(loaded, 64)
            link(V.tensor_copy(tok[:, :], c2["token_id"]))
            for t in range(TT):
                dve.wait_ge(logits_done, t + 1)
                V.tensor_tensor(L[:, t, :], ps[t][:, 0:LG], br[:, :], ALU.add).then_inc(logits_read, 1)
            dve.wait_ge(logits_read, TT)
            lg = L[:, :, 0:GROUPS]
            link(V.tensor_reduce(gmax[:, :, :], lg, AX_X, ALU.max))
            V.tensor_tensor(gval[:, :, :], lg, spread(gmax[:, :, :], GROUPS), ALU.subtract).then_inc(gmax_done, 1)
            link(V.tensor_tensor(geq[:, :, :], lg, spread(gmax[:, :, :], GROUPS), ALU.is_equal))
            link(V.tensor_tensor(gpen[:, :, :], geq[:, :, :], rows(c2["index_e_less"][:, 0:GROUPS], GROUPS), ALU.mult))
            link(V.tensor_reduce(gidx[:, :, :], gpen[:, :, :], AX_X, ALU.min))
            link(V.tensor_tensor(goh[:, :, :], rows(c2["index_e_less"][:, 0:GROUPS], GROUPS), spread(gidx[:, :, :], GROUPS),
                                 ALU.is_equal))
            link(V.tensor_scalar(gpen[:, :, :], goh[:, :, :], 1.0, -NEG, ALU.subtract, ALU.mult))
            dve.wait_ge(gexp_done, 1)
            link(V.tensor_reduce(gsum[:, :, :], gexp[:, :, :], AX_X, ALU.add))
            link(V.reciprocal(ptop[:, :, :], gsum[:, :, :]))
            for t in range(TT):
                four = lambda a: a[:, t, :].rearrange("p (g o) -> p g o", o=1).to_broadcast([P, GROUPS, PER_GROUP])
                view = lambda a: a.rearrange("p (g e) -> p g e", g=GROUPS)
                link(V.tensor_tensor(view(fine2[:, t, :]), view(L[:, t, GROUPS:LG]), four(goh), ALU.mult))
                link(V.tensor_tensor(view(fine[:, t, :]), view(fine2[:, t, :]), four(gpen), ALU.add))
            for k in range(TOP_E):
                link(V.tensor_reduce(top[k][:, :, :], fine[:, :, :], AX_X, ALU.max))
                link(V.tensor_tensor(eq[:, :, :], fine[:, :, :], spread(top[k][:, :, :], EXPERTS), ALU.is_equal))
                link(V.tensor_tensor(val[:, :, :], eq[:, :, :], rows(c2["index_e_less"], EXPERTS), ALU.mult))
                link(V.tensor_reduce(idx[k][:, :, :], val[:, :, :], AX_X, ALU.min))
                link(V.tensor_tensor(oh[k][:, :, :], rows(c2["index_e_less"], EXPERTS), spread(idx[k][:, :, :], EXPERTS), ALU.is_equal))
                if k == 0:
                    link(V.scalar_tensor_tensor(fine[:, :, :], oh[0][:, :, :], 3.0 * NEG, fine[:, :, :], ALU.mult, ALU.add))
            V.tensor_tensor(both[:, :, :], oh[0][:, :, :], oh[1][:, :, :], ALU.add).then_inc(chosen, 1)
            V.tensor_tensor(diff[:, :, :], top[1][:, :, :], top[0][:, :, :], ALU.subtract).then_inc(diff_done, 1)
            dve.wait_ge(dexp_done, 1)
            link(V.tensor_scalar(dsum[:, :, :], dexp[:, :, :], 1.0, None, ALU.add))
            link(V.reciprocal(dinv[:, :, :], dsum[:, :, :]))
            link(V.tensor_tensor(G["gate"][:, 0, :], ptop[:, :, 0], dinv[:, :, 0], ALU.mult))
            link(V.tensor_tensor(G["gate"][:, 1, :], G["gate"][:, 0, :], dexp[:, :, 0], ALU.mult))
            dve.wait_ge(ranked, 1)
            link(V.tensor_copy(rank[:, :, :], ps[4][:, 0:TT * EXPERTS].rearrange("p (t e) -> p t e", t=TT)))
            link(V.tensor_copy(cnt[:, :], ps[4][:, TT * EXPERTS:(TT + 1) * EXPERTS]))
            for m in range(MAX_BLOCKS - 1):
                link(V.tensor_scalar(more[:, m, :], cnt[:, :], float((m + 1) * P), None, ALU.is_gt))
            link(V.tensor_tensor(spare[:, :], more[:, 0, :], more[:, 1, :], ALU.add))
            link(V.tensor_tensor(spare[:, :], spare[:, :], more[:, 2, :], ALU.add))
            link(V.tensor_tensor_scan(spare_end[:, :], c2["ones"][:, 0:EXPERTS], spare[:, :], 0.0, ALU.mult, ALU.add))
            link(V.tensor_tensor(spare_start[:, :], spare_end[:, :], spare[:, :], ALU.subtract))
            link(V.tensor_tensor(ends_at[:, :, :], spare_end[:, :].rearrange("p (o e) -> p o e", o=1).to_broadcast([P, SPARE, EXPERTS]),
                                 c2["index_spare"].rearrange("p (s o) -> p s o", o=1).to_broadcast([P, SPARE, EXPERTS]), ALU.is_le))
            link(V.tensor_reduce(spare_exp[:, :], ends_at[:, :, :], AX_X, ALU.add))
            link(V.tensor_scalar(spare_exp[:, :], spare_exp[:, :], float(EXPERTS - 1), None, ALU.min))
            link(V.tensor_copy(G["spare_table"][:, 0:SPARE], spare_exp[:, :]))
            link(V.tensor_copy(G["spare_table"][:, SPARE:SPARE + 1], spare_end[:, EXPERTS - 1:EXPERTS]))
            for k in range(TOP_E):
                link(V.tensor_tensor(prod[:, :, :], rank[:, :, :], oh[k][:, :, :], ALU.mult))
                link(V.tensor_reduce(r[:, :, :], prod[:, :, :], AX_X, ALU.add))
                link(V.tensor_tensor(prod[:, :, :], rows(spare_start[:, :], EXPERTS), oh[k][:, :, :], ALU.mult))
                link(V.tensor_reduce(b[:, :, :], prod[:, :, :], AX_X, ALU.add))
                link(V.tensor_scalar(blk[:, :, :], r[:, :, :], float(P), None, ALU.is_ge))
                for m in range(1, MAX_BLOCKS - 1):
                    link(V.scalar_tensor_tensor(blk[:, :, :], r[:, :, :], float((m + 1) * P), blk[:, :, :], ALU.is_ge, ALU.add))
                link(V.scalar_tensor_tensor(local[:, :, :], blk[:, :, :], -float(P), r[:, :, :], ALU.mult, ALU.add))
                link(V.tensor_scalar(first[:, :, :], blk[:, :, :], 0.0, None, ALU.is_equal))
                link(V.tensor_tensor(blkno[:, :, :], b[:, :, :], blk[:, :, :], ALU.add))
                link(V.tensor_scalar(blkno[:, :, :], blkno[:, :, :], float(EXPERTS - 1), None, ALU.add))
                link(V.scalar_tensor_tensor(tmp[:, :, :], idx[k][:, :, :], float(EXPERTS), blkno[:, :, :], ALU.add, ALU.subtract))
                link(V.tensor_tensor(tmp[:, :, :], tmp[:, :, :], first[:, :, :], ALU.mult))
                link(V.tensor_tensor(blkno[:, :, :], blkno[:, :, :], tmp[:, :, :], ALU.add))
                link(V.scalar_tensor_tensor(place[:, :, :], local[:, :, :], float(BLOCKS), blkno[:, :, :], ALU.mult, ALU.add))
                link(V.scalar_tensor_tensor(yrow[:, :, :], blkno[:, :, :], float(P), local[:, :, :], ALU.mult, ALU.add))
                link(V.tensor_copy(G["y_row"][k][:, :], yrow[:, :, 0]))
                V.tensor_copy(place_i[k][:, :], place[:, :, 0]).then_inc(placed, 1)


def expert_phase(nc, i, G):
    PAIRS = EXPERTS // 2
    with Phase(nc, f"expert{i}") as ph:
        wg = ph.sb("w_gate", [P, 2, KD, D_EXP])
        wu = ph.sb("w_up", [P, 2, KD, D_EXP])
        wd = ph.sb("w_down", [P, 2, D_EXP // P, D])
        xg = [ph.sb(f"x_rows{s}", [P, D]) for s in range(2)]
        xgt = ph.sb("x_rows_t", [P, 2, KD, P])
        sg = ph.sb("silu", [P, 2, D_EXP])
        hid = ph.sb("hidden", [P, 2, D_EXP])
        hidt = ph.sb("hidden_t", [P, 2, D_EXP // P, P])
        y = ph.sb("y", [P, 2, D])
        up_loaded = [ph.sem(f"up_loaded{s}") for s in range(2)]
        down_loaded = [ph.sem(f"down_loaded{s}") for s in range(2)]
        rows_loaded = [ph.sem(f"rows_loaded{s}") for s in range(2)]
        rows_turned = ph.sem("rows_turned")
        rows_copied = ph.sem("rows_copied")
        up_done = ph.sem("up_done")
        silu_done = ph.sem("silu_done")
        hidden_done = ph.sem("hidden_done")
        hidden_turned = ph.sem("hidden_turned")
        hidden_copied = ph.sem("hidden_copied")
        down_done = ph.sem("down_done")
        y_by_act = ph.sem("y_by_act")
        y_by_dve = ph.sem("y_by_dve")
        stored = [ph.sem(f"stored{s}") for s in range(2)]
        ps, ident = G["ps"], G["c2"]["ident"]
        d = G["d"]
        block = ph.block()

        def load(sp, e, s):
            at = bass.ds(e, 1)
            sp.dma_start(wg[:, s, :, :], d["moe_w_gate_2"][i, at, :, :].rearrange("o (k p) n -> p (o k) n", p=P)
                         ).then_inc(up_loaded[s], 16)
            sp.dma_start(wu[:, s, :, :], d["moe_w_up_2"][i, at, :, :].rearrange("o (k p) n -> p (o k) n", p=P)
                         ).then_inc(up_loaded[s], 16)

        def load_down(sp, e, s):
            sp.dma_start(wd[:, s, :, :], d["moe_w_down_2"][i, bass.ds(e, 1), :, :].rearrange("o (k p) n -> p (o k) n", p=P)
                         ).then_inc(down_loaded[s], 16)

        @block.sync
        def _(sp):
            for s in range(2):
                load(sp, s, s)
                load_down(sp, s, s)
            with sp.Fori(1, PAIRS) as j:
                for s in range(2):
                    sp.wait_ge(up_done, j * 2 + (s - 1))
                    load(sp, j * 2 + s, s)
                    sp.wait_ge(down_done, j * 2 + (s - 1))
                    load_down(sp, j * 2 + s, s)

        @block.gpsimd
        def _(pool):
            for e in range(EXPERTS):
                if e >= 2:
                    pool.wait_ge(rows_turned, e - 1)
                pool.indirect_dma_start(xg[e % 2][:, :], None, G["h_dram"][:, :],
                                        bass.IndirectOffsetOnAxis(ap=G["slot_token"][:, e:e + 1], axis=0)
                                        ).then_inc(rows_loaded[e % 2], 16)

        @block.tensor
        def _(pe):
            def turn_rows(e, s, turns, used):
                pe.wait_ge(rows_loaded[s], turns)
                if used is not None:
                    pe.wait_ge(rows_copied, used)
                for b in range(2):
                    for n in range(4):
                        k = 4 * b + n
                        last = nc.tensor.transpose(ps[4 + b][:, n * P:(n + 1) * P], xg[s][:, k * P:(k + 1) * P], ident)
                last.then_inc(rows_turned, 1)

            def up(e, s, loads, hidden):
                pe.wait_ge(rows_copied, 2 * e + 2)
                pe.wait_ge(up_loaded[s], loads)
                if hidden is not None:
                    pe.wait_ge(hidden_done, hidden)
                for w, b in ((wg, 0), (wu, 1)):
                    for k in range(KD):
                        last = nc.tensor.matmul(ps[b][:, :], xgt[:, s, k, :], w[:, s, k, :], start=(k == 0), stop=(k == KD - 1))
                last.then_inc(up_done, 1)

            def turn_hidden(e, s, copied):
                pe.wait_ge(hidden_done, e + 1)
                if copied is not None:
                    pe.wait_ge(hidden_copied, copied)
                for k in range(D_EXP // P):
                    last = nc.tensor.transpose(ps[6][:, k * P:(k + 1) * P], hid[:, s, k * P:(k + 1) * P], ident)
                last.then_inc(hidden_turned, 1)

            def down(e, s, loads, read):
                pe.wait_ge(hidden_copied, e + 1)
                pe.wait_ge(down_loaded[s], loads)
                if read is not None:
                    pe.wait_ge(y_by_act, read)
                    pe.wait_ge(y_by_dve, read)
                for c in range(2):
                    for k in range(D_EXP // P):
                        last = nc.tensor.matmul(ps[2 + c][:, :], hidt[:, s, k, :], wd[:, s, k, c * BANK:(c + 1) * BANK],
                                                start=(k == 0), stop=(k == D_EXP // P - 1))
                last.then_inc(down_done, 1)

            turn_rows(0, 0, 16, None)
            up(0, 0, 32, None)
            turn_rows(1, 1, 16, 2)
            turn_hidden(0, 0, None)
            up(1, 1, 32, 1)
            down(0, 0, 16, None)
            with pe.Fori(1, PAIRS) as j:
                turn_rows(j * 2, 0, j * 16 + 16, j * 4)
                turn_hidden(j * 2 - 1, 1, j * 2 - 1)
                up(j * 2, 0, j * 32 + 32, j * 2)
                down(j * 2 - 1, 1, j * 16, j * 2 - 1)
                turn_rows(j * 2 + 1, 1, j * 16 + 16, j * 4 + 2)
                turn_hidden(j * 2, 0, j * 2)
                up(j * 2 + 1, 1, j * 32 + 32, j * 2 + 1)
                down(j * 2, 0, j * 16 + 16, j * 2)
            turn_hidden(EXPERTS - 1, 1, EXPERTS - 1)
            down(EXPERTS - 1, 1, 16 * PAIRS, EXPERTS - 1)

        @block.scalar
        def _(act):
            def copy_rows(e, s, used):
                act.wait_ge(rows_turned, e + 1)
                if used is not None:
                    act.wait_ge(up_done, used)
                for b in range(2):
                    nc.scalar.copy(xgt[:, s, 4 * b:4 * b + 4, :], ps[4 + b][:, :].rearrange("p (k n) -> p k n", k=4)
                                   ).then_inc(rows_copied, 1)

            def silu(e, s, used):
                act.wait_ge(up_done, e + 1)
                if used is not None:
                    act.wait_ge(hidden_done, used)
                nc.scalar.activation(sg[:, s, :], ps[0][:, :], ACT.Silu).then_inc(silu_done, 1)

            def store_half(e, s, stores):
                act.wait_ge(down_done, e + 1)
                if stores is not None:
                    act.wait_ge(stored[s], stores)
                nc.scalar.copy(y[:, s, 0:BANK], ps[2][:, :]).then_inc(y_by_act, 1)

            def store(e, s):
                act.wait_ge(y_by_act, e + 1)
                act.wait_ge(y_by_dve, e + 1)
                act.dma_start(G["y_dram"][bass.ds(e * P, P), :], y[:, s, :]).then_inc(stored[s], 16)

            copy_rows(0, 0, None)
            silu(0, 0, None)
            copy_rows(1, 1, None)
            silu(1, 1, None)
            store_half(0, 0, None)
            store(0, 0)
            copy_rows(2, 0, 1)
            silu(2, 0, 1)
            store_half(1, 1, None)
            store(1, 1)
            copy_rows(3, 1, 2)
            silu(3, 1, 2)
            with act.Fori(1, PAIRS - 1) as j:
                store_half(j * 2, 0, j * 16)
                store(j * 2, 0)
                copy_rows(j * 2 + 2, 0, j * 2 + 1)
                silu(j * 2 + 2, 0, j * 2 + 1)
                store_half(j * 2 + 1, 1, j * 16)
                store(j * 2 + 1, 1)
                copy_rows(j * 2 + 3, 1, j * 2 + 2)
                silu(j * 2 + 3, 1, j * 2 + 2)
            for s in range(2):
                e = EXPERTS - 2 + s
                store_half(e, s, 16 * (PAIRS - 1))
                store(e, s)
            for s in range(2):
                act.wait_ge(stored[s], 16 * PAIRS)

        @block.vector
        def _(dve):
            def hidden(e, s, turned):
                dve.wait_ge(silu_done, e + 1)
                if turned is not None:
                    dve.wait_ge(hidden_turned, turned)
                nc.vector.tensor_tensor(hid[:, s, :], sg[:, s, :], ps[1][:, :], ALU.mult).then_inc(hidden_done, 1)

            def copy_hidden(e, s, used):
                dve.wait_ge(hidden_turned, e + 1)
                if used is not None:
                    dve.wait_ge(down_done, used)
                nc.vector.tensor_copy(hidt[:, s, :, :], ps[6][:, :].rearrange("p (k n) -> p k n", k=D_EXP // P)
                                      ).then_inc(hidden_copied, 1)

            def store_half(e, s, stores):
                dve.wait_ge(down_done, e + 1)
                if stores is not None:
                    dve.wait_ge(stored[s], stores)
                nc.vector.tensor_copy(y[:, s, BANK:D], ps[3][:, :]).then_inc(y_by_dve, 1)

            hidden(0, 0, None)
            copy_hidden(0, 0, None)
            hidden(1, 1, None)
            store_half(0, 0, None)
            copy_hidden(1, 1, None)
            hidden(2, 0, 1)
            store_half(1, 1, None)
            copy_hidden(2, 0, 1)
            hidden(3, 1, 2)
            with dve.Fori(1, PAIRS - 1) as j:
                store_half(j * 2, 0, j * 16)
                copy_hidden(j * 2 + 1, 1, j * 2)
                hidden(j * 2 + 2, 0, j * 2 + 1)
                store_half(j * 2 + 1, 1, j * 16)
                copy_hidden(j * 2 + 2, 0, j * 2 + 1)
                hidden(j * 2 + 3, 1, j * 2 + 2)
            store_half(EXPERTS - 2, 0, 16 * (PAIRS - 1))
            copy_hidden(EXPERTS - 1, 1, EXPERTS - 2)
            store_half(EXPERTS - 1, 1, 16 * (PAIRS - 1))


def spare_phase(nc, i, G):
    with ExitStack() as regs:
        table = G["spare_table"]
        used = nc.values_load(table[0:1, SPARE:SPARE + 1], min_val=0, max_val=SPARE)
        with nc.Fori(0, SPARE) as j:
            with nc.If(used > j):
                spare_block(nc, i, j, G)


def spare_block(nc, i, j, G):
    with Phase(nc, f"spare{i}") as ph:
        wg = ph.sb("w_gate", [P, KD, D_EXP])
        wu = ph.sb("w_up", [P, KD, D_EXP])
        wd = ph.sb("w_down", [P, D_EXP // P, D])
        col = ph.sb("slot_col", [P, 1], I32)
        xg = ph.sb("x_rows", [P, D])
        xgt = ph.sb("x_rows_t", [P, KD, P])
        sg = ph.sb("silu", [P, D_EXP])
        hid = ph.sb("hidden", [P, D_EXP])
        hidt = ph.sb("hidden_t", [P, D_EXP // P, P])
        y = ph.sb("y", [P, D])
        w_loaded = ph.sem("w_loaded")
        col_set = ph.sem("col_set")
        rows_loaded = ph.sem("rows_loaded")
        rows_turned = ph.sem("rows_turned")
        rows_copied = ph.sem("rows_copied")
        up_done = ph.sem("up_done")
        silu_done = ph.sem("silu_done")
        hidden_done = ph.sem("hidden_done")
        hidden_turned = ph.sem("hidden_turned")
        hidden_copied = ph.sem("hidden_copied")
        down_done = ph.sem("down_done")
        y_done = ph.sem("y_done")
        stored = ph.sem("stored")
        ps, ident, d = G["ps"], G["c2"]["ident"], G["d"]
        block = ph.block()

        @block.sync
        def _(sp):
            e = sp.value_load(G["spare_table"][0:1, bass.ds(j, 1)], min_val=0, max_val=EXPERTS - 1)
            for w, name in ((wg, "moe_w_gate_2"), (wu, "moe_w_up_2"), (wd, "moe_w_down_2")):
                sp.dma_start(w[:, :, :], d[name][i, bass.ds(e, 1), :, :].rearrange("o (k p) n -> p (o k) n", p=P)
                             ).then_inc(w_loaded, 16)
            sp.wait_ge(y_done, 2)
            sp.dma_start(G["y_dram"][bass.ds(j * P + EXPERTS * P, P), :], y[:, :]).then_inc(stored, 16)
            sp.wait_ge(stored, 16)

        @block.gpsimd
        def _(pool):
            nc.gpsimd.tensor_copy(col[:, :], G["slot_token"][:, bass.ds(j + EXPERTS, 1)]).then_inc(col_set, 1)
            pool.wait_ge(col_set, 1)
            pool.indirect_dma_start(xg[:, :], None, G["h_dram"][:, :],
                                    bass.IndirectOffsetOnAxis(ap=col[:, 0:1], axis=0)).then_inc(rows_loaded, 16)

        @block.tensor
        def _(pe):
            pe.wait_ge(rows_loaded, 16)
            for k in range(KD):
                last = nc.tensor.transpose(ps[4 + k // 4][:, (k % 4) * P:(k % 4 + 1) * P], xg[:, k * P:(k + 1) * P], ident)
            last.then_inc(rows_turned, 1)
            pe.wait_ge(rows_copied, 2)
            pe.wait_ge(w_loaded, 48)
            for w, b in ((wg, 0), (wu, 1)):
                for k in range(KD):
                    last = nc.tensor.matmul(ps[b][:, :], xgt[:, k, :], w[:, k, :], start=(k == 0), stop=(k == KD - 1))
            last.then_inc(up_done, 1)
            pe.wait_ge(hidden_done, 1)
            for k in range(D_EXP // P):
                last = nc.tensor.transpose(ps[6][:, k * P:(k + 1) * P], hid[:, k * P:(k + 1) * P], ident)
            last.then_inc(hidden_turned, 1)
            pe.wait_ge(hidden_copied, 1)
            for c in range(2):
                for k in range(D_EXP // P):
                    last = nc.tensor.matmul(ps[2 + c][:, :], hidt[:, k, :], wd[:, k, c * BANK:(c + 1) * BANK], start=(k == 0),
                                            stop=(k == D_EXP // P - 1))
            last.then_inc(down_done, 1)

        @block.scalar
        def _(act):
            act.wait_ge(rows_turned, 1)
            for b in range(2):
                nc.scalar.copy(xgt[:, 4 * b:4 * b + 4, :], ps[4 + b][:, :].rearrange("p (k n) -> p k n", k=4)).then_inc(rows_copied, 1)
            act.wait_ge(up_done, 1)
            nc.scalar.activation(sg[:, :], ps[0][:, :], ACT.Silu).then_inc(silu_done, 1)
            act.wait_ge(down_done, 1)
            for c in range(2):
                nc.scalar.copy(y[:, c * BANK:(c + 1) * BANK], ps[2 + c][:, :]).then_inc(y_done, 1)

        @block.vector
        def _(dve):
            dve.wait_ge(silu_done, 1)
            nc.vector.tensor_tensor(hid[:, :], sg[:, :], ps[1][:, :], ALU.mult).then_inc(hidden_done, 1)
            dve.wait_ge(hidden_turned, 1)
            nc.vector.tensor_copy(hidt[:, :, :], ps[6][:, :].rearrange("p (k n) -> p k n", k=D_EXP // P)).then_inc(hidden_copied, 1)


def combine_phase(nc, i, G, gate_row):
    with Phase(nc, f"combine{i}") as ph:
        rows = [ph.sb(f"y_rows{k}", [P, TT, D]) for k in range(TOP_E)]
        gathered = [ph.sem(f"gathered{k}") for k in range(TOP_E)]
        scaled = ph.sem("scaled")
        summed = ph.sem("summed")
        gated = ph.sem("gated")
        added = ph.sem("added")
        X = G["X"]
        block = ph.block()

        @block.gpsimd
        def _(pool):
            for t in range(TT):
                for k in range(TOP_E):
                    pool.indirect_dma_start(rows[k][:, t, :], None, G["y_dram"][:, :],
                                            bass.IndirectOffsetOnAxis(ap=G["y_row"][k][:, t:t + 1], axis=0)).then_inc(gathered[k], 16)
            for t in range(TT):
                pool.wait_ge(summed, t + 1)
                nc.gpsimd.tensor_tensor(rows[1][:, t, :], rows[1][:, t, :], gate_row, ALU.mult).then_inc(gated, 1)

        @block.scalar
        def _(act):
            for t in range(TT):
                act.wait_ge(gathered[0], 16 * TT)
                nc.scalar.mul(rows[0][:, t, :], rows[0][:, t, :], G["gate"][:, 0, t:t + 1]).then_inc(scaled, 1)

        @block.vector
        def _(dve):
            dve.wait_ge(gathered[1], 16 * TT)
            for t in range(TT):
                dve.wait_ge(scaled, t + 1)
                nc.vector.scalar_tensor_tensor(rows[1][:, t, :], rows[1][:, t, :], G["gate"][:, 1, t:t + 1], rows[0][:, t, :],
                                               ALU.mult, ALU.add).then_inc(summed, 1)
            for t in range(TT):
                dve.wait_ge(gated, t + 1)
                nc.vector.tensor_tensor(X[:, t, :], X[:, t, :], rows[1][:, t, :], ALU.add).then_inc(added, 1)


def moe(nc, i, G):
    mod = lambda n: G["mod"][:, n * D:(n + 1) * D]
    norm_mod_phase(nc, f"norm{i}b", G, G["d"]["norm_g_2"][i, 1:2, :], mod(3), mod(4), h_dram=G["h_dram"])
    router_phase(nc, i, G)
    expert_phase(nc, i, G)
    spare_phase(nc, i, G)
    combine_phase(nc, i, G, mod(5))


def bias_phase(nc, G):
    BF16 = mybir.dt.bfloat16
    M = HEADS_ALL * TT
    PER = 4
    BANKS = 6
    with Phase(nc, "bias") as ph:
        pos_i = ph.sb("pos_i", [P, SEQ], I32)
        pos = ph.sb("pos", [P, SEQ])
        reach = ph.sb("reach", [P, P])
        table = ph.sb("table", [P, HEADS_ALL])
        below = ph.sb("table_below", [P, HEADS_ALL])
        step_t = ph.sb("table_steps", [P, HEADS_ALL])
        wide = ph.sb("steps_wide", [P, HEADS_ALL, TT])
        rest = ph.sb("steps_rest", [P, HEADS_ALL, TT])
        part = ph.sb("step_parts", [P, 3, HEADS_ALL, TT], BF16)
        hit = ph.sb("steps_reached", [P, 4, SEQ], BF16)
        out = ph.sb("bias_rows", [M, 2, PER, SEQ])
        loaded = ph.sem("loaded")
        zero_set = ph.sem("zero_set")
        below_loaded = ph.sem("below_loaded")
        dve_step = ph.sem("dve_step")
        parts_done = ph.sem("parts_done")
        hit_done = ph.sem("hit_done")
        summed = ph.sem("summed")
        copied = ph.sem("copied")
        stored = [ph.sem(f"stored{s}") for s in range(2)]
        ps, c2, d = G["ps"], G["c2"], G["d"]
        block = ph.block()

        @block.sync
        def _(sp):
            sp.dma_start(pos_i[:, :], row_of(d["positions_2"][0:1, :], SEQ)).then_inc(loaded, 16)
            sp.wait_ge(zero_set, 1)
            for t in range(TT):
                sp.dma_start(table[t * BUCKETS:(t + 1) * BUCKETS, :], d["rel_bias_2"][:, :]).then_inc(loaded, 16)
                sp.dma_start(below[t * BUCKETS + 1:(t + 1) * BUCKETS, :], d["rel_bias_2"][0:BUCKETS - 1, :]).then_inc(below_loaded, 16)
            for b in range(P // PER):
                sp.wait_ge(copied, PER * (b + 1))
                sp.dma_start(G["bias_dram"][:, b * PER:(b + 1) * PER, :], out[:, b % 2, :, :]).then_inc(stored[b % 2], 16)
            for s in range(2):
                sp.wait_ge(stored[s], 16 * (P // PER // 2))

        @block.vector
        def _(dve):
            V = nc.vector
            link = Chain(dve, dve_step).link
            V.memset(below[:, :], 0.0).then_inc(zero_set, 1)
            dve.wait_ge(loaded, 16 * (1 + TT))
            dve.wait_ge(below_loaded, 16 * TT)
            link(V.tensor_copy(pos[:, :], pos_i[:, :]))
            for t in range(TT):
                rows = slice(t * BUCKETS, (t + 1) * BUCKETS)
                link(V.tensor_scalar(reach[rows, :], pos[rows, t * P:(t + 1) * P], c2["bucket_start"][rows, :], None, ALU.subtract))
            link(V.tensor_tensor(step_t[:, :], table[:, :], below[:, :], ALU.subtract))
            link(V.tensor_tensor(wide[:, :, :], step_t[:, :].rearrange("p (h o) -> p h o", o=1).to_broadcast([P, HEADS_ALL, TT]),
                                 c2["tile_block"].rearrange("p (o t) -> p o t", o=1).to_broadcast([P, HEADS_ALL, TT]), ALU.mult))
            link(V.tensor_copy(part[:, 0, :, :], wide[:, :, :]))
            link(V.tensor_tensor(rest[:, :, :], wide[:, :, :], part[:, 0, :, :], ALU.subtract))
            link(V.tensor_copy(part[:, 1, :, :], rest[:, :, :]))
            link(V.tensor_tensor(rest[:, :, :], rest[:, :, :], part[:, 1, :, :], ALU.subtract))
            V.tensor_copy(part[:, 2, :, :], rest[:, :, :]).then_inc(parts_done, 1)
            for j in range(P):
                if j >= 4:
                    dve.wait_ge(summed, j - 3)
                V.tensor_scalar(hit[:, j % 4, :], pos[:, :], reach[:, j:j + 1], None, ALU.is_le).then_inc(hit_done, 1)

        @block.tensor
        def _(pe):
            pe.wait_ge(parts_done, 1)
            for j in range(P):
                pe.wait_ge(hit_done, j + 1)
                if j >= BANKS:
                    pe.wait_ge(copied, j - BANKS + 1)
                for n in range(3):
                    last = nc.tensor.matmul(ps[j % BANKS][0:M, :], part[:, n, :, :], hit[:, j % 4, :], start=(n == 0), stop=(n == 2))
                last.then_inc(summed, 1)

        @block.scalar
        def _(act):
            for j in range(P):
                b = j // PER
                act.wait_ge(summed, j + 1)
                if b >= 2:
                    act.wait_ge(stored[b % 2], 16 * (b // 2))
                nc.scalar.copy(out[:, b % 2, j % PER, :], ps[j % BANKS][0:M, :]).then_inc(copied, 1)


COL_QC, COL_KC, COL_VC, COL_QI = 0, 512, 1024, 1536
COL_KI = COL_QI + IDX_HEADS * IDX_DIM
COL_WI = COL_KI + IDX_DIM
COL_QD = COL_WI + IDX_HEADS
COL_KD, COL_VD = COL_QD + 512, COL_QD + 1024


def attn_project_phase(nc, G, S):
    RING = 3
    BANKS = 4
    chunks = [("QC", COL_QC, FM), ("KC", COL_KC, FM), ("VC", COL_VC, TM), ("QD", COL_QD, FM), ("KD", COL_KD, FM),
              ("VD", COL_VD, TM)]
    K_AT = IDX_HEADS * IDX_DIM
    W_AT = K_AT + P
    jobs = [("QI", 0, 0), ("QI", 1, 0), ("KI", 0, 0)] + [("WI", t, 0) for t in range(TT)]
    N_FIRST = len(jobs)
    jobs += [(name, m, c + 1) for c, (name, _, _) in enumerate(chunks) for m in range(4)]
    kinds = {name: kind for name, _, kind in chunks}
    units = [(t, h) for t in range(TT) for h in range(IDX_HEADS)]
    PER_JOB = 2
    with Phase(nc, "attn_project") as ph:
        W = ph.sb("w_ring", [P, RING, KD, BANK])
        qi = ph.sb("q_index", [P, 2, SEQ])
        ki = ph.sb("k_index", [P, SEQ])
        wi = ph.sb("w_index", [P, TT, IDX_HEADS])
        pos_i = ph.sb("pos_i", [P, SEQ], I32)
        pos = ph.sb("pos", [P, SEQ])
        posq_i = ph.sb("pos_q_i", [P, TT], I32)
        posq = ph.sb("pos_q", [P, TT])
        relu = ph.sb("relu", [P, 4, SEQ])
        score = ph.sb("score", [P, 2, SEQ])
        top8 = ph.sb("top8", [P, 8])
        w_loaded = [ph.sem(f"w_loaded{r}") for r in range(RING)]
        pos_loaded = ph.sem("pos_loaded")
        product_done = ph.sem("product_done")
        evacuated = ph.sem("evacuated")
        index_done = ph.sem("index_done")
        relu_done = ph.sem("relu_done")
        weighted = ph.sem("weighted")
        dve_step = ph.sem("dve_step")
        ps, XT, d = G["ps"], G["XT"], G["d"]
        w_in = lambda c0, c1: d["cd_w_in_2"][0, :, c0:c1].rearrange("(k p) n -> p k n", p=P)
        block = ph.block()

        @block.sync
        def _(sp):
            sp.dma_start(W[:, 0, :, 0:K_AT], w_in(COL_QI, COL_KI)).then_inc(w_loaded[0], 16)
            for g in range(4):
                sp.dma_start(W[:, 0, :, K_AT + g * IDX_DIM:K_AT + (g + 1) * IDX_DIM], w_in(COL_KI, COL_WI)).then_inc(w_loaded[0], 16)
            sp.dma_start(W[:, 0, :, W_AT:W_AT + IDX_HEADS], w_in(COL_WI, COL_QD)).then_inc(w_loaded[0], 16)
            sp.dma_start(pos_i[:, :], row_of(d["positions_2"][0:1, :], SEQ)).then_inc(pos_loaded, 16)
            sp.dma_start(posq_i[:, :], d["positions_2"][0, :].rearrange("(t p) -> p t", p=P),
                         allow_slow_non_contiguous=True).then_inc(pos_loaded, 16)
            for c, (_, col, _) in enumerate(chunks):
                n = c + 1
                if n >= RING:
                    sp.wait_ge(product_done, N_FIRST + 4 * (n - RING))
                sp.dma_start(W[:, n % RING, :, :], w_in(col, col + BANK)).then_inc(w_loaded[n % RING], 16)

        @block.tensor
        def _(pe):
            def index(u):
                t, h = units[u]
                r = IDX_DIM * (h % 4)
                pe.wait_ge(evacuated, N_FIRST)
                if u >= 4:
                    pe.wait_ge(relu_done, u - 3)
                nc.tensor.matmul(ps[4 + h % 4][:, :], qi[r:r + IDX_DIM, h // 4, t * P:(t + 1) * P], ki[r:r + IDX_DIM, :],
                                 start=True, stop=True, tile_position=(r, 0)).then_inc(index_done, 1)

            u = 0
            for i, (name, m, c) in enumerate(jobs):
                first = 96 if c % RING == 0 else 0
                pe.wait_ge(w_loaded[c % RING], first + 16 * ((c // RING) if c % RING == 0 else c // RING + 1))
                if i >= BANKS:
                    pe.wait_ge(evacuated, i - BANKS + 1)
                for k in range(KD):
                    flags = dict(start=(k == 0), stop=(k == KD - 1))
                    tok = XT[:, k, m * P:(m + 1) * P]
                    if name == "QI":
                        last = nc.tensor.matmul(ps[i % BANKS][:, :], W[:, 0, k, m * P:(m + 1) * P], XT[:, k, :], **flags)
                    elif name == "KI":
                        last = nc.tensor.matmul(ps[i % BANKS][:, :], W[:, 0, k, K_AT:K_AT + P], XT[:, k, :], **flags)
                    elif name == "WI":
                        last = nc.tensor.matmul(ps[i % BANKS][:, 0:IDX_HEADS], tok, W[:, 0, k, W_AT:W_AT + IDX_HEADS], **flags)
                    elif kinds[name] == TM:
                        last = nc.tensor.matmul(ps[i % BANKS][:, :], tok, W[:, c % RING, k, :], **flags)
                    else:
                        last = nc.tensor.matmul(ps[i % BANKS][:, :], W[:, c % RING, k, m * P:(m + 1) * P], XT[:, k, :], **flags)
                last.then_inc(product_done, 1)
                if i >= N_FIRST + 1:
                    for _ in range(PER_JOB):
                        if u < len(units):
                            index(u)
                            u += 1

        @block.scalar
        def _(act):
            u = 0

            def rectify(u):
                t, h = units[u]
                act.wait_ge(index_done, u + 1)
                if u >= 4:
                    act.wait_ge(weighted, u - 3)
                nc.scalar.activation(relu[:, u % 4, :], ps[4 + h % 4][:, :], ACT.Relu).then_inc(relu_done, 1)

            for i, (name, m, c) in enumerate(jobs):
                act.wait_ge(product_done, i + 1)
                if name == "WI":
                    nc.scalar.copy(wi[:, m, :], ps[i % BANKS][:, 0:IDX_HEADS]).then_inc(evacuated, 1)
                else:
                    dest = {"QI": qi[:, m, :], "KI": ki[:, :]}[name] if c == 0 else S[name][:, m, :]
                    nc.scalar.copy(dest, ps[i % BANKS][:, :]).then_inc(evacuated, 1)
                if i >= N_FIRST + 2:
                    for _ in range(PER_JOB):
                        if u < len(units):
                            rectify(u)
                            u += 1
            while u < len(units):
                rectify(u)
                u += 1

        @block.vector
        def _(dve):
            V = nc.vector
            link = Chain(dve, dve_step).link
            dve.wait_ge(pos_loaded, 32)
            link(V.tensor_copy(pos[:, :], pos_i[:, :]))
            link(V.tensor_copy(posq[:, :], posq_i[:, :]))
            for t in range(TT):
                link(V.tensor_scalar(S["causal"][:, t, :], pos[:, :], posq[:, t:t + 1], NEG, ALU.is_gt, ALU.mult))
            dve.wait_ge(evacuated, N_FIRST)
            for t in range(TT):
                s = score[:, t % 2, :]
                for h in range(IDX_HEADS):
                    u = t * IDX_HEADS + h
                    dve.wait_ge(relu_done, u + 1)
                    V.scalar_tensor_tensor(s, relu[:, u % 4, :], wi[:, t, h:h + 1], S["causal"][:, t, :] if h == 0 else s,
                                           ALU.mult, ALU.add).then_inc(weighted, 1)
                    dve.wait_ge(weighted, u + 1)
                for n in range(TOPK // 8):
                    link(V.max(top8[:, :], s))
                    link(V.match_replace(s, top8[:, :], s, DROPPED))
                link(V.tensor_scalar(s, s, DROPPED / 2, NEG, ALU.is_gt, ALU.mult))
                link(V.tensor_tensor(S["chosen"][:, t, :], s, S["causal"][:, t, :], ALU.add))


def chosen_attention_phase(nc, G, S):
    units = [(h, t) for h in range(HEADS_C) for t in range(TT)]
    N = len(units)
    with Phase(nc, "chosen") as ph:
        bias = ph.sb("bias", [P, 4, SEQ])
        add = ph.sb("bias_masked", [P, 2, SEQ])
        SL = ph.sb("scores", [P, 2, SEQ])
        PR = ph.sb("probs", [P, 2, SEQ])
        PT = ph.sb("probs_t", [P, 2, TT, P])
        neg_max = ph.sb("neg_max", [P, N])
        row_sum = ph.sb("row_sum", [P, N])
        inv_sum = ph.sb("inv_sum", [P, N])
        bias_loaded = [ph.sem(f"bias_loaded{r}") for r in range(4)]
        masked = ph.sem("masked")
        scores_done = ph.sem("scores_done")
        biased = ph.sem("biased")
        max_done = ph.sem("max_done")
        exp_done = ph.sem("exp_done")
        turned = ph.sem("turned")
        turned_copied = ph.sem("turned_copied")
        mixed = ph.sem("mixed")
        inv_done = ph.sem("inv_done")
        out_done = ph.sem("out_done")
        ps, ident = G["ps"], G["c2"]["ident"]
        block = ph.block()

        @block.sync
        def _(sp):
            for u, (h, t) in enumerate(units):
                if u >= 4:
                    sp.wait_ge(masked, u - 3)
                sp.dma_start(bias[:, u % 4, :], G["bias_dram"][h * TT + t, :, :]).then_inc(bias_loaded[u % 4], 16)

        @block.gpsimd
        def _(pool):
            for u, (h, t) in enumerate(units):
                pool.wait_ge(bias_loaded[u % 4], 16 * (u // 4 + 1))
                if u >= 2:
                    pool.wait_ge(biased, u - 1)
                nc.gpsimd.tensor_tensor(add[:, u % 2, :], bias[:, u % 4, :], S["chosen"][:, t, :], ALU.add).then_inc(masked, 1)

        @block.tensor
        def _(pe):
            def scores(u):
                h, t = units[u]
                r = HD_C * (h % 2)
                if u >= 2:
                    pe.wait_ge(biased, u - 1)
                nc.tensor.matmul(ps[u % 2][:, :], S["QC"][r:r + HD_C, h // 2, t * P:(t + 1) * P], S["KC"][r:r + HD_C, h // 2, :],
                                 start=True, stop=True).then_inc(scores_done, 1)

            def turn(u):
                pe.wait_ge(exp_done, u + 1)
                if u >= 2:
                    pe.wait_ge(turned_copied, u - 1)
                for k in range(TT):
                    last = nc.tensor.transpose(ps[2 + u % 2][:, k * P:(k + 1) * P], PR[:, u % 2, k * P:(k + 1) * P], ident)
                last.then_inc(turned, 1)

            def mix(u):
                h, t = units[u]
                pe.wait_ge(turned_copied, u + 1)
                if u >= 2:
                    pe.wait_ge(out_done, u - 1)
                for k in range(TT):
                    last = nc.tensor.matmul(ps[4 + u % 2][:, 0:HD_C], PT[:, u % 2, k, :], S["VC"][:, k, h * HD_C:(h + 1) * HD_C],
                                            start=(k == 0), stop=(k == TT - 1))
                last.then_inc(mixed, 1)

            for i in range(N + 2):
                if i < N:
                    scores(i)
                if 1 <= i <= N:
                    turn(i - 1)
                if i >= 2:
                    mix(i - 2)

        @block.vector
        def _(dve):
            def finish(u):
                h, t = units[u]
                dve.wait_ge(exp_done, u + 1)
                nc.vector.reciprocal(inv_sum[:, u:u + 1], row_sum[:, u:u + 1]).then_inc(inv_done, 1)
                dve.wait_ge(inv_done, u + 1)
                dve.wait_ge(mixed, u + 1)
                nc.vector.tensor_scalar(S["Y"][:, t, h * HD_C:(h + 1) * HD_C], ps[4 + u % 2][:, 0:HD_C], inv_sum[:, u:u + 1], None,
                                        ALU.mult).then_inc(out_done, 1)

            for u in range(N):
                dve.wait_ge(scores_done, u + 1)
                dve.wait_ge(masked, u + 1)
                if u >= 2:
                    dve.wait_ge(exp_done, u - 1)
                nc.vector.scalar_tensor_tensor(SL[:, u % 2, :], ps[u % 2][:, :], HD_C ** -0.5, add[:, u % 2, :], ALU.mult, ALU.add
                                               ).then_inc(biased, 1)
                dve.wait_ge(biased, u + 1)
                nc.vector.tensor_reduce(neg_max[:, u:u + 1], SL[:, u % 2, :], AX_X, ALU.max, negate=True).then_inc(max_done, 1)
                if u >= 2:
                    finish(u - 2)
            finish(N - 2)
            finish(N - 1)

        @block.scalar
        def _(act):
            def copy(u):
                act.wait_ge(turned, u + 1)
                if u >= 2:
                    act.wait_ge(mixed, u - 1)
                nc.scalar.copy(PT[:, u % 2, :, :], ps[2 + u % 2][:, :].rearrange("p (k n) -> p k n", n=P)).then_inc(turned_copied, 1)

            for u in range(N):
                act.wait_ge(max_done, u + 1)
                if u >= 2:
                    act.wait_ge(turned, u - 1)
                nc.scalar.activation(PR[:, u % 2, :], SL[:, u % 2, :], ACT.Exp, bias=neg_max[:, u:u + 1],
                                     accum_out=row_sum[:, u:u + 1]).then_inc(exp_done, 1)
                if u >= 1:
                    copy(u - 1)
            copy(N - 1)


def differential_phase(nc, G, S):
    units = [(h, t) for h in range(HEADS_D) for t in range(TT)]
    N = len(units)
    VW = 2 * HD_D
    with Phase(nc, "differential") as ph:
        bias = ph.sb("bias", [P, 4, SEQ])
        add = ph.sb("bias_masked", [P, 2, SEQ])
        SL = ph.sb("scores", [P, 2, 2, SEQ])
        PR = ph.sb("probs", [P, 2, 2, SEQ])
        second = ph.sb("second_part", [P, 2, SEQ])
        attn = ph.sb("attn", [P, 2, SEQ])
        PT = ph.sb("attn_t", [P, 2, TT, P])
        neg_max = ph.sb("neg_max", [P, N, 2])
        row_sum = ph.sb("row_sum", [P, N, 2])
        inv = ph.sb("inv_sum", [P, N, 2])
        coef = ph.sb("second_coef", [P, N])
        lam = ph.sb("lam", [P, 4, HD_D])
        lam_prod = ph.sb("lam_prod", [P, 2, HD_D])
        lam_sum = ph.sb("lam_sum", [P, 2])
        lam_exp = ph.sb("lam_exp", [P, 2])
        neg_lam = ph.sb("neg_lam", [P, 1])
        gain = ph.sb("gain", [P, VW])
        sq = ph.sb("squares", [P, VW])
        ss = ph.sb("square_sum", [P, N])
        std = ph.sb("std", [P, N])
        rstd = ph.sb("rstd", [P, N])
        bias_loaded = [ph.sem(f"bias_loaded{r}") for r in range(4)]
        lam_loaded = ph.sem("lam_loaded")
        lam_summed = ph.sem("lam_summed")
        lam_exp_done = ph.sem("lam_exp_done")
        dve_step = ph.sem("dve_step")
        masked = ph.sem("masked")
        scores_done = ph.sem("scores_done")
        biased = ph.sem("biased")
        max_done = ph.sem("max_done")
        exp_done = ph.sem("exp_done")
        coef_done = ph.sem("coef_done")
        second_done = ph.sem("second_done")
        attn_done = ph.sem("attn_done")
        turned = ph.sem("turned")
        turned_copied = ph.sem("turned_copied")
        mixed = ph.sem("mixed")
        out_done = ph.sem("out_done")
        squared = ph.sem("squared")
        std_done = ph.sem("std_done")
        normed = ph.sem("normed")
        ps, ident, d = G["ps"], G["c2"]["ident"], G["d"]
        out = lambda u: S["Y"][:, units[u][1], 512 + units[u][0] * VW:512 + (units[u][0] + 1) * VW]
        block = ph.block()

        @block.sync
        def _(sp):
            sp.dma_start(lam[:, :, :], d["diff_lam_2"][0:1, :, :].to_broadcast([P, 4, HD_D])).then_inc(lam_loaded, 16)
            sp.dma_start(gain[:, :], row_of(d["diff_norm_g_2"][0:1, :], VW)).then_inc(lam_loaded, 16)
            for u, (h, t) in enumerate(units):
                if u >= 4:
                    sp.wait_ge(masked, u - 3)
                sp.dma_start(bias[:, u % 4, :], G["bias_dram"][(HEADS_C + h) * TT + t, :, :]).then_inc(bias_loaded[u % 4], 16)

        @block.gpsimd
        def _(pool):
            def scale_second(u):
                pool.wait_ge(coef_done, u + 1)
                if u >= 2:
                    pool.wait_ge(attn_done, u - 1)
                nc.gpsimd.tensor_scalar(second[:, u % 2, :], PR[:, u % 2, 1, :], coef[:, u:u + 1], None, ALU.mult).then_inc(second_done, 1)

            for u, (h, t) in enumerate(units):
                pool.wait_ge(bias_loaded[u % 4], 16 * (u // 4 + 1))
                if u >= 2:
                    pool.wait_ge(biased, 2 * (u - 1))
                nc.gpsimd.tensor_tensor(add[:, u % 2, :], bias[:, u % 4, :], S["causal"][:, t, :], ALU.add).then_inc(masked, 1)
                if u >= 1:
                    scale_second(u - 1)
            scale_second(N - 1)

        @block.tensor
        def _(pe):
            def scores(u):
                h, t = units[u]
                if u >= 2:
                    pe.wait_ge(biased, 2 * (u - 1))
                for m in range(2):
                    r = HD_D * m
                    last = nc.tensor.matmul(ps[2 * (u % 2) + m][:, :], S["QD"][r:r + HD_D, h, t * P:(t + 1) * P], S["KD"][r:r + HD_D, h, :],
                                            start=True, stop=True)
                last.then_inc(scores_done, 1)

            def turn(u):
                pe.wait_ge(attn_done, u + 1)
                if u >= 2:
                    pe.wait_ge(turned_copied, u - 1)
                for k in range(TT):
                    last = nc.tensor.transpose(ps[4 + u % 2][:, k * P:(k + 1) * P], attn[:, u % 2, k * P:(k + 1) * P], ident)
                last.then_inc(turned, 1)

            def mix(u):
                h, t = units[u]
                pe.wait_ge(turned_copied, u + 1)
                if u >= 2:
                    pe.wait_ge(out_done, u - 1)
                for k in range(TT):
                    last = nc.tensor.matmul(ps[6 + u % 2][:, 0:VW], PT[:, u % 2, k, :], S["VD"][:, k, h * VW:(h + 1) * VW],
                                            start=(k == 0), stop=(k == TT - 1))
                last.then_inc(mixed, 1)

            for i in range(N + 2):
                if i < N:
                    scores(i)
                if 1 <= i <= N:
                    turn(i - 1)
                if i >= 2:
                    mix(i - 2)

        @block.vector
        def _(dve):
            V = nc.vector
            link = Chain(dve, dve_step).link

            def combine(u):
                dve.wait_ge(exp_done, 2 * u + 2)
                link(V.reciprocal(inv[:, u, :], row_sum[:, u, :]))
                V.tensor_tensor(coef[:, u:u + 1], inv[:, u, 1:2], neg_lam[:, :], ALU.mult).then_inc(coef_done, 1)
                dve.wait_ge(second_done, u + 1)
                if u >= 2:
                    dve.wait_ge(turned, u - 1)
                V.scalar_tensor_tensor(attn[:, u % 2, :], PR[:, u % 2, 0, :], inv[:, u, 0:1], second[:, u % 2, :], ALU.mult, ALU.add
                                       ).then_inc(attn_done, 1)

            dve.wait_ge(lam_loaded, 32)
            pairs = lam[:, :, :].rearrange("p (a b) e -> p a b e", b=2)
            link(V.tensor_tensor(lam_prod[:, :, :], pairs[:, :, 0, :], pairs[:, :, 1, :], ALU.mult))
            V.tensor_reduce(lam_sum[:, :], lam_prod[:, :, :], AX_X, ALU.add).then_inc(lam_summed, 1)
            link(V.tensor_scalar(gain[:, :], gain[:, :], 1.0 - LAMBDA_INIT, None, ALU.mult))
            dve.wait_ge(lam_exp_done, 1)
            link(V.tensor_tensor(neg_lam[:, :], lam_exp[:, 1:2], lam_exp[:, 0:1], ALU.subtract))
            link(V.tensor_scalar(neg_lam[:, :], neg_lam[:, :], LAMBDA_INIT, None, ALU.subtract))
            for u in range(N):
                dve.wait_ge(scores_done, u + 1)
                dve.wait_ge(masked, u + 1)
                for m in range(2):
                    if u >= 2:
                        dve.wait_ge(exp_done, 2 * (u - 2) + m + 1)
                    V.scalar_tensor_tensor(SL[:, u % 2, m, :], ps[2 * (u % 2) + m][:, :], HD_D ** -0.5, add[:, u % 2, :], ALU.mult, ALU.add
                                           ).then_inc(biased, 1)
                for m in range(2):
                    dve.wait_ge(biased, 2 * u + m + 1)
                    V.tensor_reduce(neg_max[:, u, m:m + 1], SL[:, u % 2, m, :], AX_X, ALU.max, negate=True).then_inc(max_done, 1)
                if u >= 1:
                    combine(u - 1)
            combine(N - 1)
            dve.wait_ge(std_done, 1)
            link(V.reciprocal(rstd[:, :], std[:, :]))
            for u in range(N):
                V.scalar_tensor_tensor(out(u), out(u), rstd[:, u:u + 1], gain[:, :], ALU.mult, ALU.mult).then_inc(normed, 1)

        @block.scalar
        def _(act):
            def copy(u):
                act.wait_ge(turned, u + 1)
                if u >= 2:
                    act.wait_ge(mixed, u - 1)
                nc.scalar.copy(PT[:, u % 2, :, :], ps[4 + u % 2][:, :].rearrange("p (k n) -> p k n", n=P)).then_inc(turned_copied, 1)

            def take(u):
                act.wait_ge(mixed, u + 1)
                nc.scalar.copy(out(u), ps[6 + u % 2][:, 0:VW]).then_inc(out_done, 1)
                act.wait_ge(out_done, u + 1)
                if u >= 1:
                    act.wait_ge(squared, u)
                nc.scalar.activation(sq[:, :], out(u), ACT.Square, accum_out=ss[:, u:u + 1]).then_inc(squared, 1)

            act.wait_ge(lam_summed, 1)
            nc.scalar.activation(lam_exp[:, :], lam_sum[:, :], ACT.Exp).then_inc(lam_exp_done, 1)
            for u in range(N):
                for m in range(2):
                    act.wait_ge(max_done, 2 * u + m + 1)
                    if u >= 2:
                        act.wait_ge(attn_done, u - 1)
                    nc.scalar.activation(PR[:, u % 2, m, :], SL[:, u % 2, m, :], ACT.Exp, bias=neg_max[:, u, m:m + 1],
                                         accum_out=row_sum[:, u, m:m + 1]).then_inc(exp_done, 1)
                if u >= 1:
                    copy(u - 1)
                if u >= 2:
                    take(u - 2)
            copy(N - 1)
            take(N - 2)
            take(N - 1)
            act.wait_ge(squared, N)
            nc.scalar.activation(std[:, :], ss[:, :], ACT.Sqrt, scale=1.0 / VW, bias=G["eps_norm"][:, :]).then_inc(std_done, 1)


def turn_phase(nc, G, Y, YT):
    with Phase(nc, "turn") as ph:
        turned = ph.sem("turned")
        copied = ph.sem("copied")
        ps = G["ps"]
        block = ph.block()

        @block.tensor
        def _(pe):
            for t in range(TT):
                for j in range(2):
                    for n in range(4):
                        k = 4 * j + n
                        last = nc.tensor.transpose(ps[2 * t + j][:, n * P:(n + 1) * P], Y[:, t, k * P:(k + 1) * P], G["c2"]["ident"])
                    last.then_inc(turned, 1)

        @block.scalar
        def _(act):
            for t in range(TT):
                for j in range(2):
                    act.wait_ge(turned, 2 * t + j + 1)
                    nc.scalar.copy(YT[:, 4 * j:4 * j + 4, t * P:(t + 1) * P],
                                   ps[2 * t + j][:, :].rearrange("p (k n) -> p k n", k=4)).then_inc(copied, 1)


def final_phase(nc, G):
    with Phase(nc, "final") as ph:
        gain = ph.sb("gain", [P, D])
        sq = ph.sb("squares", [P, D])
        ss = ph.sb("square_sum", [P, TT])
        std = ph.sb("std", [P, TT])
        rstd = ph.sb("rstd", [P, TT])
        out = ph.sb("out", [P, TT, D])
        loaded = ph.sem("loaded")
        squared = ph.sem("squared")
        std_done = ph.sem("std_done")
        inv_done = ph.sem("inv_done")
        scaled = ph.sem("scaled")
        stored = ph.sem("stored")
        X, d = G["X"], G["d"]
        block = ph.block()

        @block.sync
        def _(sp):
            sp.dma_start(gain[:, :], row_of(d["final_norm_g_2"].rearrange("(o n) -> o n", o=1), D)).then_inc(loaded, 16)
            for t in range(TT):
                sp.wait_ge(scaled, t + 1)
                sp.dma_start(d["out"][0, t * P:(t + 1) * P, :], out[:, t, :]).then_inc(stored, 16)
            sp.wait_ge(stored, 16 * TT)

        @block.scalar
        def _(act):
            for t in range(TT):
                if t:
                    act.wait_ge(squared, t)
                nc.scalar.activation(sq[:, :], X[:, t, :], ACT.Square, accum_out=ss[:, t:t + 1]).then_inc(squared, 1)
            act.wait_ge(squared, TT)
            nc.scalar.activation(std[:, :], ss[:, :], ACT.Sqrt, scale=1.0 / D, bias=G["eps_norm"][:, :]).then_inc(std_done, 1)

        @block.vector
        def _(dve):
            dve.wait_ge(std_done, 1)
            nc.vector.reciprocal(rstd[:, :], std[:, :]).then_inc(inv_done, 1)
            dve.wait_ge(inv_done, 1)
            dve.wait_ge(loaded, 16)
            for t in range(TT):
                nc.vector.scalar_tensor_tensor(out[:, t, :], X[:, t, :], rstd[:, t:t + 1], gain[:, :], ALU.mult, ALU.mult
                                               ).then_inc(scaled, 1)


def second_block(nc, G):
    d = G["d"]
    mod = lambda n: G["mod"][:, n * D:(n + 1) * D]
    second_load_phase(nc, G)
    bias_phase(nc, G)
    ada_phase(nc, 0, G)
    norm_mod_phase(nc, "norm0a", G, d["norm_g_2"][0, 0:1, :], mod(0), mod(1))
    with ExitStack() as ctx:
        YT = ctx.enter_context(nc.sbuf_tensor("conv_mixed_t", [P, KD, SEQ], F32))
        conv_mix_phase(nc, G, YT)
        gated_residual_phase(nc, "conv_out", G, YT, d["ab_w_out_2"][0], mod(2))
    moe(nc, 0, G)
    ada_phase(nc, 1, G)
    norm_mod_phase(nc, "norm1a", G, d["norm_g_2"][1, 0:1, :], mod(0), mod(1))
    with ExitStack() as ctx:
        sb = lambda name, shape: ctx.enter_context(nc.sbuf_tensor(name, shape, F32))
        S = {n: sb(n, [P, 4, SEQ]) for n in ("QC", "KC", "VC", "QD", "KD", "VD", "causal", "chosen")}
        attn_project_phase(nc, G, S)
        S["Y"] = sb("attn_mixed", [P, TT, D])
        chosen_attention_phase(nc, G, S)
        differential_phase(nc, G, S)
        YT = sb("attn_mixed_t", [P, KD, SEQ])
        turn_phase(nc, G, S["Y"], YT)
        gated_residual_phase(nc, "attn_out", G, YT, d["cd_w_out_2"][0], mod(2))
    moe(nc, 1, G)
    final_phase(nc, G)


def build(nc, d, parts, parts2):
    with ExitStack() as ctx:
        G = {"d": d}
        G["ps"] = [ctx.enter_context(nc.psum_tensor(f"bank{i}", [P, BANK], F32)) for i in range(8)]
        sb = lambda name, shape, dt=F32: ctx.enter_context(nc.sbuf_tensor(name, shape, dt))
        G["X"] = sb("x_tokens", [P, TT, D])
        G["XT"] = sb("x_features", [P, KD, SEQ])
        G["ones_col"] = sb("ones_col", [P, 1])
        G["eps_ln"] = sb("eps_ln", [P, 1])
        G["eps_norm"] = sb("eps_norm", [P, 1])

        def views(tile, of):
            found, at = {}, 0
            for name, a in of.items():
                found[name] = tile[:, at:at + a.shape[1]]
                at += a.shape[1]
            return found

        with ExitStack() as first:
            G["consts"] = first.enter_context(nc.sbuf_tensor("consts", list(d["consts"].shape), F32))
            G["c"] = views(G["consts"], parts)
            load_phase(nc, G)
            first_block(nc, G)
        G["consts2"] = sb("consts2", list(d["consts2"].shape))
        G["c2"] = views(G["consts2"], parts2)
        G["cond"] = sb("cond", [P, KD, P])
        G["mod"] = sb("modulation", [P, 6 * D])
        G["slot_token"] = sb("slot_token", [P, BLOCKS], I32)
        G["gate"] = sb("gate", [P, TOP_E, TT])
        G["y_row"] = [sb(f"y_row{k}", [P, TT], I32) for k in range(TOP_E)]
        G["spare_table"] = sb("spare_table", [P, SPARE + 1], I32)
        G["h_dram"] = nc.dram_tensor("h_rows", [SEQ, D], F32).ap()
        G["y_dram"] = nc.dram_tensor("y_rows", [BLOCKS * P, D], F32).ap()
        G["slot_dram"] = nc.dram_tensor("slot_tokens", [P * BLOCKS, 1], I32).ap()
        G["bias_dram"] = nc.dram_tensor("bias_rows", [HEADS_ALL * TT, P, SEQ], F32).ap()
        second_block(nc, G)


_INS = ["x", "w_in", "w_alpha", "b_alpha", "mix_scale", "w_out", "ln1_g", "ln1_b", "w_up", "conv_w", "conv_b", "w_down",
        "ln2_g", "ln2_b", "c_2", "positions_2", "rel_bias_2", "norm_g_2", "final_norm_g_2", "ada_w_2", "ada_b_2",
        "ab_w_in_2", "ab_conv_a_2", "ab_conv_b_2", "ab_conv_b_bias_2", "ab_ln_g_2", "ab_ln_b_2", "ab_w_out_2",
        "cd_w_in_2", "diff_lam_2", "diff_norm_g_2", "cd_w_out_2", "moe_wr_g_2", "moe_br_g_2", "moe_wr_e_2",
        "moe_br_e_2", "moe_w_gate_2", "moe_w_up_2", "moe_w_down_2"]


def kernel(**inputs):
    import numpy as _np
    import concourse.bacc as _bacc
    from concourse import mybir as _mybir
    from concourse.bass_utils import run_bass_kernel_spmd as _run

    nc = _bacc.Bacc("TRN2", target_bir_lowering=False, num_devices=1)
    arrays, d = {}, {}
    parts, parts2 = constant_parts(), constant_parts_2()
    given = {name: inputs[name] for name in _INS}
    given["consts"] = _np.concatenate(list(parts.values()), axis=1)
    given["consts2"] = _np.concatenate(list(parts2.values()), axis=1)
    for name, a in given.items():
        a = _np.ascontiguousarray(a)
        arrays[f"in_{name}_dram"] = a
        d[name] = nc.dram_tensor(f"in_{name}_dram", a.shape, _mybir.dt.from_np(a.dtype), kind="ExternalInput").ap()
    d["out"] = nc.dram_tensor("out_0_dram", (1, SEQ, D), F32, kind="ExternalOutput").ap()
    build(nc, d, parts, parts2)
    r = _run(nc, [arrays], core_ids=[0])
    return r.results[0]["out_0_dram"]
```

```python
from contextlib import ExitStack

import numpy as np
import concourse.bass as bass
from concourse import mybir

F32 = mybir.dt.float32
I32 = mybir.dt.int32
F32R = mybir.dt.float32r
ALU = mybir.AluOpType
ACT = mybir.ActivationFunctionType
AX_X = mybir.AxisListType.X

P = 128
SEQ = 512
D = 1024
DEPTH = 2
TT = SEQ // P
KD = D // P
BANK = 512

HEADS_A, HD_A = 8, 64
HEADS_R, QK_R = 4, 32
HEADS_G, QK_G = 4, 32
GLA_CHUNK = 64
N_CHUNKS = SEQ // GLA_CHUNK
LOW_RANK = 16
COL_QA, COL_KA, COL_VA = 0, 512, 1024
COL_QR, COL_VR, COL_QG, COL_VG, COL_AG = 1536, 1792, 2304, 2560, 3072
PROJ = COL_AG + LOW_RANK
D_FF = P * ((8 * D // 3 + P - 1) // P)
FT = D_FF // P
ALPHA = (2 * DEPTH) ** 0.25
LN_EPS = 1e-5
NORM_EPS = 1e-6
NEG = -1.0e30


def rope_pair(dim, rows):
    inv = np.float32(1.0) / (np.float32(10000.0) ** (np.arange(0, dim, 2, dtype=np.float32) / np.float32(dim)))
    ang = np.arange(SEQ, dtype=np.float32)[:, None] * inv[None, :]
    half = dim // 2
    r = np.arange(rows) % dim
    cos = np.cos(ang).T[r % half]
    sin = np.sin(ang).T[r % half] * np.where(r < half, -1.0, 1.0)[:, None]
    other = np.where(r < half, np.arange(rows) + half, np.arange(rows) - half)
    perm = np.zeros((rows, rows), np.float32)
    perm[other, np.arange(rows)] = 1.0
    return cos.astype(np.float32), sin.astype(np.float32), perm


def constant_parts():
    parts = {}
    parts["cos_a"], parts["sin_a"], parts["perm_a"] = rope_pair(HD_A, P)
    parts["cos_r"], parts["sin_r"], parts["perm_r"] = rope_pair(QK_R, P)
    q = np.arange(SEQ)[:, None]
    k = np.arange(SEQ)[None, :]
    d = q - k
    count = ((d >= 0) & (d <= 128)).astype(np.float64) + ((d >= 0) & (d % 4 == 0)) + ((d >= 0) & (d % 16 == 0))
    logc = np.where(count > 0, np.log(np.maximum(count, 1)), NEG).astype(np.float32)
    parts["log_count"] = logc.reshape(TT, P, SEQ).transpose(1, 0, 2).reshape(P, TT * SEQ)
    lg = np.log(np.float32(1.0) - np.float32(2.0) ** (np.float32(-5.0) - np.arange(HEADS_R, dtype=np.float32)))
    dist = np.arange(SEQ)[None, :] - np.arange(P)[:, None]
    dec = np.where(dist[:, None, :] >= 0, np.exp(lg.astype(np.float64)[None, :, None] * np.maximum(dist, 0)[:, None, :]), 0.0)
    parts["decay"] = (dec * QK_R ** -0.5).astype(np.float32).reshape(P, HEADS_R * SEQ)
    kk = np.arange(P)[:, None]
    qq = np.arange(P)[None, :]
    same = kk // GLA_CHUNK == qq // GLA_CHUNK
    parts["gla_causal"] = ((kk <= qq) & same).astype(np.float32)
    t = np.arange(SEQ)
    parts["chunk_keep"] = np.broadcast_to((t % GLA_CHUNK != 0).astype(np.float32), (P, SEQ))
    parts["even_chunk"] = np.broadcast_to((t // GLA_CHUNK % 2 == 0).astype(np.float32), (P, SEQ))
    parts["odd_chunk"] = np.broadcast_to((t // GLA_CHUNK % 2 == 1).astype(np.float32), (P, SEQ))
    parts["head_block"] = (np.arange(P)[:, None] // QK_G == np.arange(256)[None, :] // 64).astype(np.float32)
    return parts


class Phase:

    def __init__(self, nc, name):
        self.nc, self.name = nc, name
        self.stack = ExitStack()
        self.sems = []

    def sem(self, name):
        s = self.nc.alloc_semaphore(f"{self.name}_{name}")
        self.sems.append(s)
        return s

    def sb(self, name, shape, dt=F32):
        return self.stack.enter_context(self.nc.sbuf_tensor(f"{self.name}_{name}", shape, dt))

    def block(self):
        return self.stack.enter_context(self.nc.Block(no_gpsimd_drain=True))

    def __enter__(self):
        return self

    def __exit__(self, *failed):
        if failed[0] is None:
            self.stack.close()
            self.nc.clear_and_free_semaphores(self.sems)
            self.nc.all_engine_barrier(sem_only=True)


class Chain:

    def __init__(self, eng, sem):
        self.eng, self.sem, self.n = eng, sem, 0

    def link(self, ins):
        self.n += 1
        ins.then_inc(self.sem, 1)
        self.eng.wait_ge(self.sem, self.n)



def rounded(a):
    return a.bitcast(F32R)


def split_product(nc, out, st, mv, start, stop):
    nc.tensor.matmul(out, rounded(st[0]), rounded(mv[0]), start=start, stop=False)
    nc.tensor.matmul(out, rounded(st[0]), rounded(mv[1]), start=False, stop=False)
    return nc.tensor.matmul(out, rounded(st[1]), rounded(mv[0]), start=False, stop=stop)


class Weights:
    RING = 2
    SLOT = 2048

    def __init__(self, nc, G, name, loads):
        self.nc, self.G, self.loads = nc, G, loads
        sem = lambda n: nc.alloc_semaphore(f"{name}_{n}")
        self.loaded = [sem(f"w_loaded{r}") for r in range(self.RING)]
        self.high = sem("w_high")
        self.split = sem("w_split")
        self.used = sem("w_used")
        self.sems = self.loaded + [self.high, self.split, self.used]
        self.issued = 0

    def load(self, eng, upto=None):
        while self.issued < min(upto or len(self.loads), len(self.loads)):
            s = self.issued
            if s >= self.RING:
                eng.wait_ge(self.split, s - self.RING + 1)
            raw = self.G["w_raw"][:, s % self.RING, :]
            for col, n, step, src in self.loads[s]:
                at = col % step
                to = raw[:, col - at:col - at + n * step].rearrange("p (k n) -> p k n", k=n)
                eng.dma_start(to[:, :, at:at + src.shape[2]], src).then_inc(self.loaded[s % self.RING], 16)
            self.issued += 1

    def then_prefetch(self, eng, following):
        eng.wait_ge(self.split, len(self.loads))
        following.load(eng, self.RING)

    def split_high(self, act, s, last_user):
        n, r = self.columns(s), s % self.RING
        act.wait_ge(self.loaded[r], self.loads_done(s))
        if s >= self.RING:
            act.wait_ge(*last_user(s - self.RING))
        self.nc.scalar.copy(rounded(self.G["w_high"][:, r, 0:n]), self.G["w_raw"][:, r, 0:n]).then_inc(self.high, 1)

    def split_low(self, pool, s):
        n, r = self.columns(s), s % self.RING
        pool.wait_ge(self.high, s + 1)
        self.nc.gpsimd.tensor_tensor(rounded(self.G["w_low"][:, r, 0:n]), self.G["w_raw"][:, r, 0:n], self.G["w_high"][:, r, 0:n],
                                     ALU.subtract).then_inc(self.split, 1)

    def columns(self, s):
        return max((col // step + k) * step for col, k, step, _ in self.loads[s])

    def loads_done(self, s):
        return 16 * sum(len(self.loads[i]) for i in range(s % self.RING, s + 1, self.RING))

    def split_slot(self, dve, s, last_user=None):
        if s >= len(self.loads):
            return
        n, r = self.columns(s), s % self.RING
        raw, high, low = [self.G[w][:, r, 0:n] for w in ("w_raw", "w_high", "w_low")]
        dve.wait_ge(self.loaded[r], self.loads_done(s))
        if s >= self.RING:
            dve.wait_ge(*(last_user(s - self.RING) if last_user else (self.used, s - self.RING + 1)))
        self.nc.vector.tensor_copy(rounded(high), raw).then_inc(self.high, 1)
        dve.wait_ge(self.high, s + 1)
        self.nc.vector.tensor_tensor(rounded(low), raw, high, ALU.subtract).then_inc(self.split, 1)

    def parts(self, s, col, n):
        return [self.G[w][:, s % self.RING, col:col + n] for w in ("w_high", "w_low")]


def k_slots(w, col, width, step=None, parts=2):
    n = KD // parts
    return [[(0, n, step or width, w(h * n * P, (h + 1) * n * P, col, col + width))] for h in range(parts)]


class Split:

    def __init__(self, nc, ph, G, turned, bank):
        self.nc, self.G, self.turned, self.bank = nc, G, turned, bank
        self.high, self.low = ph.sem("high_done"), ph.sem("low_done")

    def places(self, t, j):
        at = lambda a: a[:, 4 * j:4 * j + 4, t * P:(t + 1) * P]
        return self.bank(t, j)[:, :].rearrange("p (k n) -> p k n", k=4), at(self.G["XH"]), at(self.G["XL"])

    def high_parts(self, act):
        for t in range(TT):
            for j in range(2):
                x, high, _ = self.places(t, j)
                act.wait_ge(self.turned, 2 * t + j + 1)
                self.nc.scalar.copy(rounded(high), x).then_inc(self.high, 1)

    def low_parts(self, dve, t):
        for j in range(2):
            x, high, low = self.places(t, j)
            dve.wait_ge(self.high, 2 * t + j + 1)
            self.nc.vector.tensor_tensor(rounded(low), x, high, ALU.subtract).then_inc(self.low, 1)


def load_phase(nc, G):
    with Phase(nc, "load") as ph:
        ident_loaded = ph.sem("ident_loaded")
        x_loaded = ph.sem("x_loaded")
        transposed = ph.sem("transposed")
        ones_set = ph.sem("ones_set")
        c_rows = ph.sb("c_rows", [KD, P])
        c_silu = ph.sb("c_silu", [KD, P])
        c_loaded = ph.sem("c_loaded")
        c_silu_done = ph.sem("c_silu_done")
        c_turned = ph.sem("c_turned")
        c_copied = ph.sem("c_copied")
        X, ps, ident = G["X"], G["ps"], G["ident"]
        split = Split(nc, ph, G, transposed, lambda t, j: ps[2 * t + j])
        block = ph.block()

        @block.sync
        def _(sp):
            sp.dma_start(ident, G["d"]["ident"][:, :]).then_inc(ident_loaded, 16)
            sp.dma_start(X[:, :, :], G["d"]["x"][0].rearrange("(t p) n -> p t n", p=P)).then_inc(x_loaded, 16)
            sp.dma_start(c_rows[:, :], G["d"]["c_2"][:, :].rearrange("o (k p) -> (o k) p", p=P)).then_inc(c_loaded, 16)

        @block.vector
        def _(dve):
            nc.vector.memset(G["ones_col"][:, :], 1.0).then_inc(ones_set, 1)
            nc.vector.memset(G["eps_ln"][:, :], LN_EPS).then_inc(ones_set, 1)
            nc.vector.memset(G["eps_norm"][:, :], NORM_EPS).then_inc(ones_set, 1)
            for t in range(TT):
                split.low_parts(dve, t)
            dve.wait_ge(c_turned, 1)
            nc.vector.tensor_copy(G["cond"][:, :], ps[0][:, 0:KD]).then_inc(c_copied, 1)

        @block.tensor
        def _(pe):
            pe.wait_ge(ident_loaded, 16)
            pe.wait_ge(x_loaded, 16)
            for t in range(TT):
                for j in range(2):
                    for i in range(4):
                        k = 4 * j + i
                        last = nc.tensor.transpose(ps[2 * t + j][:, i * P:(i + 1) * P], X[:, t, k * P:(k + 1) * P], ident)
                    last.then_inc(transposed, 1)
            pe.wait_ge(c_silu_done, 1)
            pe.wait_ge(split.low, 1)
            nc.tensor.transpose(ps[0][:, 0:KD], c_silu[:, :], ident[0:KD, 0:KD]).then_inc(c_turned, 1)

        @block.scalar
        def _(act):
            split.high_parts(act)
            act.wait_ge(c_loaded, 16)
            nc.scalar.activation(c_silu[:, :], c_rows[:, :], ACT.Silu).then_inc(c_silu_done, 1)


FM, TM, ROPE = "feature-major", "token-major", "feature-major, rotated"
PROJ_CHUNKS = [(COL_QA, 512, ROPE), (COL_KA, 512, ROPE), (COL_VA, 512, TM), (COL_QR, 256, ROPE),
               (COL_VR, 512, TM), (COL_QG, 256, FM), (COL_VG, 512, TM), (COL_AG, LOW_RANK, FM)]


def project_weights(nc, l, G):
    w = lambda r0, r1, c0, c1: G["d"]["w_in"][bass.ds(l, 1), r0:r1, c0:c1].rearrange("o (k p) n -> p (o k) n", p=P)
    return Weights(nc, G, "project", [s for col, width, _ in PROJ_CHUNKS
                                        for s in k_slots(w, col, width, step=max(width, P))])


def project_phase(nc, l, G, S, weights):
    jobs = []
    for c, (col, width, kind) in enumerate(PROJ_CHUNKS):
        for m in range(TT if kind == TM else -(-width // P)):
            jobs.append((c, m, kind, col))
    of_chunk = [[i for i, j in enumerate(jobs) if j[0] == c] for c in range(len(PROJ_CHUNKS))]
    ropes = [i for i, j in enumerate(jobs) if j[2] == ROPE]
    BANKS = 6
    SLOTS = 2
    KS = KD // SLOTS

    def rope_dest(i):
        c, m, _, col = jobs[i]
        if col == COL_QR:
            return (S["QR"] if m == 0 else S["KR"])[:, :]
        return (S["QA"] if col == COL_QA else S["KA"])[:, m, :]

    def plain_dest(i):
        c, m, kind, col = jobs[i]
        if kind == TM:
            return {COL_VA: S["VA"], COL_VR: S["VR"], COL_VG: S["VG"]}[col][:, m, :]
        if col == COL_QG:
            return (S["QG"] if m == 0 else S["KG"])[:, :]
        return S["AG"][:, :]

    with Phase(nc, "project") as ph:
        ph.sems += weights.sems
        raw = lambda r: S["Y"][:, r % 4, 0:SEQ]
        cosp = lambda r: S["Y"][:, r % 2, SEQ:2 * SEQ]
        sinp = lambda r: S["Y"][:, 2 + r % 2, SEQ:2 * SEQ]
        consts_loaded = ph.sem("consts_loaded")
        product_done = ph.sem("product_done")
        evacuated = ph.sem("evacuated")
        rotated = ph.sem("rotated")
        cos_done = ph.sem("cos_done")
        sin_done = ph.sem("sin_done")
        rope_done = ph.sem("rope_done")
        ps, XH, XL = G["ps"], G["XH"], G["XL"]
        block = ph.block()

        @block.sync
        def _(sp):
            weights.load(sp, 2)
            sp.dma_start(G["consts"][:, :], G["d"]["consts"][:, :]).then_inc(consts_loaded, 16)
            weights.load(sp)

        @block.tensor
        def _(pe):
            def turn(r):
                i = ropes[r]
                if r == 0:
                    pe.wait_ge(consts_loaded, 16)
                pe.wait_ge(evacuated, i + 1)
                if r >= 2:
                    pe.wait_ge(sin_done, r - 1)
                perm = G["c"]["perm_r" if jobs[i][3] == COL_QR else "perm_a"]
                nc.tensor.matmul(ps[6 + r % 2][:, :], perm, raw(r), start=True, stop=True).then_inc(rotated, 1)

            r = 0
            for c, (col, width, kind) in enumerate(PROJ_CHUNKS):
                for half in range(SLOTS):
                    s = SLOTS * c + half
                    pe.wait_ge(weights.split, s + 1)
                    for i in of_chunk[c]:
                        m = jobs[i][1]
                        if half == 0 and i >= BANKS:
                            pe.wait_ge(evacuated, i - BANKS + 1)
                        for kk in range(KS):
                            k = half * KS + kk
                            if kind == TM:
                                toks = slice(m * P, (m + 1) * P)
                                last = split_product(nc, ps[i % BANKS][:, 0:width], (XH[:, k, toks], XL[:, k, toks]),
                                                     weights.parts(s, kk * width, width), k == 0, k == KD - 1)
                            else:
                                last = split_product(nc, ps[i % BANKS][:, :], weights.parts(s, kk * max(width, P) + m * P, P),
                                                     (XH[:, k, :], XL[:, k, :]), k == 0, k == KD - 1)
                        if half == SLOTS - 1:
                            last.then_inc(product_done, 1)
                        elif i == of_chunk[c][-1]:
                            last.then_inc(weights.used, 1)
                        if r < len(ropes) and ropes[r] < of_chunk[c][0]:
                            turn(r)
                            r += 1

        @block.scalar
        def _(act):
            r = 0
            for i, (c, m, kind, col) in enumerate(jobs):
                act.wait_ge(product_done, i + 1)
                if kind == ROPE:
                    if r >= 4:
                        act.wait_ge(rotated, r - 3)
                        act.wait_ge(cos_done, r - 3)
                    nc.scalar.copy(raw(r), ps[i % BANKS][:, :]).then_inc(evacuated, 1)
                    r += 1
                elif col == COL_QG and m == 0:
                    nc.scalar.mul(plain_dest(i), ps[i % BANKS][:, :], QK_G ** -0.5).then_inc(evacuated, 1)
                elif col == COL_AG:
                    nc.scalar.copy(plain_dest(i), ps[i % BANKS][0:LOW_RANK, :]).then_inc(evacuated, 1)
                else:
                    nc.scalar.copy(plain_dest(i), ps[i % BANKS][:, :]).then_inc(evacuated, 1)

        @block.gpsimd
        def _(pool):
            pool.wait_ge(consts_loaded, 16)
            for r, i in enumerate(ropes):
                cos = G["c"]["cos_r" if jobs[i][3] == COL_QR else "cos_a"]
                pool.wait_ge(evacuated, i + 1)
                if r >= 2:
                    pool.wait_ge(rope_done, r - 1)
                nc.gpsimd.tensor_tensor(cosp(r), raw(r), cos, ALU.mult).then_inc(cos_done, 1)

        @block.vector
        def _(dve):
            last_user = lambda s: (product_done, of_chunk[s // SLOTS][-1] + 1) if s % SLOTS == SLOTS - 1 else (weights.used, s // SLOTS + 1)

            def rope(r):
                i = ropes[r]
                sin = G["c"]["sin_r" if jobs[i][3] == COL_QR else "sin_a"]
                dve.wait_ge(rotated, r + 1)
                if r >= 2:
                    dve.wait_ge(rope_done, r - 1)
                nc.vector.tensor_tensor(sinp(r), ps[6 + r % 2][:, :], sin, ALU.mult).then_inc(sin_done, 1)
                dve.wait_ge(sin_done, r + 1)
                dve.wait_ge(cos_done, r + 1)
                nc.vector.tensor_tensor(rope_dest(i), sinp(r), cosp(r), ALU.add).then_inc(rope_done, 1)

            r = 0
            for s in range(len(weights.loads)):
                weights.split_slot(dve, s, last_user)
                if s == 0:
                    dve.wait_ge(consts_loaded, 16)
                while r < len(ropes) and SLOTS * jobs[ropes[r]][0] + SLOTS + 1 <= s:
                    rope(r)
                    r += 1
            while r < len(ropes):
                rope(r)
                r += 1


def dilated_phase(nc, G, S):
    units = [(h, t) for h in range(HEADS_A) for t in range(TT)]
    SCORE_BANKS = (0, 1, 6)
    with Phase(nc, "dilated") as ph:
        rows = G["w_raw"][:, :, :].rearrange("p r (j n) -> p (r j) n", n=SEQ)
        SL, PR = rows[:, 0:3, :], rows[:, 3:6, :]
        PT = ph.sb("probs_t", [P, 2, TT, P])
        neg_max = ph.sb("neg_max", [P, len(units)])
        row_sum = ph.sb("row_sum", [P, len(units)])
        inv_sum = ph.sb("inv_sum", [P, len(units)])
        scores_done = ph.sem("scores_done")
        biased = ph.sem("biased")
        max_done = ph.sem("max_done")
        exp_done = ph.sem("exp_done")
        turned = ph.sem("turned")
        turned_copied = ph.sem("turned_copied")
        mixed = ph.sem("mixed")
        inv_done = ph.sem("inv_done")
        out_done = ph.sem("out_done")
        ps, ident = G["ps"], G["ident"]
        logc = G["c"]["log_count"].rearrange("p (t n) -> p t n", t=TT)
        block = ph.block()

        @block.tensor
        def _(pe):
            def scores(u):
                h, t = units[u]
                r = HD_A * (h % 2)
                if u >= 3:
                    pe.wait_ge(biased, u - 2)
                nc.tensor.matmul(ps[SCORE_BANKS[u % 3]][:, 0:(t + 1) * P], S["QA"][r:r + HD_A, h // 2, t * P:(t + 1) * P],
                                 S["KA"][r:r + HD_A, h // 2, 0:(t + 1) * P], start=True, stop=True).then_inc(scores_done, 1)

            def turn(u):
                h, t = units[u]
                pe.wait_ge(exp_done, u + 1)
                if u >= 2:
                    pe.wait_ge(turned_copied, u - 1)
                for k in range(t + 1):
                    last = nc.tensor.transpose(ps[2 + u % 2][:, k * P:(k + 1) * P], PR[:, u % 3, k * P:(k + 1) * P], ident)
                last.then_inc(turned, 1)

            def mix(u):
                h, t = units[u]
                pe.wait_ge(turned_copied, u + 1)
                if u >= 2:
                    pe.wait_ge(out_done, u - 1)
                for k in range(t + 1):
                    last = nc.tensor.matmul(ps[4 + u % 2][:, 0:HD_A], PT[:, u % 2, k, :],
                                            S["VA"][:, k, h * HD_A:(h + 1) * HD_A], start=(k == 0), stop=(k == t))
                last.then_inc(mixed, 1)

            for i in range(len(units) + 3):
                if i < len(units):
                    scores(i)
                if 2 <= i < len(units) + 2:
                    turn(i - 2)
                if i >= 3:
                    mix(i - 3)

        @block.vector
        def _(dve):
            def finish(u):
                h, t = units[u]
                dve.wait_ge(exp_done, u + 1)
                nc.vector.reciprocal(inv_sum[:, u:u + 1], row_sum[:, u:u + 1]).then_inc(inv_done, 1)
                dve.wait_ge(inv_done, u + 1)
                dve.wait_ge(mixed, u + 1)
                nc.vector.tensor_scalar(S["Y"][:, t, h * HD_A:(h + 1) * HD_A], ps[4 + u % 2][:, 0:HD_A],
                                        inv_sum[:, u:u + 1], None, ALU.mult).then_inc(out_done, 1)

            for u, (h, t) in enumerate(units):
                n = (t + 1) * P
                dve.wait_ge(scores_done, u + 1)
                if u >= 3:
                    dve.wait_ge(exp_done, u - 2)
                nc.vector.scalar_tensor_tensor(SL[:, u % 3, 0:n], ps[SCORE_BANKS[u % 3]][:, 0:n], HD_A ** -0.5, logc[:, t, 0:n],
                                               ALU.mult, ALU.add).then_inc(biased, 1)
                dve.wait_ge(biased, u + 1)
                nc.vector.tensor_reduce(neg_max[:, u:u + 1], SL[:, u % 3, 0:n], AX_X, ALU.max, negate=True
                                        ).then_inc(max_done, 1)
                if u >= 3:
                    finish(u - 3)
            finish(len(units) - 3)
            finish(len(units) - 2)
            finish(len(units) - 1)

        @block.scalar
        def _(act):
            def copy(u):
                n = units[u][1] + 1
                act.wait_ge(turned, u + 1)
                if u >= 2:
                    act.wait_ge(mixed, u - 1)
                nc.scalar.copy(PT[:, u % 2, 0:n, :], ps[2 + u % 2][:, 0:n * P].rearrange("p (k n) -> p k n", n=P)
                               ).then_inc(turned_copied, 1)

            for u, (h, t) in enumerate(units):
                n = (t + 1) * P
                act.wait_ge(max_done, u + 1)
                if u >= 3:
                    act.wait_ge(turned, u - 2)
                nc.scalar.activation(PR[:, u % 3, 0:n], SL[:, u % 3, 0:n], ACT.Exp, bias=neg_max[:, u:u + 1],
                                     accum_out=row_sum[:, u:u + 1]).then_inc(exp_done, 1)
                if u >= 2:
                    copy(u - 2)
            copy(len(units) - 2)
            copy(len(units) - 1)


def retention_phase(nc, G, S):
    units = [(k, h) for k in range(TT) for h in range(HEADS_R)]
    with Phase(nc, "retention") as ph:
        SD = ph.sb("decayed", [P, TT, HEADS_R, SEQ])
        scores_done = ph.sem("scores_done")
        decayed = ph.sem("decayed_done")
        mixed = ph.sem("mixed")
        copied = ph.sem("copied")
        ps = G["ps"]
        decay = G["c"]["decay"].rearrange("p (h n) -> p h n", h=HEADS_R)
        block = ph.block()

        @block.tensor
        def _(pe):
            for u, (k, h) in enumerate(units):
                r = QK_R * h
                if u >= 4:
                    pe.wait_ge(decayed, u - 3)
                nc.tensor.matmul(ps[u % 4][:, 0:SEQ - k * P], S["KR"][r:r + QK_R, k * P:(k + 1) * P],
                                 S["QR"][r:r + QK_R, k * P:SEQ], start=True, stop=True, tile_position=(r, 0)
                                 ).then_inc(scores_done, 1)
            pe.wait_ge(decayed, len(units))
            for t in range(TT):
                for h in range(HEADS_R):
                    for k in range(t + 1):
                        last = nc.tensor.matmul(ps[4 + t][:, h * 64:(h + 1) * 64], SD[:, k, h, (t - k) * P:(t - k + 1) * P],
                                                S["VR"][:, k, h * 64:(h + 1) * 64], start=(k == 0), stop=(k == t))
                last.then_inc(mixed, 1)

        @block.vector
        def _(dve):
            for u, (k, h) in enumerate(units):
                n = SEQ - k * P
                dve.wait_ge(scores_done, u + 1)
                nc.vector.tensor_tensor(SD[:, k, h, 0:n], ps[u % 4][:, 0:n], decay[:, h, 0:n], ALU.mult).then_inc(decayed, 1)

        @block.scalar
        def _(act):
            for t in range(TT):
                act.wait_ge(mixed, t + 1)
                nc.scalar.copy(S["Y"][:, t, 512:768], ps[4 + t][:, 0:256]).then_inc(copied, 1)


def gla_phase(nc, l, G, S):
    with Phase(nc, "gla") as ph:
        wal = ph.sb("w_alpha", [LOW_RANK, P])
        bal = ph.sb("b_alpha", [P, 1])
        z = ph.sb("z", [P, SEQ])
        za = ph.sb("z_abs", [P, SEQ])
        ze = ph.sb("z_exp", [P, SEQ])
        zl = ph.sb("z_ln", [P, SEQ])
        zm = ph.sb("z_min", [P, SEQ])
        la = ph.sb("log_alpha", [P, SEQ])
        kv = G["w_raw"][:, 0, :].rearrange("p (n e) -> p n e", n=N_CHUNKS)
        state = G["w_raw"][:, 1, :].rearrange("p (n e) -> p n e", n=N_CHUNKS)
        att = G["c"]["log_count"].rearrange("p (h t n) -> p h t n", h=HEADS_G, t=TT)
        cum, rest, grow, shrink = [G["c"]["decay"][:, j * SEQ:(j + 1) * SEQ] for j in range(4)]
        rest_exp = ph.sb("exp_rest", [P, SEQ])
        qt = ph.sb("q_t", [P, SEQ])
        qe = ph.sb("q_even", [P, SEQ])
        qo = ph.sb("q_odd", [P, SEQ])
        kt = ph.sb("k_t", [P, SEQ])
        kd = ph.sb("k_rest", [P, SEQ])
        kdt = ph.sb("k_rest_t", [P, TT, P])
        loaded = ph.sem("loaded")
        z_done = ph.sem("z_done")
        act_step = ph.sem("act_step")
        ln_done = ph.sem("ln_done")
        dve_step = ph.sem("dve_step")
        cum_done = ph.sem("cum_done")
        rest_done = ph.sem("rest_done")
        grow_done = ph.sem("grow_done")
        shrink_done = ph.sem("shrink_done")
        rest_exp_done = ph.sem("rest_exp_done")
        keys_done = ph.sem("keys_done")
        queries_done = ph.sem("queries_done")
        k_rest_done = ph.sem("k_rest_done")
        k_rest_turned = ph.sem("k_rest_turned")
        k_rest_copied = ph.sem("k_rest_copied")
        kv_done = ph.sem("kv_done")
        state_done = ph.sem("state_done")
        att_done = ph.sem("att_done")
        masked = ph.sem("masked")
        mixed = ph.sem("mixed")
        copied = ph.sem("copied")
        split_done = ph.sem("split_done")
        ps, c = G["ps"], G["c"]
        kv_bank = lambda n: ps[(5, 7, 5, 7, 6, 4, 6, 4)[n]][:, 256 * (n // 2 % 2):256 * (n // 2 % 2) + 256]
        by_chunk = lambda a: a[:, :].rearrange("p (n s) -> p n s", s=GLA_CHUNK)
        block = ph.block()

        @block.sync
        def _(sp):
            sp.dma_start(wal[:, :], G["d"]["w_alpha"][bass.ds(l, 1), :, :].rearrange("o r n -> (o r) n")).then_inc(loaded, 16)
            sp.dma_start(bal[:, :], G["d"]["b_alpha"][bass.ds(l, 1), :].rearrange("o p -> p o")).then_inc(loaded, 16)

        @block.tensor
        def _(pe):
            pe.wait_ge(loaded, 32)
            nc.tensor.matmul(ps[0][:, :], wal[:, :], S["AG"][:, :], start=True, stop=True).then_inc(z_done, 1)
            pe.wait_ge(queries_done, 1)
            pe.wait_ge(keys_done, 1)
            for h in range(HEADS_G):
                r = QK_G * h
                for t in range(TT):
                    last = nc.tensor.matmul(ps[h][:, t * P:(t + 1) * P], kt[r:r + QK_G, t * P:(t + 1) * P],
                                            qt[r:r + QK_G, t * P:(t + 1) * P], start=True, stop=True, tile_position=(r, 0))
                last.then_inc(att_done, 1)
            pe.wait_ge(k_rest_done, 1)
            for t in range(TT):
                last = nc.tensor.transpose(ps[4][:, t * P:(t + 1) * P], kd[:, t * P:(t + 1) * P], G["ident"])
            last.then_inc(k_rest_turned, 1)
            pe.wait_ge(k_rest_copied, 1)
            for n in range(N_CHUNKS):
                r = GLA_CHUNK * (n % 2)
                nc.tensor.matmul(kv_bank(n), kdt[r:r + GLA_CHUNK, n // 2, :],
                                 S["VG"][r:r + GLA_CHUNK, n // 2, 0:256], start=True, stop=True).then_inc(kv_done, 1)
            pe.wait_ge(masked, HEADS_G)
            pe.wait_ge(split_done, 2)
            for t in range(TT):
                pe.wait_ge(state_done, 2 * t + 2)
                o = ps[t % 2]
                if t >= 2:
                    pe.wait_ge(copied, t - 1)
                nc.tensor.matmul(o[:, 0:256], qe[:, t * P:(t + 1) * P], state[:, 2 * t, :], start=True, stop=False,
                                 skip_group_check=True)
                nc.tensor.matmul(o[:, 0:256], qo[:, t * P:(t + 1) * P], state[:, 2 * t + 1, :], start=False, stop=False,
                                 skip_group_check=True)
                for h in range(HEADS_G):
                    last = nc.tensor.matmul(o[:, h * 64:(h + 1) * 64], att[:, h, t, :], S["VG"][:, t, h * 64:(h + 1) * 64],
                                            start=False, stop=True, skip_group_check=True)
                last.then_inc(mixed, 1)

        @block.scalar
        def _(act):
            chain = Chain(act, act_step)
            act.wait_ge(loaded, 32)
            act.wait_ge(z_done, 1)
            chain.link(nc.scalar.activation(z[:, :], ps[0][:, :], ACT.Identity, bias=bal[:, :]))
            chain.link(nc.scalar.activation(za[:, :], z[:, :], ACT.Abs))
            chain.link(nc.scalar.activation(ze[:, :], za[:, :], ACT.Exp, scale=-1.0))
            nc.scalar.activation(zl[:, :], ze[:, :], ACT.Ln, bias=G["ones_col"][:, :]).then_inc(ln_done, 1)
            act.wait_ge(cum_done, 1)
            nc.scalar.activation(grow[:, :], cum[:, :], ACT.Exp).then_inc(grow_done, 1)
            nc.scalar.activation(shrink[:, :], cum[:, :], ACT.Exp, scale=-1.0).then_inc(shrink_done, 1)
            act.wait_ge(rest_done, 1)
            nc.scalar.activation(rest_exp[:, :], rest[:, :], ACT.Exp).then_inc(rest_exp_done, 1)
            act.wait_ge(k_rest_turned, 1)
            nc.scalar.copy(kdt[:, :, :], ps[4][:, :].rearrange("p (t n) -> p t n", t=TT)).then_inc(k_rest_copied, 1)
            for t in range(TT):
                act.wait_ge(mixed, t + 1)
                nc.scalar.copy(S["Y"][:, t, 768:1024], ps[t % 2][:, 0:256]).then_inc(copied, 1)

        @block.vector
        def _(dve):
            chain = Chain(dve, dve_step)
            dve.wait_ge(act_step, 1)
            chain.link(nc.vector.tensor_scalar(zm[:, :], z[:, :], 0.0, 1.0 / 16.0, ALU.min, ALU.mult))
            dve.wait_ge(ln_done, 1)
            chain.link(nc.vector.scalar_tensor_tensor(la[:, :], zl[:, :], -1.0 / 16.0, zm[:, :], ALU.mult, ALU.add))
            nc.vector.tensor_tensor_scan(cum[:, :], c["chunk_keep"], la[:, :], 0.0, ALU.mult, ALU.add).then_inc(cum_done, 1)
            dve.wait_ge(cum_done, 1)
            last = by_chunk(cum)[:, :, GLA_CHUNK - 1:GLA_CHUNK].to_broadcast([P, N_CHUNKS, GLA_CHUNK])
            nc.vector.tensor_tensor(by_chunk(rest), last, by_chunk(cum), ALU.subtract).then_inc(rest_done, 1)
            dve.wait_ge(grow_done, 1)
            nc.vector.tensor_tensor(qt[:, :], S["QG"][:, :], grow[:, :], ALU.mult).then_inc(queries_done, 1)
            dve.wait_ge(shrink_done, 1)
            nc.vector.tensor_tensor(kt[:, :], S["KG"][:, :], shrink[:, :], ALU.mult).then_inc(keys_done, 1)
            dve.wait_ge(rest_exp_done, 1)
            nc.vector.tensor_tensor(kd[:, :], S["KG"][:, :], rest_exp[:, :], ALU.mult).then_inc(k_rest_done, 1)
            mask = c["gla_causal"].rearrange("p (o n) -> p o n", o=1).to_broadcast([P, TT, P])
            for h in range(HEADS_G):
                dve.wait_ge(att_done, h + 1)
                nc.vector.tensor_tensor(att[:, h, :, :], ps[h][:, :].rearrange("p (t n) -> p t n", t=TT), mask, ALU.mult
                                        ).then_inc(masked, 1)
            nc.vector.memset(state[:, 0, :], 0.0).then_inc(state_done, 1)
            for n in range(N_CHUNKS - 1):
                dve.wait_ge(kv_done, 4 * (n // 4) + 4)
                chain.link(nc.vector.tensor_tensor(kv[:, n, :], kv_bank(n), c["head_block"], ALU.mult))
                dve.wait_ge(state_done, n + 1)
                e = n * GLA_CHUNK + GLA_CHUNK - 1
                nc.vector.scalar_tensor_tensor(state[:, n + 1, :], state[:, n, :], grow[:, e:e + 1], kv[:, n, :],
                                               ALU.mult, ALU.add).then_inc(state_done, 1)

        @block.gpsimd
        def _(pool):
            pool.wait_ge(queries_done, 1)
            nc.gpsimd.tensor_tensor(qe[:, :], qt[:, :], c["even_chunk"], ALU.mult).then_inc(split_done, 1)
            nc.gpsimd.tensor_tensor(qo[:, :], qt[:, :], c["odd_chunk"], ALU.mult).then_inc(split_done, 1)


def head_norm_phase(nc, l, G, S, next_weights):
    HN = 16
    with Phase(nc, "head_norm") as ph:
        sums = ph.sb("sums", [P, TT, HN])
        mean = ph.sb("mean", [P, TT, HN])
        cen = ph.sb("centred", [P, TT, D])
        sq = ph.sb("squares", [P, 2, D])
        sqs = ph.sb("square_sums", [P, TT, HN])
        std = ph.sb("std", [P, TT, HN])
        rstd = ph.sb("rstd", [P, TT, HN])
        gates = ph.sb("gates", [P, TT, 512])
        nrm = cen
        scale_rows = ph.sb("scale_rows", [KD, P])
        scale = ph.sb("scale", [P, KD])
        loaded = ph.sem("loaded")
        dve_step = ph.sem("dve_step")
        centred = ph.sem("centred_done")
        squared = ph.sem("squared")
        squares_summed = ph.sem("squares_summed")
        std_done = ph.sem("std_done")
        gate_done = ph.sem("gate_done")
        normed = ph.sem("normed_done")
        gated = ph.sem("gated")
        low_done = ph.sem("low_done")
        scale_turned = ph.sem("scale_turned")
        scale_done = ph.sem("scale_done")
        turned = ph.sem("turned")
        copied = ph.sem("copied")
        ps, ident = G["ps"], G["ident"]
        heads = lambda a: a.rearrange("p (h e) -> p h e", h=HN)
        spread = lambda a: a.rearrange("p (h o) -> p h o", o=1).to_broadcast([P, HN, 64])
        block = ph.block()

        @block.sync
        def _(sp):
            next_weights.load(sp, Weights.RING)
            sp.dma_start(scale_rows[:, :], G["d"]["mix_scale"][bass.ds(l, 1), :].rearrange("o (k p) -> (o k) p", p=P)
                         ).then_inc(loaded, 16)

        @block.vector
        def _(dve):
            chain = Chain(dve, dve_step)
            for t in range(TT):
                y = heads(S["Y"][:, t, :])
                chain.link(nc.vector.tensor_reduce(sums[:, t, :], y, AX_X, ALU.add))
                chain.link(nc.vector.tensor_scalar(mean[:, t, :], sums[:, t, :], 1.0 / 64, None, ALU.mult))
                nc.vector.tensor_tensor(heads(cen[:, t, :]), y, spread(mean[:, t, :]), ALU.subtract).then_inc(centred, 1)
            for t in range(TT):
                dve.wait_ge(squared, t + 1)
                nc.vector.tensor_reduce(sqs[:, t, :], heads(sq[:, t % 2, :]), AX_X, ALU.add).then_inc(squares_summed, 1)
            for t in range(TT):
                dve.wait_ge(std_done, 1)
                chain.link(nc.vector.reciprocal(rstd[:, t, :], std[:, t, :]))
                nc.vector.tensor_tensor(heads(nrm[:, t, :]), heads(cen[:, t, :]), spread(rstd[:, t, :]), ALU.mult
                                        ).then_inc(normed, 1)
            for t in range(TT):
                for k in range(KD):
                    dve.wait_ge(copied, KD * t + 4 * (k // 4 + 1))
                    toks = slice(t * P, (t + 1) * P)
                    nc.vector.scalar_tensor_tensor(rounded(G["XL"][:, k, toks]), ps[2 * (t % 2) + k // 4][:, (k % 4) * P:(k % 4 + 1) * P],
                                                   scale[:, k:k + 1], G["XH"][:, k, toks], ALU.mult, ALU.subtract).then_inc(low_done, 1)

        @block.scalar
        def _(act):
            for t in range(TT):
                act.wait_ge(centred, t + 1)
                if t >= 2:
                    act.wait_ge(squares_summed, t - 1)
                nc.scalar.activation(sq[:, t % 2, :], cen[:, t, :], ACT.Square).then_inc(squared, 1)
            for t in range(TT):
                nc.scalar.activation(gates[:, t, 0:256], S["VR"][:, t, 256:512], ACT.Silu).then_inc(gate_done, 1)
                nc.scalar.activation(gates[:, t, 256:512], S["VG"][:, t, 256:512], ACT.Silu).then_inc(gate_done, 1)
            act.wait_ge(squares_summed, TT)
            nc.scalar.activation(std[:, :, :], sqs[:, :, :], ACT.Sqrt, scale=1.0 / 64, bias=G["eps_norm"][:, :]
                                 ).then_inc(std_done, 1)
            act.wait_ge(scale_turned, 1)
            nc.scalar.copy(scale[:, :], ps[7][:, 0:KD]).then_inc(scale_done, 1)
            act.wait_ge(scale_done, 1)
            for t in range(TT):
                for k in range(KD):
                    act.wait_ge(turned, 2 * t + k // 4 + 1)
                    nc.scalar.activation(rounded(G["XH"][:, k, t * P:(t + 1) * P]),
                                         ps[2 * (t % 2) + k // 4][:, (k % 4) * P:(k % 4 + 1) * P], ACT.Copy,
                                         scale=scale[:, k:k + 1]).then_inc(copied, 1)

        @block.gpsimd
        def _(pool):
            pool.wait_ge(gate_done, 2 * TT)
            for t in range(TT):
                pool.wait_ge(normed, t + 1)
                nc.gpsimd.tensor_tensor(nrm[:, t, 512:1024], nrm[:, t, 512:1024], gates[:, t, :], ALU.mult).then_inc(gated, 1)

        @block.tensor
        def _(pe):
            pe.wait_ge(loaded, 16)
            nc.tensor.transpose(ps[7][:, 0:KD], scale_rows[:, :], ident[0:KD, 0:KD]).then_inc(scale_turned, 1)
            for t in range(TT):
                pe.wait_ge(normed, t + 1)
                pe.wait_ge(gated, t + 1)
                if t >= 2:
                    pe.wait_ge(low_done, KD * (t - 1))
                for j in range(2):
                    for i in range(4):
                        k = 4 * j + i
                        last = nc.tensor.transpose(ps[2 * (t % 2) + j][:, i * P:(i + 1) * P], nrm[:, t, k * P:(k + 1) * P], ident)
                    last.then_inc(turned, 1)


ROW_TILES = Weights.SLOT // D


def row_weights(nc, name, w, KT, G):
    return Weights(nc, G, name, [[(0, ROW_TILES, D, w(k * P, (k + ROW_TILES) * P))] for k in range(0, KT, ROW_TILES)])


def layer_rows(w_dram, l):
    return lambda r0, r1: w_dram[bass.ds(l, 1), r0:r1, :].rearrange("o (k p) n -> p (o k) n", p=P)


def row_products(nc, pe, ps, weights, acts, acts_ready, product_done):
    slots = len(weights.loads)

    def tile(s, t):
        for c in range(2):
            for k in range(ROW_TILES):
                last = split_product(nc, ps[2 * t + c][:, :], acts(s, k, slice(t * P, (t + 1) * P)),
                                     weights.parts(s, k * D + c * BANK, BANK), s == 0 and k == 0,
                                     s == slots - 1 and k == ROW_TILES - 1)
            if s == slots - 1:
                last.then_inc(product_done, 1)
        return last

    for s in range(slots - 2):
        pe.wait_ge(weights.split, s + 1)
        if acts_ready is not None:
            pe.wait_ge(acts_ready, s + 1)
        for t in range(TT):
            last = tile(s, t)
        last.then_inc(weights.used, 1)
    for t in range(TT):
        for s in (slots - 2, slots - 1):
            pe.wait_ge(weights.split, s + 1)
            if acts_ready is not None:
                pe.wait_ge(acts_ready, s + 1)
            tile(s, t)


def output_norm_phase(nc, name, l, G, H, weights, g_dram, b_dram, next_weights=None):
    slots = len(weights.loads)
    with Phase(nc, name) as ph:
        ph.sems += weights.sems
        g_row = ph.sb("g_row", [P, D])
        b_row = ph.sb("b_row", [P, D])
        stats = ph.sb("stats", [P, TT, 2, 6])
        mv = ph.sb("mean_var", [P, TT, 2])
        std = ph.sb("std", [P, TT])
        rstd = ph.sb("rstd", [P, TT])
        rows_loaded = ph.sem("rows_loaded")
        product_done = ph.sem("product_done")
        summed = ph.sem("summed")
        dve_step = ph.sem("dve_step")
        var_done = ph.sem("var_done")
        std_done = ph.sem("std_done")
        normed = ph.sem("normed")
        scaled = ph.sem("scaled")
        shifted = ph.sem("shifted")
        turned = ph.sem("turned")
        ps, X, XL, XH, ident = G["ps"], G["X"], G["XL"], G["XH"], G["ident"]
        split = Split(nc, ph, G, turned, lambda t, j: ps[2 * t + j])
        if H is None:
            acts = lambda s, k, toks: (XH[:, ROW_TILES * s + k, toks], XL[:, ROW_TILES * s + k, toks])
            acts_low = None
        else:
            hidden_high = ph.sb("hidden_high", [P, 2, ROW_TILES, SEQ])
            acts_high = ph.sem("acts_high")
            acts_low = ph.sem("acts_low")
            hidden_low = ph.sb("hidden_low", [P, 2, ROW_TILES, SEQ])
            acts = lambda s, k, toks: (hidden_high[:, s % 2, k, toks], hidden_low[:, s % 2, k, toks])
        block = ph.block()

        @block.sync
        def _(sp):
            weights.load(sp, Weights.RING)
            sp.dma_start(g_row[:, :], g_dram[bass.ds(l, 1), :].to_broadcast([P, D])).then_inc(rows_loaded, 16)
            sp.dma_start(b_row[:, :], b_dram[bass.ds(l, 1), :].to_broadcast([P, D])).then_inc(rows_loaded, 16)
            weights.load(sp)
            if next_weights is not None:
                weights.then_prefetch(sp, next_weights)

        @block.tensor
        def _(pe):
            row_products(nc, pe, ps, weights, acts, acts_low, product_done)
            for t in range(TT):
                pe.wait_ge(shifted, t + 1)
                for j in range(2):
                    for i in range(4):
                        k = 4 * j + i
                        last = nc.tensor.transpose(ps[2 * t + j][:, i * P:(i + 1) * P], X[:, t, k * P:(k + 1) * P], ident)
                    last.then_inc(turned, 1)

        @block.vector
        def _(dve):
            chain = Chain(dve, dve_step)

            def stats_of(t):
                for c in range(2):
                    dve.wait_ge(product_done, 2 * t + c + 1)
                    half = X[:, t, c * BANK:(c + 1) * BANK]
                    nc.vector.scalar_tensor_tensor(half, half, ALPHA, ps[2 * t + c][:, :], ALU.mult, ALU.add).then_inc(summed, 1)
                    dve.wait_ge(summed, 2 * t + c + 1)
                    chain.link(nc.vector.bn_stats(stats[:, t, c, :], half))
                nc.vector.bn_aggr(mv[:, t, :], stats[:, t, :, :]).then_inc(var_done, 1)

            def norm(t):
                dve.wait_ge(std_done, t + 1)
                chain.link(nc.vector.reciprocal(rstd[:, t:t + 1], std[:, t:t + 1]))
                nc.vector.tensor_scalar(X[:, t, :], X[:, t, :], mv[:, t, 0:1], rstd[:, t:t + 1], ALU.subtract, ALU.mult
                                        ).then_inc(normed, 1)
                dve.wait_ge(normed, t + 1)
                dve.wait_ge(rows_loaded, 32)
                nc.vector.tensor_tensor(X[:, t, :], X[:, t, :], g_row[:, :], ALU.mult).then_inc(scaled, 1)

            for s in range(slots):
                if H is not None:
                    if s >= 2:
                        dve.wait_ge(weights.used, s - 1)
                    nc.vector.tensor_copy(rounded(hidden_high[:, s % 2, :, :]), H[:, ROW_TILES * s:ROW_TILES * (s + 1), :]).then_inc(acts_high, 1)
                weights.split_slot(dve, s)
            for t in range(TT):
                stats_of(t)
                if t >= 1:
                    norm(t - 1)
            norm(TT - 1)
            for t in range(TT):
                split.low_parts(dve, t)

        @block.scalar
        def _(act):
            for t in range(TT):
                act.wait_ge(var_done, t + 1)
                nc.scalar.activation(std[:, t:t + 1], mv[:, t, 1:2], ACT.Sqrt, bias=G["eps_ln"][:, :]).then_inc(std_done, 1)
            split.high_parts(act)

        @block.gpsimd
        def _(pool):
            if H is not None:
                for s in range(slots):
                    pool.wait_ge(acts_high, s + 1)
                    if s >= 2:
                        pool.wait_ge(weights.used, s - 1)
                    nc.gpsimd.tensor_tensor(rounded(hidden_low[:, s % 2, :, :]), H[:, ROW_TILES * s:ROW_TILES * (s + 1), :],
                                            hidden_high[:, s % 2, :, :], ALU.subtract).then_inc(acts_low, 1)
            pool.wait_ge(rows_loaded, 32)
            for t in range(TT):
                pool.wait_ge(scaled, t + 1)
                nc.gpsimd.tensor_tensor(X[:, t, :], X[:, t, :], b_row[:, :], ALU.add).then_inc(shifted, 1)


def up_weights(nc, l, G):
    w = lambda c: G["d"]["w_up"][bass.ds(l, 1), :, c:c + P].rearrange("o (k p) n -> p (o k) n", p=P)
    return Weights(nc, G, "ffn_up", [[(0, KD, P, w(j * P)), (KD * P, KD, P, w(D_FF + j * P))] for j in range(FT)])


MOD = 6 * D
MOD_COLS = MOD // 3
MOD_CHUNKS = [(g, k) for g in range(MOD // MOD_COLS) for k in range(KD)]


def ffn_up_phase(nc, l, G, H, weights, next_weights):
    mod_step = lambda j: range(j * len(MOD_CHUNKS) // (FT - 1), min((j + 1) * len(MOD_CHUNKS) // (FT - 1), len(MOD_CHUNKS)))
    jobs = [(j, v) for j in range(FT) for v in range(2)]
    BANKS = 6
    with Phase(nc, "ffn_up") as ph:
        ph.sems += weights.sems
        taps_rows = ph.sb("taps_rows", [2 * FT, 4, P])
        taps = ph.sb("taps", [P, 4, 2 * FT])
        conv = ph.sb("conv", [P, 6, SEQ])
        gate = ph.sb("gate", [P, 2, SEQ])
        mod_w = ph.sb("mod_w", [P, 2, MOD_COLS])
        mod_sum = ph.sb("mod_sum", [P, MOD])
        mod_loaded = [ph.sem(f"mod_loaded{r}") for r in range(2)]
        mod_added = ph.sem("mod_added")
        mod_stored = ph.sem("mod_stored")
        taps_loaded = ph.sem("taps_loaded")
        taps_turned = ph.sem("taps_turned")
        taps_copied = ph.sem("taps_copied")
        product_done = ph.sem("product_done")
        last_tap = ph.sem("last_tap")
        dve_tap = ph.sem("dve_tap")
        conv_done = ph.sem("conv_done")
        silu_done = ph.sem("silu_done")
        glu_done = ph.sem("glu_done")
        ps, XH, XL, ident = G["ps"], G["XH"], G["XL"], G["ident"]
        block = ph.block()

        @block.sync
        def _(sp):
            weights.load(sp, Weights.RING)
            sp.dma_start(taps_rows[:, 0:3, :], G["d"]["conv_w"][bass.ds(l, 1), :, :].rearrange("o w (j p) -> j (o w) p", p=P)
                         ).then_inc(taps_loaded, 16)
            sp.dma_start(taps_rows[:, 3:4, :], G["d"]["conv_b"][bass.ds(l, 1), :].rearrange("o (j p) -> j o p", p=P)
                         ).then_inc(taps_loaded, 16)

            def load_mod(n):
                g, k = MOD_CHUNKS[n]
                if n >= 2:
                    sp.wait_ge(mod_added, n - 1)
                sp.dma_start(mod_w[:, n % 2, :], G["d"]["ada_w_2"][bass.ds(l, 1), k * P:(k + 1) * P, g * MOD_COLS:(g + 1) * MOD_COLS]
                             .rearrange("o p n -> p (o n)")).then_inc(mod_loaded[n % 2], 16)

            def store_mod(g):
                sp.wait_ge(mod_added, KD * (g + 1))
                cols = slice(g * MOD_COLS, (g + 1) * MOD_COLS)
                sp.dma_start(G["mod_dram"][bass.ds(l, 1), :, cols].rearrange("o p n -> p (o n)"), mod_sum[:, cols]
                             ).then_inc(mod_stored, 16)

            load_mod(0)
            load_mod(1)
            for j in range(FT):
                weights.load(sp, j + 4)
                for n in mod_step(j):
                    if n + 2 < len(MOD_CHUNKS):
                        load_mod(n + 2)
                    if n % KD == KD - 1:
                        store_mod(n // KD)
            weights.then_prefetch(sp, next_weights)
            sp.wait_ge(mod_stored, 16 * (MOD // MOD_COLS))

        @block.tensor
        def _(pe):
            pe.wait_ge(taps_loaded, 32)
            for w in range(4):
                last = nc.tensor.transpose(ps[7][:, w * P:w * P + 2 * FT], taps_rows[:, w, :], ident[0:2 * FT, 0:2 * FT])
            last.then_inc(taps_turned, 1)
            for i, (j, v) in enumerate(jobs):
                pe.wait_ge(weights.split, j + 1)
                if i >= BANKS:
                    pe.wait_ge(conv_done, i - BANKS + 1)
                for k in range(KD):
                    last = split_product(nc, ps[i % BANKS][:, :], weights.parts(j, (v * KD + k) * P, P), (XH[:, k, :], XL[:, k, :]),
                                         k == 0, k == KD - 1)
                last.then_inc(product_done, 1)

        @block.scalar
        def _(act):
            act.wait_ge(taps_turned, 1)
            nc.scalar.copy(taps[:, :, :], ps[7][:, :].rearrange("p (w j) -> p w j", w=4)[:, :, 0:2 * FT]).then_inc(taps_copied, 1)
            act.wait_ge(taps_copied, 1)

            def silu(j):
                act.wait_ge(conv_done, 2 * j + 1)
                if j >= 2:
                    act.wait_ge(glu_done, j - 1)
                nc.scalar.activation(gate[:, j % 2, :], conv[:, (2 * j) % 6, :], ACT.Silu).then_inc(silu_done, 1)

            for i, (j, v) in enumerate(jobs):
                ch = v * FT + j
                act.wait_ge(product_done, i + 1)
                if i >= 6:
                    act.wait_ge(glu_done, (i - 6) // 2 + 1)
                nc.scalar.activation(conv[:, i % 6, :], ps[i % BANKS][:, :], ACT.Identity, bias=taps[:, 3, ch:ch + 1],
                                     scale=taps[:, 2, ch:ch + 1]).then_inc(last_tap, 1)
                if v == 1:
                    silu(j)

        @block.vector
        def _(dve):
            last_user = lambda s: (product_done, 2 * (s + 1))
            weights.split_slot(dve, 0)
            weights.split_slot(dve, 1)
            dve.wait_ge(taps_copied, 1)
            for i, (j, v) in enumerate(jobs):
                ch = v * FT + j
                u = ps[i % BANKS]
                dve.wait_ge(last_tap, i + 1)
                nc.vector.scalar_tensor_tensor(conv[:, i % 6, 1:SEQ], u[:, 0:SEQ - 1], taps[:, 1, ch:ch + 1],
                                               conv[:, i % 6, 1:SEQ], ALU.mult, ALU.add).then_inc(dve_tap, 1)
                dve.wait_ge(dve_tap, i + 1)
                nc.vector.scalar_tensor_tensor(conv[:, i % 6, 2:SEQ], u[:, 0:SEQ - 2], taps[:, 0, ch:ch + 1],
                                               conv[:, i % 6, 2:SEQ], ALU.mult, ALU.add).then_inc(conv_done, 1)
                if v == 1:
                    weights.split_slot(dve, j + 2, last_user)
                    for n in mod_step(j):
                        g, k = MOD_CHUNKS[n]
                        total = mod_sum[:, g * MOD_COLS:(g + 1) * MOD_COLS]
                        dve.wait_ge(mod_loaded[n % 2], 16 * (n // 2 + 1))
                        if k == 0:
                            add = nc.vector.tensor_scalar(total, mod_w[:, n % 2, :], G["cond"][:, k:k + 1], None, ALU.mult)
                        else:
                            dve.wait_ge(mod_added, n)
                            add = nc.vector.scalar_tensor_tensor(total, mod_w[:, n % 2, :], G["cond"][:, k:k + 1], total,
                                                                 ALU.mult, ALU.add)
                        add.then_inc(mod_added, 1)

        @block.gpsimd
        def _(pool):
            for j in range(FT):
                pool.wait_ge(silu_done, j + 1)
                pool.wait_ge(conv_done, 2 * j + 2)
                nc.gpsimd.tensor_tensor(H[:, j, :], gate[:, j % 2, :], conv[:, (2 * j + 1) % 6, :], ALU.mult).then_inc(glu_done, 1)


def views(tile, parts):
    found, at = {}, 0
    for name, a in parts.items():
        found[name] = tile[:, at:at + a.shape[1]]
        at += a.shape[1]
    return found


def parts_room(nc, ctx, G, name):
    sb = lambda n, shape: ctx.enter_context(nc.sbuf_tensor(f"{name}_{n}", shape, F32))
    for n in ("XH", "XL"):
        G[n] = sb(n, [P, KD, SEQ])
    for n in ("w_raw", "w_high", "w_low"):
        G[n] = sb(n, [P, Weights.RING, Weights.SLOT])


def first_block(nc, G, parts):
    d = G["d"]
    with nc.Fori(0, DEPTH) as l:
        with ExitStack() as ctx:
            sb = lambda name, shape: ctx.enter_context(nc.sbuf_tensor(name, shape, F32))
            G["consts"] = sb("consts", list(d["consts"].shape))
            G["c"] = views(G["consts"], parts)
            S = {"Y": sb("mixed", [P, TT, D])}
            for n in ("VR", "VG"):
                S[n] = sb(n, [P, TT, 512])
            with ExitStack() as heads:
                sh = lambda name, shape: heads.enter_context(nc.sbuf_tensor(name, shape, F32))
                for n in ("QR", "KR", "QG", "KG"):
                    S[n] = sh(n, [P, SEQ])
                S["AG"] = sh("AG", [LOW_RANK, SEQ])
                with ExitStack() as wide:
                    for n in ("QA", "KA", "VA"):
                        S[n] = wide.enter_context(nc.sbuf_tensor(n, [P, 4, SEQ], F32))
                    project_phase(nc, l, G, S, project_weights(nc, l, G))
                    dilated_phase(nc, G, S)
                retention_phase(nc, G, S)
                gla_phase(nc, l, G, S)
            mix_weights = row_weights(nc, "mix_out", layer_rows(d["w_out"], l), KD, G)
            head_norm_phase(nc, l, G, S, mix_weights)
        up = up_weights(nc, l, G)
        output_norm_phase(nc, "mix_out", l, G, None, mix_weights, d["ln1_g"], d["ln1_b"], up)
        with ExitStack() as ctx:
            H = ctx.enter_context(nc.sbuf_tensor("hidden", [P, FT, SEQ], F32))
            down = row_weights(nc, "ffn_down", layer_rows(d["w_down"], l), FT, G)
            ffn_up_phase(nc, l, G, H, up, down)
            output_norm_phase(nc, "ffn_down", l, G, H, down, d["ln2_g"], d["ln2_b"])


A_W = 512
CONV_A, CONV_B = 3, 31
HEADS_C, HD_C = 8, 64
IDX_HEADS, IDX_DIM = 8, 32
TOPK = min(256, SEQ // 4)
HEADS_D, HD_D = 4, 64
BUCKETS, MAX_DIST = 32, 128
HEADS_ALL = HEADS_C + HEADS_D
GROUPS, PER_GROUP = 4, 8
EXPERTS = GROUPS * PER_GROUP
D_EXP = 512
TOP_E = 2
SLOT_ROWS = P
MAX_BLOCKS = -(-SEQ // SLOT_ROWS)
SPARE = (SEQ * TOP_E - 1) // (SLOT_ROWS + 1)
BLOCKS = EXPERTS + SPARE
LAMBDA_INIT = 0.8 - 0.6 * float(np.exp(-0.3 * 1))
DROPPED = -3.0e38
FAR = float(2 ** 30)


def bucket_starts():
    n = np.arange(4 * MAX_DIST)
    exact = BUCKETS // 2
    ratio = np.log(np.maximum(n, 1).astype(np.float32) / np.float32(exact)) / np.float32(np.log(MAX_DIST / exact))
    large = exact + (ratio * np.float32(BUCKETS - exact)).astype(np.int32)
    b = np.where(n < exact, n, np.minimum(large, BUCKETS - 1))
    starts = np.array([np.flatnonzero(b >= i)[0] for i in range(BUCKETS)], np.float64)
    starts[0] = -FAR
    return starts


def constant_parts_2():
    parts = {}
    parts["ones"] = np.ones((P, P), np.float32)
    parts["before"] = (np.arange(P)[:, None] < np.arange(P)[None, :]).astype(np.float32)
    parts["bucket_start"] = np.tile(bucket_starts(), P // BUCKETS)[:, None].astype(np.float32)
    parts["tile_block"] = (np.arange(P)[:, None] // BUCKETS == np.arange(TT)[None, :]).astype(np.float32)
    parts["index_e"] = np.broadcast_to(np.arange(EXPERTS, dtype=np.float32), (P, EXPERTS))
    parts["index_e_less"] = np.broadcast_to(np.arange(EXPERTS, dtype=np.float32) - EXPERTS, (P, EXPERTS))
    parts["index_spare"] = np.broadcast_to(np.arange(SPARE, dtype=np.float32), (P, SPARE))
    parts["token_id"] = (np.arange(TT)[None, :] * P + np.arange(P)[:, None]).astype(np.float32)
    return parts


def row_of(ap, n):
    return ap.to_broadcast([P, n])


def second_load_phase(nc, G):
    with Phase(nc, "second_load") as ph:
        loaded = ph.sem("loaded")
        zero_rows = ph.sb("zero_rows", [P, D])
        zero_set = ph.sem("zero_set")
        cleared = ph.sem("cleared")
        block = ph.block()

        @block.sync
        def _(sp):
            sp.dma_start(G["consts2"][:, :], G["d"]["consts2"][:, :]).then_inc(loaded, 16)
            sp.wait_ge(zero_set, 1)
            for b in range(EXPERTS, BLOCKS):
                sp.dma_start(G["y_dram"][b * P:(b + 1) * P, :], zero_rows[:, :]).then_inc(cleared, 16)
            sp.wait_ge(loaded, 16)
            sp.wait_ge(cleared, 16 * SPARE)

        @block.gpsimd
        def _(pool):
            nc.gpsimd.memset(zero_rows[:, :], 0.0).then_inc(zero_set, 1)


def ada_phase(nc, i, G):
    CH = MOD // BANK
    PIECES = 3
    with Phase(nc, f"ada{i}") as ph:
        part = ph.sb("partial_sums", [P, MOD])
        bias = ph.sb("bias", [1, MOD])
        part_loaded = [ph.sem(f"part_loaded{r}") for r in range(PIECES)]
        bias_loaded = ph.sem("bias_loaded")
        sum_done = ph.sem("sum_done")
        copied = ph.sem("copied")
        ps = G["ps"]
        block = ph.block()

        @block.sync
        def _(sp):
            for r in range(PIECES):
                cols = slice(r * MOD // PIECES, (r + 1) * MOD // PIECES)
                sp.dma_start(part[:, cols], G["mod_dram"][i, :, cols]).then_inc(part_loaded[r], 16)
                if r == 0:
                    sp.dma_start(bias[:, :], G["d"]["ada_b_2"][i:i + 1, :]).then_inc(bias_loaded, 16)

        @block.tensor
        def _(pe):
            pe.wait_ge(bias_loaded, 16)
            for c in range(CH):
                cols = slice(c * BANK, (c + 1) * BANK)
                pe.wait_ge(part_loaded[c * PIECES // CH], 16)
                if c >= 8:
                    pe.wait_ge(copied, c - 7)
                nc.tensor.matmul(ps[c % 8][:, :], G["c2"]["ones"], part[:, cols], start=True, stop=False)
                nc.tensor.matmul(ps[c % 8][:, :], G["c2"]["ones"][0:1, :], bias[:, cols], start=False, stop=True).then_inc(sum_done, 1)

        @block.scalar
        def _(act):
            for c in range(CH):
                act.wait_ge(sum_done, c + 1)
                nc.scalar.copy(G["mod"][:, c * BANK:(c + 1) * BANK], ps[c % 8][:, :]).then_inc(copied, 1)


def norm_mod_phase(nc, name, G, g_dram, shift, scale, XT=None, h_dram=None, following=None, room=None):
    with Phase(nc, name) as ph:
        gain = ph.sb("gain", [P, D])
        both = ph.sb("gain_scaled", [P, D])
        sq = ph.sb("squares", [P, D])
        ss = ph.sb("square_sum", [P, TT])
        std = ph.sb("std", [P, TT])
        rstd = ph.sb("rstd", [P, TT])
        part, h = room if room is not None else (ph.sb("scaled_rows", [P, TT, D]), ph.sb("rows", [P, TT, D]))
        loaded = ph.sem("loaded")
        squared = ph.sem("squared")
        std_done = ph.sem("std_done")
        gain_done = ph.sem("gain_done")
        inv_done = ph.sem("inv_done")
        scaled = ph.sem("scaled")
        shifted = ph.sem("shifted")
        turned = ph.sem("turned")
        copied = ph.sem("copied")
        stored = ph.sem("stored")
        ps, X = G["ps"], G["X"]
        split = Split(nc, ph, G, turned, lambda t, j: ps[2 * t + j])
        block = ph.block()

        @block.sync
        def _(sp):
            sp.dma_start(gain[:, :], row_of(g_dram, D)).then_inc(loaded, 16)
            if following is not None:
                following.load(sp, Weights.RING)
            if h_dram is not None:
                for t in range(TT):
                    sp.wait_ge(shifted, t + 1)
                    sp.dma_start(h_dram[t * P:(t + 1) * P, :], h[:, t, :]).then_inc(stored, 16)
                sp.wait_ge(stored, 16 * TT)

        @block.scalar
        def _(act):
            for t in range(TT):
                if t:
                    act.wait_ge(squared, t)
                nc.scalar.activation(sq[:, :], X[:, t, :], ACT.Square, accum_out=ss[:, t:t + 1]).then_inc(squared, 1)
            act.wait_ge(squared, TT)
            nc.scalar.activation(std[:, :], ss[:, :], ACT.Sqrt, scale=1.0 / D, bias=G["eps_norm"][:, :]).then_inc(std_done, 1)
            if XT is None:
                split.high_parts(act)
                return
            for t in range(TT):
                for j in range(2):
                    act.wait_ge(turned, 2 * t + j + 1)
                    nc.scalar.copy(XT[:, 4 * j:4 * j + 4, t * P:(t + 1) * P],
                                   ps[2 * t + j][:, :].rearrange("p (k n) -> p k n", k=4)).then_inc(copied, 1)

        @block.vector
        def _(dve):
            dve.wait_ge(loaded, 16)
            nc.vector.scalar_tensor_tensor(both[:, :], scale, 1.0, gain[:, :], ALU.add, ALU.mult).then_inc(gain_done, 1)
            dve.wait_ge(std_done, 1)
            nc.vector.reciprocal(rstd[:, :], std[:, :]).then_inc(inv_done, 1)
            dve.wait_ge(inv_done, 1)
            dve.wait_ge(gain_done, 1)
            for t in range(TT):
                nc.vector.scalar_tensor_tensor(part[:, t, :], X[:, t, :], rstd[:, t:t + 1], both[:, :], ALU.mult, ALU.mult
                                               ).then_inc(scaled, 1)
            if XT is None:
                for t in range(TT):
                    split.low_parts(dve, t)

        @block.gpsimd
        def _(pool):
            for t in range(TT):
                pool.wait_ge(scaled, t + 1)
                nc.gpsimd.tensor_tensor(h[:, t, :], part[:, t, :], shift, ALU.add).then_inc(shifted, 1)

        @block.tensor
        def _(pe):
            for t in range(TT):
                pe.wait_ge(shifted, t + 1)
                for j in range(2):
                    for n in range(4):
                        k = 4 * j + n
                        last = nc.tensor.transpose(ps[2 * t + j][:, n * P:(n + 1) * P], h[:, t, k * P:(k + 1) * P], G["ident"])
                    last.then_inc(turned, 1)


GATE_B, GATE_C, X_A, VAL_B, GLU = range(5)
CONV_ORDER = [GLU, VAL_B, GATE_C, X_A, GATE_B]


def conv_weights(nc, G):
    w = lambda r0, r1, c0, c1: G["d"]["ab_w_in_2"][0, r0:r1, c0:c1].rearrange("(k p) n -> p k n", p=P)
    return Weights(nc, G, "conv_mix", [s for part in CONV_ORDER for s in k_slots(w, part * A_W, A_W)])


def conv_mix_phase(nc, G, weights, following):
    order = CONV_ORDER
    SLOTS = 2
    KS = KD // SLOTS
    FIRST_TAPS = 17
    jobs = [(c, m) for c in range(5) for m in range(4)]
    BANKS = 6
    ROWS = 4 * CONV_B
    PAD_A, PAD_B = CONV_A - 1, CONV_B - 1
    with Phase(nc, "conv_mix") as ph:
        ph.sems += weights.sems
        ta_rows = ph.sb("taps_a_rows", [4 * CONV_A, P])
        tb_rows = ph.sb("taps_b_rows", [ROWS, P])
        vec_rows = ph.sb("vector_rows", [12, P])
        taps_a = ph.sb("taps_a", [P, 4 * CONV_A])
        taps_b = ph.sb("taps_b", [P, ROWS])
        vecs = ph.sb("vectors", [P, 12])
        mean_w = ph.sb("mean_weights", [P, P])
        glu = ph.sb("glu", [P, 4, SEQ])
        gc = ph.sb("gate_c", [P, 4, SEQ])
        ub = ph.sb("u_b", [P, 4, PAD_B + SEQ])
        pa = ph.sb("p_a", [P, 4, PAD_A + SEQ])
        ca = ph.sb("conv_a", [P, 4, SEQ])
        cb = ph.sb("conv_b", [P, 4, SEQ])
        sq = ph.sb("squares", [P, 4, SEQ])
        std = ph.sb("std", [P, SEQ])
        rstd = ph.sb("rstd", [P, SEQ])
        rows_loaded = ph.sem("rows_loaded")
        rows_turned = ph.sem("rows_turned")
        rows_copied = ph.sem("rows_copied")
        mix_high = ph.sem("mix_high")
        mix_low = ph.sem("mix_low")
        pads_set = ph.sem("pads_set")
        product_done = ph.sem("product_done")
        by_act = ph.sem("evacuated_by_act")
        by_dve = ph.sem("evacuated_by_dve")
        a_step = ph.sem("a_step")
        b_step = ph.sem("b_step")
        b_conv_done = ph.sem("b_conv_done")
        mean_done = ph.sem("mean_done")
        centred = ph.sem("centred")
        squared = ph.sem("squared")
        var_done = ph.sem("var_done")
        std_done = ph.sem("std_done")
        inv_done = ph.sem("inv_done")
        normed = ph.sem("normed")
        out_done = ph.sem("out_done")
        ps, XH, XL, ident = G["ps"], G["XH"], G["XL"], G["ident"]
        mixed = [glu[:, m, :] for m in range(4)] + [gc[:, m, :] for m in range(4)]
        last_user = lambda s: (product_done, 4 * (s // SLOTS + 1)) if s % SLOTS == SLOTS - 1 else (weights.used, s // SLOTS + 1)
        reader = ["act" if order[c] in (GLU, GATE_C) else "dve" for c, _ in jobs]
        count = {"act": 0, "dve": 0}
        freed = []
        for r in reader:
            count[r] += 1
            freed.append(count[r])
        block = ph.block()

        @block.sync
        def _(sp):
            sp.dma_start(ta_rows[:, :], G["d"]["ab_conv_a_2"][0].rearrange("w (m p) -> (w m) p", p=P)).then_inc(rows_loaded, 16)
            sp.dma_start(tb_rows[:, :], G["d"]["ab_conv_b_2"][0].rearrange("w (m p) -> (w m) p", p=P)).then_inc(rows_loaded, 16)
            for v, name in enumerate(("ab_conv_b_bias_2", "ab_ln_g_2", "ab_ln_b_2")):
                sp.dma_start(vec_rows[4 * v:4 * v + 4, :], G["d"][name][0:1, :].rearrange("o (m p) -> (o m) p", p=P)
                             ).then_inc(rows_loaded, 16)
            weights.load(sp)
            weights.then_prefetch(sp, following)

        @block.tensor
        def _(pe):
            pe.wait_ge(rows_loaded, 80)
            nc.tensor.transpose(ps[7][:, 0:ROWS], tb_rows[:, :], ident[0:ROWS, 0:ROWS])
            nc.tensor.transpose(ps[7][:, 128:128 + 12], ta_rows[:, :], ident[0:12, 0:12])
            nc.tensor.transpose(ps[7][:, 256:256 + 12], vec_rows[:, :], ident[0:12, 0:12]).then_inc(rows_turned, 1)
            for sl in range(SLOTS * len(order)):
                c, half = sl // SLOTS, sl % SLOTS
                pe.wait_ge(weights.split, sl + 1)
                for m in range(4):
                    i = 4 * c + m
                    if half == 0 and i >= BANKS:
                        j = i - BANKS
                        pe.wait_ge(by_act if reader[j] == "act" else by_dve, freed[j])
                    for kk in range(KS):
                        k = half * KS + kk
                        last = split_product(nc, ps[i % BANKS][:, :], weights.parts(sl, kk * A_W + m * P, P),
                                             (XH[:, k, :], XL[:, k, :]), k == 0, k == KD - 1)
                    if half == SLOTS - 1:
                        last.then_inc(product_done, 1)
                if half < SLOTS - 1:
                    last.then_inc(weights.used, 1)
            pe.wait_ge(by_dve, count["dve"])
            for m in range(4):
                pe.wait_ge(b_conv_done, m + 1)
                last = nc.tensor.matmul(ps[6][:, :], mean_w[:, :], cb[:, m, :], start=(m == 0), stop=(m == 3))
            last.then_inc(mean_done, 1)
            for m in range(4):
                pe.wait_ge(squared, m + 1)
                last = nc.tensor.matmul(ps[7][:, :], mean_w[:, :], sq[:, m, :], start=(m == 0), stop=(m == 3))
            last.then_inc(var_done, 1)

        @block.scalar
        def _(act):
            act.wait_ge(rows_turned, 1)
            nc.scalar.copy(taps_b[:, :], ps[7][:, 0:ROWS]).then_inc(rows_copied, 1)
            nc.scalar.copy(taps_a[:, :], ps[7][:, 128:140]).then_inc(rows_copied, 1)
            nc.scalar.copy(vecs[:, :], ps[7][:, 256:268]).then_inc(rows_copied, 1)
            for sl in range(SLOTS * len(order)):
                weights.split_high(act, sl, last_user)
                for i, (c, m) in enumerate(jobs):
                    if sl != SLOTS * c + SLOTS or reader[i] != "act":
                        continue
                    act.wait_ge(product_done, i + 1)
                    if order[c] == GLU:
                        nc.scalar.activation(glu[:, m, :], ps[i % BANKS][:, :], ACT.Sigmoid).then_inc(by_act, 1)
                    else:
                        nc.scalar.copy(gc[:, m, :], ps[i % BANKS][:, :]).then_inc(by_act, 1)
            for m in range(4):
                act.wait_ge(centred, m + 1)
                nc.scalar.activation(sq[:, m, :], cb[:, m, :], ACT.Square).then_inc(squared, 1)
            act.wait_ge(var_done, 1)
            nc.scalar.activation(std[:, :], ps[7][:, :], ACT.Sqrt, bias=G["eps_norm"][:, :]).then_inc(std_done, 1)
            act.wait_ge(rows_copied, 3)
            for m in range(4):
                act.wait_ge(normed, m + 1)
                nc.scalar.activation(mixed[4 + m], cb[:, m, :], ACT.Silu, scale=vecs[:, 4 + m:5 + m], bias=vecs[:, 8 + m:9 + m]
                                     ).then_inc(out_done, 1)

        @block.gpsimd
        def _(pool):
            nc.gpsimd.memset(ub[:, :, 0:PAD_B], 0.0).then_inc(pads_set, 1)
            nc.gpsimd.memset(pa[:, :, 0:PAD_A], 0.0).then_inc(pads_set, 1)
            nc.gpsimd.memset(mean_w[:, :], 1.0 / A_W).then_inc(pads_set, 1)
            for sl in range(SLOTS * len(order)):
                weights.split_low(pool, sl)
            for m in range(8):
                pool.wait_ge(mix_high, m + 1)
                nc.gpsimd.tensor_tensor(rounded(XL[:, m, :]), mixed[m], XH[:, m, :], ALU.subtract).then_inc(mix_low, 1)

        @block.vector
        def _(dve):
            achain, bchain = Chain(dve, a_step), Chain(dve, b_step)
            dve.wait_ge(rows_copied, 3)
            dve.wait_ge(pads_set, 3)
            evac = 0

            def conv_b(m, first, last_tap):
                for w in range(first, last_tap):
                    tap = taps_b[:, 4 * w + m:4 * w + m + 1]
                    if w == 0:
                        bchain.link(nc.vector.tensor_scalar(cb[:, m, :], ub[:, m, 0:SEQ], tap, vecs[:, m:m + 1], ALU.mult, ALU.add))
                    else:
                        ins = nc.vector.scalar_tensor_tensor(cb[:, m, :], ub[:, m, w:w + SEQ], tap, cb[:, m, :], ALU.mult, ALU.add)
                        if w == CONV_B - 1:
                            ins.then_inc(b_conv_done, 1)
                        else:
                            bchain.link(ins)

            for i, (c, m) in enumerate(jobs):
                if reader[i] == "act":
                    continue
                evac += 1
                dve.wait_ge(product_done, i + 1)
                if order[c] == VAL_B:
                    dve.wait_ge(by_act, m + 1)
                    nc.vector.tensor_tensor(ub[:, m, PAD_B:], ps[i % BANKS][:, :], glu[:, m, :], ALU.mult).then_inc(by_dve, 1)
                    dve.wait_ge(by_dve, evac)
                    conv_b(m, 0, FIRST_TAPS)
                elif order[c] == X_A:
                    dve.wait_ge(by_act, 4 + m + 1)
                    nc.vector.tensor_tensor(pa[:, m, PAD_A:], ps[i % BANKS][:, :], gc[:, m, :], ALU.mult).then_inc(by_dve, 1)
                    dve.wait_ge(by_dve, evac)
                    achain.link(nc.vector.tensor_scalar(ca[:, m, :], pa[:, m, 0:SEQ], taps_a[:, m:m + 1], None, ALU.mult))
                    for w in range(1, CONV_A):
                        achain.link(nc.vector.scalar_tensor_tensor(ca[:, m, :], pa[:, m, w:w + SEQ],
                                                                   taps_a[:, 4 * w + m:4 * w + m + 1], ca[:, m, :],
                                                                   ALU.mult, ALU.add))
                    conv_b(m, FIRST_TAPS, CONV_B)
                else:
                    nc.vector.tensor_tensor(mixed[m], ps[i % BANKS][:, :], ca[:, m, :], ALU.mult).then_inc(by_dve, 1)
            dve.wait_ge(by_dve, count["dve"])
            for m in range(4):
                nc.vector.tensor_copy(rounded(XH[:, m, :]), mixed[m]).then_inc(mix_high, 1)
            dve.wait_ge(mean_done, 1)
            for m in range(4):
                nc.vector.tensor_tensor(cb[:, m, :], cb[:, m, :], ps[6][:, :], ALU.subtract).then_inc(centred, 1)
            dve.wait_ge(std_done, 1)
            nc.vector.reciprocal(rstd[:, :], std[:, :]).then_inc(inv_done, 1)
            dve.wait_ge(inv_done, 1)
            dve.wait_ge(squared, 4)
            for m in range(4):
                nc.vector.tensor_tensor(cb[:, m, :], cb[:, m, :], rstd[:, :], ALU.mult).then_inc(normed, 1)
            for m in range(4):
                dve.wait_ge(out_done, m + 1)
                nc.vector.tensor_copy(rounded(XH[:, 4 + m, :]), mixed[4 + m]).then_inc(mix_high, 1)


def gated_residual_phase(nc, name, G, weights, gate, part=None):
    with Phase(nc, name) as ph:
        ph.sems += weights.sems
        part = part if part is not None else ph.sb("gated", [P, 4, BANK])
        product_done = ph.sem("product_done")
        gated = ph.sem("gated_done")
        added = ph.sem("added")
        ps, X, XH, XL = G["ps"], G["X"], G["XH"], G["XL"]
        block = ph.block()

        @block.sync
        def _(sp):
            weights.load(sp)

        @block.tensor
        def _(pe):
            acts = lambda s, k, toks: (XH[:, ROW_TILES * s + k, toks], XL[:, ROW_TILES * s + k, toks])
            row_products(nc, pe, ps, weights, acts, None, product_done)

        @block.vector
        def _(dve):
            for s in range(len(weights.loads)):
                weights.split_slot(dve, s)
            for j in range(2 * TT):
                c = j % 2
                dve.wait_ge(product_done, j + 1)
                if j >= 4:
                    dve.wait_ge(added, j - 3)
                nc.vector.tensor_tensor(part[:, j % 4, :], ps[j][:, :], gate[:, c * BANK:(c + 1) * BANK], ALU.mult
                                        ).then_inc(gated, 1)

        @block.gpsimd
        def _(pool):
            for j in range(2 * TT):
                t, c = j // 2, j % 2
                pool.wait_ge(gated, j + 1)
                xs = X[:, t, c * BANK:(c + 1) * BANK]
                nc.gpsimd.tensor_tensor(xs, xs, part[:, j % 4, :], ALU.add).then_inc(added, 1)


def router_phase(nc, i, G, XT):
    LG = GROUPS + EXPERTS
    with Phase(nc, f"router{i}") as ph:
        wr = ph.sb("w_router", [P, KD, LG])
        br = ph.sb("b_router", [P, LG])
        L = ph.sb("logits", [P, TT, LG])
        small = lambda name, n=1: ph.sb(name, [P, TT, n])
        gmax, gexp, gsum, ptop = small("gmax"), small("gexp", GROUPS), small("gsum"), small("ptop")
        geq, gval, gidx, goh, gpen = (small("geq", GROUPS), small("gval", GROUPS), small("gidx"), small("goh", GROUPS),
                                      small("gpen", GROUPS))
        fine, fine2 = small("fine", EXPERTS), small("fine2", EXPERTS)
        top = [small("top0"), small("top1")]
        eq, val = small("eq", EXPERTS), small("val", EXPERTS)
        idx = [small("idx0"), small("idx1")]
        oh = [small("oh0", EXPERTS), small("oh1", EXPERTS)]
        both = small("both", EXPERTS)
        diff, dexp, dsum, dinv = small("diff"), small("dexp"), small("dsum"), small("dinv")
        rank = small("rank", EXPERTS)
        cnt = ph.sb("count", [P, EXPERTS])
        more = ph.sb("more", [P, 3, EXPERTS])
        spare = ph.sb("spare", [P, EXPERTS])
        spare_end = ph.sb("spare_end", [P, EXPERTS])
        spare_start = ph.sb("spare_start", [P, EXPERTS])
        ends_at = ph.sb("ends_at", [P, SPARE, EXPERTS])
        spare_exp = ph.sb("spare_expert", [P, SPARE])
        prod = small("prod", EXPERTS)
        r, b, blk, first, tmp, blkno, local = (small("r"), small("b"), small("blk"), small("first"), small("tmp"),
                                               small("blkno"), small("local"))
        place, yrow = small("place"), small("yrow")
        place_i = [ph.sb(f"place_i{k}", [P, TT], I32) for k in range(TOP_E)]
        tok = ph.sb("token_id", [P, TT], I32)
        zero = ph.sb("zero", [P, BLOCKS], I32)
        loaded = ph.sem("loaded")
        zero_set = ph.sem("zero_set")
        cleared = ph.sem("cleared")
        logits_done = ph.sem("logits_done")
        logits_read = ph.sem("logits_read")
        dve_step = ph.sem("dve_step")
        gmax_done = ph.sem("gmax_done")
        gexp_done = ph.sem("gexp_done")
        diff_done = ph.sem("diff_done")
        dexp_done = ph.sem("dexp_done")
        chosen = ph.sem("chosen")
        ranked = ph.sem("ranked")
        placed = ph.sem("placed")
        scattered = ph.sem("scattered")
        read_back = ph.sem("read_back")
        ps, c2 = G["ps"], G["c2"]
        spread = lambda a, n: a.to_broadcast([P, TT, n])
        rows = lambda a, n: a.rearrange("p (o n) -> p o n", o=1).to_broadcast([P, TT, n])
        block = ph.block()

        @block.sync
        def _(sp):
            sp.dma_start(wr[:, :, 0:GROUPS], G["d"]["moe_wr_g_2"][i].rearrange("(k p) n -> p k n", p=P)).then_inc(loaded, 16)
            sp.dma_start(wr[:, :, GROUPS:LG], G["d"]["moe_wr_e_2"][i].rearrange("(k p) n -> p k n", p=P)).then_inc(loaded, 16)
            sp.dma_start(br[:, 0:GROUPS], row_of(G["d"]["moe_br_g_2"][i:i + 1, :], GROUPS)).then_inc(loaded, 16)
            sp.dma_start(br[:, GROUPS:LG], row_of(G["d"]["moe_br_e_2"][i:i + 1, :], EXPERTS)).then_inc(loaded, 16)
            sp.wait_ge(zero_set, 1)
            sp.dma_start(G["slot_dram"][:, :].rearrange("(p b) o -> p (b o)", p=P), zero[:, :]).then_inc(cleared, 16)
            sp.wait_ge(scattered, 16 * TT * TOP_E)
            sp.dma_start(G["slot_token"][:, :], G["slot_dram"][:, :].rearrange("(p b) o -> p (b o)", p=P)).then_inc(read_back, 16)
            sp.wait_ge(read_back, 16)

        @block.tensor
        def _(pe):
            pe.wait_ge(loaded, 64)
            for t in range(TT):
                for k in range(KD):
                    last = nc.tensor.matmul(ps[t][:, 0:LG], XT[:, k, t * P:(t + 1) * P], wr[:, k, :], start=(k == 0),
                                            stop=(k == KD - 1))
                last.then_inc(logits_done, 1)
            pe.wait_ge(chosen, 1)
            for t in range(TT + 1):
                for s in range(min(t + 1, TT)):
                    last = nc.tensor.matmul(ps[4][:, t * EXPERTS:(t + 1) * EXPERTS], c2["before" if s == t else "ones"],
                                            both[:, s, :], start=(s == 0), stop=(s == min(t, TT - 1)))
            last.then_inc(ranked, 1)

        @block.scalar
        def _(act):
            act.wait_ge(gmax_done, 1)
            nc.scalar.activation(gexp[:, :, :], gval[:, :, :], ACT.Exp).then_inc(gexp_done, 1)
            act.wait_ge(diff_done, 1)
            nc.scalar.activation(dexp[:, :, :], diff[:, :, :], ACT.Exp).then_inc(dexp_done, 1)

        @block.gpsimd
        def _(pool):
            nc.gpsimd.memset(zero[:, :], 0).then_inc(zero_set, 1)
            pool.wait_ge(cleared, 16)
            for k in range(TOP_E):
                pool.wait_ge(placed, k + 1)
                for t in range(TT):
                    pool.indirect_dma_start(G["slot_dram"][:, :], bass.IndirectOffsetOnAxis(ap=place_i[k][:, t:t + 1], axis=0),
                                            tok[:, t:t + 1], None).then_inc(scattered, 16)

        @block.vector
        def _(dve):
            V = nc.vector
            link = Chain(dve, dve_step).link
            dve.wait_ge(loaded, 64)
            link(V.tensor_copy(tok[:, :], c2["token_id"]))
            for t in range(TT):
                dve.wait_ge(logits_done, t + 1)
                V.tensor_tensor(L[:, t, :], ps[t][:, 0:LG], br[:, :], ALU.add).then_inc(logits_read, 1)
            dve.wait_ge(logits_read, TT)
            lg = L[:, :, 0:GROUPS]
            link(V.tensor_reduce(gmax[:, :, :], lg, AX_X, ALU.max))
            V.tensor_tensor(gval[:, :, :], lg, spread(gmax[:, :, :], GROUPS), ALU.subtract).then_inc(gmax_done, 1)
            link(V.tensor_tensor(geq[:, :, :], lg, spread(gmax[:, :, :], GROUPS), ALU.is_equal))
            link(V.tensor_tensor(gpen[:, :, :], geq[:, :, :], rows(c2["index_e_less"][:, 0:GROUPS], GROUPS), ALU.mult))
            link(V.tensor_reduce(gidx[:, :, :], gpen[:, :, :], AX_X, ALU.min))
            link(V.tensor_tensor(goh[:, :, :], rows(c2["index_e_less"][:, 0:GROUPS], GROUPS), spread(gidx[:, :, :], GROUPS),
                                 ALU.is_equal))
            link(V.tensor_scalar(gpen[:, :, :], goh[:, :, :], 1.0, -NEG, ALU.subtract, ALU.mult))
            dve.wait_ge(gexp_done, 1)
            link(V.tensor_reduce(gsum[:, :, :], gexp[:, :, :], AX_X, ALU.add))
            link(V.reciprocal(ptop[:, :, :], gsum[:, :, :]))
            for t in range(TT):
                four = lambda a: a[:, t, :].rearrange("p (g o) -> p g o", o=1).to_broadcast([P, GROUPS, PER_GROUP])
                view = lambda a: a.rearrange("p (g e) -> p g e", g=GROUPS)
                link(V.tensor_tensor(view(fine2[:, t, :]), view(L[:, t, GROUPS:LG]), four(goh), ALU.mult))
                link(V.tensor_tensor(view(fine[:, t, :]), view(fine2[:, t, :]), four(gpen), ALU.add))
            for k in range(TOP_E):
                link(V.tensor_reduce(top[k][:, :, :], fine[:, :, :], AX_X, ALU.max))
                link(V.tensor_tensor(eq[:, :, :], fine[:, :, :], spread(top[k][:, :, :], EXPERTS), ALU.is_equal))
                link(V.tensor_tensor(val[:, :, :], eq[:, :, :], rows(c2["index_e_less"], EXPERTS), ALU.mult))
                link(V.tensor_reduce(idx[k][:, :, :], val[:, :, :], AX_X, ALU.min))
                link(V.tensor_tensor(oh[k][:, :, :], rows(c2["index_e_less"], EXPERTS), spread(idx[k][:, :, :], EXPERTS), ALU.is_equal))
                if k == 0:
                    link(V.scalar_tensor_tensor(fine[:, :, :], oh[0][:, :, :], 3.0 * NEG, fine[:, :, :], ALU.mult, ALU.add))
            V.tensor_tensor(both[:, :, :], oh[0][:, :, :], oh[1][:, :, :], ALU.add).then_inc(chosen, 1)
            V.tensor_tensor(diff[:, :, :], top[1][:, :, :], top[0][:, :, :], ALU.subtract).then_inc(diff_done, 1)
            dve.wait_ge(dexp_done, 1)
            link(V.tensor_scalar(dsum[:, :, :], dexp[:, :, :], 1.0, None, ALU.add))
            link(V.reciprocal(dinv[:, :, :], dsum[:, :, :]))
            link(V.tensor_tensor(G["gate"][:, 0, :], ptop[:, :, 0], dinv[:, :, 0], ALU.mult))
            link(V.tensor_tensor(G["gate"][:, 1, :], G["gate"][:, 0, :], dexp[:, :, 0], ALU.mult))
            dve.wait_ge(ranked, 1)
            link(V.tensor_copy(rank[:, :, :], ps[4][:, 0:TT * EXPERTS].rearrange("p (t e) -> p t e", t=TT)))
            link(V.tensor_copy(cnt[:, :], ps[4][:, TT * EXPERTS:(TT + 1) * EXPERTS]))
            for m in range(MAX_BLOCKS - 1):
                link(V.tensor_scalar(more[:, m, :], cnt[:, :], float((m + 1) * P), None, ALU.is_gt))
            link(V.tensor_tensor(spare[:, :], more[:, 0, :], more[:, 1, :], ALU.add))
            link(V.tensor_tensor(spare[:, :], spare[:, :], more[:, 2, :], ALU.add))
            link(V.tensor_tensor_scan(spare_end[:, :], c2["ones"][:, 0:EXPERTS], spare[:, :], 0.0, ALU.mult, ALU.add))
            link(V.tensor_tensor(spare_start[:, :], spare_end[:, :], spare[:, :], ALU.subtract))
            link(V.tensor_tensor(ends_at[:, :, :], spare_end[:, :].rearrange("p (o e) -> p o e", o=1).to_broadcast([P, SPARE, EXPERTS]),
                                 c2["index_spare"].rearrange("p (s o) -> p s o", o=1).to_broadcast([P, SPARE, EXPERTS]), ALU.is_le))
            link(V.tensor_reduce(spare_exp[:, :], ends_at[:, :, :], AX_X, ALU.add))
            link(V.tensor_scalar(spare_exp[:, :], spare_exp[:, :], float(EXPERTS - 1), None, ALU.min))
            link(V.tensor_copy(G["spare_table"][:, 0:SPARE], spare_exp[:, :]))
            link(V.tensor_copy(G["spare_table"][:, SPARE:SPARE + 1], spare_end[:, EXPERTS - 1:EXPERTS]))
            for k in range(TOP_E):
                link(V.tensor_tensor(prod[:, :, :], rank[:, :, :], oh[k][:, :, :], ALU.mult))
                link(V.tensor_reduce(r[:, :, :], prod[:, :, :], AX_X, ALU.add))
                link(V.tensor_tensor(prod[:, :, :], rows(spare_start[:, :], EXPERTS), oh[k][:, :, :], ALU.mult))
                link(V.tensor_reduce(b[:, :, :], prod[:, :, :], AX_X, ALU.add))
                link(V.tensor_scalar(blk[:, :, :], r[:, :, :], float(P), None, ALU.is_ge))
                for m in range(1, MAX_BLOCKS - 1):
                    link(V.scalar_tensor_tensor(blk[:, :, :], r[:, :, :], float((m + 1) * P), blk[:, :, :], ALU.is_ge, ALU.add))
                link(V.scalar_tensor_tensor(local[:, :, :], blk[:, :, :], -float(P), r[:, :, :], ALU.mult, ALU.add))
                link(V.tensor_scalar(first[:, :, :], blk[:, :, :], 0.0, None, ALU.is_equal))
                link(V.tensor_tensor(blkno[:, :, :], b[:, :, :], blk[:, :, :], ALU.add))
                link(V.tensor_scalar(blkno[:, :, :], blkno[:, :, :], float(EXPERTS - 1), None, ALU.add))
                link(V.scalar_tensor_tensor(tmp[:, :, :], idx[k][:, :, :], float(EXPERTS), blkno[:, :, :], ALU.add, ALU.subtract))
                link(V.tensor_tensor(tmp[:, :, :], tmp[:, :, :], first[:, :, :], ALU.mult))
                link(V.tensor_tensor(blkno[:, :, :], blkno[:, :, :], tmp[:, :, :], ALU.add))
                link(V.scalar_tensor_tensor(place[:, :, :], local[:, :, :], float(BLOCKS), blkno[:, :, :], ALU.mult, ALU.add))
                link(V.scalar_tensor_tensor(yrow[:, :, :], blkno[:, :, :], float(P), local[:, :, :], ALU.mult, ALU.add))
                link(V.tensor_copy(G["y_row"][k][:, :], yrow[:, :, 0]))
                V.tensor_copy(place_i[k][:, :], place[:, :, 0]).then_inc(placed, 1)


class Step:

    def __init__(self, odd, j=None):
        self.odd, self.j = odd, j
        self.parity = odd % 2

    def at(self, times, plus=0):
        here = times * self.odd + plus
        return here if self.j is None else self.j * (2 * times) + here

    def least(self):
        return self.odd if self.j is None else PEELED + self.odd


PEELED = 4


def expert_steps(eng, step):
    for e in range(PEELED):
        step(Step(e))
    with eng.Fori(PEELED // 2, EXPERTS // 2 - 1) as j:
        for odd in range(2):
            step(Step(odd, j))
    for e in range(EXPERTS - 2, EXPERTS + 1):
        step(Step(e))


def expert_phase(nc, i, G):
    UP, DOWN, PARTS = 4, 2, 3
    PLACES = UP + DOWN
    KU = KD // 2
    KDN = D_EXP // P // DOWN
    with Phase(nc, f"expert{i}") as ph:
        raw = ph.sb("w_raw", [P, PLACES, Weights.SLOT])
        high = ph.sb("w_high", [P, PARTS, Weights.SLOT])
        low = ph.sb("w_low", [P, PARTS, Weights.SLOT])
        xg = [ph.sb(f"x_rows{s}", [P, D]) for s in range(2)]
        xh = ph.sb("x_high", [P, 2, KD, P])
        xl = ph.sb("x_low", [P, 2, KD, P])
        sg = ph.sb("silu", [P, D_EXP])
        hid = ph.sb("hidden", [P, D_EXP])
        hh = ph.sb("hidden_high", [P, D_EXP // P, P])
        hl = ph.sb("hidden_low", [P, D_EXP // P, P])
        y = ph.sb("y", [P, 2, D])
        loaded = [ph.sem(f"w_loaded{r}") for r in range(PLACES)]
        w_high = ph.sem("w_high_done")
        w_split = ph.sem("w_split")
        used = ph.sem("w_used")
        rows_loaded = [ph.sem(f"rows_loaded{s}") for s in range(2)]
        rows_turned = ph.sem("rows_turned")
        x_high = ph.sem("x_high_done")
        x_low = ph.sem("x_low_done")
        silu_done = ph.sem("silu_done")
        hidden_done = ph.sem("hidden_done")
        hidden_turned = ph.sem("hidden_turned")
        hidden_high = ph.sem("hidden_high_done")
        hidden_low = ph.sem("hidden_low_done")
        y_by_act = ph.sem("y_by_act")
        y_by_dve = ph.sem("y_by_dve")
        stored = [ph.sem(f"stored{s}") for s in range(2)]
        ps, ident, d = G["ps"], G["ident"], G["d"]
        X_BANK, HIDDEN_BANK = 6, 7
        gate_bank = lambda parity, w: ps[2 * parity + w]
        down_bank = lambda c: ps[4 + c]
        block = ph.block()

        def slot(e, n):
            if e.j is None and e.odd == 0 and n < UP:
                return n, n, 1
            number = e.at(PLACES, n - DOWN)
            if e.j is None and e.odd == EXPERTS:
                return number, UP + n, EXPERTS
            if n < UP:
                return number, n, e.at(1, 1)
            if n < PLACES:
                return number, n, e.at(1)
            if e.j is None and e.odd == EXPERTS - 1:
                return number, UP + n - PLACES, EXPERTS
            return number, n - PLACES, e.at(1, 2)

        def part_of(e, n):
            return n % PARTS if e.j is None and e.odd == 0 and n < UP else (n + PLACES - DOWN) % PARTS

        @block.sync
        def _(sp):
            def load_up(e):
                w = "moe_w_gate_2", "moe_w_up_2"
                ex = bass.ds(e.at(1), 1)
                for r in range(UP):
                    if e.least() == 1:
                        sp.wait_ge(w_split, r + 1)
                    elif e.least() >= 2:
                        sp.wait_ge(w_split, e.at(PLACES, r - PLACES - 1))
                    k0 = r % 2 * KU * P
                    sp.dma_start(raw[:, r, :].rearrange("p (k n) -> p k n", k=KU),
                                 d[w[r // 2]][i, ex, k0:k0 + KU * P, :].rearrange("o (k p) n -> p (o k) n", p=P)
                                 ).then_inc(loaded[r], 16)

            def load_down(e):
                ex = bass.ds(e.at(1, -1), 1)
                for r in range(UP, PLACES):
                    if e.least() >= 2:
                        sp.wait_ge(w_split, e.at(PLACES, r - PLACES - 1))
                    k0 = (r - UP) * KDN * P
                    sp.dma_start(raw[:, r, :].rearrange("p (k n) -> p k n", k=KDN),
                                 d["moe_w_down_2"][i, ex, k0:k0 + KDN * P, :].rearrange("o (k p) n -> p (o k) n", p=P)
                                 ).then_inc(loaded[r], 16)

            def store(e):
                sp.wait_ge(y_by_act, e.at(1, -2))
                sp.wait_ge(y_by_dve, e.at(1, -2))
                par = (e.parity + 1) % 2
                sp.dma_start(G["y_dram"][bass.ds(e.at(P, -3 * P), P), :], y[:, par, :]).then_inc(stored[par], 16)

            def step(e):
                if e.least() >= 3:
                    store(e)
                if e.least() < EXPERTS:
                    load_up(e)
                if e.least() >= 1:
                    load_down(e)

            expert_steps(sp, step)
            store(Step(EXPERTS + 1))
            store(Step(EXPERTS + 2))
            for s in range(2):
                sp.wait_ge(stored[s], 16 * EXPERTS // 2)

        @block.gpsimd
        def _(pool):
            for e in range(EXPERTS):
                if e >= 2:
                    pool.wait_ge(rows_turned, 2 * (e - 1))
                pool.indirect_dma_start(xg[e % 2][:, :], None, G["h_dram"][:, :],
                                        bass.IndirectOffsetOnAxis(ap=G["slot_token"][:, e:e + 1], axis=0)
                                        ).then_inc(rows_loaded[e % 2], 16)

        @block.tensor
        def _(pe):
            def turn_rows(e, half, first):
                n = 0 if first else e.at(2, 2)
                par = 0 if first else (e.parity + 1) % 2
                if half == 0:
                    pe.wait_ge(rows_loaded[par], 16 if first or e.least() == 0 else 16 * ((e.odd + 1) // 2 + 1) if e.j is None
                               else e.j * 16 + 16 * ((e.odd + 1) // 2 + 1))
                if not first or half:
                    pe.wait_ge(x_low, n + half)
                for k in range(KU):
                    last = nc.tensor.transpose(ps[X_BANK][:, k * P:(k + 1) * P], xg[par][:, (KU * half + k) * P:(KU * half + k + 1) * P], ident)
                last.then_inc(rows_turned, 1)

            def turn_hidden(e):
                pe.wait_ge(hidden_done, e.at(1))
                if e.least() >= 2:
                    pe.wait_ge(hidden_low, e.at(1, -1))
                for k in range(D_EXP // P):
                    last = nc.tensor.transpose(ps[HIDDEN_BANK][:, k * P:(k + 1) * P], hid[:, k * P:(k + 1) * P], ident)
                last.then_inc(hidden_turned, 1)

            def up_slot(e, r):
                half = r % 2
                pe.wait_ge(w_split, slot(e, r)[0] + 1)
                if r < 2:
                    pe.wait_ge(x_low, e.at(2, half + 1))
                if half == 0 and e.least() >= 2:
                    pe.wait_ge(hidden_done, e.at(1, -1))
                for k in range(KU):
                    kk = half * KU + k
                    cols = slice(k * D_EXP, (k + 1) * D_EXP)
                    parts = [w[:, part_of(e, r), cols] for w in (high, low)]
                    last = split_product(nc, gate_bank(e.parity, r // 2)[:, :], [x[:, e.parity, kk, :] for x in (xh, xl)], parts,
                                         kk == 0, kk == KD - 1)
                last.then_inc(used, 1)

            def down_slot(e, n, r):
                pe.wait_ge(w_split, slot(e, n)[0] + 1)
                if r == 0:
                    pe.wait_ge(hidden_low, e.at(1))
                    if e.least() >= 2:
                        pe.wait_ge(y_by_act, e.at(1, -1))
                        pe.wait_ge(y_by_dve, e.at(1, -1))
                for c in range(2):
                    for k in range(KDN):
                        kk = r * KDN + k
                        cols = slice(k * D + c * BANK, k * D + (c + 1) * BANK)
                        last = split_product(nc, down_bank(c)[:, :], [x[:, kk, :] for x in (hh, hl)],
                                             [w[:, part_of(e, n), cols] for w in (high, low)], kk == 0, kk == D_EXP // P - 1)
                last.then_inc(used, 1)

            def step(e):
                if e.least() == EXPERTS:
                    turn_hidden(e)
                    for r in range(DOWN):
                        down_slot(e, r, r)
                    return
                for r in range(UP):
                    up_slot(e, r)
                    if r % 2 == 0 and not (e.j is None and e.odd == EXPERTS - 1):
                        turn_rows(e, r // 2, False)
                    if r == 1 and e.least() >= 1:
                        turn_hidden(e)
                if e.least() >= 1:
                    for r in range(DOWN):
                        down_slot(e, UP + r, r)

            for half in range(2):
                turn_rows(None, half, True)
            expert_steps(pe, step)

        def turns(e, weight, rows, hidden_parts, gate, down_rows):
            last_up = e.j is None and e.odd == EXPERTS - 1
            if e.least() == EXPERTS:
                hidden_parts(e)
                down_rows(e)
                return
            weight(e, 3)
            if not last_up:
                rows(e, 0)
            if e.least() >= 1:
                weight(e, 4)
                hidden_parts(e)
                weight(e, 5)
            if not last_up:
                rows(e, 1)
            weight(e, 6)
            gate(e)
            weight(e, 7)
            if not last_up:
                weight(e, 8)
            if e.least() >= 1:
                down_rows(e)

        @block.scalar
        def _(act):
            def weight(e, n):
                number, place, loads = slot(e, n)
                act.wait_ge(loaded[place], loads * 16)
                if not (e.j is None and e.odd == 0 and n < PARTS):
                    act.wait_ge(used, number - PARTS + 1)
                nc.scalar.copy(rounded(high[:, part_of(e, n), :]), raw[:, place, :]).then_inc(w_high, 1)

            def rows(e, half):
                n = 0 if e is None else e.at(2, 2)
                par = 0 if e is None else (e.parity + 1) % 2
                act.wait_ge(rows_turned, n + half + 1)
                nc.scalar.copy(rounded(xh[:, par, KU * half:KU * half + KU, :]), ps[X_BANK][:, :].rearrange("p (k n) -> p k n", k=KU)
                               ).then_inc(x_high, 1)

            def hidden_parts(e):
                act.wait_ge(hidden_turned, e.at(1))
                nc.scalar.copy(rounded(hh[:, :, :]), ps[HIDDEN_BANK][:, :].rearrange("p (k n) -> p k n", k=D_EXP // P)).then_inc(hidden_high, 1)

            def gate(e):
                act.wait_ge(used, slot(e, UP - 1)[0] + 1)
                if e.least() >= 1:
                    act.wait_ge(hidden_done, e.at(1))
                nc.scalar.activation(sg[:, :], gate_bank(e.parity, 0)[:, :], ACT.Silu).then_inc(silu_done, 1)

            def down_rows(e):
                par = (e.parity + 1) % 2
                act.wait_ge(used, EXPERTS * PLACES if e.least() == EXPERTS else e.at(PLACES, PLACES - DOWN))
                if e.least() >= 3:
                    act.wait_ge(stored[par], 16 * ((e.odd - 1) // 2) if e.j is None else e.j * 16 + 16 * ((e.odd - 1) // 2))
                nc.scalar.copy(y[:, par, 0:BANK], down_bank(0)[:, :]).then_inc(y_by_act, 1)

            for n in range(PARTS):
                weight(Step(0), n)
            for half in range(2):
                rows(None, half)
            expert_steps(act, lambda e: turns(e, weight, rows, hidden_parts, gate, down_rows))

        @block.vector
        def _(dve):
            def weight(e, n):
                number, place, _ = slot(e, n)
                dve.wait_ge(w_high, number + 1)
                nc.vector.tensor_tensor(rounded(low[:, part_of(e, n), :]), raw[:, place, :], high[:, part_of(e, n), :], ALU.subtract
                                        ).then_inc(w_split, 1)

            def rows(e, half):
                n = 0 if e is None else e.at(2, 2)
                par = 0 if e is None else (e.parity + 1) % 2
                at = slice(KU * half, KU * half + KU)
                dve.wait_ge(x_high, n + half + 1)
                nc.vector.tensor_tensor(rounded(xl[:, par, at, :]), ps[X_BANK][:, :].rearrange("p (k n) -> p k n", k=KU),
                                        xh[:, par, at, :], ALU.subtract).then_inc(x_low, 1)

            def hidden_parts(e):
                dve.wait_ge(hidden_high, e.at(1))
                nc.vector.tensor_tensor(rounded(hl[:, :, :]), ps[HIDDEN_BANK][:, :].rearrange("p (k n) -> p k n", k=D_EXP // P), hh[:, :, :],
                                        ALU.subtract).then_inc(hidden_low, 1)

            def gate(e):
                dve.wait_ge(silu_done, e.at(1, 1))
                if e.least() >= 1:
                    dve.wait_ge(hidden_turned, e.at(1))
                nc.vector.tensor_tensor(hid[:, :], sg[:, :], gate_bank(e.parity, 1)[:, :], ALU.mult).then_inc(hidden_done, 1)

            def down_rows(e):
                par = (e.parity + 1) % 2
                dve.wait_ge(used, EXPERTS * PLACES if e.least() == EXPERTS else e.at(PLACES, PLACES - DOWN))
                if e.least() >= 3:
                    dve.wait_ge(stored[par], 16 * ((e.odd - 1) // 2) if e.j is None else e.j * 16 + 16 * ((e.odd - 1) // 2))
                nc.vector.tensor_copy(y[:, par, BANK:D], down_bank(1)[:, :]).then_inc(y_by_dve, 1)

            for n in range(PARTS):
                weight(Step(0), n)
            for half in range(2):
                rows(None, half)
            expert_steps(dve, lambda e: turns(e, weight, rows, hidden_parts, gate, down_rows))


def spare_phase(nc, i, G):
    with ExitStack() as regs:
        table = G["spare_table"]
        used = nc.values_load(table[0:1, SPARE:SPARE + 1], min_val=0, max_val=SPARE)
        with nc.Fori(0, SPARE) as j:
            with nc.If(used > j):
                spare_block(nc, i, j, G)


def spare_block(nc, i, j, G):
    with Phase(nc, f"spare{i}") as ph:
        wg = ph.sb("w_gate", [P, KD, D_EXP])
        wu = ph.sb("w_up", [P, KD, D_EXP])
        wd = ph.sb("w_down", [P, D_EXP // P, D])
        col = ph.sb("slot_col", [P, 1], I32)
        xg = ph.sb("x_rows", [P, D])
        xgt = ph.sb("x_rows_t", [P, KD, P])
        sg = ph.sb("silu", [P, D_EXP])
        hid = ph.sb("hidden", [P, D_EXP])
        hidt = ph.sb("hidden_t", [P, D_EXP // P, P])
        y = ph.sb("y", [P, D])
        w_loaded = ph.sem("w_loaded")
        col_set = ph.sem("col_set")
        rows_loaded = ph.sem("rows_loaded")
        rows_turned = ph.sem("rows_turned")
        rows_copied = ph.sem("rows_copied")
        up_done = ph.sem("up_done")
        silu_done = ph.sem("silu_done")
        hidden_done = ph.sem("hidden_done")
        hidden_turned = ph.sem("hidden_turned")
        hidden_copied = ph.sem("hidden_copied")
        down_done = ph.sem("down_done")
        y_done = ph.sem("y_done")
        stored = ph.sem("stored")
        ps, ident, d = G["ps"], G["ident"], G["d"]
        block = ph.block()

        @block.sync
        def _(sp):
            e = sp.value_load(G["spare_table"][0:1, bass.ds(j, 1)], min_val=0, max_val=EXPERTS - 1)
            for w, name in ((wg, "moe_w_gate_2"), (wu, "moe_w_up_2"), (wd, "moe_w_down_2")):
                sp.dma_start(w[:, :, :], d[name][i, bass.ds(e, 1), :, :].rearrange("o (k p) n -> p (o k) n", p=P)
                             ).then_inc(w_loaded, 16)
            sp.wait_ge(y_done, 2)
            sp.dma_start(G["y_dram"][bass.ds(j * P + EXPERTS * P, P), :], y[:, :]).then_inc(stored, 16)
            sp.wait_ge(stored, 16)

        @block.gpsimd
        def _(pool):
            nc.gpsimd.tensor_copy(col[:, :], G["slot_token"][:, bass.ds(j + EXPERTS, 1)]).then_inc(col_set, 1)
            pool.wait_ge(col_set, 1)
            pool.indirect_dma_start(xg[:, :], None, G["h_dram"][:, :],
                                    bass.IndirectOffsetOnAxis(ap=col[:, 0:1], axis=0)).then_inc(rows_loaded, 16)

        @block.tensor
        def _(pe):
            pe.wait_ge(rows_loaded, 16)
            for k in range(KD):
                last = nc.tensor.transpose(ps[4 + k // 4][:, (k % 4) * P:(k % 4 + 1) * P], xg[:, k * P:(k + 1) * P], ident)
            last.then_inc(rows_turned, 1)
            pe.wait_ge(rows_copied, 2)
            pe.wait_ge(w_loaded, 48)
            for w, b in ((wg, 0), (wu, 1)):
                for k in range(KD):
                    last = nc.tensor.matmul(ps[b][:, :], xgt[:, k, :], w[:, k, :], start=(k == 0), stop=(k == KD - 1))
            last.then_inc(up_done, 1)
            pe.wait_ge(hidden_done, 1)
            for k in range(D_EXP // P):
                last = nc.tensor.transpose(ps[6][:, k * P:(k + 1) * P], hid[:, k * P:(k + 1) * P], ident)
            last.then_inc(hidden_turned, 1)
            pe.wait_ge(hidden_copied, 1)
            for c in range(2):
                for k in range(D_EXP // P):
                    last = nc.tensor.matmul(ps[2 + c][:, :], hidt[:, k, :], wd[:, k, c * BANK:(c + 1) * BANK], start=(k == 0),
                                            stop=(k == D_EXP // P - 1))
            last.then_inc(down_done, 1)

        @block.scalar
        def _(act):
            act.wait_ge(rows_turned, 1)
            for b in range(2):
                nc.scalar.copy(xgt[:, 4 * b:4 * b + 4, :], ps[4 + b][:, :].rearrange("p (k n) -> p k n", k=4)).then_inc(rows_copied, 1)
            act.wait_ge(up_done, 1)
            nc.scalar.activation(sg[:, :], ps[0][:, :], ACT.Silu).then_inc(silu_done, 1)
            act.wait_ge(down_done, 1)
            for c in range(2):
                nc.scalar.copy(y[:, c * BANK:(c + 1) * BANK], ps[2 + c][:, :]).then_inc(y_done, 1)

        @block.vector
        def _(dve):
            dve.wait_ge(silu_done, 1)
            nc.vector.tensor_tensor(hid[:, :], sg[:, :], ps[1][:, :], ALU.mult).then_inc(hidden_done, 1)
            dve.wait_ge(hidden_turned, 1)
            nc.vector.tensor_copy(hidt[:, :, :], ps[6][:, :].rearrange("p (k n) -> p k n", k=D_EXP // P)).then_inc(hidden_copied, 1)


def combine_phase(nc, i, G, gate_row):
    with Phase(nc, f"combine{i}") as ph:
        rows = [ph.sb(f"y_rows{k}", [P, TT, D]) for k in range(TOP_E)]
        gathered = [ph.sem(f"gathered{k}") for k in range(TOP_E)]
        scaled = ph.sem("scaled")
        summed = ph.sem("summed")
        gated = ph.sem("gated")
        added = ph.sem("added")
        X = G["X"]
        block = ph.block()

        @block.gpsimd
        def _(pool):
            for t in range(TT):
                for k in range(TOP_E):
                    pool.indirect_dma_start(rows[k][:, t, :], None, G["y_dram"][:, :],
                                            bass.IndirectOffsetOnAxis(ap=G["y_row"][k][:, t:t + 1], axis=0)).then_inc(gathered[k], 16)
            for t in range(TT):
                pool.wait_ge(summed, t + 1)
                nc.gpsimd.tensor_tensor(rows[1][:, t, :], rows[1][:, t, :], gate_row, ALU.mult).then_inc(gated, 1)

        @block.scalar
        def _(act):
            for t in range(TT):
                act.wait_ge(gathered[0], 16 * TT)
                nc.scalar.mul(rows[0][:, t, :], rows[0][:, t, :], G["gate"][:, 0, t:t + 1]).then_inc(scaled, 1)

        @block.vector
        def _(dve):
            dve.wait_ge(gathered[1], 16 * TT)
            for t in range(TT):
                dve.wait_ge(scaled, t + 1)
                nc.vector.scalar_tensor_tensor(rows[1][:, t, :], rows[1][:, t, :], G["gate"][:, 1, t:t + 1], rows[0][:, t, :],
                                               ALU.mult, ALU.add).then_inc(summed, 1)
            for t in range(TT):
                dve.wait_ge(gated, t + 1)
                nc.vector.tensor_tensor(X[:, t, :], X[:, t, :], rows[1][:, t, :], ALU.add).then_inc(added, 1)


def moe(nc, i, G):
    mod = lambda n: G["mod"][:, n * D:(n + 1) * D]
    with ExitStack() as ctx:
        XT = ctx.enter_context(nc.sbuf_tensor(f"x_features{i}", [P, KD, SEQ], F32))
        norm_mod_phase(nc, f"norm{i}b", G, G["d"]["norm_g_2"][i, 1:2, :], mod(3), mod(4), XT=XT, h_dram=G["h_dram"])
        router_phase(nc, i, G, XT)
    expert_phase(nc, i, G)
    spare_phase(nc, i, G)
    combine_phase(nc, i, G, mod(5))


def bias_phase(nc, G):
    BF16 = mybir.dt.bfloat16
    M = HEADS_ALL * TT
    PER = 4
    BANKS = 6
    with Phase(nc, "bias") as ph:
        pos_i = ph.sb("pos_i", [P, SEQ], I32)
        pos = ph.sb("pos", [P, SEQ])
        reach = ph.sb("reach", [P, P])
        table = ph.sb("table", [P, HEADS_ALL])
        below = ph.sb("table_below", [P, HEADS_ALL])
        step_t = ph.sb("table_steps", [P, HEADS_ALL])
        wide = ph.sb("steps_wide", [P, HEADS_ALL, TT])
        rest = ph.sb("steps_rest", [P, HEADS_ALL, TT])
        part = ph.sb("step_parts", [P, 3, HEADS_ALL, TT], BF16)
        hit = ph.sb("steps_reached", [P, 4, SEQ], BF16)
        out = ph.sb("bias_rows", [M, 2, PER, SEQ])
        loaded = ph.sem("loaded")
        zero_set = ph.sem("zero_set")
        below_loaded = ph.sem("below_loaded")
        dve_step = ph.sem("dve_step")
        parts_done = ph.sem("parts_done")
        hit_done = ph.sem("hit_done")
        summed = ph.sem("summed")
        copied = ph.sem("copied")
        stored = [ph.sem(f"stored{s}") for s in range(2)]
        ps, c2, d = G["ps"], G["c2"], G["d"]
        block = ph.block()

        @block.sync
        def _(sp):
            sp.dma_start(pos_i[:, :], row_of(d["positions_2"][0:1, :], SEQ)).then_inc(loaded, 16)
            sp.wait_ge(zero_set, 1)
            for t in range(TT):
                sp.dma_start(table[t * BUCKETS:(t + 1) * BUCKETS, :], d["rel_bias_2"][:, :]).then_inc(loaded, 16)
                sp.dma_start(below[t * BUCKETS + 1:(t + 1) * BUCKETS, :], d["rel_bias_2"][0:BUCKETS - 1, :]).then_inc(below_loaded, 16)
            for b in range(P // PER):
                sp.wait_ge(copied, PER * (b + 1))
                sp.dma_start(G["bias_dram"][:, b * PER:(b + 1) * PER, :], out[:, b % 2, :, :]).then_inc(stored[b % 2], 16)
            for s in range(2):
                sp.wait_ge(stored[s], 16 * (P // PER // 2))

        @block.vector
        def _(dve):
            V = nc.vector
            link = Chain(dve, dve_step).link
            V.memset(below[:, :], 0.0).then_inc(zero_set, 1)
            dve.wait_ge(loaded, 16 * (1 + TT))
            dve.wait_ge(below_loaded, 16 * TT)
            link(V.tensor_copy(pos[:, :], pos_i[:, :]))
            for t in range(TT):
                rows = slice(t * BUCKETS, (t + 1) * BUCKETS)
                link(V.tensor_scalar(reach[rows, :], pos[rows, t * P:(t + 1) * P], c2["bucket_start"][rows, :], None, ALU.subtract))
            link(V.tensor_tensor(step_t[:, :], table[:, :], below[:, :], ALU.subtract))
            link(V.tensor_tensor(wide[:, :, :], step_t[:, :].rearrange("p (h o) -> p h o", o=1).to_broadcast([P, HEADS_ALL, TT]),
                                 c2["tile_block"].rearrange("p (o t) -> p o t", o=1).to_broadcast([P, HEADS_ALL, TT]), ALU.mult))
            link(V.tensor_copy(part[:, 0, :, :], wide[:, :, :]))
            link(V.tensor_tensor(rest[:, :, :], wide[:, :, :], part[:, 0, :, :], ALU.subtract))
            link(V.tensor_copy(part[:, 1, :, :], rest[:, :, :]))
            link(V.tensor_tensor(rest[:, :, :], rest[:, :, :], part[:, 1, :, :], ALU.subtract))
            V.tensor_copy(part[:, 2, :, :], rest[:, :, :]).then_inc(parts_done, 1)
            for j in range(P):
                if j >= 4:
                    dve.wait_ge(summed, j - 3)
                V.tensor_scalar(hit[:, j % 4, :], pos[:, :], reach[:, j:j + 1], None, ALU.is_le).then_inc(hit_done, 1)

        @block.tensor
        def _(pe):
            pe.wait_ge(parts_done, 1)
            for j in range(P):
                pe.wait_ge(hit_done, j + 1)
                if j >= BANKS:
                    pe.wait_ge(copied, j - BANKS + 1)
                for n in range(3):
                    last = nc.tensor.matmul(ps[j % BANKS][0:M, :], part[:, n, :, :], hit[:, j % 4, :], start=(n == 0), stop=(n == 2))
                last.then_inc(summed, 1)

        @block.scalar
        def _(act):
            for j in range(P):
                b = j // PER
                act.wait_ge(summed, j + 1)
                if b >= 2:
                    act.wait_ge(stored[b % 2], 16 * (b // 2))
                nc.scalar.copy(out[:, b % 2, j % PER, :], ps[j % BANKS][0:M, :]).then_inc(copied, 1)


COL_QC, COL_KC, COL_VC, COL_QI = 0, 512, 1024, 1536
COL_KI = COL_QI + IDX_HEADS * IDX_DIM
COL_WI = COL_KI + IDX_DIM
COL_QD = COL_WI + IDX_HEADS
COL_KD, COL_VD = COL_QD + 512, COL_QD + 1024


ATTN_CHUNKS = [("QC", COL_QC, FM), ("KC", COL_KC, FM), ("VC", COL_VC, TM), ("QD", COL_QD, FM), ("KD", COL_KD, FM),
               ("VD", COL_VD, TM)]
K_AT = IDX_HEADS * IDX_DIM
W_AT = K_AT + P
FIRST_STEP = W_AT + IDX_HEADS


def attn_weights(nc, G):
    w = lambda r0, r1, c0, c1: G["d"]["cd_w_in_2"][0, r0:r1, c0:c1].rearrange("(k p) n -> p k n", p=P)
    pieces = [(0, COL_QI, COL_KI)] + [(K_AT + g * IDX_DIM, COL_KI, COL_WI) for g in range(4)] + [(W_AT, COL_WI, COL_QD)]
    n = KD // 2
    first = [[(at, n, FIRST_STEP, w(h * n * P, (h + 1) * n * P, c0, c1)) for at, c0, c1 in pieces] for h in range(2)]
    return Weights(nc, G, "attn_project", first + [s for _, col, _ in ATTN_CHUNKS for s in k_slots(w, col, BANK)])


def attn_project_phase(nc, G, S, weights):
    chunks = [[("QI", 0), ("QI", 1), ("KI", 0)] + [("WI", t) for t in range(TT)]]
    chunks += [[(name, m) for m in range(4)] for name, _, _ in ATTN_CHUNKS]
    N_FIRST = len(chunks[0])
    number = lambda c, n: n if c == 0 else N_FIRST + 4 * (c - 1) + n
    bank = lambda c, n: n if c or n < 3 else n + 1
    kinds = {name: kind for name, _, kind in ATTN_CHUNKS}
    SLOTS = 2
    KS = KD // SLOTS
    N_SLOTS = SLOTS * len(chunks)
    units = [(t, h) for t in range(TT) for h in range(IDX_HEADS)]
    PER_JOB = IDX_HEADS // 4
    index_tile = lambda s: (s - SLOTS) // 3 if s >= SLOTS and (s - SLOTS) % 3 == 0 and (s - SLOTS) // 3 < TT else None
    with Phase(nc, "attn_project") as ph:
        ph.sems += weights.sems
        qi = ph.sb("q_index", [P, 2, SEQ])
        ki = ph.sb("k_index", [P, SEQ])
        wi = ph.sb("w_index", [P, TT, IDX_HEADS])
        pos_i = ph.sb("pos_i", [P, SEQ], I32)
        pos = ph.sb("pos", [P, SEQ])
        posq_i = ph.sb("pos_q_i", [P, TT], I32)
        posq = ph.sb("pos_q", [P, TT])
        relu = S["VD"]
        score = ph.sb("score", [P, 2, SEQ])
        top8 = ph.sb("top8", [P, 8])
        pos_loaded = ph.sem("pos_loaded")
        product_done = ph.sem("product_done")
        evacuated = ph.sem("evacuated")
        index_done = ph.sem("index_done")
        relu_done = ph.sem("relu_done")
        weighted = ph.sem("weighted")
        dve_step = ph.sem("dve_step")
        ps, XH, XL, d = G["ps"], G["XH"], G["XL"], G["d"]
        last_user = lambda s: ((product_done, number(s // SLOTS, len(chunks[s // SLOTS]) - 1) + 1) if s % SLOTS == SLOTS - 1
                               else (weights.used, s // SLOTS + 1))
        block = ph.block()

        @block.sync
        def _(sp):
            weights.load(sp, Weights.RING)
            sp.dma_start(pos_i[:, :], row_of(d["positions_2"][0:1, :], SEQ)).then_inc(pos_loaded, 16)
            sp.dma_start(posq_i[:, :], d["positions_2"][0, :].rearrange("(t p) -> p t", p=P),
                         allow_slow_non_contiguous=True).then_inc(pos_loaded, 16)
            weights.load(sp)

        @block.tensor
        def _(pe):
            def index(u):
                t, h = units[u]
                r = IDX_DIM * (h % 4)
                pe.wait_ge(evacuated, N_FIRST)
                if u >= 4:
                    pe.wait_ge(relu_done, u - 3)
                nc.tensor.matmul(ps[4 + h % 4][:, :], qi[r:r + IDX_DIM, h // 4, t * P:(t + 1) * P], ki[r:r + IDX_DIM, :],
                                 start=True, stop=True, tile_position=(r, 0)).then_inc(index_done, 1)

            for s in range(N_SLOTS):
                c, half = s // SLOTS, s % SLOTS
                pe.wait_ge(weights.split, s + 1)
                for n, (name, m) in enumerate(chunks[c]):
                    if half == 0 and (c >= 2 or c == 1 and n < 3):
                        pe.wait_ge(evacuated, number(c, n) - 3 if c >= 2 else n + 1)
                    out = ps[bank(c, n)]
                    for kk in range(KS):
                        k = half * KS + kk
                        flags = (k == 0, k == KD - 1)
                        tok = [a[:, k, m * P:(m + 1) * P] for a in (XH, XL)]
                        features = [a[:, k, :] for a in (XH, XL)]
                        if name == "WI":
                            last = split_product(nc, out[:, 0:IDX_HEADS], tok, weights.parts(s, kk * FIRST_STEP + W_AT, IDX_HEADS), *flags)
                        elif name == "KI":
                            last = split_product(nc, out[:, :], weights.parts(s, kk * FIRST_STEP + K_AT, P), features, *flags)
                        elif kinds.get(name) == TM:
                            last = split_product(nc, out[:, :], tok, weights.parts(s, kk * BANK, BANK), *flags)
                        else:
                            last = split_product(nc, out[:, :], weights.parts(s, kk * (BANK if c else FIRST_STEP) + m * P, P), features, *flags)
                    if half == SLOTS - 1:
                        last.then_inc(product_done, 1)
                    elif n == len(chunks[c]) - 1:
                        last.then_inc(weights.used, 1)
                    if index_tile(s) is not None:
                        for h in range(PER_JOB * n, PER_JOB * (n + 1)):
                            index(index_tile(s) * IDX_HEADS + h)

        @block.scalar
        def _(act):
            def rectify(u):
                t, h = units[u]
                act.wait_ge(index_done, u + 1)
                if u >= 4:
                    act.wait_ge(weighted, u - 3)
                nc.scalar.activation(relu[:, u % 4, :], ps[4 + h % 4][:, :], ACT.Relu).then_inc(relu_done, 1)

            weights.split_high(act, 0, last_user)
            weights.split_high(act, 1, last_user)
            for s in range(N_SLOTS):
                c, half = s // SLOTS, s % SLOTS
                if index_tile(s) is not None:
                    for h in range(IDX_HEADS):
                        rectify(index_tile(s) * IDX_HEADS + h)
                if half == SLOTS - 1:
                    for n, (name, m) in enumerate(chunks[c]):
                        act.wait_ge(product_done, number(c, n) + 1)
                        if name == "WI":
                            nc.scalar.copy(wi[:, m, :], ps[bank(c, n)][:, 0:IDX_HEADS]).then_inc(evacuated, 1)
                            continue
                        if name == "VD":
                            act.wait_ge(weighted, len(units))
                        dest = {"QI": qi[:, m, :], "KI": ki[:, :]}[name] if c == 0 else S[name][:, m, :]
                        nc.scalar.copy(dest, ps[bank(c, n)][:, :]).then_inc(evacuated, 1)
                if s + 2 < N_SLOTS:
                    weights.split_high(act, s + 2, last_user)

        @block.gpsimd
        def _(pool):
            for s in range(N_SLOTS):
                weights.split_low(pool, s)

        @block.vector
        def _(dve):
            V = nc.vector
            link = Chain(dve, dve_step).link
            dve.wait_ge(pos_loaded, 32)
            link(V.tensor_copy(pos[:, :], pos_i[:, :]))
            link(V.tensor_copy(posq[:, :], posq_i[:, :]))
            for t in range(TT):
                link(V.tensor_scalar(S["causal"][:, t, :], pos[:, :], posq[:, t:t + 1], NEG, ALU.is_gt, ALU.mult))
            dve.wait_ge(evacuated, N_FIRST)
            for t in range(TT):
                s = score[:, t % 2, :]
                for h in range(IDX_HEADS):
                    u = t * IDX_HEADS + h
                    dve.wait_ge(relu_done, u + 1)
                    V.scalar_tensor_tensor(s, relu[:, u % 4, :], wi[:, t, h:h + 1], S["causal"][:, t, :] if h == 0 else s,
                                           ALU.mult, ALU.add).then_inc(weighted, 1)
                    dve.wait_ge(weighted, u + 1)
                for n in range(TOPK // 8):
                    link(V.max(top8[:, :], s))
                    link(V.match_replace(s, top8[:, :], s, DROPPED))
                link(V.tensor_scalar(s, s, DROPPED / 2, NEG, ALU.is_gt, ALU.mult))
                link(V.tensor_tensor(S["chosen"][:, t, :], s, S["causal"][:, t, :], ALU.add))


def chosen_attention_phase(nc, G, S):
    units = [(h, t) for h in range(HEADS_C) for t in range(TT)]
    N = len(units)
    SCORE_BANKS = (0, 1, 6)
    with Phase(nc, "chosen") as ph:
        bias = ph.sb("bias", [P, 4, SEQ])
        add = ph.sb("bias_masked", [P, 3, SEQ])
        SL = ph.sb("scores", [P, 3, SEQ])
        PR = ph.sb("probs", [P, 3, SEQ])
        PT = ph.sb("probs_t", [P, 2, TT, P])
        neg_max = ph.sb("neg_max", [P, N])
        row_sum = ph.sb("row_sum", [P, N])
        inv_sum = ph.sb("inv_sum", [P, N])
        bias_loaded = [ph.sem(f"bias_loaded{r}") for r in range(4)]
        masked = ph.sem("masked")
        scores_done = ph.sem("scores_done")
        biased = ph.sem("biased")
        max_done = ph.sem("max_done")
        exp_done = ph.sem("exp_done")
        turned = ph.sem("turned")
        turned_copied = ph.sem("turned_copied")
        mixed = ph.sem("mixed")
        inv_done = ph.sem("inv_done")
        out_done = ph.sem("out_done")
        ps, ident = G["ps"], G["ident"]
        block = ph.block()

        @block.sync
        def _(sp):
            for u, (h, t) in enumerate(units):
                if u >= 4:
                    sp.wait_ge(masked, u - 3)
                sp.dma_start(bias[:, u % 4, :], G["bias_dram"][h * TT + t, :, :]).then_inc(bias_loaded[u % 4], 16)

        @block.gpsimd
        def _(pool):
            for u, (h, t) in enumerate(units):
                pool.wait_ge(bias_loaded[u % 4], 16 * (u // 4 + 1))
                if u >= 3:
                    pool.wait_ge(biased, u - 2)
                nc.gpsimd.tensor_tensor(add[:, u % 3, :], bias[:, u % 4, :], S["chosen"][:, t, :], ALU.add).then_inc(masked, 1)

        @block.tensor
        def _(pe):
            def scores(u):
                h, t = units[u]
                r = HD_C * (h % 2)
                if u >= 3:
                    pe.wait_ge(biased, u - 2)
                nc.tensor.matmul(ps[SCORE_BANKS[u % 3]][:, :], S["QC"][r:r + HD_C, h // 2, t * P:(t + 1) * P], S["KC"][r:r + HD_C, h // 2, :],
                                 start=True, stop=True).then_inc(scores_done, 1)

            def turn(u):
                pe.wait_ge(exp_done, u + 1)
                if u >= 2:
                    pe.wait_ge(turned_copied, u - 1)
                for k in range(TT):
                    last = nc.tensor.transpose(ps[2 + u % 2][:, k * P:(k + 1) * P], PR[:, u % 3, k * P:(k + 1) * P], ident)
                last.then_inc(turned, 1)

            def mix(u):
                h, t = units[u]
                pe.wait_ge(turned_copied, u + 1)
                if u >= 2:
                    pe.wait_ge(out_done, u - 1)
                for k in range(TT):
                    last = nc.tensor.matmul(ps[4 + u % 2][:, 0:HD_C], PT[:, u % 2, k, :], S["VC"][:, k, h * HD_C:(h + 1) * HD_C],
                                            start=(k == 0), stop=(k == TT - 1))
                last.then_inc(mixed, 1)

            for i in range(N + 3):
                if i < N:
                    scores(i)
                if 2 <= i < N + 2:
                    turn(i - 2)
                if i >= 3:
                    mix(i - 3)

        @block.vector
        def _(dve):
            def finish(u):
                h, t = units[u]
                dve.wait_ge(exp_done, u + 1)
                nc.vector.reciprocal(inv_sum[:, u:u + 1], row_sum[:, u:u + 1]).then_inc(inv_done, 1)
                dve.wait_ge(inv_done, u + 1)
                dve.wait_ge(mixed, u + 1)
                nc.vector.tensor_scalar(S["Y"][:, t, h * HD_C:(h + 1) * HD_C], ps[4 + u % 2][:, 0:HD_C], inv_sum[:, u:u + 1], None,
                                        ALU.mult).then_inc(out_done, 1)

            for u in range(N):
                dve.wait_ge(scores_done, u + 1)
                dve.wait_ge(masked, u + 1)
                if u >= 3:
                    dve.wait_ge(exp_done, u - 2)
                nc.vector.scalar_tensor_tensor(SL[:, u % 3, :], ps[SCORE_BANKS[u % 3]][:, :], HD_C ** -0.5, add[:, u % 3, :], ALU.mult, ALU.add
                                               ).then_inc(biased, 1)
                dve.wait_ge(biased, u + 1)
                nc.vector.tensor_reduce(neg_max[:, u:u + 1], SL[:, u % 3, :], AX_X, ALU.max, negate=True).then_inc(max_done, 1)
                if u >= 3:
                    finish(u - 3)
            finish(N - 3)
            finish(N - 2)
            finish(N - 1)

        @block.scalar
        def _(act):
            def copy(u):
                act.wait_ge(turned, u + 1)
                if u >= 2:
                    act.wait_ge(mixed, u - 1)
                nc.scalar.copy(PT[:, u % 2, :, :], ps[2 + u % 2][:, :].rearrange("p (k n) -> p k n", n=P)).then_inc(turned_copied, 1)

            for u in range(N):
                act.wait_ge(max_done, u + 1)
                if u >= 3:
                    act.wait_ge(turned, u - 2)
                nc.scalar.activation(PR[:, u % 3, :], SL[:, u % 3, :], ACT.Exp, bias=neg_max[:, u:u + 1],
                                     accum_out=row_sum[:, u:u + 1]).then_inc(exp_done, 1)
                if u >= 2:
                    copy(u - 2)
            copy(N - 2)
            copy(N - 1)


def differential_phase(nc, G, S):
    units = [(h, t) for h in range(HEADS_D) for t in range(TT)]
    N = len(units)
    VW = 2 * HD_D
    with Phase(nc, "differential") as ph:
        bias = ph.sb("bias", [P, 4, SEQ])
        add = ph.sb("bias_masked", [P, 3, SEQ])
        SL = ph.sb("scores", [P, 3, 2, SEQ])
        PR = ph.sb("probs", [P, 4, 2, SEQ])
        second = ph.sb("second_part", [P, 2, SEQ])
        attn = ph.sb("attn", [P, 2, SEQ])
        PT = ph.sb("attn_t", [P, 2, TT, P])
        neg_max = ph.sb("neg_max", [P, N, 2])
        row_sum = ph.sb("row_sum", [P, N, 2])
        inv = ph.sb("inv_sum", [P, N, 2])
        coef = ph.sb("second_coef", [P, N])
        lam = ph.sb("lam", [P, 4, HD_D])
        lam_prod = ph.sb("lam_prod", [P, 2, HD_D])
        lam_sum = ph.sb("lam_sum", [P, 2])
        lam_exp = ph.sb("lam_exp", [P, 2])
        neg_lam = ph.sb("neg_lam", [P, 1])
        gain = ph.sb("gain", [P, VW])
        sq = ph.sb("squares", [P, VW])
        ss = ph.sb("square_sum", [P, N])
        std = ph.sb("std", [P, N])
        rstd = ph.sb("rstd", [P, N])
        bias_loaded = [ph.sem(f"bias_loaded{r}") for r in range(4)]
        lam_loaded = ph.sem("lam_loaded")
        lam_summed = ph.sem("lam_summed")
        lam_exp_done = ph.sem("lam_exp_done")
        dve_step = ph.sem("dve_step")
        masked = ph.sem("masked")
        scores_done = ph.sem("scores_done")
        biased = ph.sem("biased")
        max_done = ph.sem("max_done")
        exp_done = ph.sem("exp_done")
        coef_done = ph.sem("coef_done")
        second_done = ph.sem("second_done")
        attn_done = ph.sem("attn_done")
        turned = ph.sem("turned")
        turned_copied = ph.sem("turned_copied")
        mixed = ph.sem("mixed")
        out_done = ph.sem("out_done")
        squared = ph.sem("squared")
        std_done = ph.sem("std_done")
        normed = ph.sem("normed")
        ps, ident, d = G["ps"], G["ident"], G["d"]
        out = lambda u: S["Y"][:, units[u][1], 512 + units[u][0] * VW:512 + (units[u][0] + 1) * VW]
        block = ph.block()

        @block.sync
        def _(sp):
            sp.dma_start(lam[:, :, :], d["diff_lam_2"][0:1, :, :].to_broadcast([P, 4, HD_D])).then_inc(lam_loaded, 16)
            sp.dma_start(gain[:, :], row_of(d["diff_norm_g_2"][0:1, :], VW)).then_inc(lam_loaded, 16)
            for u, (h, t) in enumerate(units):
                if u >= 4:
                    sp.wait_ge(masked, u - 3)
                sp.dma_start(bias[:, u % 4, :], G["bias_dram"][(HEADS_C + h) * TT + t, :, :]).then_inc(bias_loaded[u % 4], 16)

        @block.gpsimd
        def _(pool):
            def scale_second(u):
                pool.wait_ge(coef_done, u + 1)
                if u >= 2:
                    pool.wait_ge(attn_done, u - 1)
                nc.gpsimd.tensor_scalar(second[:, u % 2, :], PR[:, u % 4, 1, :], coef[:, u:u + 1], None, ALU.mult).then_inc(second_done, 1)

            for u, (h, t) in enumerate(units):
                pool.wait_ge(bias_loaded[u % 4], 16 * (u // 4 + 1))
                if u >= 3:
                    pool.wait_ge(biased, 2 * (u - 2))
                nc.gpsimd.tensor_tensor(add[:, u % 3, :], bias[:, u % 4, :], S["causal"][:, t, :], ALU.add).then_inc(masked, 1)
                if u >= 2:
                    scale_second(u - 2)
            scale_second(N - 2)
            scale_second(N - 1)

        @block.tensor
        def _(pe):
            def scores(u):
                h, t = units[u]
                if u >= 2:
                    pe.wait_ge(biased, 2 * (u - 1))
                for m in range(2):
                    r = HD_D * m
                    last = nc.tensor.matmul(ps[2 * (u % 2) + m][:, :], S["QD"][r:r + HD_D, h, t * P:(t + 1) * P], S["KD"][r:r + HD_D, h, :],
                                            start=True, stop=True)
                last.then_inc(scores_done, 1)

            def turn(u):
                pe.wait_ge(attn_done, u + 1)
                if u >= 2:
                    pe.wait_ge(turned_copied, u - 1)
                for k in range(TT):
                    last = nc.tensor.transpose(ps[4 + u % 2][:, k * P:(k + 1) * P], attn[:, u % 2, k * P:(k + 1) * P], ident)
                last.then_inc(turned, 1)

            def mix(u):
                h, t = units[u]
                pe.wait_ge(turned_copied, u + 1)
                if u >= 2:
                    pe.wait_ge(out_done, u - 1)
                for k in range(TT):
                    last = nc.tensor.matmul(ps[6 + u % 2][:, 0:VW], PT[:, u % 2, k, :], S["VD"][:, k, h * VW:(h + 1) * VW],
                                            start=(k == 0), stop=(k == TT - 1))
                last.then_inc(mixed, 1)

            scores(0)
            for i in range(N + 3):
                if i + 1 < N:
                    scores(i + 1)
                if 2 <= i < N + 2:
                    turn(i - 2)
                if i >= 3:
                    mix(i - 3)

        @block.vector
        def _(dve):
            V = nc.vector
            link = Chain(dve, dve_step).link

            def weigh(u):
                dve.wait_ge(exp_done, 2 * u + 2)
                link(V.reciprocal(inv[:, u, :], row_sum[:, u, :]))
                V.tensor_tensor(coef[:, u:u + 1], inv[:, u, 1:2], neg_lam[:, :], ALU.mult).then_inc(coef_done, 1)

            def combine(u):
                dve.wait_ge(second_done, u + 1)
                if u >= 2:
                    dve.wait_ge(turned, u - 1)
                V.scalar_tensor_tensor(attn[:, u % 2, :], PR[:, u % 4, 0, :], inv[:, u, 0:1], second[:, u % 2, :], ALU.mult, ALU.add
                                       ).then_inc(attn_done, 1)

            dve.wait_ge(lam_loaded, 32)
            pairs = lam[:, :, :].rearrange("p (a b) e -> p a b e", b=2)
            link(V.tensor_tensor(lam_prod[:, :, :], pairs[:, :, 0, :], pairs[:, :, 1, :], ALU.mult))
            V.tensor_reduce(lam_sum[:, :], lam_prod[:, :, :], AX_X, ALU.add).then_inc(lam_summed, 1)
            link(V.tensor_scalar(gain[:, :], gain[:, :], 1.0 - LAMBDA_INIT, None, ALU.mult))
            dve.wait_ge(lam_exp_done, 1)
            link(V.tensor_tensor(neg_lam[:, :], lam_exp[:, 1:2], lam_exp[:, 0:1], ALU.subtract))
            link(V.tensor_scalar(neg_lam[:, :], neg_lam[:, :], LAMBDA_INIT, None, ALU.subtract))
            for u in range(N):
                dve.wait_ge(scores_done, u + 1)
                dve.wait_ge(masked, u + 1)
                for m in range(2):
                    if u >= 3:
                        dve.wait_ge(exp_done, 2 * (u - 3) + m + 1)
                    V.scalar_tensor_tensor(SL[:, u % 3, m, :], ps[2 * (u % 2) + m][:, :], HD_D ** -0.5, add[:, u % 3, :], ALU.mult, ALU.add
                                           ).then_inc(biased, 1)
                for m in range(2):
                    dve.wait_ge(biased, 2 * u + m + 1)
                    V.tensor_reduce(neg_max[:, u, m:m + 1], SL[:, u % 3, m, :], AX_X, ALU.max, negate=True).then_inc(max_done, 1)
                if u >= 1:
                    weigh(u - 1)
                if u >= 2:
                    combine(u - 2)
            weigh(N - 1)
            combine(N - 2)
            combine(N - 1)
            dve.wait_ge(std_done, 1)
            link(V.reciprocal(rstd[:, :], std[:, :]))
            for u in range(N):
                V.scalar_tensor_tensor(out(u), out(u), rstd[:, u:u + 1], gain[:, :], ALU.mult, ALU.mult).then_inc(normed, 1)

        @block.scalar
        def _(act):
            def copy(u):
                act.wait_ge(turned, u + 1)
                if u >= 2:
                    act.wait_ge(mixed, u - 1)
                nc.scalar.copy(PT[:, u % 2, :, :], ps[4 + u % 2][:, :].rearrange("p (k n) -> p k n", n=P)).then_inc(turned_copied, 1)

            def take(u):
                act.wait_ge(mixed, u + 1)
                nc.scalar.copy(out(u), ps[6 + u % 2][:, 0:VW]).then_inc(out_done, 1)
                act.wait_ge(out_done, u + 1)
                if u >= 1:
                    act.wait_ge(squared, u)
                nc.scalar.activation(sq[:, :], out(u), ACT.Square, accum_out=ss[:, u:u + 1]).then_inc(squared, 1)

            act.wait_ge(lam_summed, 1)
            nc.scalar.activation(lam_exp[:, :], lam_sum[:, :], ACT.Exp).then_inc(lam_exp_done, 1)
            for u in range(N):
                for m in range(2):
                    act.wait_ge(max_done, 2 * u + m + 1)
                    if u >= 4:
                        act.wait_ge(attn_done, u - 3)
                    nc.scalar.activation(PR[:, u % 4, m, :], SL[:, u % 3, m, :], ACT.Exp, bias=neg_max[:, u, m:m + 1],
                                         accum_out=row_sum[:, u, m:m + 1]).then_inc(exp_done, 1)
                if u >= 3:
                    copy(u - 3)
                if u >= 4:
                    take(u - 4)
            for u in range(N - 4, N):
                if u >= N - 3:
                    copy(u)
                take(u)
            act.wait_ge(squared, N)
            nc.scalar.activation(std[:, :], ss[:, :], ACT.Sqrt, scale=1.0 / VW, bias=G["eps_norm"][:, :]).then_inc(std_done, 1)


def turn_phase(nc, G, Y, following):
    with Phase(nc, "turn") as ph:
        turned = ph.sem("turned")
        ps = G["ps"]
        split = Split(nc, ph, G, turned, lambda t, j: ps[2 * t + j])
        block = ph.block()

        @block.sync
        def _(sp):
            following.load(sp, Weights.RING)

        @block.tensor
        def _(pe):
            for t in range(TT):
                for j in range(2):
                    for n in range(4):
                        k = 4 * j + n
                        last = nc.tensor.transpose(ps[2 * t + j][:, n * P:(n + 1) * P], Y[:, t, k * P:(k + 1) * P], G["ident"])
                    last.then_inc(turned, 1)

        @block.scalar
        def _(act):
            split.high_parts(act)

        @block.vector
        def _(dve):
            for t in range(TT):
                split.low_parts(dve, t)


def final_phase(nc, G):
    with Phase(nc, "final") as ph:
        gain = ph.sb("gain", [P, D])
        sq = ph.sb("squares", [P, D])
        ss = ph.sb("square_sum", [P, TT])
        std = ph.sb("std", [P, TT])
        rstd = ph.sb("rstd", [P, TT])
        out = ph.sb("out", [P, TT, D])
        loaded = ph.sem("loaded")
        squared = ph.sem("squared")
        std_done = ph.sem("std_done")
        inv_done = ph.sem("inv_done")
        scaled = ph.sem("scaled")
        stored = ph.sem("stored")
        X, d = G["X"], G["d"]
        block = ph.block()

        @block.sync
        def _(sp):
            sp.dma_start(gain[:, :], row_of(d["final_norm_g_2"].rearrange("(o n) -> o n", o=1), D)).then_inc(loaded, 16)
            for t in range(TT):
                sp.wait_ge(scaled, t + 1)
                sp.dma_start(d["out"][0, t * P:(t + 1) * P, :], out[:, t, :]).then_inc(stored, 16)
            sp.wait_ge(stored, 16 * TT)

        @block.scalar
        def _(act):
            for t in range(TT):
                if t:
                    act.wait_ge(squared, t)
                nc.scalar.activation(sq[:, :], X[:, t, :], ACT.Square, accum_out=ss[:, t:t + 1]).then_inc(squared, 1)
            act.wait_ge(squared, TT)
            nc.scalar.activation(std[:, :], ss[:, :], ACT.Sqrt, scale=1.0 / D, bias=G["eps_norm"][:, :]).then_inc(std_done, 1)

        @block.vector
        def _(dve):
            dve.wait_ge(std_done, 1)
            nc.vector.reciprocal(rstd[:, :], std[:, :]).then_inc(inv_done, 1)
            dve.wait_ge(inv_done, 1)
            dve.wait_ge(loaded, 16)
            for t in range(TT):
                nc.vector.scalar_tensor_tensor(out[:, t, :], X[:, t, :], rstd[:, t:t + 1], gain[:, :], ALU.mult, ALU.mult
                                               ).then_inc(scaled, 1)


def second_block(nc, G):
    d = G["d"]
    mod = lambda n: G["mod"][:, n * D:(n + 1) * D]
    second_load_phase(nc, G)
    bias_phase(nc, G)
    ada_phase(nc, 0, G)
    rows_of = lambda w: (lambda r0, r1: w[0, r0:r1, :].rearrange("(k p) n -> p k n", p=P))
    with ExitStack() as ctx:
        parts_room(nc, ctx, G, "conv")
        w_in = conv_weights(nc, G)
        norm_mod_phase(nc, "norm0a", G, d["norm_g_2"][0, 0:1, :], mod(0), mod(1), following=w_in)
        w_out = row_weights(nc, "conv_out", rows_of(d["ab_w_out_2"]), KD, G)
        conv_mix_phase(nc, G, w_in, w_out)
        gated_residual_phase(nc, "conv_out", G, w_out, mod(2))
    moe(nc, 0, G)
    ada_phase(nc, 1, G)
    with ExitStack() as ctx:
        sb = lambda name, shape: ctx.enter_context(nc.sbuf_tensor(name, shape, F32))
        names = ("QC", "KC", "VC", "QD", "KD", "VD", "causal", "chosen")
        room = sb("attn_room", [P, len(names), 4, SEQ])
        S = {n: room[:, j, :, :] for j, n in enumerate(names)}
        with ExitStack() as parts:
            parts_room(nc, parts, G, "attn")
            w_in = attn_weights(nc, G)
            rows = lambda j: room[:, j:j + 2, :, :].rearrange("p j m n -> p (j m n)").rearrange("p (t n) -> p t n", t=TT)
            norm_mod_phase(nc, "norm1a", G, d["norm_g_2"][1, 0:1, :], mod(0), mod(1), following=w_in, room=(rows(0), rows(2)))
            attn_project_phase(nc, G, S, w_in)
        S["Y"] = sb("attn_mixed", [P, TT, D])
        chosen_attention_phase(nc, G, S)
        differential_phase(nc, G, S)
        with ExitStack() as parts:
            parts_room(nc, parts, G, "attn_out")
            w_out = row_weights(nc, "attn_out", rows_of(d["cd_w_out_2"]), KD, G)
            turn_phase(nc, G, S["Y"], w_out)
            gated_residual_phase(nc, "attn_out", G, w_out, mod(2), part=S["QC"])
    moe(nc, 1, G)
    final_phase(nc, G)


def build(nc, d, parts, parts2):
    with ExitStack() as ctx:
        G = {"d": d}
        G["ps"] = [ctx.enter_context(nc.psum_tensor(f"bank{i}", [P, BANK], F32)) for i in range(8)]
        sb = lambda name, shape, dt=F32: ctx.enter_context(nc.sbuf_tensor(name, shape, dt))
        G["X"] = sb("x_tokens", [P, TT, D])
        G["ident"] = sb("ident", [P, P])[:, :]
        G["ones_col"] = sb("ones_col", [P, 1])
        G["cond"] = sb("cond", [P, KD])
        G["mod_dram"] = nc.dram_tensor("mod_partial_sums", [DEPTH, P, MOD], F32).ap()
        G["eps_ln"] = sb("eps_ln", [P, 1])
        G["eps_norm"] = sb("eps_norm", [P, 1])
        with ExitStack() as first:
            parts_room(nc, first, G, "first")
            load_phase(nc, G)
            first_block(nc, G, parts)
        G["consts2"] = sb("consts2", list(d["consts2"].shape))
        G["c2"] = views(G["consts2"], parts2)
        G["mod"] = sb("modulation", [P, 6 * D])
        G["slot_token"] = sb("slot_token", [P, BLOCKS], I32)
        G["gate"] = sb("gate", [P, TOP_E, TT])
        G["y_row"] = [sb(f"y_row{k}", [P, TT], I32) for k in range(TOP_E)]
        G["spare_table"] = sb("spare_table", [P, SPARE + 1], I32)
        G["h_dram"] = nc.dram_tensor("h_rows", [SEQ, D], F32).ap()
        G["y_dram"] = nc.dram_tensor("y_rows", [BLOCKS * P, D], F32).ap()
        G["slot_dram"] = nc.dram_tensor("slot_tokens", [P * BLOCKS, 1], I32).ap()
        G["bias_dram"] = nc.dram_tensor("bias_rows", [HEADS_ALL * TT, P, SEQ], F32).ap()
        second_block(nc, G)


_INS = ["x", "w_in", "w_alpha", "b_alpha", "mix_scale", "w_out", "ln1_g", "ln1_b", "w_up", "conv_w", "conv_b", "w_down",
        "ln2_g", "ln2_b", "c_2", "positions_2", "rel_bias_2", "norm_g_2", "final_norm_g_2", "ada_w_2", "ada_b_2",
        "ab_w_in_2", "ab_conv_a_2", "ab_conv_b_2", "ab_conv_b_bias_2", "ab_ln_g_2", "ab_ln_b_2", "ab_w_out_2",
        "cd_w_in_2", "diff_lam_2", "diff_norm_g_2", "cd_w_out_2", "moe_wr_g_2", "moe_br_g_2", "moe_wr_e_2",
        "moe_br_e_2", "moe_w_gate_2", "moe_w_up_2", "moe_w_down_2"]


def kernel(**inputs):
    import numpy as _np
    import concourse.bacc as _bacc
    from concourse import mybir as _mybir
    from concourse.bass_utils import run_bass_kernel_spmd as _run

    nc = _bacc.Bacc("TRN2", target_bir_lowering=False, num_devices=1)
    arrays, d = {}, {}
    parts, parts2 = constant_parts(), constant_parts_2()
    given = {name: inputs[name] for name in _INS}
    given["consts"] = _np.concatenate(list(parts.values()), axis=1)
    given["consts2"] = _np.concatenate(list(parts2.values()), axis=1)
    given["ident"] = _np.eye(P, dtype=_np.float32)
    for name, a in given.items():
        a = _np.ascontiguousarray(a)
        arrays[f"in_{name}_dram"] = a
        d[name] = nc.dram_tensor(f"in_{name}_dram", a.shape, _mybir.dt.from_np(a.dtype), kind="ExternalInput").ap()
    d["out"] = nc.dram_tensor("out_0_dram", (1, SEQ, D), F32, kind="ExternalOutput").ap()
    build(nc, d, parts, parts2)
    r = _run(nc, [arrays], core_ids=[0])
    return r.results[0]["out_0_dram"]
```

```python
from contextlib import ExitStack

import numpy as np
import concourse.bass as bass
from concourse import mybir

F32 = mybir.dt.float32
I32 = mybir.dt.int32
F32R = mybir.dt.float32r
ALU = mybir.AluOpType
ACT = mybir.ActivationFunctionType
AX_X = mybir.AxisListType.X

P = 128
SEQ = 512
D = 1024
DEPTH = 2
TT = SEQ // P
KD = D // P
BANK = 512

HEADS_A, HD_A = 8, 64
HEADS_R, QK_R = 4, 32
HEADS_G, QK_G = 4, 32
GLA_CHUNK = 64
N_CHUNKS = SEQ // GLA_CHUNK
LOW_RANK = 16
COL_QA, COL_KA, COL_VA = 0, 512, 1024
COL_QR, COL_VR, COL_QG, COL_VG, COL_AG = 1536, 1792, 2304, 2560, 3072
PROJ = COL_AG + LOW_RANK
D_FF = P * ((8 * D // 3 + P - 1) // P)
FT = D_FF // P
ALPHA = (2 * DEPTH) ** 0.25
LN_EPS = 1e-5
NORM_EPS = 1e-6
NEG = -1.0e30


def rope_pair(dim, rows):
    inv = np.float32(1.0) / (np.float32(10000.0) ** (np.arange(0, dim, 2, dtype=np.float32) / np.float32(dim)))
    ang = np.arange(SEQ, dtype=np.float32)[:, None] * inv[None, :]
    half = dim // 2
    r = np.arange(rows) % dim
    cos = np.cos(ang).T[r % half]
    sin = np.sin(ang).T[r % half] * np.where(r < half, -1.0, 1.0)[:, None]
    other = np.where(r < half, np.arange(rows) + half, np.arange(rows) - half)
    perm = np.zeros((rows, rows), np.float32)
    perm[other, np.arange(rows)] = 1.0
    return cos.astype(np.float32), sin.astype(np.float32), perm


def constant_parts():
    parts = {}
    parts["cos_a"], parts["sin_a"], parts["perm_a"] = rope_pair(HD_A, P)
    parts["cos_r"], parts["sin_r"], parts["perm_r"] = rope_pair(QK_R, P)
    q = np.arange(SEQ)[:, None]
    k = np.arange(SEQ)[None, :]
    d = q - k
    count = ((d >= 0) & (d <= 128)).astype(np.float64) + ((d >= 0) & (d % 4 == 0)) + ((d >= 0) & (d % 16 == 0))
    logc = np.where(count > 0, np.log(np.maximum(count, 1)), NEG).astype(np.float32)
    parts["log_count"] = logc.reshape(TT, P, SEQ).transpose(1, 0, 2).reshape(P, TT * SEQ)
    lg = np.log(np.float32(1.0) - np.float32(2.0) ** (np.float32(-5.0) - np.arange(HEADS_R, dtype=np.float32)))
    dist = np.arange(SEQ)[None, :] - np.arange(P)[:, None]
    dec = np.where(dist[:, None, :] >= 0, np.exp(lg.astype(np.float64)[None, :, None] * np.maximum(dist, 0)[:, None, :]), 0.0)
    parts["decay"] = (dec * QK_R ** -0.5).astype(np.float32).reshape(P, HEADS_R * SEQ)
    kk = np.arange(P)[:, None]
    qq = np.arange(P)[None, :]
    same = kk // GLA_CHUNK == qq // GLA_CHUNK
    parts["gla_causal"] = ((kk <= qq) & same).astype(np.float32)
    t = np.arange(SEQ)
    parts["chunk_keep"] = np.broadcast_to((t % GLA_CHUNK != 0).astype(np.float32), (P, SEQ))
    parts["even_chunk"] = np.broadcast_to((t // GLA_CHUNK % 2 == 0).astype(np.float32), (P, SEQ))
    parts["odd_chunk"] = np.broadcast_to((t // GLA_CHUNK % 2 == 1).astype(np.float32), (P, SEQ))
    parts["head_block"] = (np.arange(P)[:, None] // QK_G == np.arange(256)[None, :] // 64).astype(np.float32)
    return parts


class Phase:

    def __init__(self, nc, name):
        self.nc, self.name = nc, name
        self.stack = ExitStack()
        self.sems = []

    def sem(self, name):
        s = self.nc.alloc_semaphore(f"{self.name}_{name}")
        self.sems.append(s)
        return s

    def sb(self, name, shape, dt=F32):
        return self.stack.enter_context(self.nc.sbuf_tensor(f"{self.name}_{name}", shape, dt))

    def block(self):
        return self.stack.enter_context(self.nc.Block(no_gpsimd_drain=True))

    def __enter__(self):
        return self

    def __exit__(self, *failed):
        if failed[0] is None:
            self.stack.close()
            self.nc.clear_and_free_semaphores(self.sems)
            self.nc.all_engine_barrier(sem_only=True)


class Chain:

    def __init__(self, eng, sem):
        self.eng, self.sem, self.n = eng, sem, 0

    def link(self, ins):
        self.n += 1
        ins.then_inc(self.sem, 1)
        self.eng.wait_ge(self.sem, self.n)



def rounded(a):
    return a.bitcast(F32R)


def split_product(nc, out, st, mv, start, stop):
    nc.tensor.matmul(out, rounded(st[0]), rounded(mv[0]), start=start, stop=False)
    nc.tensor.matmul(out, rounded(st[0]), rounded(mv[1]), start=False, stop=False)
    return nc.tensor.matmul(out, rounded(st[1]), rounded(mv[0]), start=False, stop=stop)


class Weights:
    RING = 2
    SLOT = 2048

    def __init__(self, nc, G, name, loads):
        self.nc, self.G, self.loads = nc, G, loads
        sem = lambda n: nc.alloc_semaphore(f"{name}_{n}")
        self.loaded = [sem(f"w_loaded{r}") for r in range(self.RING)]
        self.high = sem("w_high")
        self.split = sem("w_split")
        self.used = sem("w_used")
        self.sems = self.loaded + [self.high, self.split, self.used]
        self.issued = 0

    def load(self, eng, upto=None):
        while self.issued < min(upto or len(self.loads), len(self.loads)):
            s = self.issued
            if s >= self.RING:
                eng.wait_ge(self.split, s - self.RING + 1)
            raw = self.G["w_raw"][:, s % self.RING, :]
            for col, n, step, src in self.loads[s]:
                at = col % step
                to = raw[:, col - at:col - at + n * step].rearrange("p (k n) -> p k n", k=n)
                eng.dma_start(to[:, :, at:at + src.shape[2]], src).then_inc(self.loaded[s % self.RING], 16)
            self.issued += 1

    def then_prefetch(self, eng, following):
        eng.wait_ge(self.split, len(self.loads))
        following.load(eng, self.RING)

    def split_high(self, act, s, last_user):
        n, r = self.columns(s), s % self.RING
        act.wait_ge(self.loaded[r], self.loads_done(s))
        if s >= self.RING:
            act.wait_ge(*last_user(s - self.RING))
        self.nc.scalar.copy(rounded(self.G["w_high"][:, r, 0:n]), self.G["w_raw"][:, r, 0:n]).then_inc(self.high, 1)

    def split_low(self, pool, s):
        n, r = self.columns(s), s % self.RING
        pool.wait_ge(self.high, s + 1)
        self.nc.gpsimd.tensor_tensor(rounded(self.G["w_low"][:, r, 0:n]), self.G["w_raw"][:, r, 0:n], self.G["w_high"][:, r, 0:n],
                                     ALU.subtract).then_inc(self.split, 1)

    def columns(self, s):
        return max((col // step + k) * step for col, k, step, _ in self.loads[s])

    def loads_done(self, s):
        return 16 * sum(len(self.loads[i]) for i in range(s % self.RING, s + 1, self.RING))

    def split_slot(self, dve, s, last_user=None):
        if s >= len(self.loads):
            return
        n, r = self.columns(s), s % self.RING
        raw, high, low = [self.G[w][:, r, 0:n] for w in ("w_raw", "w_high", "w_low")]
        dve.wait_ge(self.loaded[r], self.loads_done(s))
        if s >= self.RING:
            dve.wait_ge(*(last_user(s - self.RING) if last_user else (self.used, s - self.RING + 1)))
        self.nc.vector.tensor_copy(rounded(high), raw).then_inc(self.high, 1)
        dve.wait_ge(self.high, s + 1)
        self.nc.vector.tensor_tensor(rounded(low), raw, high, ALU.subtract).then_inc(self.split, 1)

    def parts(self, s, col, n):
        return [self.G[w][:, s % self.RING, col:col + n] for w in ("w_high", "w_low")]


def k_slots(w, col, width, step=None, parts=2):
    n = KD // parts
    return [[(0, n, step or width, w(h * n * P, (h + 1) * n * P, col, col + width))] for h in range(parts)]


class Split:

    def __init__(self, nc, ph, G, turned, bank):
        self.nc, self.G, self.turned, self.bank = nc, G, turned, bank
        self.high, self.low = ph.sem("high_done"), ph.sem("low_done")

    def places(self, t, j):
        at = lambda a: a[:, 4 * j:4 * j + 4, t * P:(t + 1) * P]
        return self.bank(t, j)[:, :].rearrange("p (k n) -> p k n", k=4), at(self.G["XH"]), at(self.G["XL"])

    def high_parts(self, act):
        for t in range(TT):
            for j in range(2):
                x, high, _ = self.places(t, j)
                act.wait_ge(self.turned, 2 * t + j + 1)
                self.nc.scalar.copy(rounded(high), x).then_inc(self.high, 1)

    def low_parts(self, dve, t):
        for j in range(2):
            x, high, low = self.places(t, j)
            dve.wait_ge(self.high, 2 * t + j + 1)
            self.nc.vector.tensor_tensor(rounded(low), x, high, ALU.subtract).then_inc(self.low, 1)


def load_phase(nc, G):
    with Phase(nc, "load") as ph:
        ident_loaded = ph.sem("ident_loaded")
        x_loaded = ph.sem("x_loaded")
        transposed = ph.sem("transposed")
        ones_set = ph.sem("ones_set")
        c_rows = ph.sb("c_rows", [KD, P])
        c_silu = ph.sb("c_silu", [KD, P])
        c_loaded = ph.sem("c_loaded")
        c_silu_done = ph.sem("c_silu_done")
        c_turned = ph.sem("c_turned")
        c_copied = ph.sem("c_copied")
        X, ps, ident = G["X"], G["ps"], G["ident"]
        split = Split(nc, ph, G, transposed, lambda t, j: ps[2 * t + j])
        block = ph.block()

        @block.sync
        def _(sp):
            sp.dma_start(ident, G["d"]["ident"][:, :]).then_inc(ident_loaded, 16)
            sp.dma_start(X[:, :, :], G["d"]["x"][0].rearrange("(t p) n -> p t n", p=P)).then_inc(x_loaded, 16)
            sp.dma_start(c_rows[:, :], G["d"]["c_2"][:, :].rearrange("o (k p) -> (o k) p", p=P)).then_inc(c_loaded, 16)

        @block.vector
        def _(dve):
            nc.vector.memset(G["ones_col"][:, :], 1.0).then_inc(ones_set, 1)
            nc.vector.memset(G["eps_ln"][:, :], LN_EPS).then_inc(ones_set, 1)
            nc.vector.memset(G["eps_norm"][:, :], NORM_EPS).then_inc(ones_set, 1)
            for t in range(TT):
                split.low_parts(dve, t)
            dve.wait_ge(c_turned, 1)
            nc.vector.tensor_copy(G["cond"][:, :], ps[0][:, 0:KD]).then_inc(c_copied, 1)

        @block.tensor
        def _(pe):
            pe.wait_ge(ident_loaded, 16)
            pe.wait_ge(x_loaded, 16)
            for t in range(TT):
                for j in range(2):
                    for i in range(4):
                        k = 4 * j + i
                        last = nc.tensor.transpose(ps[2 * t + j][:, i * P:(i + 1) * P], X[:, t, k * P:(k + 1) * P], ident)
                    last.then_inc(transposed, 1)
            pe.wait_ge(c_silu_done, 1)
            pe.wait_ge(split.low, 1)
            nc.tensor.transpose(ps[0][:, 0:KD], c_silu[:, :], ident[0:KD, 0:KD]).then_inc(c_turned, 1)

        @block.scalar
        def _(act):
            split.high_parts(act)
            act.wait_ge(c_loaded, 16)
            nc.scalar.activation(c_silu[:, :], c_rows[:, :], ACT.Silu).then_inc(c_silu_done, 1)


FM, TM, ROPE = "feature-major", "token-major", "feature-major, rotated"
PROJ_CHUNKS = [(COL_QA, 512, ROPE), (COL_KA, 512, ROPE), (COL_VA, 512, TM), (COL_QR, 256, ROPE),
               (COL_VR, 512, TM), (COL_QG, 256, FM), (COL_VG, 512, TM), (COL_AG, LOW_RANK, FM)]


def project_weights(nc, l, G):
    w = lambda r0, r1, c0, c1: G["d"]["w_in"][bass.ds(l, 1), r0:r1, c0:c1].rearrange("o (k p) n -> p (o k) n", p=P)
    return Weights(nc, G, "project", [s for col, width, _ in PROJ_CHUNKS
                                        for s in k_slots(w, col, width, step=max(width, P))])


def project_phase(nc, l, G, S, weights):
    jobs = []
    for c, (col, width, kind) in enumerate(PROJ_CHUNKS):
        for m in range(TT if kind == TM else -(-width // P)):
            jobs.append((c, m, kind, col))
    of_chunk = [[i for i, j in enumerate(jobs) if j[0] == c] for c in range(len(PROJ_CHUNKS))]
    ropes = [i for i, j in enumerate(jobs) if j[2] == ROPE]
    BANKS = 6
    SLOTS = 2
    KS = KD // SLOTS

    def rope_dest(i):
        c, m, _, col = jobs[i]
        if col == COL_QR:
            return (S["QR"] if m == 0 else S["KR"])[:, :]
        return (S["QA"] if col == COL_QA else S["KA"])[:, m, :]

    def plain_dest(i):
        c, m, kind, col = jobs[i]
        if kind == TM:
            return {COL_VA: S["VA"], COL_VR: S["VR"], COL_VG: S["VG"]}[col][:, m, :]
        if col == COL_QG:
            return (S["QG"] if m == 0 else S["KG"])[:, :]
        return S["AG"][:, :]

    with Phase(nc, "project") as ph:
        ph.sems += weights.sems
        raw = lambda r: S["Y"][:, r % 4, 0:SEQ]
        cosp = lambda r: S["Y"][:, r % 2, SEQ:2 * SEQ]
        sinp = lambda r: S["Y"][:, 2 + r % 2, SEQ:2 * SEQ]
        consts_loaded = ph.sem("consts_loaded")
        product_done = ph.sem("product_done")
        evacuated = ph.sem("evacuated")
        rotated = ph.sem("rotated")
        cos_done = ph.sem("cos_done")
        sin_done = ph.sem("sin_done")
        rope_done = ph.sem("rope_done")
        ps, XH, XL = G["ps"], G["XH"], G["XL"]
        block = ph.block()

        @block.sync
        def _(sp):
            weights.load(sp, 2)
            sp.dma_start(G["consts"][:, :], G["d"]["consts"][:, :]).then_inc(consts_loaded, 16)
            weights.load(sp)

        @block.tensor
        def _(pe):
            def turn(r):
                i = ropes[r]
                if r == 0:
                    pe.wait_ge(consts_loaded, 16)
                pe.wait_ge(evacuated, i + 1)
                if r >= 2:
                    pe.wait_ge(sin_done, r - 1)
                perm = G["c"]["perm_r" if jobs[i][3] == COL_QR else "perm_a"]
                nc.tensor.matmul(ps[6 + r % 2][:, :], perm, raw(r), start=True, stop=True).then_inc(rotated, 1)

            r = 0
            for c, (col, width, kind) in enumerate(PROJ_CHUNKS):
                for half in range(SLOTS):
                    s = SLOTS * c + half
                    pe.wait_ge(weights.split, s + 1)
                    for i in of_chunk[c]:
                        m = jobs[i][1]
                        if half == 0 and i >= BANKS:
                            pe.wait_ge(evacuated, i - BANKS + 1)
                        for kk in range(KS):
                            k = half * KS + kk
                            if kind == TM:
                                toks = slice(m * P, (m + 1) * P)
                                last = split_product(nc, ps[i % BANKS][:, 0:width], (XH[:, k, toks], XL[:, k, toks]),
                                                     weights.parts(s, kk * width, width), k == 0, k == KD - 1)
                            else:
                                last = split_product(nc, ps[i % BANKS][:, :], weights.parts(s, kk * max(width, P) + m * P, P),
                                                     (XH[:, k, :], XL[:, k, :]), k == 0, k == KD - 1)
                        if half == SLOTS - 1:
                            last.then_inc(product_done, 1)
                        elif i == of_chunk[c][-1]:
                            last.then_inc(weights.used, 1)
                        if r < len(ropes) and ropes[r] < of_chunk[c][0]:
                            turn(r)
                            r += 1

        @block.scalar
        def _(act):
            r = 0
            for i, (c, m, kind, col) in enumerate(jobs):
                act.wait_ge(product_done, i + 1)
                if kind == ROPE:
                    if r >= 4:
                        act.wait_ge(rotated, r - 3)
                        act.wait_ge(cos_done, r - 3)
                    nc.scalar.copy(raw(r), ps[i % BANKS][:, :]).then_inc(evacuated, 1)
                    r += 1
                elif col == COL_QG and m == 0:
                    nc.scalar.mul(plain_dest(i), ps[i % BANKS][:, :], QK_G ** -0.5).then_inc(evacuated, 1)
                elif col == COL_AG:
                    nc.scalar.copy(plain_dest(i), ps[i % BANKS][0:LOW_RANK, :]).then_inc(evacuated, 1)
                else:
                    nc.scalar.copy(plain_dest(i), ps[i % BANKS][:, :]).then_inc(evacuated, 1)

        @block.gpsimd
        def _(pool):
            pool.wait_ge(consts_loaded, 16)
            for r, i in enumerate(ropes):
                cos = G["c"]["cos_r" if jobs[i][3] == COL_QR else "cos_a"]
                pool.wait_ge(evacuated, i + 1)
                if r >= 2:
                    pool.wait_ge(rope_done, r - 1)
                nc.gpsimd.tensor_tensor(cosp(r), raw(r), cos, ALU.mult).then_inc(cos_done, 1)

        @block.vector
        def _(dve):
            last_user = lambda s: (product_done, of_chunk[s // SLOTS][-1] + 1) if s % SLOTS == SLOTS - 1 else (weights.used, s // SLOTS + 1)

            def rope(r):
                i = ropes[r]
                sin = G["c"]["sin_r" if jobs[i][3] == COL_QR else "sin_a"]
                dve.wait_ge(rotated, r + 1)
                if r >= 2:
                    dve.wait_ge(rope_done, r - 1)
                nc.vector.tensor_tensor(sinp(r), ps[6 + r % 2][:, :], sin, ALU.mult).then_inc(sin_done, 1)
                dve.wait_ge(sin_done, r + 1)
                dve.wait_ge(cos_done, r + 1)
                nc.vector.tensor_tensor(rope_dest(i), sinp(r), cosp(r), ALU.add).then_inc(rope_done, 1)

            r = 0
            for s in range(len(weights.loads)):
                weights.split_slot(dve, s, last_user)
                if s == 0:
                    dve.wait_ge(consts_loaded, 16)
                while r < len(ropes) and SLOTS * jobs[ropes[r]][0] + SLOTS + 1 <= s:
                    rope(r)
                    r += 1
            while r < len(ropes):
                rope(r)
                r += 1


def dilated_phase(nc, l, G, S):
    units = [(h, t) for h in range(HEADS_A) for t in range(TT)]
    SCORE_BANKS = (0, 1, 6)
    with Phase(nc, "dilated") as ph:
        rows = G["w_raw"][:, :, :].rearrange("p r (j n) -> p (r j) n", n=SEQ)
        SL, PR = rows[:, 0:3, :], rows[:, 3:6, :]
        PT = ph.sb("probs_t", [P, 2, TT, P])
        neg_max = ph.sb("neg_max", [P, len(units)])
        row_sum = ph.sb("row_sum", [P, len(units)])
        inv_sum = ph.sb("inv_sum", [P, len(units)])
        scores_done = ph.sem("scores_done")
        biased = ph.sem("biased")
        max_done = ph.sem("max_done")
        exp_done = ph.sem("exp_done")
        turned = ph.sem("turned")
        turned_copied = ph.sem("turned_copied")
        mixed = ph.sem("mixed")
        inv_done = ph.sem("inv_done")
        out_done = ph.sem("out_done")
        ps, ident = G["ps"], G["ident"]
        logc = G["c"]["log_count"].rearrange("p (t n) -> p t n", t=TT)
        zero_rows = ph.sb("zero_rows", [P, D])
        zero_set = ph.sem("zero_set")
        cleared = ph.sem("cleared")
        share = BLOCKS // DEPTH
        block = ph.block()

        @block.sync
        def _(sp):
            sp.wait_ge(zero_set, 1)
            for b in range(share):
                sp.dma_start(G["y_dram"][bass.ds(l * (share * P) + b * P, P), :], zero_rows[:, :]).then_inc(cleared, 16)
            sp.wait_ge(cleared, 16 * share)

        @block.gpsimd
        def _(pool):
            nc.gpsimd.memset(zero_rows[:, :], 0.0).then_inc(zero_set, 1)

        @block.tensor
        def _(pe):
            def scores(u):
                h, t = units[u]
                r = HD_A * (h % 2)
                if u >= 3:
                    pe.wait_ge(biased, u - 2)
                nc.tensor.matmul(ps[SCORE_BANKS[u % 3]][:, 0:(t + 1) * P], S["QA"][r:r + HD_A, h // 2, t * P:(t + 1) * P],
                                 S["KA"][r:r + HD_A, h // 2, 0:(t + 1) * P], start=True, stop=True).then_inc(scores_done, 1)

            def turn(u):
                h, t = units[u]
                pe.wait_ge(exp_done, u + 1)
                if u >= 2:
                    pe.wait_ge(turned_copied, u - 1)
                for k in range(t + 1):
                    last = nc.tensor.transpose(ps[2 + u % 2][:, k * P:(k + 1) * P], PR[:, u % 3, k * P:(k + 1) * P], ident)
                last.then_inc(turned, 1)

            def mix(u):
                h, t = units[u]
                pe.wait_ge(turned_copied, u + 1)
                if u >= 2:
                    pe.wait_ge(out_done, u - 1)
                for k in range(t + 1):
                    last = nc.tensor.matmul(ps[4 + u % 2][:, 0:P], PT[:, u % 2, k, :],
                                            S["VA"][:, k, h // 2 * P:(h // 2 + 1) * P], start=(k == 0), stop=(k == t))
                last.then_inc(mixed, 1)

            for i in range(len(units) + 3):
                if i < len(units):
                    scores(i)
                if 2 <= i < len(units) + 2:
                    turn(i - 2)
                if i >= 3:
                    mix(i - 3)

        @block.vector
        def _(dve):
            def finish(u):
                h, t = units[u]
                dve.wait_ge(exp_done, u + 1)
                nc.vector.reciprocal(inv_sum[:, u:u + 1], row_sum[:, u:u + 1]).then_inc(inv_done, 1)
                dve.wait_ge(inv_done, u + 1)
                dve.wait_ge(mixed, u + 1)
                nc.vector.tensor_scalar(S["Y"][:, t, h * HD_A:(h + 1) * HD_A], ps[4 + u % 2][:, h % 2 * HD_A:(h % 2 + 1) * HD_A],
                                        inv_sum[:, u:u + 1], None, ALU.mult).then_inc(out_done, 1)

            for u, (h, t) in enumerate(units):
                n = (t + 1) * P
                dve.wait_ge(scores_done, u + 1)
                if u >= 3:
                    dve.wait_ge(exp_done, u - 2)
                nc.vector.scalar_tensor_tensor(SL[:, u % 3, 0:n], ps[SCORE_BANKS[u % 3]][:, 0:n], HD_A ** -0.5, logc[:, t, 0:n],
                                               ALU.mult, ALU.add).then_inc(biased, 1)
                dve.wait_ge(biased, u + 1)
                nc.vector.tensor_reduce(neg_max[:, u:u + 1], SL[:, u % 3, 0:n], AX_X, ALU.max, negate=True
                                        ).then_inc(max_done, 1)
                if u >= 3:
                    finish(u - 3)
            finish(len(units) - 3)
            finish(len(units) - 2)
            finish(len(units) - 1)

        @block.scalar
        def _(act):
            def copy(u):
                n = units[u][1] + 1
                act.wait_ge(turned, u + 1)
                if u >= 2:
                    act.wait_ge(mixed, u - 1)
                nc.scalar.copy(PT[:, u % 2, 0:n, :], ps[2 + u % 2][:, 0:n * P].rearrange("p (k n) -> p k n", n=P)
                               ).then_inc(turned_copied, 1)

            for u, (h, t) in enumerate(units):
                n = (t + 1) * P
                act.wait_ge(max_done, u + 1)
                if u >= 3:
                    act.wait_ge(turned, u - 2)
                nc.scalar.activation(PR[:, u % 3, 0:n], SL[:, u % 3, 0:n], ACT.Exp, bias=neg_max[:, u:u + 1],
                                     accum_out=row_sum[:, u:u + 1]).then_inc(exp_done, 1)
                if u >= 2:
                    copy(u - 2)
            copy(len(units) - 2)
            copy(len(units) - 1)


def retention_phase(nc, G, S):
    units = [(k, h) for k in range(TT) for h in range(HEADS_R)]
    with Phase(nc, "retention") as ph:
        SD = ph.sb("decayed", [P, TT, HEADS_R, SEQ])
        scores_done = ph.sem("scores_done")
        decayed = ph.sem("decayed_done")
        mixed = ph.sem("mixed")
        copied = ph.sem("copied")
        ps = G["ps"]
        decay = G["c"]["decay"].rearrange("p (h n) -> p h n", h=HEADS_R)
        block = ph.block()

        @block.tensor
        def _(pe):
            for u, (k, h) in enumerate(units):
                r = QK_R * h
                if u >= 4:
                    pe.wait_ge(decayed, u - 3)
                nc.tensor.matmul(ps[u % 4][:, 0:SEQ - k * P], S["KR"][r:r + QK_R, k * P:(k + 1) * P],
                                 S["QR"][r:r + QK_R, k * P:SEQ], start=True, stop=True, tile_position=(r, 0)
                                 ).then_inc(scores_done, 1)
            pe.wait_ge(decayed, len(units))
            for t in range(TT):
                for h in range(HEADS_R):
                    for k in range(t + 1):
                        last = nc.tensor.matmul(ps[4 + t][:, h * 64:(h + 1) * 64], SD[:, k, h, (t - k) * P:(t - k + 1) * P],
                                                S["VR"][:, k, h * 64:(h + 1) * 64], start=(k == 0), stop=(k == t))
                last.then_inc(mixed, 1)

        @block.vector
        def _(dve):
            for u, (k, h) in enumerate(units):
                n = SEQ - k * P
                dve.wait_ge(scores_done, u + 1)
                nc.vector.tensor_tensor(SD[:, k, h, 0:n], ps[u % 4][:, 0:n], decay[:, h, 0:n], ALU.mult).then_inc(decayed, 1)

        @block.scalar
        def _(act):
            for t in range(TT):
                act.wait_ge(mixed, t + 1)
                nc.scalar.copy(S["Y"][:, t, 512:768], ps[4 + t][:, 0:256]).then_inc(copied, 1)


def gla_phase(nc, l, G, S):
    with Phase(nc, "gla") as ph:
        wal = ph.sb("w_alpha", [LOW_RANK, P])
        bal = ph.sb("b_alpha", [P, 1])
        z = ph.sb("z", [P, SEQ])
        za = ph.sb("z_abs", [P, SEQ])
        ze = ph.sb("z_exp", [P, SEQ])
        zl = ph.sb("z_ln", [P, SEQ])
        zm = ph.sb("z_min", [P, SEQ])
        la = ph.sb("log_alpha", [P, SEQ])
        kv = G["w_raw"][:, 0, :].rearrange("p (n e) -> p n e", n=N_CHUNKS)
        state = G["w_raw"][:, 1, :].rearrange("p (n e) -> p n e", n=N_CHUNKS)
        att = G["c"]["log_count"].rearrange("p (h t n) -> p h t n", h=HEADS_G, t=TT)
        cum, rest, grow, shrink = [G["c"]["decay"][:, j * SEQ:(j + 1) * SEQ] for j in range(4)]
        rest_exp = ph.sb("exp_rest", [P, SEQ])
        qt = ph.sb("q_t", [P, SEQ])
        qe = ph.sb("q_even", [P, SEQ])
        qo = ph.sb("q_odd", [P, SEQ])
        kt = ph.sb("k_t", [P, SEQ])
        kd = ph.sb("k_rest", [P, SEQ])
        kdt = ph.sb("k_rest_t", [P, TT, P])
        loaded = ph.sem("loaded")
        z_done = ph.sem("z_done")
        act_step = ph.sem("act_step")
        ln_done = ph.sem("ln_done")
        dve_step = ph.sem("dve_step")
        cum_done = ph.sem("cum_done")
        rest_done = ph.sem("rest_done")
        grow_done = ph.sem("grow_done")
        shrink_done = ph.sem("shrink_done")
        rest_exp_done = ph.sem("rest_exp_done")
        keys_done = ph.sem("keys_done")
        queries_done = ph.sem("queries_done")
        k_rest_done = ph.sem("k_rest_done")
        k_rest_turned = ph.sem("k_rest_turned")
        k_rest_copied = ph.sem("k_rest_copied")
        kv_done = ph.sem("kv_done")
        state_done = ph.sem("state_done")
        att_done = ph.sem("att_done")
        masked = ph.sem("masked")
        mixed = ph.sem("mixed")
        copied = ph.sem("copied")
        split_done = ph.sem("split_done")
        ps, c = G["ps"], G["c"]
        kv_bank = lambda n: ps[(5, 7, 5, 7, 6, 4, 6, 4)[n]][:, 256 * (n // 2 % 2):256 * (n // 2 % 2) + 256]
        by_chunk = lambda a: a[:, :].rearrange("p (n s) -> p n s", s=GLA_CHUNK)
        block = ph.block()

        @block.sync
        def _(sp):
            sp.dma_start(wal[:, :], G["d"]["w_alpha"][bass.ds(l, 1), :, :].rearrange("o r n -> (o r) n")).then_inc(loaded, 16)
            sp.dma_start(bal[:, :], G["d"]["b_alpha"][bass.ds(l, 1), :].rearrange("o p -> p o")).then_inc(loaded, 16)

        @block.tensor
        def _(pe):
            pe.wait_ge(loaded, 32)
            nc.tensor.matmul(ps[0][:, :], wal[:, :], S["AG"][:, :], start=True, stop=True).then_inc(z_done, 1)
            pe.wait_ge(queries_done, 1)
            pe.wait_ge(keys_done, 1)
            for h in range(HEADS_G):
                r = QK_G * h
                for t in range(TT):
                    last = nc.tensor.matmul(ps[h][:, t * P:(t + 1) * P], kt[r:r + QK_G, t * P:(t + 1) * P],
                                            qt[r:r + QK_G, t * P:(t + 1) * P], start=True, stop=True, tile_position=(r, 0))
                last.then_inc(att_done, 1)
            pe.wait_ge(k_rest_done, 1)
            for t in range(TT):
                last = nc.tensor.transpose(ps[4][:, t * P:(t + 1) * P], kd[:, t * P:(t + 1) * P], G["ident"])
            last.then_inc(k_rest_turned, 1)
            pe.wait_ge(k_rest_copied, 1)
            for n in range(N_CHUNKS):
                r = GLA_CHUNK * (n % 2)
                nc.tensor.matmul(kv_bank(n), kdt[r:r + GLA_CHUNK, n // 2, :],
                                 S["VG"][r:r + GLA_CHUNK, n // 2, 0:256], start=True, stop=True).then_inc(kv_done, 1)
            pe.wait_ge(masked, HEADS_G)
            pe.wait_ge(split_done, 2)
            for t in range(TT):
                pe.wait_ge(state_done, 2 * t + 2)
                o = ps[t % 2]
                if t >= 2:
                    pe.wait_ge(copied, t - 1)
                nc.tensor.matmul(o[:, 0:256], qe[:, t * P:(t + 1) * P], state[:, 2 * t, :], start=True, stop=False,
                                 skip_group_check=True)
                nc.tensor.matmul(o[:, 0:256], qo[:, t * P:(t + 1) * P], state[:, 2 * t + 1, :], start=False, stop=False,
                                 skip_group_check=True)
                for h in range(HEADS_G):
                    last = nc.tensor.matmul(o[:, h * 64:(h + 1) * 64], att[:, h, t, :], S["VG"][:, t, h * 64:(h + 1) * 64],
                                            start=False, stop=True, skip_group_check=True)
                last.then_inc(mixed, 1)

        @block.scalar
        def _(act):
            chain = Chain(act, act_step)
            act.wait_ge(loaded, 32)
            act.wait_ge(z_done, 1)
            chain.link(nc.scalar.activation(z[:, :], ps[0][:, :], ACT.Identity, bias=bal[:, :]))
            chain.link(nc.scalar.activation(za[:, :], z[:, :], ACT.Abs))
            chain.link(nc.scalar.activation(ze[:, :], za[:, :], ACT.Exp, scale=-1.0))
            nc.scalar.activation(zl[:, :], ze[:, :], ACT.Ln, bias=G["ones_col"][:, :]).then_inc(ln_done, 1)
            act.wait_ge(cum_done, 1)
            nc.scalar.activation(grow[:, :], cum[:, :], ACT.Exp).then_inc(grow_done, 1)
            nc.scalar.activation(shrink[:, :], cum[:, :], ACT.Exp, scale=-1.0).then_inc(shrink_done, 1)
            act.wait_ge(rest_done, 1)
            nc.scalar.activation(rest_exp[:, :], rest[:, :], ACT.Exp).then_inc(rest_exp_done, 1)
            act.wait_ge(k_rest_turned, 1)
            nc.scalar.copy(kdt[:, :, :], ps[4][:, :].rearrange("p (t n) -> p t n", t=TT)).then_inc(k_rest_copied, 1)
            for t in range(TT):
                act.wait_ge(mixed, t + 1)
                nc.scalar.copy(S["Y"][:, t, 768:1024], ps[t % 2][:, 0:256]).then_inc(copied, 1)

        @block.vector
        def _(dve):
            chain = Chain(dve, dve_step)
            dve.wait_ge(act_step, 1)
            chain.link(nc.vector.tensor_scalar(zm[:, :], z[:, :], 0.0, 1.0 / 16.0, ALU.min, ALU.mult))
            dve.wait_ge(ln_done, 1)
            chain.link(nc.vector.scalar_tensor_tensor(la[:, :], zl[:, :], -1.0 / 16.0, zm[:, :], ALU.mult, ALU.add))
            nc.vector.tensor_tensor_scan(cum[:, :], c["chunk_keep"], la[:, :], 0.0, ALU.mult, ALU.add).then_inc(cum_done, 1)
            dve.wait_ge(cum_done, 1)
            last = by_chunk(cum)[:, :, GLA_CHUNK - 1:GLA_CHUNK].to_broadcast([P, N_CHUNKS, GLA_CHUNK])
            nc.vector.tensor_tensor(by_chunk(rest), last, by_chunk(cum), ALU.subtract).then_inc(rest_done, 1)
            dve.wait_ge(grow_done, 1)
            nc.vector.tensor_tensor(qt[:, :], S["QG"][:, :], grow[:, :], ALU.mult).then_inc(queries_done, 1)
            dve.wait_ge(shrink_done, 1)
            nc.vector.tensor_tensor(kt[:, :], S["KG"][:, :], shrink[:, :], ALU.mult).then_inc(keys_done, 1)
            dve.wait_ge(rest_exp_done, 1)
            nc.vector.tensor_tensor(kd[:, :], S["KG"][:, :], rest_exp[:, :], ALU.mult).then_inc(k_rest_done, 1)
            mask = c["gla_causal"].rearrange("p (o n) -> p o n", o=1).to_broadcast([P, TT, P])
            for h in range(HEADS_G):
                dve.wait_ge(att_done, h + 1)
                nc.vector.tensor_tensor(att[:, h, :, :], ps[h][:, :].rearrange("p (t n) -> p t n", t=TT), mask, ALU.mult
                                        ).then_inc(masked, 1)
            nc.vector.memset(state[:, 0, :], 0.0).then_inc(state_done, 1)
            for n in range(N_CHUNKS - 1):
                dve.wait_ge(kv_done, 4 * (n // 4) + 4)
                chain.link(nc.vector.tensor_tensor(kv[:, n, :], kv_bank(n), c["head_block"], ALU.mult))
                dve.wait_ge(state_done, n + 1)
                e = n * GLA_CHUNK + GLA_CHUNK - 1
                nc.vector.scalar_tensor_tensor(state[:, n + 1, :], state[:, n, :], grow[:, e:e + 1], kv[:, n, :],
                                               ALU.mult, ALU.add).then_inc(state_done, 1)

        @block.gpsimd
        def _(pool):
            pool.wait_ge(queries_done, 1)
            nc.gpsimd.tensor_tensor(qe[:, :], qt[:, :], c["even_chunk"], ALU.mult).then_inc(split_done, 1)
            nc.gpsimd.tensor_tensor(qo[:, :], qt[:, :], c["odd_chunk"], ALU.mult).then_inc(split_done, 1)


def head_norm_phase(nc, l, G, S, next_weights):
    HN = 16
    with Phase(nc, "head_norm") as ph:
        sums = ph.sb("sums", [P, TT, HN])
        mean = ph.sb("mean", [P, TT, HN])
        cen = ph.sb("centred", [P, TT, D])
        sq = ph.sb("squares", [P, 2, D])
        sqs = ph.sb("square_sums", [P, TT, HN])
        std = ph.sb("std", [P, TT, HN])
        rstd = ph.sb("rstd", [P, TT, HN])
        gates = ph.sb("gates", [P, TT, 512])
        nrm = cen
        scale_rows = ph.sb("scale_rows", [KD, P])
        scale = ph.sb("scale", [P, KD])
        loaded = ph.sem("loaded")
        dve_step = ph.sem("dve_step")
        centred = ph.sem("centred_done")
        squared = ph.sem("squared")
        squares_summed = ph.sem("squares_summed")
        std_done = ph.sem("std_done")
        gate_done = ph.sem("gate_done")
        normed = ph.sem("normed_done")
        gated = ph.sem("gated")
        low_done = ph.sem("low_done")
        scale_turned = ph.sem("scale_turned")
        scale_done = ph.sem("scale_done")
        turned = ph.sem("turned")
        copied = ph.sem("copied")
        ps, ident = G["ps"], G["ident"]
        heads = lambda a: a.rearrange("p (h e) -> p h e", h=HN)
        spread = lambda a: a.rearrange("p (h o) -> p h o", o=1).to_broadcast([P, HN, 64])
        block = ph.block()

        @block.sync
        def _(sp):
            next_weights.load(sp, Weights.RING)
            sp.dma_start(scale_rows[:, :], G["d"]["mix_scale"][bass.ds(l, 1), :].rearrange("o (k p) -> (o k) p", p=P)
                         ).then_inc(loaded, 16)

        @block.vector
        def _(dve):
            chain = Chain(dve, dve_step)
            for t in range(TT):
                y = heads(S["Y"][:, t, :])
                chain.link(nc.vector.tensor_reduce(sums[:, t, :], y, AX_X, ALU.add))
                chain.link(nc.vector.tensor_scalar(mean[:, t, :], sums[:, t, :], 1.0 / 64, None, ALU.mult))
                nc.vector.tensor_tensor(heads(cen[:, t, :]), y, spread(mean[:, t, :]), ALU.subtract).then_inc(centred, 1)
            for t in range(TT):
                dve.wait_ge(squared, t + 1)
                nc.vector.tensor_reduce(sqs[:, t, :], heads(sq[:, t % 2, :]), AX_X, ALU.add).then_inc(squares_summed, 1)
            for t in range(TT):
                dve.wait_ge(std_done, 1)
                chain.link(nc.vector.reciprocal(rstd[:, t, :], std[:, t, :]))
                nc.vector.tensor_tensor(heads(nrm[:, t, :]), heads(cen[:, t, :]), spread(rstd[:, t, :]), ALU.mult
                                        ).then_inc(normed, 1)
            for t in range(TT):
                for k in range(KD):
                    dve.wait_ge(copied, KD * t + 4 * (k // 4 + 1))
                    toks = slice(t * P, (t + 1) * P)
                    nc.vector.scalar_tensor_tensor(rounded(G["XL"][:, k, toks]), ps[2 * (t % 2) + k // 4][:, (k % 4) * P:(k % 4 + 1) * P],
                                                   scale[:, k:k + 1], G["XH"][:, k, toks], ALU.mult, ALU.subtract).then_inc(low_done, 1)

        @block.scalar
        def _(act):
            for t in range(TT):
                act.wait_ge(centred, t + 1)
                if t >= 2:
                    act.wait_ge(squares_summed, t - 1)
                nc.scalar.activation(sq[:, t % 2, :], cen[:, t, :], ACT.Square).then_inc(squared, 1)
            for t in range(TT):
                nc.scalar.activation(gates[:, t, 0:256], S["VR"][:, t, 256:512], ACT.Silu).then_inc(gate_done, 1)
                nc.scalar.activation(gates[:, t, 256:512], S["VG"][:, t, 256:512], ACT.Silu).then_inc(gate_done, 1)
            act.wait_ge(squares_summed, TT)
            nc.scalar.activation(std[:, :, :], sqs[:, :, :], ACT.Sqrt, scale=1.0 / 64, bias=G["eps_norm"][:, :]
                                 ).then_inc(std_done, 1)
            act.wait_ge(scale_turned, 1)
            nc.scalar.copy(scale[:, :], ps[7][:, 0:KD]).then_inc(scale_done, 1)
            act.wait_ge(scale_done, 1)
            for t in range(TT):
                for k in range(KD):
                    act.wait_ge(turned, 2 * t + k // 4 + 1)
                    nc.scalar.activation(rounded(G["XH"][:, k, t * P:(t + 1) * P]),
                                         ps[2 * (t % 2) + k // 4][:, (k % 4) * P:(k % 4 + 1) * P], ACT.Copy,
                                         scale=scale[:, k:k + 1]).then_inc(copied, 1)

        @block.gpsimd
        def _(pool):
            pool.wait_ge(gate_done, 2 * TT)
            for t in range(TT):
                pool.wait_ge(normed, t + 1)
                nc.gpsimd.tensor_tensor(nrm[:, t, 512:1024], nrm[:, t, 512:1024], gates[:, t, :], ALU.mult).then_inc(gated, 1)

        @block.tensor
        def _(pe):
            pe.wait_ge(loaded, 16)
            nc.tensor.transpose(ps[7][:, 0:KD], scale_rows[:, :], ident[0:KD, 0:KD]).then_inc(scale_turned, 1)
            for t in range(TT):
                pe.wait_ge(normed, t + 1)
                pe.wait_ge(gated, t + 1)
                if t >= 2:
                    pe.wait_ge(low_done, KD * (t - 1))
                for j in range(2):
                    for i in range(4):
                        k = 4 * j + i
                        last = nc.tensor.transpose(ps[2 * (t % 2) + j][:, i * P:(i + 1) * P], nrm[:, t, k * P:(k + 1) * P], ident)
                    last.then_inc(turned, 1)


ROW_TILES = Weights.SLOT // D


def row_weights(nc, name, w, KT, G):
    return Weights(nc, G, name, [[(0, ROW_TILES, D, w(k * P, (k + ROW_TILES) * P))] for k in range(0, KT, ROW_TILES)])


def layer_rows(w_dram, l):
    return lambda r0, r1: w_dram[bass.ds(l, 1), r0:r1, :].rearrange("o (k p) n -> p (o k) n", p=P)


def row_products(nc, pe, ps, weights, acts, acts_ready, product_done):
    slots = len(weights.loads)

    def tile(s, t):
        for c in range(2):
            for k in range(ROW_TILES):
                last = split_product(nc, ps[2 * t + c][:, :], acts(s, k, slice(t * P, (t + 1) * P)),
                                     weights.parts(s, k * D + c * BANK, BANK), s == 0 and k == 0,
                                     s == slots - 1 and k == ROW_TILES - 1)
            if s == slots - 1:
                last.then_inc(product_done, 1)
        return last

    for s in range(slots - 2):
        pe.wait_ge(weights.split, s + 1)
        if acts_ready is not None:
            pe.wait_ge(acts_ready, s + 1)
        for t in range(TT):
            last = tile(s, t)
        last.then_inc(weights.used, 1)
    for t in range(TT):
        for s in (slots - 2, slots - 1):
            pe.wait_ge(weights.split, s + 1)
            if acts_ready is not None:
                pe.wait_ge(acts_ready, s + 1)
            tile(s, t)


def output_norm_phase(nc, name, l, G, H, weights, g_dram, b_dram, next_weights=None):
    slots = len(weights.loads)
    with Phase(nc, name) as ph:
        ph.sems += weights.sems
        g_row = ph.sb("g_row", [P, D])
        b_row = ph.sb("b_row", [P, D])
        stats = ph.sb("stats", [P, TT, 2, 6])
        mv = ph.sb("mean_var", [P, TT, 2])
        std = ph.sb("std", [P, TT])
        rstd = ph.sb("rstd", [P, TT])
        rows_loaded = ph.sem("rows_loaded")
        product_done = ph.sem("product_done")
        summed = ph.sem("summed")
        dve_step = ph.sem("dve_step")
        var_done = ph.sem("var_done")
        std_done = ph.sem("std_done")
        normed = ph.sem("normed")
        scaled = ph.sem("scaled")
        shifted = ph.sem("shifted")
        turned = ph.sem("turned")
        ps, X, XL, XH, ident = G["ps"], G["X"], G["XL"], G["XH"], G["ident"]
        split = Split(nc, ph, G, turned, lambda t, j: ps[2 * t + j])
        if H is None:
            acts = lambda s, k, toks: (XH[:, ROW_TILES * s + k, toks], XL[:, ROW_TILES * s + k, toks])
            acts_low = None
        else:
            hidden_high = ph.sb("hidden_high", [P, 2, ROW_TILES, SEQ])
            acts_high = ph.sem("acts_high")
            acts_low = ph.sem("acts_low")
            hidden_low = ph.sb("hidden_low", [P, 2, ROW_TILES, SEQ])
            acts = lambda s, k, toks: (hidden_high[:, s % 2, k, toks], hidden_low[:, s % 2, k, toks])
        block = ph.block()

        @block.sync
        def _(sp):
            weights.load(sp, Weights.RING)
            sp.dma_start(g_row[:, :], g_dram[bass.ds(l, 1), :].to_broadcast([P, D])).then_inc(rows_loaded, 16)
            sp.dma_start(b_row[:, :], b_dram[bass.ds(l, 1), :].to_broadcast([P, D])).then_inc(rows_loaded, 16)
            weights.load(sp)
            if next_weights is not None:
                weights.then_prefetch(sp, next_weights)

        @block.tensor
        def _(pe):
            row_products(nc, pe, ps, weights, acts, acts_low, product_done)
            for t in range(TT):
                pe.wait_ge(shifted, t + 1)
                for j in range(2):
                    for i in range(4):
                        k = 4 * j + i
                        last = nc.tensor.transpose(ps[2 * t + j][:, i * P:(i + 1) * P], X[:, t, k * P:(k + 1) * P], ident)
                    last.then_inc(turned, 1)

        @block.vector
        def _(dve):
            chain = Chain(dve, dve_step)

            def stats_of(t):
                for c in range(2):
                    dve.wait_ge(product_done, 2 * t + c + 1)
                    half = X[:, t, c * BANK:(c + 1) * BANK]
                    nc.vector.scalar_tensor_tensor(half, half, ALPHA, ps[2 * t + c][:, :], ALU.mult, ALU.add).then_inc(summed, 1)
                    dve.wait_ge(summed, 2 * t + c + 1)
                    chain.link(nc.vector.bn_stats(stats[:, t, c, :], half))
                nc.vector.bn_aggr(mv[:, t, :], stats[:, t, :, :]).then_inc(var_done, 1)

            def norm(t):
                dve.wait_ge(std_done, t + 1)
                chain.link(nc.vector.reciprocal(rstd[:, t:t + 1], std[:, t:t + 1]))
                nc.vector.tensor_scalar(X[:, t, :], X[:, t, :], mv[:, t, 0:1], rstd[:, t:t + 1], ALU.subtract, ALU.mult
                                        ).then_inc(normed, 1)
                dve.wait_ge(normed, t + 1)
                dve.wait_ge(rows_loaded, 32)
                nc.vector.tensor_tensor(X[:, t, :], X[:, t, :], g_row[:, :], ALU.mult).then_inc(scaled, 1)

            for s in range(slots):
                if H is not None:
                    if s >= 2:
                        dve.wait_ge(weights.used, s - 1)
                    nc.vector.tensor_copy(rounded(hidden_high[:, s % 2, :, :]), H[:, ROW_TILES * s:ROW_TILES * (s + 1), :]).then_inc(acts_high, 1)
                weights.split_slot(dve, s)
            for t in range(TT):
                stats_of(t)
                if t >= 1:
                    norm(t - 1)
            norm(TT - 1)
            for t in range(TT):
                split.low_parts(dve, t)

        @block.scalar
        def _(act):
            for t in range(TT):
                act.wait_ge(var_done, t + 1)
                nc.scalar.activation(std[:, t:t + 1], mv[:, t, 1:2], ACT.Sqrt, bias=G["eps_ln"][:, :]).then_inc(std_done, 1)
            split.high_parts(act)

        @block.gpsimd
        def _(pool):
            if H is not None:
                for s in range(slots):
                    pool.wait_ge(acts_high, s + 1)
                    if s >= 2:
                        pool.wait_ge(weights.used, s - 1)
                    nc.gpsimd.tensor_tensor(rounded(hidden_low[:, s % 2, :, :]), H[:, ROW_TILES * s:ROW_TILES * (s + 1), :],
                                            hidden_high[:, s % 2, :, :], ALU.subtract).then_inc(acts_low, 1)
            pool.wait_ge(rows_loaded, 32)
            for t in range(TT):
                pool.wait_ge(scaled, t + 1)
                nc.gpsimd.tensor_tensor(X[:, t, :], X[:, t, :], b_row[:, :], ALU.add).then_inc(shifted, 1)


def up_weights(nc, l, G):
    w = lambda c: G["d"]["w_up"][bass.ds(l, 1), :, c:c + P].rearrange("o (k p) n -> p (o k) n", p=P)
    return Weights(nc, G, "ffn_up", [[(0, KD, P, w(j * P)), (KD * P, KD, P, w(D_FF + j * P))] for j in range(FT)])


MOD = 6 * D
MOD_COLS = MOD // 3
MOD_CHUNKS = [(g, k) for g in range(MOD // MOD_COLS) for k in range(KD)]


def ffn_up_phase(nc, l, G, H, weights, next_weights):
    MOD_STEPS = FT - 1
    mod_step = lambda j: range(min(j * len(MOD_CHUNKS) // MOD_STEPS, len(MOD_CHUNKS)),
                               min((j + 1) * len(MOD_CHUNKS) // MOD_STEPS, len(MOD_CHUNKS)))
    GROUPS_OF = MOD // MOD_COLS
    sum_at = {next(j for j in range(FT) if KD * (g + 1) - 1 in mod_step(j)) + 2: g for g in range(GROUPS_OF)}
    jobs = [(j, v) for j in range(FT) for v in range(2)]
    BANKS = 6
    with Phase(nc, "ffn_up") as ph:
        ph.sems += weights.sems
        taps_rows = ph.sb("taps_rows", [2 * FT, 4, P])
        taps = ph.sb("taps", [P, 4, 2 * FT])
        conv = ph.sb("conv", [P, 6, SEQ])
        gate = ph.sb("gate", [P, 2, SEQ])
        mod_w = ph.sb("mod_w", [P, 2, MOD_COLS])
        mod_sum = ph.sb("mod_sum", [P, MOD])
        mod_loaded = [ph.sem(f"mod_loaded{r}") for r in range(2)]
        mod_added = ph.sem("mod_added")
        mod_cols = ph.sb("mod_cols", [P, MOD // P])
        mod_bias = ph.sb("mod_bias", [MOD // P, P])
        mod_rows = ph.sb("mod_rows", [MOD // P, P])
        mod_bias_loaded = ph.sem("mod_bias_loaded")
        mod_summed = ph.sem("mod_summed")
        mod_copied = ph.sem("mod_copied")
        mod_turned = ph.sem("mod_turned")
        mod_biased = ph.sem("mod_biased")
        mod_stored = ph.sem("mod_stored")
        taps_loaded = ph.sem("taps_loaded")
        taps_turned = ph.sem("taps_turned")
        taps_copied = ph.sem("taps_copied")
        product_done = ph.sem("product_done")
        last_tap = ph.sem("last_tap")
        dve_tap = ph.sem("dve_tap")
        conv_done = ph.sem("conv_done")
        silu_done = ph.sem("silu_done")
        glu_done = ph.sem("glu_done")
        ps, XH, XL, ident = G["ps"], G["XH"], G["XL"], G["ident"]
        block = ph.block()

        @block.sync
        def _(sp):
            weights.load(sp, Weights.RING)
            sp.dma_start(taps_rows[:, 0:3, :], G["d"]["conv_w"][bass.ds(l, 1), :, :].rearrange("o w (j p) -> j (o w) p", p=P)
                         ).then_inc(taps_loaded, 16)
            sp.dma_start(taps_rows[:, 3:4, :], G["d"]["conv_b"][bass.ds(l, 1), :].rearrange("o (j p) -> j o p", p=P)
                         ).then_inc(taps_loaded, 16)

            def load_mod(n):
                g, k = MOD_CHUNKS[n]
                if n >= 2:
                    sp.wait_ge(mod_added, n - 1)
                sp.dma_start(mod_w[:, n % 2, :], G["d"]["ada_w_2"][bass.ds(l, 1), k * P:(k + 1) * P, g * MOD_COLS:(g + 1) * MOD_COLS]
                             .rearrange("o p n -> p (o n)")).then_inc(mod_loaded[n % 2], 16)

            load_mod(0)
            load_mod(1)
            for j in range(FT):
                weights.load(sp, j + 4)
                for n in mod_step(j):
                    if n + 2 < len(MOD_CHUNKS):
                        load_mod(n + 2)
                if j == 0:
                    sp.dma_start(mod_bias[:, :], G["d"]["ada_b_2"][bass.ds(l, 1), :].rearrange("o (j p) -> (o j) p", p=P)
                                 ).then_inc(mod_bias_loaded, 16)
            weights.then_prefetch(sp, next_weights)
            sp.wait_ge(mod_biased, 1)
            sp.dma_start(G["mod_dram"][bass.ds(l, 1), :].rearrange("o (j p) -> (o j) p", p=P), mod_rows[:, :]).then_inc(mod_stored, 16)
            sp.wait_ge(mod_stored, 16)

        @block.tensor
        def _(pe):
            pe.wait_ge(taps_loaded, 32)
            for w in range(4):
                last = nc.tensor.transpose(ps[7][:, w * P:w * P + 2 * FT], taps_rows[:, w, :], ident[0:2 * FT, 0:2 * FT])
            last.then_inc(taps_turned, 1)
            def sum_mod(g):
                pe.wait_ge(mod_added, KD * (g + 1))
                for c in range(g * MOD_COLS // P, (g + 1) * MOD_COLS // P):
                    last = nc.tensor.matmul(ps[6][:, c:c + 1], mod_sum[:, c * P:(c + 1) * P], G["ones_col"][:, :], start=True, stop=True)
                last.then_inc(mod_summed, 1)

            for i, (j, v) in enumerate(jobs):
                if v == 0 and j in sum_at:
                    sum_mod(sum_at[j])
                pe.wait_ge(weights.split, j + 1)
                if i >= BANKS:
                    pe.wait_ge(conv_done, i - BANKS + 1)
                for k in range(KD):
                    last = split_product(nc, ps[i % BANKS][:, :], weights.parts(j, (v * KD + k) * P, P), (XH[:, k, :], XL[:, k, :]),
                                         k == 0, k == KD - 1)
                last.then_inc(product_done, 1)
            sum_mod(GROUPS_OF - 1)
            pe.wait_ge(mod_copied, 1)
            nc.tensor.transpose(ps[7][0:MOD // P, 0:P], mod_cols[:, :], ident).then_inc(mod_turned, 1)

        @block.scalar
        def _(act):
            act.wait_ge(taps_turned, 1)
            nc.scalar.copy(taps[:, :, :], ps[7][:, :].rearrange("p (w j) -> p w j", w=4)[:, :, 0:2 * FT]).then_inc(taps_copied, 1)
            act.wait_ge(taps_copied, 1)

            def silu(j):
                act.wait_ge(conv_done, 2 * j + 1)
                if j >= 2:
                    act.wait_ge(glu_done, j - 1)
                nc.scalar.activation(gate[:, j % 2, :], conv[:, (2 * j) % 6, :], ACT.Silu).then_inc(silu_done, 1)

            for i, (j, v) in enumerate(jobs):
                ch = v * FT + j
                act.wait_ge(product_done, i + 1)
                if i >= 6:
                    act.wait_ge(glu_done, (i - 6) // 2 + 1)
                nc.scalar.activation(conv[:, i % 6, :], ps[i % BANKS][:, :], ACT.Identity, bias=taps[:, 3, ch:ch + 1],
                                     scale=taps[:, 2, ch:ch + 1]).then_inc(last_tap, 1)
                if v == 1:
                    silu(j)
            act.wait_ge(mod_summed, GROUPS_OF)
            nc.scalar.copy(mod_cols[:, :], ps[6][:, 0:MOD // P]).then_inc(mod_copied, 1)

        @block.vector
        def _(dve):
            last_user = lambda s: (product_done, 2 * (s + 1))
            weights.split_slot(dve, 0)
            weights.split_slot(dve, 1)
            dve.wait_ge(taps_copied, 1)
            for i, (j, v) in enumerate(jobs):
                ch = v * FT + j
                u = ps[i % BANKS]
                dve.wait_ge(last_tap, i + 1)
                nc.vector.scalar_tensor_tensor(conv[:, i % 6, 1:SEQ], u[:, 0:SEQ - 1], taps[:, 1, ch:ch + 1],
                                               conv[:, i % 6, 1:SEQ], ALU.mult, ALU.add).then_inc(dve_tap, 1)
                dve.wait_ge(dve_tap, i + 1)
                nc.vector.scalar_tensor_tensor(conv[:, i % 6, 2:SEQ], u[:, 0:SEQ - 2], taps[:, 0, ch:ch + 1],
                                               conv[:, i % 6, 2:SEQ], ALU.mult, ALU.add).then_inc(conv_done, 1)
                if v == 1:
                    weights.split_slot(dve, j + 2, last_user)
                    for n in mod_step(j):
                        g, k = MOD_CHUNKS[n]
                        total = mod_sum[:, g * MOD_COLS:(g + 1) * MOD_COLS]
                        dve.wait_ge(mod_loaded[n % 2], 16 * (n // 2 + 1))
                        if k == 0:
                            add = nc.vector.tensor_scalar(total, mod_w[:, n % 2, :], G["cond"][:, k:k + 1], None, ALU.mult)
                        else:
                            dve.wait_ge(mod_added, n)
                            add = nc.vector.scalar_tensor_tensor(total, mod_w[:, n % 2, :], G["cond"][:, k:k + 1], total,
                                                                 ALU.mult, ALU.add)
                        add.then_inc(mod_added, 1)
            dve.wait_ge(mod_bias_loaded, 16)
            dve.wait_ge(mod_turned, 1)
            nc.vector.tensor_tensor(mod_rows[:, :], ps[7][0:MOD // P, 0:P], mod_bias[:, :], ALU.add).then_inc(mod_biased, 1)

        @block.gpsimd
        def _(pool):
            for j in range(FT):
                pool.wait_ge(silu_done, j + 1)
                pool.wait_ge(conv_done, 2 * j + 2)
                nc.gpsimd.tensor_tensor(H[:, j, :], gate[:, j % 2, :], conv[:, (2 * j + 1) % 6, :], ALU.mult).then_inc(glu_done, 1)


def views(tile, parts):
    found, at = {}, 0
    for name, a in parts.items():
        found[name] = tile[:, at:at + a.shape[1]]
        at += a.shape[1]
    return found


def parts_room(nc, ctx, G, name):
    sb = lambda n, shape: ctx.enter_context(nc.sbuf_tensor(f"{name}_{n}", shape, F32))
    for n in ("XH", "XL"):
        G[n] = sb(n, [P, KD, SEQ])
    for n in ("w_raw", "w_high", "w_low"):
        G[n] = sb(n, [P, Weights.RING, Weights.SLOT])


def first_block(nc, G, parts):
    d = G["d"]
    with nc.Fori(0, DEPTH) as l:
        with ExitStack() as ctx:
            sb = lambda name, shape: ctx.enter_context(nc.sbuf_tensor(name, shape, F32))
            G["consts"] = sb("consts", list(d["consts"].shape))
            G["c"] = views(G["consts"], parts)
            S = {"Y": sb("mixed", [P, TT, D])}
            for n in ("VR", "VG"):
                S[n] = sb(n, [P, TT, 512])
            with ExitStack() as heads:
                sh = lambda name, shape: heads.enter_context(nc.sbuf_tensor(name, shape, F32))
                for n in ("QR", "KR", "QG", "KG"):
                    S[n] = sh(n, [P, SEQ])
                S["AG"] = sh("AG", [LOW_RANK, SEQ])
                with ExitStack() as wide:
                    for n in ("QA", "KA", "VA"):
                        S[n] = wide.enter_context(nc.sbuf_tensor(n, [P, 4, SEQ], F32))
                    project_phase(nc, l, G, S, project_weights(nc, l, G))
                    dilated_phase(nc, l, G, S)
                retention_phase(nc, G, S)
                gla_phase(nc, l, G, S)
            mix_weights = row_weights(nc, "mix_out", layer_rows(d["w_out"], l), KD, G)
            head_norm_phase(nc, l, G, S, mix_weights)
        up = up_weights(nc, l, G)
        output_norm_phase(nc, "mix_out", l, G, None, mix_weights, d["ln1_g"], d["ln1_b"], up)
        with ExitStack() as ctx:
            H = ctx.enter_context(nc.sbuf_tensor("hidden", [P, FT, SEQ], F32))
            down = row_weights(nc, "ffn_down", layer_rows(d["w_down"], l), FT, G)
            ffn_up_phase(nc, l, G, H, up, down)
            output_norm_phase(nc, "ffn_down", l, G, H, down, d["ln2_g"], d["ln2_b"])


A_W = 512
CONV_A, CONV_B = 3, 31
HEADS_C, HD_C = 8, 64
IDX_HEADS, IDX_DIM = 8, 32
TOPK = min(256, SEQ // 4)
HEADS_D, HD_D = 4, 64
BUCKETS, MAX_DIST = 32, 128
HEADS_ALL = HEADS_C + HEADS_D
GROUPS, PER_GROUP = 4, 8
EXPERTS = GROUPS * PER_GROUP
D_EXP = 512
TOP_E = 2
SLOT_ROWS = P
MAX_BLOCKS = -(-SEQ // SLOT_ROWS)
SPARE = (SEQ * TOP_E - 1) // (SLOT_ROWS + 1)
BLOCKS = -(-(EXPERTS + SPARE) // 2) * 2
LEAST_PAIRS = SEQ * TOP_E // SLOT_ROWS // 2
LAMBDA_INIT = 0.8 - 0.6 * float(np.exp(-0.3 * 1))
DROPPED = -3.0e38
FAR = float(2 ** 30)


def bucket_starts():
    n = np.arange(4 * MAX_DIST)
    exact = BUCKETS // 2
    ratio = np.log(np.maximum(n, 1).astype(np.float32) / np.float32(exact)) / np.float32(np.log(MAX_DIST / exact))
    large = exact + (ratio * np.float32(BUCKETS - exact)).astype(np.int32)
    b = np.where(n < exact, n, np.minimum(large, BUCKETS - 1))
    starts = np.array([np.flatnonzero(b >= i)[0] for i in range(BUCKETS)], np.float64)
    starts[0] = -FAR
    return starts


def constant_parts_2():
    parts = {}
    parts["ones"] = np.ones((P, P), np.float32)
    parts["before"] = (np.arange(P)[:, None] < np.arange(P)[None, :]).astype(np.float32)
    parts["bucket_start"] = np.tile(bucket_starts(), P // BUCKETS)[:, None].astype(np.float32)
    parts["tile_block"] = (np.arange(P)[:, None] // BUCKETS == np.arange(TT)[None, :]).astype(np.float32)
    parts["index_e"] = np.broadcast_to(np.arange(EXPERTS, dtype=np.float32), (P, EXPERTS))
    parts["index_e_less"] = np.broadcast_to(np.arange(EXPERTS, dtype=np.float32) - EXPERTS, (P, EXPERTS))
    parts["index_block"] = np.broadcast_to(np.arange(BLOCKS, dtype=np.float32), (P, BLOCKS))
    parts["token_id"] = (np.arange(TT)[None, :] * P + np.arange(P)[:, None]).astype(np.float32)
    return parts


def row_of(ap, n):
    return ap.to_broadcast([P, n])


def second_load_phase(nc, G):
    with Phase(nc, "second_load") as ph:
        loaded = ph.sem("loaded")
        block = ph.block()

        @block.sync
        def _(sp):
            sp.dma_start(G["consts2"][:, :], G["d"]["consts2"][:, :]).then_inc(loaded, 16)
            sp.wait_ge(loaded, 16)


def norm_mod_phase(nc, name, G, g_dram, shift, scale, XT=None, h_dram=None, following=None, room=None, layer=None):
    with Phase(nc, name) as ph:
        gain = ph.sb("gain", [P, D])
        both = ph.sb("gain_scaled", [P, D])
        sq = ph.sb("squares", [P, D])
        ss = ph.sb("square_sum", [P, TT])
        std = ph.sb("std", [P, TT])
        rstd = ph.sb("rstd", [P, TT])
        part, h = room if room is not None else (ph.sb("scaled_rows", [P, TT, D]), ph.sb("rows", [P, TT, D]))
        loaded = ph.sem("loaded")
        squared = ph.sem("squared")
        std_done = ph.sem("std_done")
        gain_done = ph.sem("gain_done")
        inv_done = ph.sem("inv_done")
        scaled = ph.sem("scaled")
        shifted = ph.sem("shifted")
        turned = ph.sem("turned")
        copied = ph.sem("copied")
        stored = ph.sem("stored")
        mod_loaded = [ph.sem(f"mod_loaded{r}") for r in range(3)]
        ps, X = G["ps"], G["X"]
        split = Split(nc, ph, G, turned, lambda t, j: ps[2 * t + j])
        block = ph.block()

        @block.sync
        def _(sp):
            sp.dma_start(gain[:, :], row_of(g_dram, D)).then_inc(loaded, 16)
            if layer is not None:
                for r, (c0, c1) in enumerate(((D, 2 * D), (0, D), (2 * D, MOD))):
                    sp.dma_start(G["mod"][:, c0:c1], row_of(G["mod_dram"][layer:layer + 1, c0:c1], c1 - c0)).then_inc(mod_loaded[r], 16)
            if following is not None:
                following.load(sp, Weights.RING)
            if layer is not None:
                sp.wait_ge(mod_loaded[2], 16)
            if h_dram is not None:
                for t in range(TT):
                    sp.wait_ge(shifted, t + 1)
                    sp.dma_start(h_dram[t * P:(t + 1) * P, :], h[:, t, :]).then_inc(stored, 16)
                sp.wait_ge(stored, 16 * TT)

        @block.scalar
        def _(act):
            for t in range(TT):
                if t:
                    act.wait_ge(squared, t)
                nc.scalar.activation(sq[:, :], X[:, t, :], ACT.Square, accum_out=ss[:, t:t + 1]).then_inc(squared, 1)
            act.wait_ge(squared, TT)
            nc.scalar.activation(std[:, :], ss[:, :], ACT.Sqrt, scale=1.0 / D, bias=G["eps_norm"][:, :]).then_inc(std_done, 1)
            if XT is None:
                split.high_parts(act)
                return
            for t in range(TT):
                for j in range(2):
                    act.wait_ge(turned, 2 * t + j + 1)
                    nc.scalar.copy(XT[:, 4 * j:4 * j + 4, t * P:(t + 1) * P],
                                   ps[2 * t + j][:, :].rearrange("p (k n) -> p k n", k=4)).then_inc(copied, 1)

        @block.vector
        def _(dve):
            dve.wait_ge(loaded, 16)
            if layer is not None:
                dve.wait_ge(mod_loaded[0], 16)
            nc.vector.scalar_tensor_tensor(both[:, :], scale, 1.0, gain[:, :], ALU.add, ALU.mult).then_inc(gain_done, 1)
            dve.wait_ge(std_done, 1)
            nc.vector.reciprocal(rstd[:, :], std[:, :]).then_inc(inv_done, 1)
            dve.wait_ge(inv_done, 1)
            dve.wait_ge(gain_done, 1)
            for t in range(TT):
                nc.vector.scalar_tensor_tensor(part[:, t, :], X[:, t, :], rstd[:, t:t + 1], both[:, :], ALU.mult, ALU.mult
                                               ).then_inc(scaled, 1)
            if XT is None:
                for t in range(TT):
                    split.low_parts(dve, t)

        @block.gpsimd
        def _(pool):
            if layer is not None:
                pool.wait_ge(mod_loaded[1], 16)
            for t in range(TT):
                pool.wait_ge(scaled, t + 1)
                nc.gpsimd.tensor_tensor(h[:, t, :], part[:, t, :], shift, ALU.add).then_inc(shifted, 1)

        @block.tensor
        def _(pe):
            for t in range(TT):
                pe.wait_ge(shifted, t + 1)
                for j in range(2):
                    for n in range(4):
                        k = 4 * j + n
                        last = nc.tensor.transpose(ps[2 * t + j][:, n * P:(n + 1) * P], h[:, t, k * P:(k + 1) * P], G["ident"])
                    last.then_inc(turned, 1)


GATE_B, GATE_C, X_A, VAL_B, GLU = range(5)
CONV_JOBS = [job for m in range(4) for job in ((GLU, m), (VAL_B, m))]
CONV_JOBS += [job for m in range(4) for job in ((GATE_C, m), (X_A, m))]
CONV_JOBS += [(GATE_B, m) for m in range(4)]


def conv_weights(nc, G):
    w = lambda part, m: G["d"]["ab_w_in_2"][0, :, part * A_W + m * P:part * A_W + (m + 1) * P].rearrange("(k p) n -> p k n", p=P)
    return Weights(nc, G, "conv_mix", [[(0, KD, P, w(*CONV_JOBS[i])), (KD * P, KD, P, w(*CONV_JOBS[i + 1]))]
                                       for i in range(0, len(CONV_JOBS), 2)])


def conv_mix_phase(nc, G, weights, following):
    FIRST_TAPS = 17
    jobs = CONV_JOBS
    BANKS = 6
    ROWS = 4 * CONV_B
    PAD_A, PAD_B = CONV_A - 1, CONV_B - 1
    with Phase(nc, "conv_mix") as ph:
        ph.sems += weights.sems
        ta_rows = ph.sb("taps_a_rows", [4 * CONV_A, P])
        tb_rows = ph.sb("taps_b_rows", [ROWS, P])
        vec_rows = ph.sb("vector_rows", [12, P])
        taps_a = ph.sb("taps_a", [P, 4 * CONV_A])
        taps_b = ph.sb("taps_b", [P, ROWS])
        vecs = ph.sb("vectors", [P, 12])
        mean_w = ph.sb("mean_weights", [P, P])
        glu = ph.sb("glu", [P, 4, SEQ])
        gc = ph.sb("gate_c", [P, 4, SEQ])
        ub = ph.sb("u_b", [P, 4, PAD_B + SEQ])
        pa = ph.sb("p_a", [P, 4, PAD_A + SEQ])
        ca = ph.sb("conv_a", [P, 4, SEQ])
        cb = ph.sb("conv_b", [P, 4, SEQ])
        sq = ph.sb("squares", [P, 4, SEQ])
        std = ph.sb("std", [P, SEQ])
        rstd = ph.sb("rstd", [P, SEQ])
        rows_loaded = ph.sem("rows_loaded")
        rows_turned = ph.sem("rows_turned")
        rows_copied = ph.sem("rows_copied")
        mix_high = ph.sem("mix_high")
        mix_low = ph.sem("mix_low")
        pads_set = ph.sem("pads_set")
        product_done = ph.sem("product_done")
        by_act = ph.sem("evacuated_by_act")
        by_dve = ph.sem("evacuated_by_dve")
        a_step = ph.sem("a_step")
        b_step = ph.sem("b_step")
        b_conv_done = ph.sem("b_conv_done")
        mean_done = ph.sem("mean_done")
        centred = ph.sem("centred")
        squared = ph.sem("squared")
        var_done = ph.sem("var_done")
        std_done = ph.sem("std_done")
        inv_done = ph.sem("inv_done")
        normed = ph.sem("normed")
        out_done = ph.sem("out_done")
        ps, XH, XL, ident = G["ps"], G["XH"], G["XL"], G["ident"]
        mixed = [glu[:, m, :] for m in range(4)] + [gc[:, m, :] for m in range(4)]
        last_user = lambda s: (product_done, 2 * (s + 1))
        reader = ["act" if part in (GLU, GATE_C) else "dve" for part, _ in jobs]
        count = {"act": 0, "dve": 0}
        freed = []
        for r in reader:
            count[r] += 1
            freed.append(count[r])
        block = ph.block()

        @block.sync
        def _(sp):
            sp.dma_start(ta_rows[:, :], G["d"]["ab_conv_a_2"][0].rearrange("w (m p) -> (w m) p", p=P)).then_inc(rows_loaded, 16)
            sp.dma_start(tb_rows[:, :], G["d"]["ab_conv_b_2"][0].rearrange("w (m p) -> (w m) p", p=P)).then_inc(rows_loaded, 16)
            for v, name in enumerate(("ab_conv_b_bias_2", "ab_ln_g_2", "ab_ln_b_2")):
                sp.dma_start(vec_rows[4 * v:4 * v + 4, :], G["d"][name][0:1, :].rearrange("o (m p) -> (o m) p", p=P)
                             ).then_inc(rows_loaded, 16)
            weights.load(sp)
            weights.then_prefetch(sp, following)

        @block.tensor
        def _(pe):
            pe.wait_ge(rows_loaded, 80)
            nc.tensor.transpose(ps[7][:, 0:ROWS], tb_rows[:, :], ident[0:ROWS, 0:ROWS])
            nc.tensor.transpose(ps[7][:, 128:128 + 12], ta_rows[:, :], ident[0:12, 0:12])
            nc.tensor.transpose(ps[7][:, 256:256 + 12], vec_rows[:, :], ident[0:12, 0:12]).then_inc(rows_turned, 1)
            for i in range(len(jobs)):
                pe.wait_ge(weights.split, i // 2 + 1)
                if i >= BANKS:
                    j = i - BANKS
                    pe.wait_ge(by_act if reader[j] == "act" else by_dve, freed[j])
                for k in range(KD):
                    last = split_product(nc, ps[i % BANKS][:, :], weights.parts(i // 2, (i % 2 * KD + k) * P, P),
                                         (XH[:, k, :], XL[:, k, :]), k == 0, k == KD - 1)
                last.then_inc(product_done, 1)
            pe.wait_ge(by_dve, count["dve"])
            for m in range(4):
                pe.wait_ge(b_conv_done, m + 1)
                last = nc.tensor.matmul(ps[6][:, :], mean_w[:, :], cb[:, m, :], start=(m == 0), stop=(m == 3))
            last.then_inc(mean_done, 1)
            for m in range(4):
                pe.wait_ge(squared, m + 1)
                last = nc.tensor.matmul(ps[7][:, :], mean_w[:, :], sq[:, m, :], start=(m == 0), stop=(m == 3))
            last.then_inc(var_done, 1)

        @block.scalar
        def _(act):
            act.wait_ge(rows_turned, 1)
            nc.scalar.copy(taps_b[:, :], ps[7][:, 0:ROWS]).then_inc(rows_copied, 1)
            nc.scalar.copy(taps_a[:, :], ps[7][:, 128:140]).then_inc(rows_copied, 1)
            nc.scalar.copy(vecs[:, :], ps[7][:, 256:268]).then_inc(rows_copied, 1)
            act.wait_ge(weights.split, 2)
            for i, (part, m) in enumerate(jobs):
                if part == GLU:
                    act.wait_ge(product_done, i + 1)
                    nc.scalar.activation(glu[:, m, :], ps[i % BANKS][:, :], ACT.Sigmoid).then_inc(by_act, 1)
                elif part == GATE_C:
                    act.wait_ge(product_done, i + 1)
                    nc.scalar.copy(gc[:, m, :], ps[i % BANKS][:, :]).then_inc(by_act, 1)
                if i % 2 == 1 and i // 2 + 2 < len(weights.loads):
                    weights.split_high(act, i // 2 + 2, last_user)
            for m in range(4):
                act.wait_ge(centred, m + 1)
                nc.scalar.activation(sq[:, m, :], cb[:, m, :], ACT.Square).then_inc(squared, 1)
            act.wait_ge(var_done, 1)
            nc.scalar.activation(std[:, :], ps[7][:, :], ACT.Sqrt, bias=G["eps_norm"][:, :]).then_inc(std_done, 1)
            act.wait_ge(rows_copied, 3)
            for m in range(4):
                act.wait_ge(normed, m + 1)
                nc.scalar.activation(mixed[4 + m], cb[:, m, :], ACT.Silu, scale=vecs[:, 4 + m:5 + m], bias=vecs[:, 8 + m:9 + m]
                                     ).then_inc(out_done, 1)

        @block.gpsimd
        def _(pool):
            nc.gpsimd.memset(ub[:, :, 0:PAD_B], 0.0).then_inc(pads_set, 1)
            nc.gpsimd.memset(pa[:, :, 0:PAD_A], 0.0).then_inc(pads_set, 1)
            nc.gpsimd.memset(mean_w[:, :], 1.0 / A_W).then_inc(pads_set, 1)
            for sl in range(2, len(weights.loads)):
                weights.split_low(pool, sl)
            for m in range(8):
                pool.wait_ge(mix_high, m + 1)
                nc.gpsimd.tensor_tensor(rounded(XL[:, m, :]), mixed[m], XH[:, m, :], ALU.subtract).then_inc(mix_low, 1)

        @block.vector
        def _(dve):
            achain, bchain = Chain(dve, a_step), Chain(dve, b_step)
            for sl in range(2):
                weights.split_slot(dve, sl)
            dve.wait_ge(rows_copied, 3)
            dve.wait_ge(pads_set, 3)
            evac = 0

            def conv_b(m, first, last_tap):
                for w in range(first, last_tap):
                    tap = taps_b[:, 4 * w + m:4 * w + m + 1]
                    if w == 0:
                        bchain.link(nc.vector.tensor_scalar(cb[:, m, :], ub[:, m, 0:SEQ], tap, vecs[:, m:m + 1], ALU.mult, ALU.add))
                    else:
                        ins = nc.vector.scalar_tensor_tensor(cb[:, m, :], ub[:, m, w:w + SEQ], tap, cb[:, m, :], ALU.mult, ALU.add)
                        if w == CONV_B - 1:
                            ins.then_inc(b_conv_done, 1)
                        else:
                            bchain.link(ins)

            for i, (part, m) in enumerate(jobs):
                if reader[i] == "act":
                    continue
                evac += 1
                dve.wait_ge(product_done, i + 1)
                if part == VAL_B:
                    dve.wait_ge(by_act, m + 1)
                    nc.vector.tensor_tensor(ub[:, m, PAD_B:], ps[i % BANKS][:, :], glu[:, m, :], ALU.mult).then_inc(by_dve, 1)
                    dve.wait_ge(by_dve, evac)
                    conv_b(m, 0, FIRST_TAPS)
                elif part == X_A:
                    dve.wait_ge(by_act, 4 + m + 1)
                    nc.vector.tensor_tensor(pa[:, m, PAD_A:], ps[i % BANKS][:, :], gc[:, m, :], ALU.mult).then_inc(by_dve, 1)
                    dve.wait_ge(by_dve, evac)
                    achain.link(nc.vector.tensor_scalar(ca[:, m, :], pa[:, m, 0:SEQ], taps_a[:, m:m + 1], None, ALU.mult))
                    for w in range(1, CONV_A):
                        achain.link(nc.vector.scalar_tensor_tensor(ca[:, m, :], pa[:, m, w:w + SEQ],
                                                                   taps_a[:, 4 * w + m:4 * w + m + 1], ca[:, m, :],
                                                                   ALU.mult, ALU.add))
                    conv_b(m, FIRST_TAPS, CONV_B)
                else:
                    nc.vector.tensor_tensor(mixed[m], ps[i % BANKS][:, :], ca[:, m, :], ALU.mult).then_inc(by_dve, 1)
            dve.wait_ge(by_dve, count["dve"])
            for m in range(4):
                nc.vector.tensor_copy(rounded(XH[:, m, :]), mixed[m]).then_inc(mix_high, 1)
            dve.wait_ge(mean_done, 1)
            for m in range(4):
                nc.vector.tensor_tensor(cb[:, m, :], cb[:, m, :], ps[6][:, :], ALU.subtract).then_inc(centred, 1)
            dve.wait_ge(std_done, 1)
            nc.vector.reciprocal(rstd[:, :], std[:, :]).then_inc(inv_done, 1)
            dve.wait_ge(inv_done, 1)
            dve.wait_ge(squared, 4)
            for m in range(4):
                nc.vector.tensor_tensor(cb[:, m, :], cb[:, m, :], rstd[:, :], ALU.mult).then_inc(normed, 1)
            for m in range(4):
                dve.wait_ge(out_done, m + 1)
                nc.vector.tensor_copy(rounded(XH[:, 4 + m, :]), mixed[4 + m]).then_inc(mix_high, 1)


def gated_residual_phase(nc, name, G, weights, gate, part=None):
    with Phase(nc, name) as ph:
        ph.sems += weights.sems
        part = part if part is not None else ph.sb("gated", [P, 4, BANK])
        product_done = ph.sem("product_done")
        gated = ph.sem("gated_done")
        added = ph.sem("added")
        ps, X, XH, XL = G["ps"], G["X"], G["XH"], G["XL"]
        block = ph.block()

        @block.sync
        def _(sp):
            weights.load(sp)

        @block.tensor
        def _(pe):
            acts = lambda s, k, toks: (XH[:, ROW_TILES * s + k, toks], XL[:, ROW_TILES * s + k, toks])
            row_products(nc, pe, ps, weights, acts, None, product_done)

        @block.vector
        def _(dve):
            for s in range(len(weights.loads)):
                weights.split_slot(dve, s)
            for j in range(2 * TT):
                c = j % 2
                dve.wait_ge(product_done, j + 1)
                if j >= 4:
                    dve.wait_ge(added, j - 3)
                nc.vector.tensor_tensor(part[:, j % 4, :], ps[j][:, :], gate[:, c * BANK:(c + 1) * BANK], ALU.mult
                                        ).then_inc(gated, 1)

        @block.gpsimd
        def _(pool):
            for j in range(2 * TT):
                t, c = j // 2, j % 2
                pool.wait_ge(gated, j + 1)
                xs = X[:, t, c * BANK:(c + 1) * BANK]
                nc.gpsimd.tensor_tensor(xs, xs, part[:, j % 4, :], ALU.add).then_inc(added, 1)


def router_phase(nc, i, G, XT, following):
    LG = GROUPS + EXPERTS
    with Phase(nc, f"router{i}") as ph:
        wr = ph.sb("w_router", [P, KD, LG])
        br = ph.sb("b_router", [P, LG])
        L = ph.sb("logits", [P, TT, LG])
        small = lambda name, n=1: ph.sb(name, [P, TT, n])
        gmax, gexp, gsum, ptop = small("gmax"), small("gexp", GROUPS), small("gsum"), small("ptop")
        geq, gval, gidx, goh, gpen = (small("geq", GROUPS), small("gval", GROUPS), small("gidx"), small("goh", GROUPS),
                                      small("gpen", GROUPS))
        fine, fine2 = small("fine", EXPERTS), small("fine2", EXPERTS)
        top = [small("top0"), small("top1")]
        eq, val = small("eq", EXPERTS), small("val", EXPERTS)
        idx = [small("idx0"), small("idx1")]
        oh = [small("oh0", EXPERTS), small("oh1", EXPERTS)]
        both = small("both", EXPERTS)
        diff, dexp, dsum, dinv = small("diff"), small("dexp"), small("dsum"), small("dinv")
        rank = small("rank", EXPERTS)
        cnt = ph.sb("count", [P, EXPERTS])
        more = ph.sb("more", [P, MAX_BLOCKS, EXPERTS])
        n_blocks = ph.sb("n_blocks", [P, EXPERTS])
        block_end = ph.sb("block_end", [P, EXPERTS])
        block_start = ph.sb("block_start", [P, EXPERTS])
        ends_at = ph.sb("ends_at", [P, BLOCKS, EXPERTS])
        block_exp = ph.sb("block_expert", [P, BLOCKS])
        half = ph.sb("half_of_blocks", [P, 1])
        pair_used = ph.sb("pair_used", [P, BLOCKS])
        pairs = ph.sb("pairs", [P, 1])
        prod = small("prod", EXPERTS)
        r, b, blk, blkno, local = small("r"), small("b"), small("blk"), small("blkno"), small("local")
        place, yrow = small("place"), small("yrow")
        place_i = [ph.sb(f"place_i{k}", [P, TT], I32) for k in range(TOP_E)]
        tok = ph.sb("token_id", [P, TT], I32)
        zero = ph.sb("zero", [P, BLOCKS], I32)
        loaded = ph.sem("loaded")
        zero_set = ph.sem("zero_set")
        cleared = ph.sem("cleared")
        logits_done = ph.sem("logits_done")
        logits_read = ph.sem("logits_read")
        dve_step = ph.sem("dve_step")
        gmax_done = ph.sem("gmax_done")
        gexp_done = ph.sem("gexp_done")
        diff_done = ph.sem("diff_done")
        dexp_done = ph.sem("dexp_done")
        chosen = ph.sem("chosen")
        ranked = ph.sem("ranked")
        placed = ph.sem("placed")
        scattered = ph.sem("scattered")
        read_back = ph.sem("read_back")
        ps, c2 = G["ps"], G["c2"]
        spread = lambda a, n: a.to_broadcast([P, TT, n])
        rows = lambda a, n: a.rearrange("p (o n) -> p o n", o=1).to_broadcast([P, TT, n])
        block = ph.block()

        @block.sync
        def _(sp):
            sp.dma_start(wr[:, :, 0:GROUPS], G["d"]["moe_wr_g_2"][i].rearrange("(k p) n -> p k n", p=P)).then_inc(loaded, 16)
            sp.dma_start(wr[:, :, GROUPS:LG], G["d"]["moe_wr_e_2"][i].rearrange("(k p) n -> p k n", p=P)).then_inc(loaded, 16)
            sp.dma_start(br[:, 0:GROUPS], row_of(G["d"]["moe_br_g_2"][i:i + 1, :], GROUPS)).then_inc(loaded, 16)
            sp.dma_start(br[:, GROUPS:LG], row_of(G["d"]["moe_br_e_2"][i:i + 1, :], EXPERTS)).then_inc(loaded, 16)
            following.first_loads(sp)
            sp.wait_ge(zero_set, 1)
            sp.dma_start(G["slot_dram"][:, :].rearrange("(p b) o -> p (b o)", p=P), zero[:, :]).then_inc(cleared, 16)
            sp.wait_ge(scattered, 16 * TT * TOP_E)
            sp.dma_start(G["slot_token"][:, :], G["slot_dram"][:, :].rearrange("(p b) o -> p (b o)", p=P)).then_inc(read_back, 16)
            sp.wait_ge(read_back, 16)

        @block.tensor
        def _(pe):
            pe.wait_ge(loaded, 64)
            for t in range(TT):
                for k in range(KD):
                    last = nc.tensor.matmul(ps[t][:, 0:LG], XT[:, k, t * P:(t + 1) * P], wr[:, k, :], start=(k == 0),
                                            stop=(k == KD - 1))
                last.then_inc(logits_done, 1)
            pe.wait_ge(chosen, 1)
            for t in range(TT + 1):
                for s in range(min(t + 1, TT)):
                    last = nc.tensor.matmul(ps[4][:, t * EXPERTS:(t + 1) * EXPERTS], c2["before" if s == t else "ones"],
                                            both[:, s, :], start=(s == 0), stop=(s == min(t, TT - 1)))
            last.then_inc(ranked, 1)

        @block.scalar
        def _(act):
            act.wait_ge(gmax_done, 1)
            nc.scalar.activation(gexp[:, :, :], gval[:, :, :], ACT.Exp).then_inc(gexp_done, 1)
            act.wait_ge(diff_done, 1)
            nc.scalar.activation(dexp[:, :, :], diff[:, :, :], ACT.Exp).then_inc(dexp_done, 1)

        @block.gpsimd
        def _(pool):
            nc.gpsimd.memset(zero[:, :], 0).then_inc(zero_set, 1)
            pool.wait_ge(cleared, 16)
            for k in range(TOP_E):
                pool.wait_ge(placed, k + 1)
                for t in range(TT):
                    pool.indirect_dma_start(G["slot_dram"][:, :], bass.IndirectOffsetOnAxis(ap=place_i[k][:, t:t + 1], axis=0),
                                            tok[:, t:t + 1], None).then_inc(scattered, 16)

        @block.vector
        def _(dve):
            V = nc.vector
            link = Chain(dve, dve_step).link
            dve.wait_ge(loaded, 64)
            link(V.tensor_copy(tok[:, :], c2["token_id"]))
            for t in range(TT):
                dve.wait_ge(logits_done, t + 1)
                V.tensor_tensor(L[:, t, :], ps[t][:, 0:LG], br[:, :], ALU.add).then_inc(logits_read, 1)
            dve.wait_ge(logits_read, TT)
            lg = L[:, :, 0:GROUPS]
            link(V.tensor_reduce(gmax[:, :, :], lg, AX_X, ALU.max))
            V.tensor_tensor(gval[:, :, :], lg, spread(gmax[:, :, :], GROUPS), ALU.subtract).then_inc(gmax_done, 1)
            link(V.tensor_tensor(geq[:, :, :], lg, spread(gmax[:, :, :], GROUPS), ALU.is_equal))
            link(V.tensor_tensor(gpen[:, :, :], geq[:, :, :], rows(c2["index_e_less"][:, 0:GROUPS], GROUPS), ALU.mult))
            link(V.tensor_reduce(gidx[:, :, :], gpen[:, :, :], AX_X, ALU.min))
            link(V.tensor_tensor(goh[:, :, :], rows(c2["index_e_less"][:, 0:GROUPS], GROUPS), spread(gidx[:, :, :], GROUPS),
                                 ALU.is_equal))
            link(V.tensor_scalar(gpen[:, :, :], goh[:, :, :], 1.0, -NEG, ALU.subtract, ALU.mult))
            dve.wait_ge(gexp_done, 1)
            link(V.tensor_reduce(gsum[:, :, :], gexp[:, :, :], AX_X, ALU.add))
            link(V.reciprocal(ptop[:, :, :], gsum[:, :, :]))
            for t in range(TT):
                four = lambda a: a[:, t, :].rearrange("p (g o) -> p g o", o=1).to_broadcast([P, GROUPS, PER_GROUP])
                view = lambda a: a.rearrange("p (g e) -> p g e", g=GROUPS)
                link(V.tensor_tensor(view(fine2[:, t, :]), view(L[:, t, GROUPS:LG]), four(goh), ALU.mult))
                link(V.tensor_tensor(view(fine[:, t, :]), view(fine2[:, t, :]), four(gpen), ALU.add))
            for k in range(TOP_E):
                link(V.tensor_reduce(top[k][:, :, :], fine[:, :, :], AX_X, ALU.max))
                link(V.tensor_tensor(eq[:, :, :], fine[:, :, :], spread(top[k][:, :, :], EXPERTS), ALU.is_equal))
                link(V.tensor_tensor(val[:, :, :], eq[:, :, :], rows(c2["index_e_less"], EXPERTS), ALU.mult))
                link(V.tensor_reduce(idx[k][:, :, :], val[:, :, :], AX_X, ALU.min))
                link(V.tensor_tensor(oh[k][:, :, :], rows(c2["index_e_less"], EXPERTS), spread(idx[k][:, :, :], EXPERTS), ALU.is_equal))
                if k == 0:
                    link(V.scalar_tensor_tensor(fine[:, :, :], oh[0][:, :, :], 3.0 * NEG, fine[:, :, :], ALU.mult, ALU.add))
            V.tensor_tensor(both[:, :, :], oh[0][:, :, :], oh[1][:, :, :], ALU.add).then_inc(chosen, 1)
            V.tensor_tensor(diff[:, :, :], top[1][:, :, :], top[0][:, :, :], ALU.subtract).then_inc(diff_done, 1)
            dve.wait_ge(dexp_done, 1)
            link(V.tensor_scalar(dsum[:, :, :], dexp[:, :, :], 1.0, None, ALU.add))
            link(V.reciprocal(dinv[:, :, :], dsum[:, :, :]))
            link(V.tensor_tensor(G["gate"][:, 0, :], ptop[:, :, 0], dinv[:, :, 0], ALU.mult))
            link(V.tensor_tensor(G["gate"][:, 1, :], G["gate"][:, 0, :], dexp[:, :, 0], ALU.mult))
            dve.wait_ge(ranked, 1)
            link(V.tensor_copy(rank[:, :, :], ps[4][:, 0:TT * EXPERTS].rearrange("p (t e) -> p t e", t=TT)))
            link(V.tensor_copy(cnt[:, :], ps[4][:, TT * EXPERTS:(TT + 1) * EXPERTS]))
            for m in range(MAX_BLOCKS):
                link(V.tensor_scalar(more[:, m, :], cnt[:, :], float(m * P), None, ALU.is_gt))
            link(V.tensor_tensor(n_blocks[:, :], more[:, 0, :], more[:, 1, :], ALU.add))
            for m in range(2, MAX_BLOCKS):
                link(V.tensor_tensor(n_blocks[:, :], n_blocks[:, :], more[:, m, :], ALU.add))
            link(V.tensor_scalar(n_blocks[:, 0:1], n_blocks[:, 0:1], 1.0, None, ALU.max))
            link(V.tensor_tensor_scan(block_end[:, :], c2["ones"][:, 0:EXPERTS], n_blocks[:, :], 0.0, ALU.mult, ALU.add))
            link(V.tensor_tensor(block_start[:, :], block_end[:, :], n_blocks[:, :], ALU.subtract))
            link(V.tensor_tensor(ends_at[:, :, :], block_end[:, :].rearrange("p (o e) -> p o e", o=1).to_broadcast([P, BLOCKS, EXPERTS]),
                                 c2["index_block"].rearrange("p (s o) -> p s o", o=1).to_broadcast([P, BLOCKS, EXPERTS]), ALU.is_le))
            link(V.tensor_reduce(block_exp[:, :], ends_at[:, :, :], AX_X, ALU.add))
            link(V.tensor_scalar(block_exp[:, :], block_exp[:, :], float(EXPERTS - 1), None, ALU.min))
            link(V.tensor_copy(G["block_table"][:, 0:BLOCKS], block_exp[:, :]))
            link(V.tensor_scalar(half[:, :], block_end[:, EXPERTS - 1:EXPERTS], 0.5, None, ALU.mult))
            link(V.tensor_tensor(pair_used[:, :], c2["index_block"], half[:, :].to_broadcast([P, BLOCKS]), ALU.is_lt))
            link(V.tensor_reduce(pairs[:, :], pair_used[:, :], AX_X, ALU.add))
            link(V.tensor_scalar(pairs[:, :], pairs[:, :], float(LEAST_PAIRS), None, ALU.subtract))
            link(V.tensor_copy(G["block_table"][:, BLOCKS:BLOCKS + 1], pairs[:, :]))
            for k in range(TOP_E):
                link(V.tensor_tensor(prod[:, :, :], rank[:, :, :], oh[k][:, :, :], ALU.mult))
                link(V.tensor_reduce(r[:, :, :], prod[:, :, :], AX_X, ALU.add))
                link(V.tensor_tensor(prod[:, :, :], rows(block_start[:, :], EXPERTS), oh[k][:, :, :], ALU.mult))
                link(V.tensor_reduce(b[:, :, :], prod[:, :, :], AX_X, ALU.add))
                link(V.tensor_scalar(blk[:, :, :], r[:, :, :], float(P), None, ALU.is_ge))
                for m in range(1, MAX_BLOCKS - 1):
                    link(V.scalar_tensor_tensor(blk[:, :, :], r[:, :, :], float((m + 1) * P), blk[:, :, :], ALU.is_ge, ALU.add))
                link(V.scalar_tensor_tensor(local[:, :, :], blk[:, :, :], -float(P), r[:, :, :], ALU.mult, ALU.add))
                link(V.tensor_tensor(blkno[:, :, :], b[:, :, :], blk[:, :, :], ALU.add))
                link(V.scalar_tensor_tensor(place[:, :, :], local[:, :, :], float(BLOCKS), blkno[:, :, :], ALU.mult, ALU.add))
                link(V.scalar_tensor_tensor(yrow[:, :, :], blkno[:, :, :], float(P), local[:, :, :], ALU.mult, ALU.add))
                link(V.tensor_copy(G["y_row"][k][:, :], yrow[:, :, 0]))
                V.tensor_copy(place_i[k][:, :], place[:, :, 0]).then_inc(placed, 1)


class Step:

    def __init__(self, odd, j=None, lowest=0, last=False, end=False):
        self.odd, self.j, self.lowest = odd, j, lowest
        self.last, self.end = last, end
        self.parity = odd % 2

    def at(self, times, plus=0):
        here = times * self.odd + plus
        return here if self.j is None else self.j * (2 * times) + here

    def halved(self, times, plus):
        here = times * ((self.odd + plus) // 2)
        return here if self.j is None else self.j * times + here

    def least(self):
        return 2 * self.lowest + self.odd


PEELED = 4


def further_pairs(eng, G):
    return eng.value_load(G["block_table"][0:1, BLOCKS:BLOCKS + 1], min_val=0, max_val=BLOCKS // 2 - LEAST_PAIRS)


def block_steps(eng, further, step):
    for e in range(PEELED):
        step(Step(e))
    with eng.Fori(PEELED // 2, BLOCKS // 2 - 1) as j:
        with eng.If(further + (LEAST_PAIRS - 1) > j):
            for odd in range(2):
                step(Step(odd, j, PEELED // 2))
    fewest = 2 * LEAST_PAIRS
    step(Step(fewest - 2, further))
    step(Step(fewest - 1, further, last=True))
    step(Step(fewest, further, end=True))


UP_SLOTS, DOWN_SLOTS, PART_PLACES = 4, 2, 3
PLACES = UP_SLOTS + DOWN_SLOTS
KU = KD // 2
KDN = D_EXP // P // DOWN_SLOTS


class ExpertWeights:

    def __init__(self, nc, ctx, i, G):
        self.i, self.d = i, G["d"]
        self.raw = ctx.enter_context(nc.sbuf_tensor(f"expert{i}_w_raw", [P, PLACES, Weights.SLOT], F32))
        self.loaded = [nc.alloc_semaphore(f"expert{i}_w_loaded{r}") for r in range(PLACES)]

    def load(self, sp, r, e):
        name = ("moe_w_gate_2", "moe_w_gate_2", "moe_w_up_2", "moe_w_up_2", "moe_w_down_2", "moe_w_down_2")[r]
        tiles = KU if r < UP_SLOTS else KDN
        k0 = r % 2 * tiles * P
        sp.dma_start(self.raw[:, r, :].rearrange("p (k n) -> p k n", k=tiles),
                     self.d[name][self.i, bass.ds(e, 1), k0:k0 + tiles * P, :].rearrange("o (k p) n -> p (o k) n", p=P)
                     ).then_inc(self.loaded[r], 16)

    def first_loads(self, sp):
        for r in range(PLACES):
            self.load(sp, r, 0)


def expert_phase(nc, i, G, weights):
    UP, DOWN, PARTS = UP_SLOTS, DOWN_SLOTS, PART_PLACES
    with Phase(nc, f"expert{i}") as ph:
        raw, loaded = weights.raw, weights.loaded
        ph.sems += loaded
        high = ph.sb("w_high", [P, PARTS, Weights.SLOT])
        low = ph.sb("w_low", [P, PARTS, Weights.SLOT])
        xg = [ph.sb(f"x_rows{s}", [P, D]) for s in range(2)]
        xh = ph.sb("x_high", [P, 2, KD, P])
        xl = ph.sb("x_low", [P, 2, KD, P])
        sg = ph.sb("silu", [P, D_EXP])
        hid = ph.sb("hidden", [P, D_EXP])
        hh = ph.sb("hidden_high", [P, D_EXP // P, P])
        hl = ph.sb("hidden_low", [P, D_EXP // P, P])
        y = ph.sb("y", [P, 2, D])
        w_high = ph.sem("w_high_done")
        w_split = ph.sem("w_split")
        used = ph.sem("w_used")
        rows_loaded = [ph.sem(f"rows_loaded{s}") for s in range(2)]
        rows_turned = ph.sem("rows_turned")
        x_high = ph.sem("x_high_done")
        x_low = ph.sem("x_low_done")
        silu_done = ph.sem("silu_done")
        hidden_done = ph.sem("hidden_done")
        hidden_turned = ph.sem("hidden_turned")
        hidden_high = ph.sem("hidden_high_done")
        hidden_low = ph.sem("hidden_low_done")
        y_by_act = ph.sem("y_by_act")
        y_by_dve = ph.sem("y_by_dve")
        stored = [ph.sem(f"stored{s}") for s in range(2)]
        last_stored = ph.sem("last_stored")
        ps, ident, d = G["ps"], G["ident"], G["d"]
        X_BANK, HIDDEN_BANK = 6, 7
        gate_bank = lambda parity, w: ps[2 * parity + w]
        down_bank = lambda c: ps[4 + c]
        block = ph.block()

        def slot(e, n):
            if e.j is None and e.odd == 0 and n < UP:
                return n, n, 1
            number = e.at(PLACES, n - DOWN)
            if e.end:
                return number, UP + n, e.at(1)
            if n < UP:
                return number, n, e.at(1, 1)
            if n < PLACES:
                return number, n, e.at(1)
            if e.last:
                return number, UP + n - PLACES, e.at(1, 1)
            return number, n - PLACES, e.at(1, 2)

        def part_of(e, n):
            return n % PARTS if e.j is None and e.odd == 0 and n < UP else (n + PLACES - DOWN) % PARTS

        @block.sync
        def _(sp):
            table = G["block_table"]
            further = further_pairs(sp, G)

            def expert_of(block):
                at = slice(block, block + 1) if isinstance(block, int) else bass.ds(block, 1)
                return sp.value_load(table[0:1, at], min_val=0, max_val=EXPERTS - 1)

            def load_up(e, expert):
                for r in range(UP):
                    if e.least() == 1:
                        sp.wait_ge(w_split, r + 1)
                    else:
                        sp.wait_ge(w_split, e.at(PLACES, r - PLACES - 1))
                    weights.load(sp, r, expert)

            def load_down(e, expert):
                for r in range(UP, PLACES):
                    sp.wait_ge(w_split, e.at(PLACES, r - PLACES - 1))
                    weights.load(sp, r, expert)

            def store(e, done=None):
                sp.wait_ge(y_by_act, e.at(1, -2))
                sp.wait_ge(y_by_dve, e.at(1, -2))
                par = (e.parity + 1) % 2
                sp.dma_start(G["y_dram"][bass.ds(e.at(P, -3 * P), P), :], y[:, par, :]).then_inc(done or stored[par], 16)

            def step(e):
                this = expert_of(e.at(1)) if e.least() >= 1 and not e.end else None
                before = expert_of(e.at(1, -1)) if e.least() >= 2 else None
                if e.least() >= 3:
                    store(e)
                if this is not None:
                    load_up(e, this)
                if before is not None:
                    load_down(e, before)

            block_steps(sp, further, step)
            for after in (1, 2):
                store(Step(2 * LEAST_PAIRS + after, further), last_stored)
            sp.wait_ge(last_stored, 32)

        @block.gpsimd
        def _(pool):
            def gather(e):
                if e >= 2:
                    pool.wait_ge(rows_turned, 2 * (e - 1))
                pool.indirect_dma_start(xg[e % 2][:, :], None, G["h_dram"][:, :],
                                        bass.IndirectOffsetOnAxis(ap=G["slot_token"][:, e:e + 1], axis=0)
                                        ).then_inc(rows_loaded[e % 2], 16)

            further = further_pairs(pool, G)
            for e in range(2 * LEAST_PAIRS):
                gather(e)
            for pair in range(LEAST_PAIRS, BLOCKS // 2):
                with pool.If(further > pair - LEAST_PAIRS):
                    for odd in range(2):
                        gather(2 * pair + odd)

        @block.tensor
        def _(pe):
            def turn_rows(e, half, first):
                n = 0 if first else e.at(2, 2)
                par = 0 if first else (e.parity + 1) % 2
                if half == 0:
                    pe.wait_ge(rows_loaded[par], 16 if first else e.halved(16, 3))
                if not first or half:
                    pe.wait_ge(x_low, n + half)
                for k in range(KU):
                    last = nc.tensor.transpose(ps[X_BANK][:, k * P:(k + 1) * P], xg[par][:, (KU * half + k) * P:(KU * half + k + 1) * P], ident)
                last.then_inc(rows_turned, 1)

            def turn_hidden(e):
                pe.wait_ge(hidden_done, e.at(1))
                if e.least() >= 2:
                    pe.wait_ge(hidden_low, e.at(1, -1))
                for k in range(D_EXP // P):
                    last = nc.tensor.transpose(ps[HIDDEN_BANK][:, k * P:(k + 1) * P], hid[:, k * P:(k + 1) * P], ident)
                last.then_inc(hidden_turned, 1)

            def up_slot(e, r):
                half = r % 2
                pe.wait_ge(w_split, slot(e, r)[0] + 1)
                if r < 2:
                    pe.wait_ge(x_low, e.at(2, half + 1))
                if half == 0 and e.least() >= 2:
                    pe.wait_ge(hidden_done, e.at(1, -1))
                for k in range(KU):
                    kk = half * KU + k
                    cols = slice(k * D_EXP, (k + 1) * D_EXP)
                    parts = [w[:, part_of(e, r), cols] for w in (high, low)]
                    last = split_product(nc, gate_bank(e.parity, r // 2)[:, :], [x[:, e.parity, kk, :] for x in (xh, xl)], parts,
                                         kk == 0, kk == KD - 1)
                last.then_inc(used, 1)

            def down_slot(e, n, r):
                pe.wait_ge(w_split, slot(e, n)[0] + 1)
                if r == 0:
                    pe.wait_ge(hidden_low, e.at(1))
                    if e.least() >= 2:
                        pe.wait_ge(y_by_act, e.at(1, -1))
                        pe.wait_ge(y_by_dve, e.at(1, -1))
                for c in range(2):
                    for k in range(KDN):
                        kk = r * KDN + k
                        cols = slice(k * D + c * BANK, k * D + (c + 1) * BANK)
                        last = split_product(nc, down_bank(c)[:, :], [x[:, kk, :] for x in (hh, hl)],
                                             [w[:, part_of(e, n), cols] for w in (high, low)], kk == 0, kk == D_EXP // P - 1)
                last.then_inc(used, 1)

            def step(e):
                if e.end:
                    turn_hidden(e)
                    for r in range(DOWN):
                        down_slot(e, r, r)
                    return
                for r in range(UP):
                    up_slot(e, r)
                    if r % 2 == 0 and not e.last:
                        turn_rows(e, r // 2, False)
                    if r == 1 and e.least() >= 1:
                        turn_hidden(e)
                if e.least() >= 1:
                    for r in range(DOWN):
                        down_slot(e, UP + r, r)

            for half in range(2):
                turn_rows(None, half, True)
            block_steps(pe, further_pairs(pe, G), step)

        def turns(e, weight, rows, hidden_parts, gate, down_rows):
            if e.end:
                hidden_parts(e)
                down_rows(e)
                return
            weight(e, 3)
            if not e.last:
                rows(e, 0)
            if e.least() >= 1:
                weight(e, 4)
                hidden_parts(e)
                weight(e, 5)
            if not e.last:
                rows(e, 1)
            weight(e, 6)
            gate(e)
            weight(e, 7)
            if not e.last:
                weight(e, 8)
            if e.least() >= 1:
                down_rows(e)

        @block.scalar
        def _(act):
            def weight(e, n):
                number, place, loads = slot(e, n)
                act.wait_ge(loaded[place], loads * 16)
                if not (e.j is None and e.odd == 0 and n < PARTS):
                    act.wait_ge(used, number - PARTS + 1)
                nc.scalar.copy(rounded(high[:, part_of(e, n), :]), raw[:, place, :]).then_inc(w_high, 1)

            def rows(e, half):
                n = 0 if e is None else e.at(2, 2)
                par = 0 if e is None else (e.parity + 1) % 2
                act.wait_ge(rows_turned, n + half + 1)
                nc.scalar.copy(rounded(xh[:, par, KU * half:KU * half + KU, :]), ps[X_BANK][:, :].rearrange("p (k n) -> p k n", k=KU)
                               ).then_inc(x_high, 1)

            def hidden_parts(e):
                act.wait_ge(hidden_turned, e.at(1))
                nc.scalar.copy(rounded(hh[:, :, :]), ps[HIDDEN_BANK][:, :].rearrange("p (k n) -> p k n", k=D_EXP // P)).then_inc(hidden_high, 1)

            def gate(e):
                act.wait_ge(used, slot(e, UP - 1)[0] + 1)
                if e.least() >= 1:
                    act.wait_ge(hidden_done, e.at(1))
                nc.scalar.activation(sg[:, :], gate_bank(e.parity, 0)[:, :], ACT.Silu).then_inc(silu_done, 1)

            def down_rows(e):
                par = (e.parity + 1) % 2
                act.wait_ge(used, e.at(PLACES, 0 if e.end else PLACES - DOWN))
                if e.least() >= 3:
                    act.wait_ge(stored[par], e.halved(16, -1))
                nc.scalar.copy(y[:, par, 0:BANK], down_bank(0)[:, :]).then_inc(y_by_act, 1)

            for n in range(PARTS):
                weight(Step(0), n)
            for half in range(2):
                rows(None, half)
            block_steps(act, further_pairs(act, G), lambda e: turns(e, weight, rows, hidden_parts, gate, down_rows))

        @block.vector
        def _(dve):
            def weight(e, n):
                number, place, _ = slot(e, n)
                dve.wait_ge(w_high, number + 1)
                nc.vector.tensor_tensor(rounded(low[:, part_of(e, n), :]), raw[:, place, :], high[:, part_of(e, n), :], ALU.subtract
                                        ).then_inc(w_split, 1)

            def rows(e, half):
                n = 0 if e is None else e.at(2, 2)
                par = 0 if e is None else (e.parity + 1) % 2
                at = slice(KU * half, KU * half + KU)
                dve.wait_ge(x_high, n + half + 1)
                nc.vector.tensor_tensor(rounded(xl[:, par, at, :]), ps[X_BANK][:, :].rearrange("p (k n) -> p k n", k=KU),
                                        xh[:, par, at, :], ALU.subtract).then_inc(x_low, 1)

            def hidden_parts(e):
                dve.wait_ge(hidden_high, e.at(1))
                nc.vector.tensor_tensor(rounded(hl[:, :, :]), ps[HIDDEN_BANK][:, :].rearrange("p (k n) -> p k n", k=D_EXP // P), hh[:, :, :],
                                        ALU.subtract).then_inc(hidden_low, 1)

            def gate(e):
                dve.wait_ge(silu_done, e.at(1, 1))
                if e.least() >= 1:
                    dve.wait_ge(hidden_turned, e.at(1))
                nc.vector.tensor_tensor(hid[:, :], sg[:, :], gate_bank(e.parity, 1)[:, :], ALU.mult).then_inc(hidden_done, 1)

            def down_rows(e):
                par = (e.parity + 1) % 2
                dve.wait_ge(used, e.at(PLACES, 0 if e.end else PLACES - DOWN))
                if e.least() >= 3:
                    dve.wait_ge(stored[par], e.halved(16, -1))
                nc.vector.tensor_copy(y[:, par, BANK:D], down_bank(1)[:, :]).then_inc(y_by_dve, 1)

            for n in range(PARTS):
                weight(Step(0), n)
            for half in range(2):
                rows(None, half)
            block_steps(dve, further_pairs(dve, G), lambda e: turns(e, weight, rows, hidden_parts, gate, down_rows))


def combine_phase(nc, i, G, gate_row):
    with Phase(nc, f"combine{i}") as ph:
        rows = [ph.sb(f"y_rows{k}", [P, TT, D]) for k in range(TOP_E)]
        gathered = [[ph.sem(f"gathered{k}_{t}") for t in range(TT)] for k in range(TOP_E)]
        scaled = ph.sem("scaled")
        summed = ph.sem("summed")
        by_pool = ph.sem("gated_by_pool")
        by_dve = ph.sem("gated_by_dve")
        added = ph.sem("added")
        X = G["X"]
        block = ph.block()

        @block.gpsimd
        def _(pool):
            for t in range(TT):
                for k in range(TOP_E):
                    pool.indirect_dma_start(rows[k][:, t, :], None, G["y_dram"][:, :],
                                            bass.IndirectOffsetOnAxis(ap=G["y_row"][k][:, t:t + 1], axis=0)).then_inc(gathered[k][t], 16)
            for t in range(0, TT, 2):
                pool.wait_ge(summed, t + 1)
                nc.gpsimd.tensor_tensor(rows[1][:, t, :], rows[1][:, t, :], gate_row, ALU.mult).then_inc(by_pool, 1)

        @block.scalar
        def _(act):
            for t in range(TT):
                act.wait_ge(gathered[0][t], 16)
                nc.scalar.mul(rows[0][:, t, :], rows[0][:, t, :], G["gate"][:, 0, t:t + 1]).then_inc(scaled, 1)

        @block.vector
        def _(dve):
            def add(t):
                if t % 2 == 0:
                    dve.wait_ge(by_pool, t // 2 + 1)
                else:
                    dve.wait_ge(by_dve, t // 2 + 1)
                nc.vector.tensor_tensor(X[:, t, :], X[:, t, :], rows[1][:, t, :], ALU.add).then_inc(added, 1)

            for t in range(TT):
                dve.wait_ge(gathered[1][t], 16)
                dve.wait_ge(scaled, t + 1)
                nc.vector.scalar_tensor_tensor(rows[1][:, t, :], rows[1][:, t, :], G["gate"][:, 1, t:t + 1], rows[0][:, t, :],
                                               ALU.mult, ALU.add).then_inc(summed, 1)
                if t % 2 == 1:
                    dve.wait_ge(summed, t + 1)
                    nc.vector.tensor_tensor(rows[1][:, t, :], rows[1][:, t, :], gate_row, ALU.mult).then_inc(by_dve, 1)
                if t >= 1:
                    add(t - 1)
            add(TT - 1)


def moe(nc, i, G):
    mod = lambda n: G["mod"][:, n * D:(n + 1) * D]
    with ExitStack() as stream:
        weights = ExpertWeights(nc, stream, i, G)
        with ExitStack() as ctx:
            XT = ctx.enter_context(nc.sbuf_tensor(f"x_features{i}", [P, KD, SEQ], F32))
            norm_mod_phase(nc, f"norm{i}b", G, G["d"]["norm_g_2"][i, 1:2, :], mod(3), mod(4), XT=XT, h_dram=G["h_dram"])
            router_phase(nc, i, G, XT, weights)
        expert_phase(nc, i, G, weights)
    combine_phase(nc, i, G, mod(5))


def bias_phase(nc, G):
    M = HEADS_ALL * TT
    PER = 4
    OUTS = 4
    BANKS = 8
    with Phase(nc, "bias") as ph:
        pos_i = ph.sb("pos_i", [P, SEQ], I32)
        pos = ph.sb("pos", [P, SEQ])
        reach = ph.sb("reach", [P, P])
        table = ph.sb("table", [P, HEADS_ALL])
        below = ph.sb("table_below", [P, HEADS_ALL])
        step_t = ph.sb("table_steps", [P, HEADS_ALL])
        wide = ph.sb("steps_wide", [P, P])
        part = ph.sb("step_parts", [P, 2, P])
        hit = ph.sb("steps_reached", [P, 4, SEQ])
        out = ph.sb("bias_rows", [M, OUTS, PER, SEQ])
        loaded = ph.sem("loaded")
        zero_set = ph.sem("zero_set")
        below_loaded = ph.sem("below_loaded")
        dve_step = ph.sem("dve_step")
        parts_done = ph.sem("parts_done")
        hit_done = ph.sem("hit_done")
        summed = ph.sem("summed")
        copied = ph.sem("copied")
        stored = [ph.sem(f"stored{s}") for s in range(OUTS)]
        ps, c2, d = G["ps"], G["c2"], G["d"]
        block = ph.block()

        @block.sync
        def _(sp):
            sp.dma_start(pos_i[:, :], row_of(d["positions_2"][0:1, :], SEQ)).then_inc(loaded, 16)
            sp.wait_ge(zero_set, 1)
            for t in range(TT):
                sp.dma_start(table[t * BUCKETS:(t + 1) * BUCKETS, :], d["rel_bias_2"][:, :]).then_inc(loaded, 16)
                sp.dma_start(below[t * BUCKETS + 1:(t + 1) * BUCKETS, :], d["rel_bias_2"][0:BUCKETS - 1, :]).then_inc(below_loaded, 16)
            for b in range(P // PER):
                sp.wait_ge(copied, PER * (b + 1))
                sp.dma_start(G["bias_dram"][:, b * PER:(b + 1) * PER, :], out[:, b % OUTS, :, :]).then_inc(stored[b % OUTS], 16)
            for s in range(OUTS):
                sp.wait_ge(stored[s], 16 * (P // PER // OUTS))

        @block.vector
        def _(dve):
            V = nc.vector
            link = Chain(dve, dve_step).link
            V.memset(below[:, :], 0.0).then_inc(zero_set, 1)
            dve.wait_ge(loaded, 16 * (1 + TT))
            dve.wait_ge(below_loaded, 16 * TT)
            link(V.tensor_copy(pos[:, :], pos_i[:, :]))
            for t in range(TT):
                rows = slice(t * BUCKETS, (t + 1) * BUCKETS)
                link(V.tensor_scalar(reach[rows, :], pos[rows, t * P:(t + 1) * P], c2["bucket_start"][rows, :], None, ALU.subtract))
            link(V.tensor_tensor(step_t[:, :], table[:, :], below[:, :], ALU.subtract))
            link(V.memset(wide[:, :], 0.0))
            link(V.tensor_tensor(wide[:, 0:M].rearrange("p (h t) -> p h t", t=TT),
                                 step_t[:, :].rearrange("p (h o) -> p h o", o=1).to_broadcast([P, HEADS_ALL, TT]),
                                 c2["tile_block"].rearrange("p (o t) -> p o t", o=1).to_broadcast([P, HEADS_ALL, TT]), ALU.mult))
            link(V.tensor_copy(rounded(part[:, 0, :]), wide[:, :]))
            V.tensor_tensor(rounded(part[:, 1, :]), wide[:, :], part[:, 0, :], ALU.subtract).then_inc(parts_done, 1)
            for j in range(P):
                if j >= 4:
                    dve.wait_ge(summed, j - 3)
                V.tensor_scalar(rounded(hit[:, j % 4, :]), pos[:, :], reach[:, j:j + 1], None, ALU.is_le).then_inc(hit_done, 1)

        @block.tensor
        def _(pe):
            pe.wait_ge(parts_done, 1)
            for j in range(P):
                pe.wait_ge(hit_done, j + 1)
                if j >= BANKS:
                    pe.wait_ge(copied, j - BANKS + 1)
                for n in range(2):
                    last = nc.tensor.matmul(ps[j % BANKS][:, :], rounded(part[:, n, :]), rounded(hit[:, j % 4, :]), start=(n == 0), stop=(n == 1))
                last.then_inc(summed, 1)

        @block.scalar
        def _(act):
            for j in range(P):
                b = j // PER
                act.wait_ge(summed, j + 1)
                if b >= OUTS:
                    act.wait_ge(stored[b % OUTS], 16 * (b // OUTS))
                nc.scalar.copy(out[:, b % OUTS, j % PER, :], ps[j % BANKS][0:M, :]).then_inc(copied, 1)


COL_QC, COL_KC, COL_VC, COL_QI = 0, 512, 1024, 1536
COL_KI = COL_QI + IDX_HEADS * IDX_DIM
COL_WI = COL_KI + IDX_DIM
COL_QD = COL_WI + IDX_HEADS
COL_KD, COL_VD = COL_QD + 512, COL_QD + 1024


ATTN_CHUNKS = [("QC", COL_QC, FM), ("KC", COL_KC, FM), ("VC", COL_VC, TM), ("QD", COL_QD, FM), ("KD", COL_KD, FM),
               ("VD", COL_VD, TM)]
K_AT = IDX_HEADS * IDX_DIM
W_AT = K_AT + P
FIRST_STEP = W_AT + IDX_HEADS


def attn_weights(nc, G):
    w = lambda r0, r1, c0, c1: G["d"]["cd_w_in_2"][0, r0:r1, c0:c1].rearrange("(k p) n -> p k n", p=P)
    pieces = [(0, COL_QI, COL_KI)] + [(K_AT + g * IDX_DIM, COL_KI, COL_WI) for g in range(4)] + [(W_AT, COL_WI, COL_QD)]
    n = KD // 2
    first = [[(at, n, FIRST_STEP, w(h * n * P, (h + 1) * n * P, c0, c1)) for at, c0, c1 in pieces] for h in range(2)]
    return Weights(nc, G, "attn_project", first + [s for _, col, _ in ATTN_CHUNKS for s in k_slots(w, col, BANK)])


def attn_project_phase(nc, G, S, weights):
    chunks = [[("QI", 0), ("QI", 1), ("KI", 0)] + [("WI", t) for t in range(TT)]]
    chunks += [[(name, m) for m in range(4)] for name, _, _ in ATTN_CHUNKS]
    N_FIRST = len(chunks[0])
    number = lambda c, n: n if c == 0 else N_FIRST + 4 * (c - 1) + n
    bank = lambda c, n: n if c or n < 3 else n + 1
    kinds = {name: kind for name, _, kind in ATTN_CHUNKS}
    SLOTS = 2
    KS = KD // SLOTS
    N_SLOTS = SLOTS * len(chunks)
    units = [(t, h) for t in range(TT) for h in range(IDX_HEADS)]
    PER_JOB = IDX_HEADS // 4
    index_tile = lambda s: (s - SLOTS) // 3 if s >= SLOTS and (s - SLOTS) % 3 == 0 and (s - SLOTS) // 3 < TT else None
    with Phase(nc, "attn_project") as ph:
        ph.sems += weights.sems
        qi = ph.sb("q_index", [P, 2, SEQ])
        ki = ph.sb("k_index", [P, SEQ])
        wi = ph.sb("w_index", [P, TT, IDX_HEADS])
        pos_i = ph.sb("pos_i", [P, SEQ], I32)
        pos = ph.sb("pos", [P, SEQ])
        posq_i = ph.sb("pos_q_i", [P, TT], I32)
        posq = ph.sb("pos_q", [P, TT])
        relu = S["VD"]
        score = ph.sb("score", [P, 2, SEQ])
        top8 = ph.sb("top8", [P, 8])
        pos_loaded = ph.sem("pos_loaded")
        product_done = ph.sem("product_done")
        evacuated = ph.sem("evacuated")
        index_done = ph.sem("index_done")
        relu_done = ph.sem("relu_done")
        weighted = ph.sem("weighted")
        dve_step = ph.sem("dve_step")
        ps, XH, XL, d = G["ps"], G["XH"], G["XL"], G["d"]
        last_user = lambda s: ((product_done, number(s // SLOTS, len(chunks[s // SLOTS]) - 1) + 1) if s % SLOTS == SLOTS - 1
                               else (weights.used, s // SLOTS + 1))
        block = ph.block()

        @block.sync
        def _(sp):
            weights.load(sp, Weights.RING)
            sp.dma_start(pos_i[:, :], row_of(d["positions_2"][0:1, :], SEQ)).then_inc(pos_loaded, 16)
            sp.dma_start(posq_i[:, :], d["positions_2"][0, :].rearrange("(t p) -> p t", p=P),
                         allow_slow_non_contiguous=True).then_inc(pos_loaded, 16)
            weights.load(sp)

        @block.tensor
        def _(pe):
            def index(u):
                t, h = units[u]
                r = IDX_DIM * (h % 4)
                pe.wait_ge(evacuated, N_FIRST)
                if u >= 4:
                    pe.wait_ge(relu_done, u - 3)
                nc.tensor.matmul(ps[4 + h % 4][:, :], qi[r:r + IDX_DIM, h // 4, t * P:(t + 1) * P], ki[r:r + IDX_DIM, :],
                                 start=True, stop=True, tile_position=(r, 0)).then_inc(index_done, 1)

            for s in range(N_SLOTS):
                c, half = s // SLOTS, s % SLOTS
                pe.wait_ge(weights.split, s + 1)
                for n, (name, m) in enumerate(chunks[c]):
                    if half == 0 and (c >= 2 or c == 1 and n < 3):
                        pe.wait_ge(evacuated, number(c, n) - 3 if c >= 2 else n + 1)
                    out = ps[bank(c, n)]
                    for kk in range(KS):
                        k = half * KS + kk
                        flags = (k == 0, k == KD - 1)
                        tok = [a[:, k, m * P:(m + 1) * P] for a in (XH, XL)]
                        features = [a[:, k, :] for a in (XH, XL)]
                        if name == "WI":
                            last = split_product(nc, out[:, 0:IDX_HEADS], tok, weights.parts(s, kk * FIRST_STEP + W_AT, IDX_HEADS), *flags)
                        elif name == "KI":
                            last = split_product(nc, out[:, :], weights.parts(s, kk * FIRST_STEP + K_AT, P), features, *flags)
                        elif kinds.get(name) == TM:
                            last = split_product(nc, out[:, :], tok, weights.parts(s, kk * BANK, BANK), *flags)
                        else:
                            last = split_product(nc, out[:, :], weights.parts(s, kk * (BANK if c else FIRST_STEP) + m * P, P), features, *flags)
                    if half == SLOTS - 1:
                        last.then_inc(product_done, 1)
                    elif n == len(chunks[c]) - 1:
                        last.then_inc(weights.used, 1)
                    if index_tile(s) is not None:
                        for h in range(PER_JOB * n, PER_JOB * (n + 1)):
                            index(index_tile(s) * IDX_HEADS + h)

        @block.scalar
        def _(act):
            def rectify(u):
                t, h = units[u]
                act.wait_ge(index_done, u + 1)
                if u >= 4:
                    act.wait_ge(weighted, u - 3)
                nc.scalar.activation(relu[:, u % 4, :], ps[4 + h % 4][:, :], ACT.Relu).then_inc(relu_done, 1)

            act.wait_ge(weights.split, 2)
            for s in range(N_SLOTS):
                c, half = s // SLOTS, s % SLOTS
                if index_tile(s) is not None:
                    for h in range(IDX_HEADS):
                        rectify(index_tile(s) * IDX_HEADS + h)
                if half == SLOTS - 1:
                    for n, (name, m) in enumerate(chunks[c]):
                        act.wait_ge(product_done, number(c, n) + 1)
                        if name == "WI":
                            nc.scalar.copy(wi[:, m, :], ps[bank(c, n)][:, 0:IDX_HEADS]).then_inc(evacuated, 1)
                            continue
                        if name == "VD":
                            act.wait_ge(weighted, len(units))
                        dest = {"QI": qi[:, m, :], "KI": ki[:, :]}[name] if c == 0 else S[name][:, m, :]
                        nc.scalar.copy(dest, ps[bank(c, n)][:, :]).then_inc(evacuated, 1)
                if s + 2 < N_SLOTS:
                    weights.split_high(act, s + 2, last_user)

        @block.gpsimd
        def _(pool):
            for s in range(2, N_SLOTS):
                weights.split_low(pool, s)

        @block.vector
        def _(dve):
            V = nc.vector
            link = Chain(dve, dve_step).link
            for s in range(2):
                weights.split_slot(dve, s)
            dve.wait_ge(pos_loaded, 32)
            link(V.tensor_copy(pos[:, :], pos_i[:, :]))
            link(V.tensor_copy(posq[:, :], posq_i[:, :]))
            for t in range(TT):
                link(V.tensor_scalar(S["causal"][:, t, :], pos[:, :], posq[:, t:t + 1], NEG, ALU.is_gt, ALU.mult))
            dve.wait_ge(evacuated, N_FIRST)
            for t in range(TT):
                s = score[:, t % 2, :]
                for h in range(IDX_HEADS):
                    u = t * IDX_HEADS + h
                    dve.wait_ge(relu_done, u + 1)
                    V.scalar_tensor_tensor(s, relu[:, u % 4, :], wi[:, t, h:h + 1], S["causal"][:, t, :] if h == 0 else s,
                                           ALU.mult, ALU.add).then_inc(weighted, 1)
                    dve.wait_ge(weighted, u + 1)
                for n in range(TOPK // 8):
                    link(V.max(top8[:, :], s))
                    link(V.match_replace(s, top8[:, :], s, DROPPED))
                link(V.tensor_scalar(s, s, DROPPED / 2, NEG, ALU.is_gt, ALU.mult))
                link(V.tensor_tensor(S["chosen"][:, t, :], s, S["causal"][:, t, :], ALU.add))


def chosen_attention_phase(nc, G, S):
    units = [(h, t) for h in range(HEADS_C) for t in range(TT)]
    N = len(units)
    SCORE_BANKS = (0, 1, 6)
    with Phase(nc, "chosen") as ph:
        bias = ph.sb("bias", [P, 4, SEQ])
        add = ph.sb("bias_masked", [P, 3, SEQ])
        SL = ph.sb("scores", [P, 3, SEQ])
        PR = ph.sb("probs", [P, 3, SEQ])
        PT = ph.sb("probs_t", [P, 2, TT, P])
        neg_max = ph.sb("neg_max", [P, N])
        row_sum = ph.sb("row_sum", [P, N])
        inv_sum = ph.sb("inv_sum", [P, N])
        bias_loaded = [ph.sem(f"bias_loaded{r}") for r in range(4)]
        masked = ph.sem("masked")
        scores_done = ph.sem("scores_done")
        biased = ph.sem("biased")
        max_done = ph.sem("max_done")
        exp_done = ph.sem("exp_done")
        turned = ph.sem("turned")
        turned_copied = ph.sem("turned_copied")
        mixed = ph.sem("mixed")
        inv_done = ph.sem("inv_done")
        out_done = ph.sem("out_done")
        ps, ident = G["ps"], G["ident"]
        block = ph.block()

        @block.sync
        def _(sp):
            for u, (h, t) in enumerate(units):
                if u >= 4:
                    sp.wait_ge(masked, u - 3)
                sp.dma_start(bias[:, u % 4, :], G["bias_dram"][h * TT + t, :, :]).then_inc(bias_loaded[u % 4], 16)

        @block.gpsimd
        def _(pool):
            for u, (h, t) in enumerate(units):
                pool.wait_ge(bias_loaded[u % 4], 16 * (u // 4 + 1))
                if u >= 3:
                    pool.wait_ge(biased, u - 2)
                nc.gpsimd.tensor_tensor(add[:, u % 3, :], bias[:, u % 4, :], S["chosen"][:, t, :], ALU.add).then_inc(masked, 1)

        @block.tensor
        def _(pe):
            def scores(u):
                h, t = units[u]
                r = HD_C * (h % 2)
                if u >= 3:
                    pe.wait_ge(biased, u - 2)
                nc.tensor.matmul(ps[SCORE_BANKS[u % 3]][:, :], S["QC"][r:r + HD_C, h // 2, t * P:(t + 1) * P], S["KC"][r:r + HD_C, h // 2, :],
                                 start=True, stop=True).then_inc(scores_done, 1)

            def turn(u):
                pe.wait_ge(exp_done, u + 1)
                if u >= 2:
                    pe.wait_ge(turned_copied, u - 1)
                for k in range(TT):
                    last = nc.tensor.transpose(ps[2 + u % 2][:, k * P:(k + 1) * P], PR[:, u % 3, k * P:(k + 1) * P], ident)
                last.then_inc(turned, 1)

            def mix(u):
                h, t = units[u]
                pe.wait_ge(turned_copied, u + 1)
                if u >= 2:
                    pe.wait_ge(out_done, u - 1)
                for k in range(TT):
                    last = nc.tensor.matmul(ps[4 + u % 2][:, 0:P], PT[:, u % 2, k, :], S["VC"][:, k, h // 2 * P:(h // 2 + 1) * P],
                                            start=(k == 0), stop=(k == TT - 1))
                last.then_inc(mixed, 1)

            for i in range(N + 3):
                if i < N:
                    scores(i)
                if 2 <= i < N + 2:
                    turn(i - 2)
                if i >= 3:
                    mix(i - 3)

        @block.vector
        def _(dve):
            def finish(u):
                h, t = units[u]
                dve.wait_ge(exp_done, u + 1)
                nc.vector.reciprocal(inv_sum[:, u:u + 1], row_sum[:, u:u + 1]).then_inc(inv_done, 1)
                dve.wait_ge(inv_done, u + 1)
                dve.wait_ge(mixed, u + 1)
                nc.vector.tensor_scalar(S["Y"][:, t, h * HD_C:(h + 1) * HD_C], ps[4 + u % 2][:, h % 2 * HD_C:(h % 2 + 1) * HD_C], inv_sum[:, u:u + 1], None,
                                        ALU.mult).then_inc(out_done, 1)

            for u in range(N):
                dve.wait_ge(scores_done, u + 1)
                dve.wait_ge(masked, u + 1)
                if u >= 3:
                    dve.wait_ge(exp_done, u - 2)
                nc.vector.scalar_tensor_tensor(SL[:, u % 3, :], ps[SCORE_BANKS[u % 3]][:, :], HD_C ** -0.5, add[:, u % 3, :], ALU.mult, ALU.add
                                               ).then_inc(biased, 1)
                dve.wait_ge(biased, u + 1)
                nc.vector.tensor_reduce(neg_max[:, u:u + 1], SL[:, u % 3, :], AX_X, ALU.max, negate=True).then_inc(max_done, 1)
                if u >= 3:
                    finish(u - 3)
            finish(N - 3)
            finish(N - 2)
            finish(N - 1)

        @block.scalar
        def _(act):
            def copy(u):
                act.wait_ge(turned, u + 1)
                if u >= 2:
                    act.wait_ge(mixed, u - 1)
                nc.scalar.copy(PT[:, u % 2, :, :], ps[2 + u % 2][:, :].rearrange("p (k n) -> p k n", n=P)).then_inc(turned_copied, 1)

            for u in range(N):
                act.wait_ge(max_done, u + 1)
                if u >= 3:
                    act.wait_ge(turned, u - 2)
                nc.scalar.activation(PR[:, u % 3, :], SL[:, u % 3, :], ACT.Exp, bias=neg_max[:, u:u + 1],
                                     accum_out=row_sum[:, u:u + 1]).then_inc(exp_done, 1)
                if u >= 2:
                    copy(u - 2)
            copy(N - 2)
            copy(N - 1)


def differential_phase(nc, G, S):
    units = [(h, t) for h in range(HEADS_D) for t in range(TT)]
    N = len(units)
    VW = 2 * HD_D
    with Phase(nc, "differential") as ph:
        bias = ph.sb("bias", [P, 4, SEQ])
        add = ph.sb("bias_masked", [P, 3, SEQ])
        SL = ph.sb("scores", [P, 3, 2, SEQ])
        PR = ph.sb("probs", [P, 4, 2, SEQ])
        second = ph.sb("second_part", [P, 2, SEQ])
        attn = ph.sb("attn", [P, 2, SEQ])
        PT = ph.sb("attn_t", [P, 2, TT, P])
        neg_max = ph.sb("neg_max", [P, N, 2])
        row_sum = ph.sb("row_sum", [P, N, 2])
        inv = ph.sb("inv_sum", [P, N, 2])
        coef = ph.sb("second_coef", [P, N])
        lam = ph.sb("lam", [P, 4, HD_D])
        lam_prod = ph.sb("lam_prod", [P, 2, HD_D])
        lam_sum = ph.sb("lam_sum", [P, 2])
        lam_exp = ph.sb("lam_exp", [P, 2])
        neg_lam = ph.sb("neg_lam", [P, 1])
        gain = ph.sb("gain", [P, VW])
        sq = ph.sb("squares", [P, VW])
        ss = ph.sb("square_sum", [P, N])
        std = ph.sb("std", [P, N])
        rstd = ph.sb("rstd", [P, N])
        bias_loaded = [ph.sem(f"bias_loaded{r}") for r in range(4)]
        lam_loaded = ph.sem("lam_loaded")
        lam_summed = ph.sem("lam_summed")
        lam_exp_done = ph.sem("lam_exp_done")
        dve_step = ph.sem("dve_step")
        masked = ph.sem("masked")
        scores_done = ph.sem("scores_done")
        biased = ph.sem("biased")
        max_done = ph.sem("max_done")
        exp_done = ph.sem("exp_done")
        coef_done = ph.sem("coef_done")
        second_done = ph.sem("second_done")
        attn_done = ph.sem("attn_done")
        turned = ph.sem("turned")
        turned_copied = ph.sem("turned_copied")
        mixed = ph.sem("mixed")
        out_done = ph.sem("out_done")
        squared = ph.sem("squared")
        std_done = ph.sem("std_done")
        normed = ph.sem("normed")
        ps, ident, d = G["ps"], G["ident"], G["d"]
        out = lambda u: S["Y"][:, units[u][1], 512 + units[u][0] * VW:512 + (units[u][0] + 1) * VW]
        block = ph.block()

        @block.sync
        def _(sp):
            sp.dma_start(lam[:, :, :], d["diff_lam_2"][0:1, :, :].to_broadcast([P, 4, HD_D])).then_inc(lam_loaded, 16)
            sp.dma_start(gain[:, :], row_of(d["diff_norm_g_2"][0:1, :], VW)).then_inc(lam_loaded, 16)
            for u, (h, t) in enumerate(units):
                if u >= 4:
                    sp.wait_ge(masked, u - 3)
                sp.dma_start(bias[:, u % 4, :], G["bias_dram"][(HEADS_C + h) * TT + t, :, :]).then_inc(bias_loaded[u % 4], 16)

        @block.gpsimd
        def _(pool):
            def scale_second(u):
                pool.wait_ge(coef_done, u + 1)
                if u >= 2:
                    pool.wait_ge(attn_done, u - 1)
                nc.gpsimd.tensor_scalar(second[:, u % 2, :], PR[:, u % 4, 1, :], coef[:, u:u + 1], None, ALU.mult).then_inc(second_done, 1)

            for u, (h, t) in enumerate(units):
                pool.wait_ge(bias_loaded[u % 4], 16 * (u // 4 + 1))
                if u >= 3:
                    pool.wait_ge(biased, 2 * (u - 2))
                nc.gpsimd.tensor_tensor(add[:, u % 3, :], bias[:, u % 4, :], S["causal"][:, t, :], ALU.add).then_inc(masked, 1)
                if u >= 2:
                    scale_second(u - 2)
            scale_second(N - 2)
            scale_second(N - 1)

        @block.tensor
        def _(pe):
            def scores(u):
                h, t = units[u]
                if u >= 2:
                    pe.wait_ge(biased, 2 * (u - 1))
                for m in range(2):
                    r = HD_D * m
                    last = nc.tensor.matmul(ps[2 * (u % 2) + m][:, :], S["QD"][r:r + HD_D, h, t * P:(t + 1) * P], S["KD"][r:r + HD_D, h, :],
                                            start=True, stop=True)
                last.then_inc(scores_done, 1)

            def turn(u):
                pe.wait_ge(attn_done, u + 1)
                if u >= 2:
                    pe.wait_ge(turned_copied, u - 1)
                for k in range(TT):
                    last = nc.tensor.transpose(ps[4 + u % 2][:, k * P:(k + 1) * P], attn[:, u % 2, k * P:(k + 1) * P], ident)
                last.then_inc(turned, 1)

            def mix(u):
                h, t = units[u]
                pe.wait_ge(turned_copied, u + 1)
                if u >= 2:
                    pe.wait_ge(out_done, u - 1)
                for k in range(TT):
                    last = nc.tensor.matmul(ps[6 + u % 2][:, 0:VW], PT[:, u % 2, k, :], S["VD"][:, k, h * VW:(h + 1) * VW],
                                            start=(k == 0), stop=(k == TT - 1))
                last.then_inc(mixed, 1)

            scores(0)
            for i in range(N + 3):
                if i + 1 < N:
                    scores(i + 1)
                if 2 <= i < N + 2:
                    turn(i - 2)
                if i >= 3:
                    mix(i - 3)

        @block.vector
        def _(dve):
            V = nc.vector
            link = Chain(dve, dve_step).link

            def weigh(u):
                dve.wait_ge(exp_done, 2 * u + 2)
                link(V.reciprocal(inv[:, u, :], row_sum[:, u, :]))
                V.tensor_tensor(coef[:, u:u + 1], inv[:, u, 1:2], neg_lam[:, :], ALU.mult).then_inc(coef_done, 1)

            def combine(u):
                dve.wait_ge(second_done, u + 1)
                if u >= 2:
                    dve.wait_ge(turned, u - 1)
                V.scalar_tensor_tensor(attn[:, u % 2, :], PR[:, u % 4, 0, :], inv[:, u, 0:1], second[:, u % 2, :], ALU.mult, ALU.add
                                       ).then_inc(attn_done, 1)

            dve.wait_ge(lam_loaded, 32)
            pairs = lam[:, :, :].rearrange("p (a b) e -> p a b e", b=2)
            link(V.tensor_tensor(lam_prod[:, :, :], pairs[:, :, 0, :], pairs[:, :, 1, :], ALU.mult))
            V.tensor_reduce(lam_sum[:, :], lam_prod[:, :, :], AX_X, ALU.add).then_inc(lam_summed, 1)
            link(V.tensor_scalar(gain[:, :], gain[:, :], 1.0 - LAMBDA_INIT, None, ALU.mult))
            dve.wait_ge(lam_exp_done, 1)
            link(V.tensor_tensor(neg_lam[:, :], lam_exp[:, 1:2], lam_exp[:, 0:1], ALU.subtract))
            link(V.tensor_scalar(neg_lam[:, :], neg_lam[:, :], LAMBDA_INIT, None, ALU.subtract))
            for u in range(N):
                dve.wait_ge(scores_done, u + 1)
                dve.wait_ge(masked, u + 1)
                for m in range(2):
                    if u >= 3:
                        dve.wait_ge(exp_done, 2 * (u - 3) + m + 1)
                    V.scalar_tensor_tensor(SL[:, u % 3, m, :], ps[2 * (u % 2) + m][:, :], HD_D ** -0.5, add[:, u % 3, :], ALU.mult, ALU.add
                                           ).then_inc(biased, 1)
                for m in range(2):
                    dve.wait_ge(biased, 2 * u + m + 1)
                    V.tensor_reduce(neg_max[:, u, m:m + 1], SL[:, u % 3, m, :], AX_X, ALU.max, negate=True).then_inc(max_done, 1)
                if u >= 1:
                    weigh(u - 1)
                if u >= 2:
                    combine(u - 2)
            weigh(N - 1)
            combine(N - 2)
            combine(N - 1)
            dve.wait_ge(std_done, 1)
            link(V.reciprocal(rstd[:, :], std[:, :]))
            for u in range(N):
                V.scalar_tensor_tensor(out(u), out(u), rstd[:, u:u + 1], gain[:, :], ALU.mult, ALU.mult).then_inc(normed, 1)

        @block.scalar
        def _(act):
            def copy(u):
                act.wait_ge(turned, u + 1)
                if u >= 2:
                    act.wait_ge(mixed, u - 1)
                nc.scalar.copy(PT[:, u % 2, :, :], ps[4 + u % 2][:, :].rearrange("p (k n) -> p k n", n=P)).then_inc(turned_copied, 1)

            def take(u):
                act.wait_ge(mixed, u + 1)
                nc.scalar.copy(out(u), ps[6 + u % 2][:, 0:VW]).then_inc(out_done, 1)
                act.wait_ge(out_done, u + 1)
                if u >= 1:
                    act.wait_ge(squared, u)
                nc.scalar.activation(sq[:, :], out(u), ACT.Square, accum_out=ss[:, u:u + 1]).then_inc(squared, 1)

            act.wait_ge(lam_summed, 1)
            nc.scalar.activation(lam_exp[:, :], lam_sum[:, :], ACT.Exp).then_inc(lam_exp_done, 1)
            for u in range(N):
                for m in range(2):
                    act.wait_ge(max_done, 2 * u + m + 1)
                    if u >= 4:
                        act.wait_ge(attn_done, u - 3)
                    nc.scalar.activation(PR[:, u % 4, m, :], SL[:, u % 3, m, :], ACT.Exp, bias=neg_max[:, u, m:m + 1],
                                         accum_out=row_sum[:, u, m:m + 1]).then_inc(exp_done, 1)
                if u >= 3:
                    copy(u - 3)
                if u >= 4:
                    take(u - 4)
            for u in range(N - 4, N):
                if u >= N - 3:
                    copy(u)
                take(u)
            act.wait_ge(squared, N)
            nc.scalar.activation(std[:, :], ss[:, :], ACT.Sqrt, scale=1.0 / VW, bias=G["eps_norm"][:, :]).then_inc(std_done, 1)


def turn_phase(nc, G, Y, following):
    with Phase(nc, "turn") as ph:
        turned = ph.sem("turned")
        ps = G["ps"]
        split = Split(nc, ph, G, turned, lambda t, j: ps[2 * t + j])
        block = ph.block()

        @block.sync
        def _(sp):
            following.load(sp, Weights.RING)

        @block.tensor
        def _(pe):
            for t in range(TT):
                for j in range(2):
                    for n in range(4):
                        k = 4 * j + n
                        last = nc.tensor.transpose(ps[2 * t + j][:, n * P:(n + 1) * P], Y[:, t, k * P:(k + 1) * P], G["ident"])
                    last.then_inc(turned, 1)

        @block.scalar
        def _(act):
            split.high_parts(act)

        @block.vector
        def _(dve):
            for t in range(TT):
                split.low_parts(dve, t)


def final_phase(nc, G):
    with Phase(nc, "final") as ph:
        gain = ph.sb("gain", [P, D])
        sq = ph.sb("squares", [P, D])
        ss = ph.sb("square_sum", [P, TT])
        std = ph.sb("std", [P, TT])
        rstd = ph.sb("rstd", [P, TT])
        out = ph.sb("out", [P, TT, D])
        loaded = ph.sem("loaded")
        squared = ph.sem("squared")
        std_done = ph.sem("std_done")
        inv_done = ph.sem("inv_done")
        scaled = ph.sem("scaled")
        stored = ph.sem("stored")
        X, d = G["X"], G["d"]
        block = ph.block()

        @block.sync
        def _(sp):
            sp.dma_start(gain[:, :], row_of(d["final_norm_g_2"].rearrange("(o n) -> o n", o=1), D)).then_inc(loaded, 16)
            for t in range(TT):
                sp.wait_ge(scaled, t + 1)
                sp.dma_start(d["out"][0, t * P:(t + 1) * P, :], out[:, t, :]).then_inc(stored, 16)
            sp.wait_ge(stored, 16 * TT)

        @block.scalar
        def _(act):
            for t in range(TT):
                if t:
                    act.wait_ge(squared, t)
                nc.scalar.activation(sq[:, :], X[:, t, :], ACT.Square, accum_out=ss[:, t:t + 1]).then_inc(squared, 1)
            act.wait_ge(squared, TT)
            nc.scalar.activation(std[:, :], ss[:, :], ACT.Sqrt, scale=1.0 / D, bias=G["eps_norm"][:, :]).then_inc(std_done, 1)

        @block.vector
        def _(dve):
            dve.wait_ge(std_done, 1)
            nc.vector.reciprocal(rstd[:, :], std[:, :]).then_inc(inv_done, 1)
            dve.wait_ge(inv_done, 1)
            dve.wait_ge(loaded, 16)
            for t in range(TT):
                nc.vector.scalar_tensor_tensor(out[:, t, :], X[:, t, :], rstd[:, t:t + 1], gain[:, :], ALU.mult, ALU.mult
                                               ).then_inc(scaled, 1)


def second_block(nc, G):
    d = G["d"]
    mod = lambda n: G["mod"][:, n * D:(n + 1) * D]
    second_load_phase(nc, G)
    bias_phase(nc, G)
    rows_of = lambda w: (lambda r0, r1: w[0, r0:r1, :].rearrange("(k p) n -> p k n", p=P))
    with ExitStack() as ctx:
        parts_room(nc, ctx, G, "conv")
        w_in = conv_weights(nc, G)
        norm_mod_phase(nc, "norm0a", G, d["norm_g_2"][0, 0:1, :], mod(0), mod(1), following=w_in, layer=0)
        w_out = row_weights(nc, "conv_out", rows_of(d["ab_w_out_2"]), KD, G)
        conv_mix_phase(nc, G, w_in, w_out)
        gated_residual_phase(nc, "conv_out", G, w_out, mod(2))
    moe(nc, 0, G)
    with ExitStack() as ctx:
        sb = lambda name, shape: ctx.enter_context(nc.sbuf_tensor(name, shape, F32))
        names = ("QC", "KC", "VC", "QD", "KD", "VD", "causal", "chosen")
        room = sb("attn_room", [P, len(names), 4, SEQ])
        S = {n: room[:, j, :, :] for j, n in enumerate(names)}
        with ExitStack() as parts:
            parts_room(nc, parts, G, "attn")
            w_in = attn_weights(nc, G)
            rows = lambda j: room[:, j:j + 2, :, :].rearrange("p j m n -> p (j m n)").rearrange("p (t n) -> p t n", t=TT)
            norm_mod_phase(nc, "norm1a", G, d["norm_g_2"][1, 0:1, :], mod(0), mod(1), following=w_in, room=(rows(0), rows(2)), layer=1)
            attn_project_phase(nc, G, S, w_in)
        S["Y"] = sb("attn_mixed", [P, TT, D])
        chosen_attention_phase(nc, G, S)
        differential_phase(nc, G, S)
        with ExitStack() as parts:
            parts_room(nc, parts, G, "attn_out")
            w_out = row_weights(nc, "attn_out", rows_of(d["cd_w_out_2"]), KD, G)
            turn_phase(nc, G, S["Y"], w_out)
            gated_residual_phase(nc, "attn_out", G, w_out, mod(2), part=S["QC"])
    moe(nc, 1, G)
    final_phase(nc, G)


def build(nc, d, parts, parts2):
    with ExitStack() as ctx:
        G = {"d": d}
        G["ps"] = [ctx.enter_context(nc.psum_tensor(f"bank{i}", [P, BANK], F32)) for i in range(8)]
        sb = lambda name, shape, dt=F32: ctx.enter_context(nc.sbuf_tensor(name, shape, dt))
        G["X"] = sb("x_tokens", [P, TT, D])
        G["ident"] = sb("ident", [P, P])[:, :]
        G["ones_col"] = sb("ones_col", [P, 1])
        G["cond"] = sb("cond", [P, KD])
        G["mod_dram"] = nc.dram_tensor("modulation_rows", [DEPTH, MOD], F32).ap()
        G["eps_ln"] = sb("eps_ln", [P, 1])
        G["eps_norm"] = sb("eps_norm", [P, 1])
        G["y_dram"] = nc.dram_tensor("y_rows", [BLOCKS * P, D], F32).ap()
        with ExitStack() as first:
            parts_room(nc, first, G, "first")
            load_phase(nc, G)
            first_block(nc, G, parts)
        G["consts2"] = sb("consts2", list(d["consts2"].shape))
        G["c2"] = views(G["consts2"], parts2)
        G["mod"] = sb("modulation", [P, 6 * D])
        G["slot_token"] = sb("slot_token", [P, BLOCKS], I32)
        G["gate"] = sb("gate", [P, TOP_E, TT])
        G["y_row"] = [sb(f"y_row{k}", [P, TT], I32) for k in range(TOP_E)]
        G["block_table"] = sb("block_table", [P, BLOCKS + 1], I32)
        G["h_dram"] = nc.dram_tensor("h_rows", [SEQ, D], F32).ap()
        G["slot_dram"] = nc.dram_tensor("slot_tokens", [P * BLOCKS, 1], I32).ap()
        G["bias_dram"] = nc.dram_tensor("bias_rows", [HEADS_ALL * TT, P, SEQ], F32).ap()
        second_block(nc, G)


_INS = ["x", "w_in", "w_alpha", "b_alpha", "mix_scale", "w_out", "ln1_g", "ln1_b", "w_up", "conv_w", "conv_b", "w_down",
        "ln2_g", "ln2_b", "c_2", "positions_2", "rel_bias_2", "norm_g_2", "final_norm_g_2", "ada_w_2", "ada_b_2",
        "ab_w_in_2", "ab_conv_a_2", "ab_conv_b_2", "ab_conv_b_bias_2", "ab_ln_g_2", "ab_ln_b_2", "ab_w_out_2",
        "cd_w_in_2", "diff_lam_2", "diff_norm_g_2", "cd_w_out_2", "moe_wr_g_2", "moe_br_g_2", "moe_wr_e_2",
        "moe_br_e_2", "moe_w_gate_2", "moe_w_up_2", "moe_w_down_2"]


def kernel(**inputs):
    import numpy as _np
    import concourse.bacc as _bacc
    from concourse import mybir as _mybir
    from concourse.bass_utils import run_bass_kernel_spmd as _run

    nc = _bacc.Bacc("TRN2", target_bir_lowering=False, num_devices=1)
    arrays, d = {}, {}
    parts, parts2 = constant_parts(), constant_parts_2()
    given = {name: inputs[name] for name in _INS}
    given["consts"] = _np.concatenate(list(parts.values()), axis=1)
    given["consts2"] = _np.concatenate(list(parts2.values()), axis=1)
    given["ident"] = _np.eye(P, dtype=_np.float32)
    for name, a in given.items():
        a = _np.ascontiguousarray(a)
        arrays[f"in_{name}_dram"] = a
        d[name] = nc.dram_tensor(f"in_{name}_dram", a.shape, _mybir.dt.from_np(a.dtype), kind="ExternalInput").ap()
    d["out"] = nc.dram_tensor("out_0_dram", (1, SEQ, D), F32, kind="ExternalOutput").ap()
    build(nc, d, parts, parts2)
    r = _run(nc, [arrays], core_ids=[0])
    return r.results[0]["out_0_dram"]
```
